# Optimizing a Trainium2 kernel written in Bass

```python
import jax, jax.numpy as jnp
from jax import lax
import numpy as np
import math

D_MODEL = 1024
BATCH = 1
SEQ = 1024
DEPTH = 1

CHUNK = 64
MIX_WIDTH = D_MODEL
RET_WIDTH = MIX_WIDTH // 2
RWKV_WIDTH = MIX_WIDTH - RET_WIDTH
RET_HEADS = 4
RET_HEAD_DIM = RET_WIDTH // RET_HEADS
RWKV_HEAD_DIM = 64
RWKV_HEADS = RWKV_WIDTH // RWKV_HEAD_DIM
DECAY_LORA = 64
AAA_LORA = 64
GATE_LORA = 128
RWKV_COLS = 3 * RWKV_WIDTH + DECAY_LORA + AAA_LORA + GATE_LORA
IN_COLS = 4 * RET_WIDTH + RWKV_COLS
N_GROUPS = 4
EXPERTS_PER_GROUP = 8
N_EXPERTS = N_GROUPS * EXPERTS_PER_GROUP
TOP_K = 2
D_EXPERT = 512
MOE_BLOCK = 128
ROPE_BASE = 10000.0
NORM_EPS = 1e-6
RET_GN_EPS = 1e-5
RWKV_GN_EPS = 64e-5


def rms_norm(x, gain):
    xf = x.astype(jnp.float32)
    y = xf * lax.rsqrt(jnp.mean(xf * xf, axis=-1, keepdims=True) + NORM_EPS)
    return (y * gain.astype(jnp.float32)).astype(x.dtype)

def head_norm(y, gain, eps):
    mu = jnp.mean(y, axis=-1, keepdims=True)
    yc = y - mu
    var = jnp.mean(yc * yc, axis=-1, keepdims=True)
    return yc * lax.rsqrt(var + eps) * gain.astype(jnp.float32)

def rotary(x):
    S, d = x.shape[1], x.shape[-1]
    half = d // 2
    inv = ROPE_BASE ** (-jnp.arange(half, dtype=jnp.float32) / half)
    ang = jnp.arange(S, dtype=jnp.float32)[:, None] * inv[None, :]
    cos = jnp.cos(ang)[None, :, None, :]
    sin = jnp.sin(ang)[None, :, None, :]
    x1, x2 = x[..., :half], x[..., half:]
    return jnp.concatenate([x1 * cos - x2 * sin, x1 * sin + x2 * cos], axis=-1)

def retention(q, k, v):
    B, S, H, d = q.shape
    NC = S // CHUNK
    log_g = jnp.log(1.0 - jnp.exp2(-5.0 - jnp.arange(H, dtype=jnp.float32)))
    idx = jnp.arange(CHUNK, dtype=jnp.float32)
    intra_decay = jnp.exp(log_g[:, None, None] * jnp.abs(idx[:, None] - idx[None, :]))
    k_decay = jnp.exp(log_g[:, None] * (CHUNK - 1.0 - idx)[None, :])
    q_decay = jnp.exp(log_g[:, None] * (idx + 1.0)[None, :])
    chunk_decay = jnp.exp(log_g * CHUNK)
    qc = q.reshape(B, NC, CHUNK, H, d)
    kc = k.reshape(B, NC, CHUNK, H, d) * (d ** -0.5)
    vc = v.reshape(B, NC, CHUNK, H, d)
    scores = jnp.einsum('bnchd,bnmhd->bnhcm', qc, kc) * intra_decay[None, None]
    intra = jnp.einsum('bnhcm,bnmhe->bnche', scores, vc)
    kv = jnp.einsum('bnmhd,hm,bnmhe->bnhde', kc, k_decay, vc)

    def step(state, kv_n):
        return state * chunk_decay[None, :, None, None] + kv_n, state

    _, prev = lax.scan(step, jnp.zeros((B, H, d, d), jnp.float32), jnp.moveaxis(kv, 1, 0))
    prev = jnp.moveaxis(prev, 0, 1)
    cross = jnp.einsum('bnchd,hc,bnhde->bnche', qc, q_decay, prev)
    return (intra + cross).reshape(B, S, H, d)

def token_shift_lerp(feat, mu):
    prev = jnp.concatenate([jnp.zeros_like(feat[:, :1]), feat[:, :-1]], axis=1)
    return feat + (prev - feat) * mu

def rwkv7_time_mix(feats, mu, w0, w_up, a0, a_up, g_up, k_k, k_a, r_k, gn_gain):
    B, S, _ = feats.shape
    H, N, W = RWKV_HEADS, RWKV_HEAD_DIM, RWKV_WIDTH
    f = token_shift_lerp(feats.astype(jnp.float32), mu.astype(jnp.float32))
    r = f[..., 0:W]
    k = f[..., W:2 * W]
    v = f[..., 2 * W:3 * W]
    o = 3 * W
    w_lo = f[..., o:o + DECAY_LORA]
    a_lo = f[..., o + DECAY_LORA:o + DECAY_LORA + AAA_LORA]
    g_lo = f[..., o + DECAY_LORA + AAA_LORA:]
    w = -jax.nn.softplus(-(w0 + jnp.tanh(w_lo) @ w_up)) - 0.5
    decay = jnp.exp(-jnp.exp(w))
    a = jax.nn.sigmoid(a0 + a_lo @ a_up)
    g = jax.nn.sigmoid(g_lo) @ g_up
    kk = (k * k_k).reshape(B, S, H, N)
    kk = kk / jnp.maximum(jnp.sqrt(jnp.sum(kk * kk, axis=-1, keepdims=True)), 1e-12)
    k = k * (1.0 + (a - 1.0) * k_a)
    rh = r.reshape(B, S, H, N)
    kh = k.reshape(B, S, H, N)
    vh = v.reshape(B, S, H, N)
    ah = a.reshape(B, S, H, N)
    dh = decay.reshape(B, S, H, N)
    a_vec = -kk
    b_vec = kk * ah

    def step(state, inp):
        r_t, k_t, v_t, w_t, a_t, b_t = inp
        sa = jnp.einsum('bhvk,bhk->bhv', state, a_t)
        state = state * w_t[:, :, None, :] + sa[..., None] * b_t[:, :, None, :] + v_t[..., None] * k_t[:, :, None, :]
        return state, jnp.einsum('bhvk,bhk->bhv', state, r_t)

    xs = tuple(jnp.moveaxis(t, 1, 0) for t in (rh, kh, vh, dh, a_vec, b_vec))
    _, y = lax.scan(step, jnp.zeros((B, H, N, N), jnp.float32), xs)
    y = jnp.moveaxis(y, 0, 1)
    y = head_norm(y, gn_gain.reshape(H, N), RWKV_GN_EPS)
    bonus = jnp.sum(rh * kh * r_k[None, None].astype(jnp.float32), axis=-1, keepdims=True) * vh
    return (y + bonus).reshape(B, S, W) * g

def hier_moe(xn, w_route_group, b_route_group, w_route_expert, b_route_expert, w_gate, w_up, w_down):
    B, S, D = xn.shape
    T = B * S
    xt = xn.reshape(T, D)
    group_logits = (xt @ w_route_group).astype(jnp.float32) + b_route_group.astype(jnp.float32)
    group_prob = jax.nn.softmax(group_logits, axis=-1)
    g_idx = jnp.argmax(group_logits, axis=-1).astype(jnp.int32)
    g_p = jnp.take_along_axis(group_prob, g_idx[:, None], axis=1)
    exp_logits = ((xt @ w_route_expert).astype(jnp.float32) + b_route_expert.astype(jnp.float32)).reshape(T, N_GROUPS, EXPERTS_PER_GROUP)
    in_group = jnp.take_along_axis(exp_logits, g_idx[:, None, None], axis=1)[:, 0]
    top_v, top_i = lax.top_k(in_group, TOP_K)
    top_w = jax.nn.softmax(top_v, axis=-1) * g_p
    expert_id = (g_idx[:, None] * EXPERTS_PER_GROUP + top_i.astype(jnp.int32)).reshape(-1)
    token_id = jnp.repeat(jnp.arange(T, dtype=jnp.int32), TOP_K)
    weight = top_w.reshape(-1)
    A = T * TOP_K
    order = jnp.argsort(expert_id)
    se, st, sw = expert_id[order], token_id[order], weight[order]
    counts = jax.ops.segment_sum(jnp.ones((A,), jnp.int32), expert_id, num_segments=N_EXPERTS)
    starts = jnp.cumsum(counts) - counts
    padded = (counts + MOE_BLOCK - 1) // MOE_BLOCK * MOE_BLOCK
    pad_ends = jnp.cumsum(padded)
    pad_starts = pad_ends - padded
    dest = pad_starts[se] + jnp.arange(A, dtype=jnp.int32) - starts[se]
    P = ((A + MOE_BLOCK - 1) // MOE_BLOCK + N_EXPERTS) * MOE_BLOCK
    NB = P // MOE_BLOCK
    slot_tok = jnp.full((P,), T, jnp.int32).at[dest].set(st)
    slot_w = jnp.zeros((P,), jnp.float32).at[dest].set(sw)
    block_expert = jnp.clip(jnp.searchsorted(pad_ends, jnp.arange(NB, dtype=jnp.int32) * MOE_BLOCK, side='right'), 0, N_EXPERTS - 1)
    x_pad = jnp.concatenate([xt, jnp.zeros((1, D), xt.dtype)], axis=0)
    xb = x_pad[slot_tok].reshape(NB, MOE_BLOCK, D)

    def expert_block(args):
        xblk, e = args
        hdn = jax.nn.silu(xblk @ w_gate[e]) * (xblk @ w_up[e])
        return hdn @ w_down[e]

    yb = lax.map(expert_block, (xb, block_expert)).reshape(P, D)
    y = jax.ops.segment_sum(yb.astype(jnp.float32) * slot_w[:, None], slot_tok, num_segments=T + 1)[:T]
    return y.reshape(B, S, D).astype(xn.dtype)

def first_inputs(seed: int = 0) -> dict:
    key = jax.random.key(seed)
    ks = jax.random.split(key, 24)
    L, D = DEPTH, D_MODEL
    nrm = lambda k, shape, s: jax.random.normal(k, shape, jnp.float32) * s
    return {
        'x': nrm(ks[0], (BATCH, SEQ, D), 1.0),
        'norm1_gain': 1.0 + nrm(ks[1], (L, D), 0.02),
        'w_in': nrm(ks[2], (L, D, IN_COLS), D ** -0.5),
        'ret_gn_gain': 1.0 + nrm(ks[3], (L, RET_WIDTH), 0.02),
        'rwkv_mu': jax.random.uniform(ks[4], (L, RWKV_COLS), jnp.float32),
        'rwkv_w0': nrm(ks[5], (L, RWKV_WIDTH), 0.5) + 0.5,
        'rwkv_w_up': nrm(ks[6], (L, DECAY_LORA, RWKV_WIDTH), 0.5 * DECAY_LORA ** -0.5),
        'rwkv_a0': nrm(ks[7], (L, RWKV_WIDTH), 0.5),
        'rwkv_a_up': nrm(ks[8], (L, AAA_LORA, RWKV_WIDTH), 0.5 * AAA_LORA ** -0.5),
        'rwkv_g_up': nrm(ks[9], (L, GATE_LORA, RWKV_WIDTH), GATE_LORA ** -0.5),
        'rwkv_k_k': 0.85 + nrm(ks[10], (L, RWKV_WIDTH), 0.05),
        'rwkv_k_a': 1.0 + nrm(ks[11], (L, RWKV_WIDTH), 0.05),
        'rwkv_r_k': nrm(ks[12], (L, RWKV_HEADS, RWKV_HEAD_DIM), 0.1),
        'rwkv_gn_gain': 1.0 + nrm(ks[13], (L, RWKV_WIDTH), 0.02),
        'w_out': nrm(ks[14], (L, MIX_WIDTH, D), MIX_WIDTH ** -0.5),
        'norm2_gain': 1.0 + nrm(ks[15], (L, D), 0.02),
        'w_route_group': nrm(ks[16], (L, D, N_GROUPS), D ** -0.5),
        'b_route_group': nrm(ks[17], (L, N_GROUPS), 0.01),
        'w_route_expert': nrm(ks[18], (L, D, N_EXPERTS), D ** -0.5),
        'b_route_expert': nrm(ks[19], (L, N_EXPERTS), 0.01),
        'w_gate': nrm(ks[20], (L, N_EXPERTS, D, D_EXPERT), D ** -0.5),
        'w_up': nrm(ks[21], (L, N_EXPERTS, D, D_EXPERT), D ** -0.5),
        'w_down': nrm(ks[22], (L, N_EXPERTS, D_EXPERT, D), D_EXPERT ** -0.5),
        'final_norm_gain': 1.0 + nrm(ks[23], (D,), 0.02),
    }

def first_block(x, norm1_gain, w_in, ret_gn_gain, rwkv_mu, rwkv_w0, rwkv_w_up, rwkv_a0, rwkv_a_up, rwkv_g_up, rwkv_k_k, rwkv_k_a, rwkv_r_k, rwkv_gn_gain, w_out, norm2_gain, w_route_group, b_route_group, w_route_expert, b_route_expert, w_gate, w_up, w_down, final_norm_gain):
    B, S, _ = x.shape
    h = x
    for l in range(DEPTH):
        xn = rms_norm(h, norm1_gain[l])
        proj = xn @ w_in[l]
        rp = proj[..., :4 * RET_WIDTH].astype(jnp.float32)
        q = rotary(rp[..., 0:RET_WIDTH].reshape(B, S, RET_HEADS, RET_HEAD_DIM))
        k = rotary(rp[..., RET_WIDTH:2 * RET_WIDTH].reshape(B, S, RET_HEADS, RET_HEAD_DIM))
        v = rp[..., 2 * RET_WIDTH:3 * RET_WIDTH].reshape(B, S, RET_HEADS, RET_HEAD_DIM)
        ret = head_norm(retention(q, k, v), ret_gn_gain[l].reshape(RET_HEADS, RET_HEAD_DIM), RET_GN_EPS)
        ret = jax.nn.silu(rp[..., 3 * RET_WIDTH:]) * ret.reshape(B, S, RET_WIDTH)
        rw = rwkv7_time_mix(proj[..., 4 * RET_WIDTH:], rwkv_mu[l], rwkv_w0[l], rwkv_w_up[l], rwkv_a0[l], rwkv_a_up[l], rwkv_g_up[l], rwkv_k_k[l], rwkv_k_a[l], rwkv_r_k[l], rwkv_gn_gain[l])
        mixed = jnp.concatenate([ret, rw], axis=-1).astype(x.dtype)
        h = h + mixed @ w_out[l]
        h = h + hier_moe(rms_norm(h, norm2_gain[l]), w_route_group[l], b_route_group[l], w_route_expert[l], b_route_expert[l], w_gate[l], w_up[l], w_down[l])
    return rms_norm(h, final_norm_gain)


MLA_HEADS = 8
MLA_Q_LORA = 256
MLA_KV_LORA = 128
MLA_NOPE_DIM = 64
MLA_ROPE_DIM = 32
MLA_V_DIM = 64
ROPE_THETA = 10000.0
Q_BLOCK = 128
SC_DIM = 256
SC_WIDTH = 3
SSD_HEADS = 4
SSD_HEAD_DIM = 64
SSD_GROUPS = 2
SSD_STATE = 128
SSD_CONV_WIDTH = 4
SSD_CHUNK = 128
FFN_DIM = 2816
FFN_CONV_WIDTH = 3

MLA_QK_DIM = MLA_NOPE_DIM + MLA_ROPE_DIM
MLA_OUT = MLA_HEADS * MLA_V_DIM
SSD_DIM = SSD_HEADS * SSD_HEAD_DIM
SSD_CONV_DIM = SSD_DIM + 2 * SSD_GROUPS * SSD_STATE
SSD_IN = SSD_DIM + SSD_CONV_DIM + SSD_HEADS
IN_WIDTHS = (MLA_Q_LORA, MLA_KV_LORA, MLA_ROPE_DIM, SC_DIM, SC_DIM, SC_DIM, SSD_IN)
IN_SPLITS = tuple(int(v) for v in np.cumsum(IN_WIDTHS)[:-1])
D_IN = sum(IN_WIDTHS)
D_MIX = MLA_OUT + SC_DIM + SSD_DIM


def rms_norm_2(x, w):
    xf = x.astype(jnp.float32)
    y = xf * lax.rsqrt(jnp.mean(xf * xf, axis=-1, keepdims=True) + NORM_EPS)
    return (y * w.astype(jnp.float32)).astype(x.dtype)

def causal_dwconv(u, w):
    width = w.shape[0]
    s = u.shape[1]
    up = jnp.pad(u, ((0, 0), (width - 1, 0), (0, 0)))
    out = up[:, 0:s] * w[0]
    for i in range(1, width):
        out = out + up[:, i:i + s] * w[i]
    return out

def rope(x, cos, sin):
    x1, x2 = jnp.split(x, 2, axis=-1)
    return jnp.concatenate([x1 * cos - x2 * sin, x2 * cos + x1 * sin], axis=-1).astype(x.dtype)

def mla_mixer(c_q, c_kv, k_rope, cos, sin, q_norm, w_q_up, kv_norm, w_kv_up):
    b, s, _ = c_q.shape
    q = (rms_norm_2(c_q, q_norm) @ w_q_up).reshape(b, s, MLA_HEADS, MLA_QK_DIM)
    q_nope = q[..., :MLA_NOPE_DIM]
    q_rope = rope(q[..., MLA_NOPE_DIM:], cos[:, :, None, :], sin[:, :, None, :])
    kv = (rms_norm_2(c_kv, kv_norm) @ w_kv_up).reshape(b, s, MLA_HEADS, MLA_NOPE_DIM + MLA_V_DIM)
    k_nope = kv[..., :MLA_NOPE_DIM]
    v = kv[..., MLA_NOPE_DIM:]
    k_rope = rope(k_rope, cos, sin)
    scale = MLA_QK_DIM ** -0.5
    key_idx = jnp.arange(s)

    def block(i):
        start = i * Q_BLOCK
        qn = lax.dynamic_slice_in_dim(q_nope, start, Q_BLOCK, axis=1)
        qr = lax.dynamic_slice_in_dim(q_rope, start, Q_BLOCK, axis=1)
        sc = jnp.einsum("bqhd,bkhd->bhqk", qn, k_nope) + jnp.einsum("bqhd,bkd->bhqk", qr, k_rope)
        sc = sc.astype(jnp.float32) * scale
        causal = (start + jnp.arange(Q_BLOCK))[:, None] >= key_idx[None, :]
        p = jax.nn.softmax(jnp.where(causal, sc, -jnp.inf), axis=-1)
        return jnp.einsum("bhqk,bkhd->bqhd", p.astype(v.dtype), v)

    out = lax.map(block, jnp.arange(s // Q_BLOCK))
    return out.transpose(1, 0, 2, 3, 4).reshape(b, s, MLA_OUT)

def short_conv_mixer(gate_b, gate_c, h, conv_w):
    return gate_b * causal_dwconv(gate_c * h, conv_w)

def ssd_scan(xdt, a_dt, bh, ch):
    b, s, h, p = xdt.shape
    n = bh.shape[-1]
    L = SSD_CHUNK
    c = s // L
    xdt = xdt.reshape(b, c, L, h, p)
    bh = bh.reshape(b, c, L, h, n)
    ch = ch.reshape(b, c, L, h, n)
    a_cs = jnp.cumsum(a_dt.reshape(b, c, L, h).transpose(0, 3, 1, 2), axis=-1)
    diff = a_cs[..., :, None] - a_cs[..., None, :]
    tri = jnp.tril(jnp.ones((L, L), dtype=bool))
    decay_in = jnp.exp(jnp.where(tri, diff, -jnp.inf))
    scores = jnp.einsum("bclhn,bcshn->bhcls", ch, bh) * decay_in
    y_diag = jnp.einsum("bhcls,bcshp->bclhp", scores, xdt)
    decay_to_end = jnp.exp(a_cs[..., -1:] - a_cs).transpose(0, 2, 3, 1)
    chunk_states = jnp.einsum("bclhn,bclhp->bchpn", bh * decay_to_end[..., None], xdt)
    chunk_decay = jnp.exp(a_cs[..., -1]).transpose(2, 0, 1)

    def step(state, inp):
        st, dec = inp
        return state * dec[..., None, None] + st, state

    init = jnp.zeros((b, h, p, n), chunk_states.dtype)
    _, prev = lax.scan(step, init, (chunk_states.transpose(1, 0, 2, 3, 4), chunk_decay))
    prev = prev.transpose(1, 0, 2, 3, 4)
    decay_from_start = jnp.exp(a_cs).transpose(0, 2, 3, 1)
    y_off = jnp.einsum("bclhn,bchpn->bclhp", ch, prev) * decay_from_start[..., None]
    return (y_diag + y_off).reshape(b, s, h, p)

def ssd_mixer(zxbcdt, conv_w, conv_b, dt_bias, a_log, d_skip, norm_w):
    b, s, _ = zxbcdt.shape
    z = zxbcdt[..., :SSD_DIM]
    xbc = zxbcdt[..., SSD_DIM:SSD_DIM + SSD_CONV_DIM]
    dt = zxbcdt[..., SSD_DIM + SSD_CONV_DIM:]
    xbc = jax.nn.silu(causal_dwconv(xbc, conv_w) + conv_b)
    xs = xbc[..., :SSD_DIM].reshape(b, s, SSD_HEADS, SSD_HEAD_DIM)
    heads_per_group = SSD_HEADS // SSD_GROUPS
    gn = SSD_GROUPS * SSD_STATE
    bm = jnp.repeat(xbc[..., SSD_DIM:SSD_DIM + gn].reshape(b, s, SSD_GROUPS, SSD_STATE), heads_per_group, axis=2)
    cm = jnp.repeat(xbc[..., SSD_DIM + gn:].reshape(b, s, SSD_GROUPS, SSD_STATE), heads_per_group, axis=2)
    dt = jax.nn.softplus(dt.astype(jnp.float32) + dt_bias.astype(jnp.float32))
    a = -jnp.exp(a_log.astype(jnp.float32))
    y = ssd_scan(xs * dt[..., None], dt * a, bm, cm)
    y = y + xs * d_skip[:, None]
    y = y.reshape(b, s, SSD_DIM).astype(zxbcdt.dtype)
    return rms_norm_2(y * jax.nn.silu(z), norm_w)

def second_inputs(seed: int = 0) -> dict:
    key = jax.random.key(seed)
    ks = jax.random.split(key, 24)
    L = DEPTH

    def normal(k, shape, scale):
        return scale * jax.random.normal(k, shape, jnp.float32)

    def gain(k, n):
        return 1.0 + normal(k, (L, n), 0.02)

    dt0 = jnp.exp(jax.random.uniform(ks[15], (L, SSD_HEADS), jnp.float32, math.log(1e-3), math.log(1e-1)))
    return {
        "x": normal(ks[0], (BATCH, SEQ, D_MODEL), 1.0),
        "positions": jnp.broadcast_to(jnp.arange(SEQ, dtype=jnp.int32), (BATCH, SEQ)),
        "norm_mix_pre": gain(ks[1], D_MODEL),
        "norm_mix_post": gain(ks[2], D_MODEL),
        "norm_ffn_pre": gain(ks[3], D_MODEL),
        "norm_ffn_post": gain(ks[4], D_MODEL),
        "w_in": normal(ks[5], (L, D_MODEL, D_IN), D_MODEL ** -0.5),
        "mla_q_norm": gain(ks[6], MLA_Q_LORA),
        "mla_w_q_up": normal(ks[7], (L, MLA_Q_LORA, MLA_HEADS * MLA_QK_DIM), MLA_Q_LORA ** -0.5),
        "mla_kv_norm": gain(ks[8], MLA_KV_LORA),
        "mla_w_kv_up": normal(ks[9], (L, MLA_KV_LORA, MLA_HEADS * (MLA_NOPE_DIM + MLA_V_DIM)), MLA_KV_LORA ** -0.5),
        "sc_conv_w": normal(ks[10], (L, SC_WIDTH, SC_DIM), SC_WIDTH ** -0.5),
        "ssd_conv_w": normal(ks[11], (L, SSD_CONV_WIDTH, SSD_CONV_DIM), SSD_CONV_WIDTH ** -0.5),
        "ssd_conv_b": normal(ks[12], (L, SSD_CONV_DIM), 0.02),
        "ssd_dt_bias": dt0 + jnp.log(-jnp.expm1(-dt0)),
        "ssd_a_log": jnp.log(jax.random.uniform(ks[13], (L, SSD_HEADS), jnp.float32, 1.0, 16.0)),
        "ssd_d": 1.0 + normal(ks[14], (L, SSD_HEADS), 0.1),
        "ssd_norm": gain(ks[16], SSD_DIM),
        "w_out": normal(ks[17], (L, D_MIX, D_MODEL), D_MIX ** -0.5),
        "ffn_w_up": normal(ks[18], (L, D_MODEL, 2 * FFN_DIM), D_MODEL ** -0.5),
        "ffn_conv_w": normal(ks[19], (L, FFN_CONV_WIDTH, 2 * FFN_DIM), FFN_CONV_WIDTH ** -0.5),
        "ffn_conv_b": normal(ks[20], (L, 2 * FFN_DIM), 0.02),
        "ffn_w_down": normal(ks[21], (L, FFN_DIM, D_MODEL), FFN_DIM ** -0.5),
    }

def second_block(x, positions, norm_mix_pre, norm_mix_post, norm_ffn_pre, norm_ffn_post, w_in,
              mla_q_norm, mla_w_q_up, mla_kv_norm, mla_w_kv_up, sc_conv_w, ssd_conv_w, ssd_conv_b,
              ssd_dt_bias, ssd_a_log, ssd_d, ssd_norm, w_out, ffn_w_up, ffn_conv_w, ffn_conv_b,
              ffn_w_down):
    inv_freq = 1.0 / (ROPE_THETA ** (jnp.arange(0, MLA_ROPE_DIM, 2, dtype=jnp.float32) / MLA_ROPE_DIM))
    ang = positions.astype(jnp.float32)[..., None] * inv_freq
    cos = jnp.cos(ang).astype(x.dtype)
    sin = jnp.sin(ang).astype(x.dtype)
    for l in range(DEPTH):
        h = rms_norm_2(x, norm_mix_pre[l])
        c_q, c_kv, k_rope, sc_b, sc_c, sc_h, ssd_in = jnp.split(h @ w_in[l], IN_SPLITS, axis=-1)
        y_att = mla_mixer(c_q, c_kv, k_rope, cos, sin, mla_q_norm[l], mla_w_q_up[l], mla_kv_norm[l], mla_w_kv_up[l])
        y_conv = short_conv_mixer(sc_b, sc_c, sc_h, sc_conv_w[l])
        y_ssd = ssd_mixer(ssd_in, ssd_conv_w[l], ssd_conv_b[l], ssd_dt_bias[l], ssd_a_log[l], ssd_d[l], ssd_norm[l])
        mixed = jnp.concatenate([y_att, y_conv, y_ssd], axis=-1) @ w_out[l]
        x = x + rms_norm_2(mixed, norm_mix_post[l])
        h = rms_norm_2(x, norm_ffn_pre[l])
        u = causal_dwconv(h @ ffn_w_up[l], ffn_conv_w[l]) + ffn_conv_b[l]
        gate, up = jnp.split(u, 2, axis=-1)
        x = x + rms_norm_2((jax.nn.silu(gate) * up) @ ffn_w_down[l], norm_ffn_post[l])
    return x


def setup_inputs(seed=0):
    out = dict(first_inputs(seed))
    for name, value in second_inputs(seed + 1).items():
        if name != "x":
            out[name + "_2"] = value
    return out


def reference(
    x, norm1_gain, w_in, ret_gn_gain, rwkv_mu, rwkv_w0, rwkv_w_up, rwkv_a0, rwkv_a_up,
    rwkv_g_up, rwkv_k_k, rwkv_k_a, rwkv_r_k, rwkv_gn_gain, w_out, norm2_gain, w_route_group,
    b_route_group, w_route_expert, b_route_expert, w_gate, w_up, w_down, final_norm_gain,
    positions_2, norm_mix_pre_2, norm_mix_post_2, norm_ffn_pre_2, norm_ffn_post_2, w_in_2,
    mla_q_norm_2, mla_w_q_up_2, mla_kv_norm_2, mla_w_kv_up_2, sc_conv_w_2, ssd_conv_w_2,
    ssd_conv_b_2, ssd_dt_bias_2, ssd_a_log_2, ssd_d_2, ssd_norm_2, w_out_2, ffn_w_up_2,
    ffn_conv_w_2, ffn_conv_b_2, ffn_w_down_2,
):
    x = first_block(
        x, norm1_gain, w_in, ret_gn_gain, rwkv_mu, rwkv_w0, rwkv_w_up, rwkv_a0, rwkv_a_up,
        rwkv_g_up, rwkv_k_k, rwkv_k_a, rwkv_r_k, rwkv_gn_gain, w_out, norm2_gain, w_route_group,
        b_route_group, w_route_expert, b_route_expert, w_gate, w_up, w_down, final_norm_gain,
    )
    return second_block(
        x, positions_2, norm_mix_pre_2, norm_mix_post_2, norm_ffn_pre_2, norm_ffn_post_2,
        w_in_2, mla_q_norm_2, mla_w_q_up_2, mla_kv_norm_2, mla_w_kv_up_2, sc_conv_w_2,
        ssd_conv_w_2, ssd_conv_b_2, ssd_dt_bias_2, ssd_a_log_2, ssd_d_2, ssd_norm_2, w_out_2,
        ffn_w_up_2, ffn_conv_w_2, ffn_conv_b_2, ffn_w_down_2,
    )


_drawn_inputs = setup_inputs


def setup_inputs(seed=0):
    import zlib

    import numpy as np

    out = dict(_drawn_inputs(seed))
    spreads = {}
    factors = {'rwkv_k_k': 2.984,
     'b_route_group': 3.036,
     'norm_mix_post_2': 3.482,
     'norm_ffn_pre_2': 3.415,
     'norm_ffn_post_2': 17.771,
     'mla_q_norm_2': 8.0,
     'mla_kv_norm_2': 8.0,
     'ssd_conv_b_2': 3.513,
     'ssd_d_2': 49.375,
     'ssd_norm_2': 23.698,
     'ffn_conv_b_2': 3.478}
    for name, (base, spread) in spreads.items():
        noise = np.random.default_rng([zlib.crc32(name.encode()), seed]).standard_normal(out[name].shape)
        drawn = base * np.exp(spread * noise) if base else spread * noise
        out[name] = __import__('jax').numpy.asarray(drawn.astype(out[name].dtype))
    for name, factor in factors.items():
        out[name] = (out[name] * factor).astype(out[name].dtype)
    return out
```

```python
from contextlib import ExitStack

import concourse.bass as bass
import numpy as np
from concourse import mybir

F32 = mybir.dt.float32
I32 = mybir.dt.int32
U32 = mybir.dt.uint32
ALU = mybir.AluOpType
ACT = mybir.ActivationFunctionType
AX_X = mybir.AxisListType.X
ds = bass.ds

P = 128
D = 1024
S = 1024
KT = D // P
TT = S // P
BANK = 512
EPS = 1e-6

RET_W = 512
RET_HEADS = 4
RET_D = RET_W // RET_HEADS
RET_CHUNK = 64
RW_W = 512
RW_HEADS = 8
RW_N = RW_W // RW_HEADS
LORA = 64
RW_COLS = 3 * RW_W + 2 * LORA + 128
IN_COLS = 4 * RET_W + RW_COLS
RET_GN_EPS = 1e-5
RW_GN_EPS = 64e-5
DECAY = -float(np.exp(-0.5))
SOLVE_STEPS = (2, 4, 8, 16, 32, 64)


class Stage:

    def __init__(self, nc, name):
        self.nc, self.name, self.sems, self.ctx = nc, name, [], ExitStack()

    def __enter__(self):
        self.block_ctx = self.nc.Block()
        self.block = None
        return self

    def open(self):
        self.block = self.block_ctx.__enter__()
        return self.block

    def sem(self, name):
        s = self.nc.alloc_semaphore(name=f"{self.name}_{name}")
        self.sems.append(s)
        return s

    def sb(self, name, shape, dt=F32):
        return self.ctx.enter_context(self.nc.sbuf_tensor(f"{self.name}_{name}", shape, dt))

    def __exit__(self, *error):
        if error[0] is None:
            self.block_ctx.__exit__(None, None, None)
            self.nc.clear_and_free_semaphores(self.sems)
            self.nc.all_engine_barrier()
        self.ctx.close()


def rows(dram, cols):
    return dram.rearrange("(a n) -> a n", a=1)[:, 0:cols].partition_broadcast(P)


def flat(ap):
    return ap.rearrange("p a b -> p (a b)")


def three(ap, a):
    return ap.rearrange("p (a b) -> p a b", a=a)


def per_row(ap, n):
    return ap.unsqueeze(2).to_broadcast([ap.shape[0], ap.shape[1], n])


def per_block(ap, n):
    return ap.unsqueeze(1).to_broadcast([ap.shape[0], n, ap.shape[1]])


def load_stage(nc, x, ident, x_dram, ident_dram, zero_row_of):
    with Stage(nc, "load") as st:
        zeros = st.sb("zeros", [1, IN_COLS])
        loaded, zeroed, cleared = st.sem("loaded"), st.sem("zeroed"), st.sem("cleared")
        block = st.open()

        @block.sync
        def _(sp):
            sp.dma_start(x[:], x_dram.rearrange("(t p) d -> p t d", p=P)).then_inc(loaded, 16)
            sp.dma_start(ident[:], ident_dram).then_inc(loaded, 16)
            sp.wait_ge(zeroed, 1)
            sp.dma_start(zero_row_of, zeros[0:1, 0:zero_row_of.shape[1]]).then_inc(cleared, 16)
            sp.wait_ge(cleared, 16)
            sp.wait_ge(loaded, 32)

        @block.vector
        def _(v):
            v.memset(zeros[:], 0.0).then_inc(zeroed, 1)


def norm_stage(nc, name, bank, ident, x, gain_dram, out, rows_dram=None):
    with Stage(nc, name) as st:
        gain = st.sb("gain", [P, KT])
        junk = [st.sb(f"junk{u}", [P, D]) for u in range(2)]
        square = [st.sb(f"square{u}", [P, 1]) for u in range(2)]
        mean = [st.sb(f"mean{u}", [P, 1]) for u in range(2)]
        rstd = [st.sb(f"rstd{u}", [P, 1]) for u in range(2)]
        root = [st.sb(f"root{u}", [P, 1]) for u in range(2)]
        xs = [st.sb(f"xs{u}", [P, D]) for u in range(2)]
        gain_loaded = st.sem("gain_loaded")
        squared = [st.sem(f"squared{u}") for u in range(2)]
        mean_ready = [st.sem(f"mean_ready{u}") for u in range(2)]
        root_ready = [st.sem(f"root_ready{u}") for u in range(2)]
        rstd_ready = [st.sem(f"rstd_ready{u}") for u in range(2)]
        xs_ready = [st.sem(f"xs_ready{u}") for u in range(2)]
        turned = [st.sem(f"turned{u}") for u in range(2)]
        low_out = [st.sem(f"low_out{u}") for u in range(2)]
        high_out = [st.sem(f"high_out{u}") for u in range(2)]
        stored = [st.sem(f"stored{u}") for u in range(2)]
        block = st.open()

        @block.sync
        def _(sp):
            sp.dma_start(gain[:], gain_dram.rearrange("(k p) -> p k", p=P),
                         allow_slow_non_contiguous=True).then_inc(gain_loaded, 16)
            if rows_dram is not None:
                with sp.Fori(0, TT // 2) as j:
                    for u in range(2):
                        sp.wait_ge(xs_ready[u], j + 1)
                        sp.dma_start(rows_dram[ds((j * 2 + u) * P, P), :], xs[u][:]).then_inc(stored[u], 16)
                for u in range(2):
                    sp.wait_ge(stored[u], 16 * (TT // 2))

        @block.scalar
        def _(act):
            act.wait_ge(gain_loaded, 16)
            with act.Fori(0, TT // 2) as j:
                for u in range(2):
                    t = j * 2 + u
                    act.wait_ge(mean_ready[u], j)
                    act.activation(junk[u][:], x[:, ds(t, 1), :].rearrange("p a d -> p (a d)"), ACT.Square,
                                   accum_out=square[u][:]).then_inc(squared[u], 1)
                for u in range(2):
                    act.wait_ge(mean_ready[u], j + 1)
                    act.wait_ge(xs_ready[u], j)
                    act.activation(root[u][:], mean[u][:], ACT.Sqrt).then_inc(root_ready[u], 1)
                for u in range(2):
                    t = j * 2 + u
                    act.wait_ge(turned[u], j + 1)
                    for k in range(4, 8):
                        last = act.activation(out[:, k, ds(t * P, P)], bank[2 * u + 1][:, (k - 4) * P:(k - 3) * P],
                                              ACT.Copy, scale=gain[:, k:k + 1])
                    last.then_inc(high_out[u], 1)

        @block.vector
        def _(v):
            v.wait_ge(gain_loaded, 16)
            with v.Fori(0, TT // 2) as j:
                for u in range(2):
                    t = j * 2 + u
                    v.wait_ge(squared[u], j + 1)
                    v.wait_ge(root_ready[u], j)
                    v.tensor_scalar(mean[u][:], square[u][:], 1.0 / D, EPS, ALU.mult, ALU.add).then_inc(mean_ready[u], 1)
                    v.wait_ge(root_ready[u], j + 1)
                    v.reciprocal(rstd[u][:], root[u][:]).then_inc(rstd_ready[u], 1)
                    v.wait_ge(rstd_ready[u], j + 1)
                    v.wait_ge(turned[u], j)
                    if rows_dram is not None:
                        v.wait_ge(stored[u], j * 16)
                    v.tensor_scalar(xs[u][:], x[:, ds(t, 1), :].rearrange("p a d -> p (a d)"), rstd[u][:, 0:1], None,
                                    ALU.mult).then_inc(xs_ready[u], 1)
                for u in range(2):
                    t = j * 2 + u
                    v.wait_ge(turned[u], j + 1)
                    v.tensor_tensor(out[:, 0:4, ds(t * P, P)], three(bank[2 * u][:], 4), per_row(gain[:, 0:4], P),
                                    ALU.mult).then_inc(low_out[u], 1)

        @block.tensor
        def _(pe):
            with pe.Fori(0, TT // 2) as j:
                for u in range(2):
                    pe.wait_ge(xs_ready[u], j + 1)
                    pe.wait_ge(low_out[u], j)
                    pe.wait_ge(high_out[u], j)
                    for k in range(KT):
                        last = pe.transpose(bank[2 * u + k // 4][:, (k % 4) * P:(k % 4 + 1) * P],
                                            xs[u][:, k * P:(k + 1) * P], ident[:])
                    last.then_inc(turned[u], 1)


def project_stage(nc, name, bank, feat, w_dram, width, blocks, out_dram, idle_rows):
    half = blocks // 2
    with Stage(nc, name) as st:
        w = [st.sb(f"w{u}", [P, KT, width]) for u in range(2)]
        out = [st.sb(f"out{u}", [P, TT, width]) for u in range(2)]
        w_loaded = [st.sem(f"w_loaded{u}") for u in range(2)]
        stored = [st.sem(f"stored{u}") for u in range(2)]
        product = st.sem("product")
        even_out, odd_out = st.sem("even_out"), st.sem("odd_out")
        zeros = st.sb("zeros", [P, D])
        zeroed, cleared = st.sem("zeroed"), st.sem("cleared")
        block = st.open()

        @block.gpsimd
        def _(pool):
            pool.memset(zeros[:], 0.0).then_inc(zeroed, 1)
            pool.wait_ge(zeroed, 1)
            pool.dma_start(idle_rows.rearrange("(b p) d -> p b d", p=P),
                           per_block(zeros[:], idle_rows.shape[0] // P)).then_inc(cleared, 16)

        @block.sync
        def _(sp):
            with sp.Fori(0, half) as j:
                for u in range(2):
                    sp.wait_ge(odd_out, j * 8 + u * 4)
                    sp.dma_start(w[u][:], w_dram[:, ds((j * 2 + u) * width, width)]
                                 .rearrange("(k p) n -> p k n", p=P)).then_inc(w_loaded[u], 16)
            sp.wait_ge(cleared, 16)

        @block.tensor
        def _(pe):
            with pe.Fori(0, half) as j:
                for u in range(2):
                    b = j * 2 + u
                    pe.wait_ge(w_loaded[u], j * 16 + 16)
                    for t in range(TT):
                        if t % 2 == 0:
                            pe.wait_ge(even_out, b * 4 + t // 2 + 1)
                        else:
                            pe.wait_ge(odd_out, b * 4 + t // 2 + 1)
                        for k in range(KT):
                            last = pe.matmul(bank[t][:, 0:width], feat[:, k, t * P:(t + 1) * P], w[u][:, k, :],
                                             start=(k == 0), stop=(k == KT - 1))
                        last.then_inc(product, 1)

        @block.scalar
        def _(act):
            act.sem_inc(even_out, 4)
            with act.Fori(0, half) as j:
                for u in range(2):
                    b = j * 2 + u
                    act.wait_ge(stored[u], j * 16)
                    for t in range(0, TT, 2):
                        act.wait_ge(product, b * TT + t + 1)
                        act.activation(out[u][:, t, :], bank[t][:, 0:width], ACT.Copy).then_inc(even_out, 1)
                    act.wait_ge(even_out, b * 4 + 8)
                    act.wait_ge(odd_out, b * 4 + 8)
                    act.dma_start(out_dram[:, ds(b * width, width)].rearrange("(t p) n -> p t n", p=P),
                                  out[u][:]).then_inc(stored[u], 16)
            for u in range(2):
                act.wait_ge(stored[u], 16 * half)

        @block.vector
        def _(v):
            v.sem_inc(odd_out, 4)
            with v.Fori(0, half) as j:
                for u in range(2):
                    b = j * 2 + u
                    v.wait_ge(stored[u], j * 16)
                    for t in range(1, TT, 2):
                        v.wait_ge(product, b * TT + t + 1)
                        v.tensor_copy(out[u][:, t, :], bank[t][:, 0:width]).then_inc(odd_out, 1)


def head_norm(v, link, y, scratch, stats, heads, width, eps, gain, out, spread_ready, root_ready, count):
    total, mean, var, spread, root, rstd = (stats[:, i, 0:heads] for i in range(6))
    link(v.tensor_reduce(total, three(y, heads), AX_X, ALU.add))
    link(v.tensor_scalar(mean, total, 1.0 / width, None, ALU.mult))
    link(v.tensor_tensor(three(out, heads), three(y, heads), per_row(mean, width), ALU.subtract))
    link(v.tensor_tensor(scratch, out, out, ALU.mult))
    link(v.tensor_reduce(var, three(scratch, heads), AX_X, ALU.add))
    v.tensor_scalar(spread, var, 1.0 / width, eps, ALU.mult, ALU.add).then_inc(spread_ready, 1)
    v.wait_ge(root_ready, count)
    link(v.reciprocal(rstd, root))
    link(v.tensor_tensor(three(out, heads), three(out, heads), per_row(rstd, width), ALU.mult))
    link(v.tensor_tensor(out, out, gain, ALU.mult))


def mix_stage(nc, bank, ident, a, proj, mix):
    HG = 4
    with Stage(nc, "mix") as st:
        mu = st.sb("mu", [P, RW_COLS])
        w0, a0, k_k, k_a, r_k, rw_gain, ret_gain = (st.sb(n, [P, 512]) for n in
                                                    ("w0", "a0", "k_k", "k_a", "r_k", "rw_gain", "ret_gain"))
        lora_up = st.sb("lora_up", [P, RW_W])
        g_up = st.sb("g_up", [P, RW_W])
        incl, strict, incl_mid, strict_mid = (st.sb(n, [P, P]) for n in ("incl", "strict", "incl_mid", "strict_mid"))
        pair_mask = [st.sb(f"pair_mask{i}", [P, P]) for i in range(1 + len(SOLVE_STEPS))]
        ends = st.sb("ends", [P, 2])
        intra = st.sb("intra", [P, RET_HEADS, P])
        q_decay = st.sb("q_decay", [P, RET_HEADS, P])
        k_decay = st.sb("k_decay", [P, RET_HEADS])
        tile_decay = st.sb("tile_decay", [P, RET_HEADS])

        feat, prev = st.sb("feat", [P, RW_COLS]), st.sb("prev", [P, RW_COLS])
        ret_in = st.sb("ret_in", [P, 4 * RET_W])
        rope = st.sb("rope", [P, 2, RET_D // 2])
        f = feat
        lo = st.sb("lo", [P, 256])
        lo_t = st.sb("lo_t", [P, 256])
        sg, ag, g, p_t, p_inv, p_ex = (st.sb(n, [P, RW_W]) for n in ("sg", "ag", "g", "p_t", "p_inv", "p_ex"))
        k2, y = st.sb("k2", [P, RW_W]), st.sb("y", [P, RW_W])
        t0, t1, kk = (prev[:, i * RW_W:(i + 1) * RW_W] for i in range(3))
        tilde = [st.sb(f"tilde_{n}", [P, RW_W]) for n in "bkra"]
        tilde_t = [st.sb(f"tilde_t_{n}", [RW_N, RW_HEADS, P]) for n in "bkra"]
        stats = st.sb("stats", [P, 6, RW_HEADS])
        bonus = st.sb("bonus", [P, RW_HEADS])
        reach = st.sb("reach", [RW_N, RW_HEADS, 2])
        m, m0 = st.sb("m", [RW_N, RW_W]), st.sb("m0", [RW_N, RW_W])
        ab, ak, rb, rk = ([st.sb(f"{n}{i}", [P, HG, P]) for i in range(2)] for n in ("ab", "ak", "rb", "rk"))
        ab_step = [[st.sb(f"ab_step{i}_{s}", [P, HG, P]) for s in range(3)] for i in range(2)]
        x_t, x_n, zs = ([st.sb(f"{n}{i}", [P, HG, P]) for i in range(2)] for n in ("x_t", "x_n", "zs"))
        q1, u = st.sb("q1", [P, RW_W]), st.sb("u", [P, RW_W])
        rot = st.sb("rot", [P, 4, 512])
        qk = st.sb("qk", [P, 2 * RET_W])
        kd = rot[:, 0, :]
        q_t, k_t, qd_t, pt = (st.sb(n, [P, RET_HEADS, P]) for n in ("q_t", "k_t", "qd_t", "pt"))
        state, gate, ry = (st.sb(n, [P, RET_W]) for n in ("state", "gate", "ry"))

        names = ("const in_ready turn_done dve_order pool_order shifted lo_ready lo_turned lo_t_ready lifted w_added a_added "
                 "sg_ready a_ready g_ready run_ready exp_ready reach_ready tilde_ready tilde_turned fm_even fm_odd "
                 "scored masked ab_split x_ready x_turned x_n_ready z_made z_ready x_step "
                 "m0_ready q1_made q1_ready u_made u_ready y_made m_made rw_ready rw_turned mixed "
                 "rotated ret_turned ret_t_ready qd_ready ret_scored pt_ready ret_made kv_used gate_ready ret_ready "
                 "ret_out_turned spread_ready root_ready pe_passed").split()
        sem = {n: st.sem(n) for n in names}
        (const, in_ready, turn_done, dve_order, pool_order, shifted, lo_ready, lo_turned, lo_t_ready, lifted, w_added, a_added,
         sg_ready, a_ready, g_ready, run_ready, exp_ready, reach_ready, tilde_ready, tilde_turned, fm_even, fm_odd,
         scored, masked, ab_split, x_ready, x_turned, x_n_ready, z_made, z_ready, x_step,
         m0_ready, q1_made, q1_ready, u_made, u_ready, y_made, m_made, rw_ready, rw_turned, mixed,
         rotated, ret_turned, ret_t_ready, qd_ready, ret_scored, pt_ready, ret_made, kv_used, gate_ready, ret_ready,
         ret_out_turned, spread_ready, root_ready, pe_passed) = (sem[n] for n in names)
        NS = len(SOLVE_STEPS)
        r_, k_, v_ = f[:, 0:512], f[:, 512:1024], f[:, 1024:1536]

        def head(ap, h, n):
            return ap[:, h * n:(h + 1) * n]

        consts = [
            (mu[:], rows(a["rwkv_mu"], RW_COLS)), (w0[:], rows(a["rwkv_w0"], 512)), (a0[:], rows(a["rwkv_a0"], 512)),
            (k_k[:], rows(a["rwkv_k_k"], 512)), (k_a[:], rows(a["rwkv_k_a"], 512)),
            (r_k[:], rows(a["rwkv_r_k"].rearrange("h n -> (h n)"), 512)),
            (rw_gain[:], rows(a["rwkv_gn_gain"], 512)), (ret_gain[:], rows(a["ret_gn_gain"], 512)),
            (lora_up[0:LORA, :], a["rwkv_w_up"]), (lora_up[LORA:2 * LORA, :], a["rwkv_a_up"]), (g_up[:], a["rwkv_g_up"]),
            (incl[:], a["c_incl"]), (strict[:], a["c_strict"]), (incl_mid[:], a["c_incl_mid"]),
            (strict_mid[:], a["c_strict_mid"]), (ends[:], a["c_ends"]),
            (intra[:], a["c_ret_intra"]), (q_decay[:], a["c_ret_q"]), (k_decay[:], a["c_ret_k"]),
            (tile_decay[:], a["c_ret_tile"]),
        ] + [(pair_mask[i][:], a["c_pairs"][i]) for i in range(1 + NS)]
        block = st.open()

        @block.sync
        def _(sp):
            for to, of in consts:
                sp.dma_start(to, of).then_inc(const, 16)
            with sp.Fori(0, TT) as t:
                sp.wait_ge(turn_done, t * 4)
                sp.dma_start(feat[:], proj[ds(t * P + 1, P), 4 * RET_W:IN_COLS]).then_inc(in_ready, 16)
                sp.dma_start(prev[:], proj[ds(t * P, P), 4 * RET_W:IN_COLS]).then_inc(in_ready, 16)
                sp.dma_start(ret_in[:], proj[ds(t * P + 1, P), 0:4 * RET_W]).then_inc(in_ready, 16)
                sp.dma_start(rope[:], a["c_rope"][ds(t * P, P), :].rearrange("p (a d) -> p a d", a=2)).then_inc(in_ready, 16)

        @block.vector
        def _(v):
            PER = 35
            v.memset(m[:], 0.0).then_inc(m_made, 1)
            v.memset(state[:], 0.0).then_inc(kv_used, 1)
            v.wait_ge(m_made, 1)
            v.wait_ge(kv_used, 1)
            v.wait_ge(const, 16 * len(consts))
            with v.Fori(0, TT) as t:
                steps = [0]

                def link(ins):
                    steps[0] += 1
                    ins.then_inc(dve_order, 1)
                    v.wait_ge(dve_order, t * PER + steps[0])

                v.wait_ge(turn_done, t * 4)
                v.wait_ge(in_ready, t * 64 + 64)
                link(v.tensor_tensor(prev[:], prev[:], feat[:], ALU.subtract))
                link(v.tensor_tensor(prev[:], prev[:], mu[:], ALU.mult))
                v.tensor_tensor(f[:], feat[:], prev[:], ALU.add).then_inc(shifted, 1)
                v.wait_ge(shifted, t + 1)
                link(v.tensor_tensor(t0, k_, k_k[:], ALU.mult))
                link(v.tensor_tensor(t1, t0, t0, ALU.mult))
                v.tensor_reduce(stats[:, 0, :], three(t1, RW_HEADS), AX_X, ALU.add).then_inc(spread_ready, 1)
                v.wait_ge(root_ready, t * 3 + 1)
                link(v.tensor_scalar(stats[:, 1, :], stats[:, 1, :], 1e-12, None, ALU.max))
                link(v.reciprocal(stats[:, 2, :], stats[:, 1, :]))
                link(v.tensor_tensor(three(kk, RW_HEADS), three(t0, RW_HEADS), per_row(stats[:, 2, :], RW_N), ALU.mult))
                v.wait_ge(lifted, t + 1)
                v.tensor_tensor(p_t[:], bank[1][:], w0[:], ALU.add).then_inc(w_added, 1)
                v.tensor_tensor(p_inv[:], bank[2][:], a0[:], ALU.add).then_inc(a_added, 1)
                v.wait_ge(a_ready, t + 1)
                link(v.scalar_tensor_tensor(out=t0, in0=ag[:], scalar=-1.0, in1=k_a[:], op0=ALU.add, op1=ALU.mult))
                link(v.scalar_tensor_tensor(out=k2[:], in0=t0, scalar=1.0, in1=k_, op0=ALU.add, op1=ALU.mult))
                link(v.tensor_tensor(t1, kk, ag[:], ALU.mult))
                v.wait_ge(exp_ready, t * 3 + 3)
                v.tensor_tensor(tilde[0][:], t1, p_inv[:], ALU.mult).then_inc(tilde_ready, 1)
                v.tensor_tensor(tilde[1][:], k2[:], p_inv[:], ALU.mult).then_inc(tilde_ready, 1)
                v.tensor_tensor(tilde[2][:], r_, p_t[:], ALU.mult).then_inc(tilde_ready, 1)
                v.scalar_tensor_tensor(out=tilde[3][:], in0=kk, scalar=-1.0, in1=p_ex[:], op0=ALU.mult,
                                       op1=ALU.mult).then_inc(tilde_ready, 1)
                v.wait_ge(reach_ready, t + 1)
                v.tensor_tensor(three(m0[:], RW_HEADS), three(m[:], RW_HEADS), per_row(reach[:, :, 0], RW_N),
                                ALU.mult).then_inc(m0_ready, 1)
                for n in range(1, 8, 2):
                    v.wait_ge(tilde_turned, t * 8 + n + 1)
                    v.tensor_copy(tilde_t[n // 2][:, 4 * (n % 2):4 * (n % 2) + 4, :],
                                  three(bank[n][0:RW_N, :], HG)).then_inc(fm_odd, 1)
                v.wait_ge(tilde_ready, t * 4 + 4)
                link(v.tensor_tensor(t0, r_, k2[:], ALU.mult))
                link(v.tensor_tensor(t0, t0, r_k[:], ALU.mult))
                link(v.tensor_reduce(bonus[:], three(t0, RW_HEADS), AX_X, ALU.add))
                for gr in range(2):
                    for n, (to, mask) in enumerate(((ab, strict), (rb, incl), (ak, strict), (rk, incl))):
                        v.wait_ge(scored, t * 8 + 4 * gr + n + 1)
                        v.tensor_tensor(to[gr][:], three(bank[4 * gr + n][:], HG), per_block(mask[:], HG),
                                        ALU.mult).then_inc(masked, 1)
                for gr in range(2):
                    v.wait_ge(ab_split, t * 2 * (NS + 1) + gr + 1)
                    v.tensor_tensor(x_t[gr][:], ab_step[gr][0][:], per_block(ident[:], HG), ALU.add).then_inc(x_ready, 1)
                for s in range(NS):
                    for gr in range(2):
                        v.wait_ge(x_step, t * 2 * NS + 2 * s + gr + 1)
                        v.wait_ge(x_ready, t * 2 * (NS + 1) + 2 * s + gr + 1)
                        v.tensor_tensor(x_t[gr][:], x_t[gr][:], three(bank[4 * gr + 2][:], HG), ALU.add).then_inc(x_ready, 1)
                v.wait_ge(m_made, t + 2)
                v.wait_ge(m0_ready, t + 1)
                link(v.tensor_tensor(m[:], m0[:], bank[4][0:RW_N, :], ALU.add))
                link(v.tensor_tensor(three(m[:], RW_HEADS), three(m[:], RW_HEADS), per_row(reach[:, :, 1], RW_N), ALU.mult))
                v.wait_ge(y_made, t + 1)
                head_norm(v, link, bank[0][:], t1, stats, RW_HEADS, RW_N, RW_GN_EPS, rw_gain[:], y[:],
                          spread_ready, root_ready, t * 3 + 2)
                link(v.tensor_tensor(three(t0, RW_HEADS), three(v_, RW_HEADS), per_row(bonus[:], RW_N), ALU.mult))
                link(v.tensor_tensor(y[:], y[:], t0, ALU.add))
                v.wait_ge(g_ready, t + 1)
                v.tensor_tensor(y[:], y[:], g[:], ALU.mult).then_inc(rw_ready, 1)
                v.wait_ge(ret_t_ready, t * 2 + 1)
                v.tensor_tensor(qd_t[:], q_t[:], q_decay[:], ALU.mult).then_inc(qd_ready, 1)
                v.wait_ge(ret_scored, t + 1)
                v.tensor_tensor(pt[:], three(bank[5][:], RET_HEADS), intra[:], ALU.mult).then_inc(pt_ready, 1)
                v.wait_ge(ret_made, t + 1)
                link(v.tensor_tensor(three(state[:], RET_HEADS), three(state[:], RET_HEADS),
                                     per_row(tile_decay[:], RET_D), ALU.mult))
                link(v.tensor_tensor(state[:], state[:], bank[7][:], ALU.add))
                head_norm(v, link, bank[6][:], t1, stats, RET_HEADS, RET_D, RET_GN_EPS, ret_gain[:], ry[:],
                          spread_ready, root_ready, t * 3 + 3)
                v.wait_ge(gate_ready, t + 1)
                v.tensor_tensor(ry[:], ry[:], gate[:], ALU.mult).then_inc(ret_ready, 1)
                v.wait_ge(ret_ready, t + 1)
                v.wait_ge(rw_ready, t + 1)
                v.sem_inc(turn_done, 1)
                assert steps[0] == PER

        @block.gpsimd
        def _(pool):
            half = RET_D // 2
            pool.wait_ge(const, 16 * len(consts))
            with pool.Fori(0, TT) as t:
                steps = [0]

                def link(ins):
                    steps[0] += 1
                    ins.then_inc(pool_order, 1)
                    pool.wait_ge(pool_order, t * 6 + steps[0])

                pool.wait_ge(turn_done, t * 4)
                pool.wait_ge(in_ready, t * 64 + 64)
                both = ret_in[:, 0:2 * RET_W].rearrange("p (h c d) -> p h c d", c=2, d=half)
                to = qk[:].rearrange("p (h c d) -> p h c d", c=2, d=half)
                cos, sin = (per_block(rope[:, i, :], 2 * RET_HEADS) for i in range(2))
                parts = [three(rot[:, i, :], 2 * RET_HEADS) for i in range(4)]
                link(pool.tensor_tensor(parts[0], both[:, :, 0, :], cos, ALU.mult))
                link(pool.tensor_tensor(parts[1], both[:, :, 1, :], sin, ALU.mult))
                link(pool.tensor_tensor(parts[2], both[:, :, 0, :], sin, ALU.mult))
                link(pool.tensor_tensor(parts[3], both[:, :, 1, :], cos, ALU.mult))
                link(pool.tensor_tensor(to[:, :, 0, :], parts[0], parts[1], ALU.subtract))
                link(pool.tensor_tensor(to[:, :, 1, :], parts[2], parts[3], ALU.add))
                pool.tensor_tensor(three(kd, RET_HEADS), three(qk[:, RET_W:2 * RET_W], RET_HEADS),
                                   per_row(k_decay[:], RET_D), ALU.mult).then_inc(rotated, 1)
                for s in range(NS + 1):
                    for gr in range(2):
                        if s == 0:
                            pool.wait_ge(masked, t * 8 + gr * 4 + 1)
                        elif s == 3:
                            pool.wait_ge(x_ready, t * 2 * (NS + 1) + gr + 1)
                        elif s > 3:
                            pool.wait_ge(z_made, t * 2 * NS + 2 * (s - 4) + gr + 1)
                        pool.tensor_tensor(ab_step[gr][s % 3][:], ab[gr][:], per_block(pair_mask[s][:], HG),
                                           ALU.mult).then_inc(ab_split, 1)
                pool.wait_ge(ab_split, t * 2 * (NS + 1) + 2 * (NS + 1))
                pool.wait_ge(rotated, t + 1)
                pool.sem_inc(turn_done, 1)

        @block.scalar
        def _(act):
            act.wait_ge(const, 16 * len(consts))
            with act.Fori(0, TT) as t:
                act.wait_ge(turn_done, t * 4)
                act.wait_ge(shifted, t + 1)
                act.activation(lo[:, 0:LORA], f[:, 1536:1536 + LORA], ACT.Tanh).then_inc(lo_ready, 1)
                act.activation(lo[:, LORA:2 * LORA], f[:, 1536 + LORA:1536 + 2 * LORA], ACT.Copy).then_inc(lo_ready, 1)
                act.activation(lo[:, 2 * LORA:256], f[:, 1536 + 2 * LORA:RW_COLS], ACT.Sigmoid).then_inc(lo_ready, 1)
                act.wait_ge(spread_ready, t * 3 + 1)
                act.activation(stats[:, 1, :], stats[:, 0, :], ACT.Sqrt).then_inc(root_ready, 1)
                act.wait_ge(lo_turned, t + 1)
                act.activation(lo_t[:], bank[0][:, 0:256], ACT.Copy).then_inc(lo_t_ready, 1)
                act.wait_ge(w_added, t + 1)
                act.activation(sg[:], p_t[:], ACT.Sigmoid).then_inc(sg_ready, 1)
                act.wait_ge(a_added, t + 1)
                act.activation(ag[:], p_inv[:], ACT.Sigmoid).then_inc(a_ready, 1)
                act.activation(g[:], bank[3][:], ACT.Copy).then_inc(g_ready, 1)
                act.wait_ge(in_ready, t * 64 + 64)
                act.activation(gate[:], ret_in[:, 3 * RET_W:4 * RET_W], ACT.Silu).then_inc(gate_ready, 1)
                act.wait_ge(a_ready, t + 1)
                act.wait_ge(sg_ready, t + 1)
                act.wait_ge(run_ready, t + 1)
                act.activation(p_t[:], bank[4][:], ACT.Exp, scale=DECAY).then_inc(exp_ready, 1)
                act.activation(p_inv[:], bank[4][:], ACT.Exp, scale=-DECAY).then_inc(exp_ready, 1)
                act.activation(p_ex[:], bank[5][:], ACT.Exp, scale=DECAY).then_inc(exp_ready, 1)
                act.activation(reach[:], three(bank[6][0:RW_N, 0:2 * RW_HEADS], RW_HEADS), ACT.Exp,
                               scale=DECAY).then_inc(reach_ready, 1)
                for n in range(0, 8, 2):
                    act.wait_ge(tilde_turned, t * 8 + n + 1)
                    act.activation(tilde_t[n // 2][:, 0:4, :], three(bank[n][0:RW_N, :], HG), ACT.Copy).then_inc(fm_even, 1)
                for s in range(NS):
                    for gr in range(2):
                        act.wait_ge(x_turned, t * 2 * NS + 2 * s + gr + 1)
                        act.activation(x_n[gr][:], three(bank[4 * gr][:], HG), ACT.Copy).then_inc(x_n_ready, 1)
                    for gr in range(2):
                        act.wait_ge(z_made, t * 2 * NS + 2 * s + gr + 1)
                        act.activation(zs[gr][:], three(bank[4 * gr + 1][:], HG), ACT.Copy).then_inc(z_ready, 1)
                act.wait_ge(q1_made, t + 1)
                act.activation(q1[:], bank[3][:], ACT.Copy).then_inc(q1_ready, 1)
                act.wait_ge(u_made, t + 1)
                act.activation(u[:], bank[7][:], ACT.Copy).then_inc(u_ready, 1)
                for n in range(2):
                    act.wait_ge(ret_turned, t * 2 + n + 1)
                    act.activation((q_t, k_t)[n][:], three(bank[2 + n][:], RET_HEADS), ACT.Copy).then_inc(ret_t_ready, 1)
                act.wait_ge(spread_ready, t * 3 + 2)
                act.activation(stats[:, 4, :], stats[:, 3, :], ACT.Sqrt).then_inc(root_ready, 1)
                act.wait_ge(rw_turned, t + 1)
                act.activation(mix[:, 4:8, ds(t * P, P)], three(bank[1][:], 4), ACT.Copy).then_inc(mixed, 1)
                act.wait_ge(spread_ready, t * 3 + 3)
                act.activation(stats[:, 4, 0:RET_HEADS], stats[:, 3, 0:RET_HEADS], ACT.Sqrt).then_inc(root_ready, 1)
                act.wait_ge(ret_out_turned, t + 1)
                act.activation(mix[:, 0:4, ds(t * P, P)], three(bank[4][:], 4), ACT.Copy).then_inc(mixed, 1)
                act.wait_ge(mixed, t * 2 + 2)
                act.sem_inc(turn_done, 1)

        @block.tensor
        def _(pe):
            pe.wait_ge(const, 16 * len(consts))
            with pe.Fori(0, TT) as t:
                pe.wait_ge(turn_done, t * 4)
                pe.wait_ge(lo_ready, t * 3 + 3)
                pe.transpose(bank[0][:, 0:P], lo[:, 0:P], ident[:])
                pe.transpose(bank[0][:, P:2 * P], lo[:, P:2 * P], ident[:]).then_inc(lo_turned, 1)
                pe.wait_ge(lo_t_ready, t + 1)
                pe.matmul(bank[1][:], lo_t[0:LORA, 0:P], lora_up[0:LORA, :], start=True, stop=True)
                pe.matmul(bank[2][:], lo_t[LORA:2 * LORA, 0:P], lora_up[LORA:2 * LORA, :], start=True, stop=True)
                pe.matmul(bank[3][:], lo_t[:, P:2 * P], g_up[:], start=True, stop=True).then_inc(lifted, 1)
                pe.wait_ge(sg_ready, t + 1)
                pe.matmul(bank[4][:], incl_mid[:], sg[:], start=True, stop=True)
                pe.matmul(bank[5][:], strict_mid[:], sg[:], start=True, stop=True)
                for h in range(RW_HEADS):
                    last = pe.matmul(bank[6][0:RW_N, 2 * h:2 * h + 2], head(sg, h, RW_N), ends[:], start=True, stop=True)
                last.then_inc(run_ready, 1)
                pe.wait_ge(g_ready, t + 1)
                pe.wait_ge(a_added, t + 1)
                pe.wait_ge(exp_ready, t * 3 + 3)
                pe.wait_ge(reach_ready, t + 1)
                for n in range(8):
                    pe.wait_ge(tilde_ready, t * 4 + n // 2 + 1)
                    pe.sem_inc(pe_passed, 1)
                    for h in range(HG):
                        last = pe.transpose(bank[n][0:RW_N, h * P:(h + 1) * P],
                                            head(tilde[n // 2], HG * (n % 2) + h, RW_N), ident[:])
                    last.then_inc(tilde_turned, 1)
                b_t, kt_t, r_t, a_t = tilde_t
                pe.wait_ge(fm_even, t * 4 + 4)
                pe.wait_ge(fm_odd, t * 4 + 4)
                for gr in range(2):
                    for left, at in ((b_t, 0), (kt_t, 2)):
                        for n, right in enumerate((a_t, r_t)):
                            for h in range(HG):
                                hh = HG * gr + h
                                last = pe.matmul(bank[4 * gr + at + n][:, h * P:(h + 1) * P], left[:, hh, :],
                                                 right[:, hh, :], start=True, stop=True)
                            last.then_inc(scored, 1)
                pe.wait_ge(masked, t * 8 + 8)
                for s in range(NS):
                    for gr in range(2):
                        pe.wait_ge(x_ready, t * 2 * (NS + 1) + 2 * s + gr + 1)
                        for h in range(HG):
                            last = pe.transpose(bank[4 * gr][:, h * P:(h + 1) * P], x_t[gr][:, h, :], ident[:])
                        last.then_inc(x_turned, 1)
                    for gr in range(2):
                        pe.wait_ge(x_n_ready, t * 2 * NS + 2 * s + gr + 1)
                        pe.wait_ge(ab_split, t * 2 * (NS + 1) + 2 * (s + 1) + gr + 1)
                        for h in range(HG):
                            last = pe.matmul(bank[4 * gr + 1][:, h * P:(h + 1) * P], ab_step[gr][(1 + s) % 3][:, h, :],
                                             x_n[gr][:, h, :], start=True, stop=True)
                        last.then_inc(z_made, 1)
                    for gr in range(2):
                        pe.wait_ge(z_ready, t * 2 * NS + 2 * s + gr + 1)
                        for h in range(HG):
                            last = pe.matmul(bank[4 * gr + 2][:, h * P:(h + 1) * P], zs[gr][:, h, :], x_t[gr][:, h, :],
                                             start=True, stop=True)
                        last.then_inc(x_step, 1)
                pe.wait_ge(m0_ready, t + 1)
                for h in range(RW_HEADS):
                    to = head(bank[3], h, RW_N)
                    pe.matmul(to, a_t[:, h, :], head(m0, h, RW_N), start=True, stop=False)
                    last = pe.matmul(to, ak[h // HG][:, h % HG, :], head(v_, h, RW_N), start=False, stop=True)
                last.then_inc(q1_made, 1)
                pe.wait_ge(q1_ready, t + 1)
                pe.wait_ge(x_ready, t * 2 * (NS + 1) + 2 * (NS + 1))
                for h in range(RW_HEADS):
                    last = pe.matmul(head(bank[7], h, RW_N), x_t[h // HG][:, h % HG, :], head(q1, h, RW_N),
                                     start=True, stop=True)
                last.then_inc(u_made, 1)
                pe.wait_ge(u_ready, t + 1)
                for h in range(RW_HEADS):
                    to = head(bank[4], h, RW_N)[0:RW_N, :]
                    pe.matmul(to, head(tilde[0], h, RW_N), head(u, h, RW_N), start=True, stop=False)
                    last = pe.matmul(to, head(tilde[1], h, RW_N), head(v_, h, RW_N), start=False, stop=True)
                last.then_inc(m_made, 1)
                for h in range(RW_HEADS):
                    to = head(bank[0], h, RW_N)
                    pe.matmul(to, r_t[:, h, :], head(m0, h, RW_N), start=True, stop=False)
                    pe.matmul(to, rb[h // HG][:, h % HG, :], head(u, h, RW_N), start=False, stop=False)
                    last = pe.matmul(to, rk[h // HG][:, h % HG, :], head(v_, h, RW_N), start=False, stop=True)
                last.then_inc(y_made, 1)
                pe.wait_ge(rotated, t + 1)
                for n in range(2):
                    for h in range(RET_HEADS):
                        last = pe.transpose(bank[2 + n][:, h * P:(h + 1) * P], head(qk[:, n * RET_W:(n + 1) * RET_W], h, RET_D),
                                            ident[:])
                    last.then_inc(ret_turned, 1)
                pe.wait_ge(ret_t_ready, t * 2 + 2)
                for h in range(RET_HEADS):
                    last = pe.matmul(bank[5][:, h * P:(h + 1) * P], k_t[:, h, :], q_t[:, h, :], start=True, stop=True)
                last.then_inc(ret_scored, 1)
                pe.wait_ge(pt_ready, t + 1)
                pe.wait_ge(qd_ready, t + 1)
                ret_v = ret_in[:, 2 * RET_W:3 * RET_W]
                for h in range(RET_HEADS):
                    to = head(bank[6], h, RET_D)
                    pe.matmul(to, pt[:, h, :], head(ret_v, h, RET_D), start=True, stop=False)
                    pe.matmul(to, qd_t[:, h, :], head(state, h, RET_D), start=False, stop=True)
                for h in range(RET_HEADS):
                    last = pe.matmul(head(bank[7], h, RET_D), head(kd, h, RET_D), head(ret_v, h, RET_D), start=True, stop=True)
                last.then_inc(ret_made, 1)
                pe.wait_ge(rw_ready, t + 1)
                for n in range(4):
                    last = pe.transpose(bank[1][:, n * P:(n + 1) * P], y[:, n * P:(n + 1) * P], ident[:])
                last.then_inc(rw_turned, 1)
                pe.wait_ge(ret_ready, t + 1)
                for n in range(4):
                    last = pe.transpose(bank[4][:, n * P:(n + 1) * P], ry[:, n * P:(n + 1) * P], ident[:])
                last.then_inc(ret_out_turned, 1)
                pe.wait_ge(mixed, t * 2 + 2)
                pe.sem_inc(turn_done, 1)


def constants():
    i = np.arange(P)
    incl = (i[:, None] <= i[None, :]).astype(np.float32)
    strict = (i[:, None] < i[None, :]).astype(np.float32)
    first = (i < P // 2).astype(np.float32)[:, None]
    pairs = [((i[:, None] // (2 * s) == i[None, :] // (2 * s)) & (i[:, None] % (2 * s) < s) & (i[None, :] % (2 * s) >= s))
             for s in (1,) + SOLVE_STEPS]
    log_g = np.log(1.0 - np.exp2(-5.0 - np.arange(RET_HEADS)))
    gap = i[None, :] - i[:, None]
    chunk = i // RET_CHUNK
    seen = chunk[None, :] >= chunk[:, None]
    intra = np.exp(log_g[:, None, None] * np.abs(gap)) * seen * RET_D ** -0.5
    half = RET_D // 2
    angle = np.arange(S, dtype=np.float32)[:, None] * (np.float32(10000.0) ** (-np.arange(half, dtype=np.float32) / np.float32(half)))[None, :]
    angle = angle.astype(np.float32).astype(np.float64)
    out = {
        "c_ident": np.eye(P), "c_incl": incl, "c_strict": strict,
        "c_incl_mid": incl - first, "c_strict_mid": strict - first,
        "c_ends": np.concatenate([first, 1.0 - first], axis=1),
        "c_pairs": np.stack(pairs), "c_ret_intra": intra.transpose(1, 0, 2),
        "c_ret_q": np.broadcast_to(np.exp(log_g[:, None] * (i + 1.0)), (P, RET_HEADS, P)),
        "c_ret_k": (np.exp(log_g[None, :] * (P - 1.0 - i)[:, None]) * RET_D ** -0.5),
        "c_ret_tile": np.broadcast_to(np.exp(log_g * P), (P, RET_HEADS)),
        "c_prefer": np.broadcast_to(8.0 - np.arange(8), (P, 8)),
        "c_expert_no": np.broadcast_to(np.arange(EXPERTS), (P, EXPERTS)),
        "c_fulls": np.broadcast_to(SLOT_BLOCK * np.arange(1, FULL_STEPS + 1), (P, FULL_STEPS)),
        "c_earlier": np.broadcast_to(np.tril(np.ones((EXPERTS, EXPERTS)), -1), (P, EXPERTS, EXPERTS)),
        "c_more_no": np.arange(MORE_BLOCKS)[None, :],
        "c_future": np.where(i[None, :] > i[:, None], -FAR, 0.0),
        "c_inv_freq": np.broadcast_to(1.0 / (np.float32(10000.0) ** (np.arange(0, ROPE, 2, dtype=np.float32) / np.float32(ROPE))),
                                      (P, ROPE // 2)),
        "c_rope": np.concatenate([np.cos(angle), np.sin(angle)], axis=1),
    }
    out = {k: np.ascontiguousarray(v, dtype=np.float32) for k, v in out.items()}
    out["c_token_ids"] = (np.arange(TT)[None, :] * P + i[:, None]).astype(np.int32)
    return out


def lay_out(inputs):
    out = {}
    for name, value in inputs.items():
        value = np.ascontiguousarray(value)
        out[name] = value[0] if value.ndim > 1 else value
    out.update(constants())
    return out


def add_product_stage(nc, name, bank, feat, w_dram, x, x_dram=None, post_gain=None):
    halves = D // BANK
    with Stage(nc, name) as st:
        w = st.sb("w", [P, KT, D])
        gain = st.sb("gain", [P, D])
        junk = [st.sb(f"junk{i}", [P, D]) for i in range(2)]
        scaled = [st.sb(f"scaled{i}", [P, D]) for i in range(2)]
        stats = st.sb("stats", [P, TT, 6])
        w_loaded, x_loaded, gain_loaded = st.sem("w_loaded"), st.sem("x_loaded"), st.sem("gain_loaded")
        product, squared, mean_ready, root_ready, dve_order, added = (
            st.sem(n) for n in ("product", "squared", "mean_ready", "root_ready", "dve_order", "added"))
        block = st.open()

        @block.sync
        def _(sp):
            sp.dma_start(w[:], w_dram.rearrange("(k p) n -> p k n", p=P)).then_inc(w_loaded, 16)
            if x_dram is not None:
                sp.dma_start(x[:], x_dram.rearrange("(t p) d -> p t d", p=P)).then_inc(x_loaded, 16)
            if post_gain is not None:
                sp.dma_start(gain[:], rows(post_gain, D)).then_inc(gain_loaded, 16)

        @block.tensor
        def _(pe):
            pe.wait_ge(w_loaded, 16)
            for t in range(TT):
                for n in range(halves):
                    if t >= 2:
                        pe.wait_ge(added, t - 1)
                    for k in range(KT):
                        last = pe.matmul(bank[2 * (t % 2) + n][:], feat[:, k, t * P:(t + 1) * P],
                                         w[:, k, n * BANK:(n + 1) * BANK], start=(k == 0), stop=(k == KT - 1))
                    last.then_inc(product, 1)

        if post_gain is not None:
            @block.scalar
            def _(act):
                for t in range(TT):
                    for n in range(halves):
                        act.wait_ge(product, 2 * t + n + 1)
                        if t >= 2:
                            act.wait_ge(squared, 2 * t - 2)
                        act.activation(junk[t % 2][:, n * BANK:(n + 1) * BANK], bank[2 * (t % 2) + n][:], ACT.Square,
                                       accum_out=stats[:, t, n:n + 1]).then_inc(squared, 1)
                    act.wait_ge(mean_ready, t + 1)
                    act.activation(stats[:, t, 4:5], stats[:, t, 3:4], ACT.Sqrt).then_inc(root_ready, 1)

        @block.vector
        def _(v):
            steps = [0]

            def link(ins):
                steps[0] += 1
                ins.then_inc(dve_order, 1)
                v.wait_ge(dve_order, steps[0])

            if x_dram is not None:
                v.wait_ge(x_loaded, 16)
            if post_gain is not None:
                v.wait_ge(gain_loaded, 16)
            for t in range(TT):
                if post_gain is not None:
                    v.wait_ge(squared, 2 * t + 2)
                    link(v.tensor_tensor(stats[:, t, 2:3], stats[:, t, 0:1], stats[:, t, 1:2], ALU.add))
                    v.tensor_scalar(stats[:, t, 3:4], stats[:, t, 2:3], 1.0 / D, EPS, ALU.mult, ALU.add).then_inc(mean_ready, 1)
                    v.wait_ge(root_ready, t + 1)
                    link(v.reciprocal(stats[:, t, 5:6], stats[:, t, 4:5]))
                for n in range(halves):
                    cols = slice(n * BANK, (n + 1) * BANK)
                    v.wait_ge(product, 2 * t + n + 1)
                    if post_gain is None:
                        link(v.tensor_tensor(x[:, t, cols], x[:, t, cols], bank[2 * (t % 2) + n][:], ALU.add))
                    else:
                        link(v.scalar_tensor_tensor(out=scaled[t % 2][:, cols], in0=bank[2 * (t % 2) + n][:],
                                                    scalar=stats[:, t, 5:6], in1=gain[:, cols], op0=ALU.mult, op1=ALU.mult))
                        link(v.tensor_tensor(x[:, t, cols], x[:, t, cols], scaled[t % 2][:, cols], ALU.add))
                v.sem_inc(added, 1)


GROUPS, PER_GROUP = 4, 8
EXPERTS = GROUPS * PER_GROUP
SLOT_BLOCK = 128
MORE_BLOCKS = 2 * S // SLOT_BLOCK - 1
SLOT_BLOCKS = EXPERTS + MORE_BLOCKS
FULL_STEPS = S // SLOT_BLOCK - 1
FAR = 1e30


def route_stage(nc, bank, a, feat, token_ids, slot_weight, slot_index, more, slot_token):
    with Stage(nc, "route") as st:
        w = st.sb("w", [P, KT, GROUPS + EXPERTS])
        bias = st.sb("bias", [P, GROUPS + EXPERTS])
        strict, ones = st.sb("strict", [P, P]), st.sb("ones", [P, P])
        prefer, expert_no = st.sb("prefer", [P, PER_GROUP]), st.sb("expert_no", [P, EXPERTS])
        fulls = st.sb("fulls", [P, FULL_STEPS])
        earlier = st.sb("earlier", [P, EXPERTS, EXPERTS])
        more_no = st.sb("more_no", [1, MORE_BLOCKS])
        logit = st.sb("logit", [P, TT, GROUPS + EXPERTS])
        g_shift, g_hot = st.sb("g_shift", [P, TT, GROUPS]), st.sb("g_hot", [P, TT, GROUPS])
        spread = st.sb("spread", [P, TT, GROUPS, PER_GROUP])
        inside, left, e_hot1, e_hot2, eq = (st.sb(n, [P, TT, PER_GROUP]) for n in ("inside", "left", "e_hot1", "e_hot2", "eq"))
        hot = [st.sb(f"hot{i}", [P, TT, EXPERTS]) for i in range(2)]
        both, rank, weighed = (st.sb(n, [P, TT, EXPERTS]) for n in ("both", "rank", "weighed"))
        carry = st.sb("carry", [P, TT + 1, EXPERTS])
        g_max, g_sum, g_prob, top1, top2, pick, gap, e_gap, denom = (
            st.sb(n, [P, TT]) for n in ("g_max", "g_sum", "g_prob", "top1", "top2", "pick", "gap", "e_gap", "denom"))
        over = st.sb("over", [P, EXPERTS, FULL_STEPS])
        blocks, first, last_of = (st.sb(n, [P, EXPERTS]) for n in ("blocks", "first", "last_of"))
        ahead = st.sb("ahead", [P, EXPERTS, EXPERTS])
        own, place, full, far, shift, where = (st.sb(n, [P, 2, TT]) for n in ("own", "place", "full", "far", "shift", "where"))
        start = st.sb("start", [P, 2, TT])
        past = st.sb("past", [P, 2 * TT, FULL_STEPS])
        passed = st.sb("passed", [1, MORE_BLOCKS, EXPERTS])
        more_f = st.sb("more_f", [1, 2, MORE_BLOCKS])
        used = st.sb("used", [1, 1])
        no_token = st.sb("no_token", [P, SLOT_BLOCKS], I32)
        (const, gate_const, logits_made, dve_order, g_shifted, g_exp_ready, gap_ready, gap_exp_ready, hot_ready, ranked,
         slots_ready, cleared, cleared_ready, scattered) = (st.sem(n) for n in (
             "const", "gate_const", "logits_made", "dve_order", "g_shifted", "g_exp_ready", "gap_ready", "gap_exp_ready",
             "hot_ready", "ranked", "slots_ready", "cleared", "cleared_ready", "scattered"))
        consts = [(w[:, :, 0:GROUPS], a["w_route_group"].rearrange("(k p) n -> p k n", p=P)),
                  (w[:, :, GROUPS:], a["w_route_expert"].rearrange("(k p) n -> p k n", p=P)),
                  (bias[:, 0:GROUPS], rows(a["b_route_group"], GROUPS)), (bias[:, GROUPS:], rows(a["b_route_expert"], EXPERTS)),
                  (strict[:], a["c_strict"]), (prefer[:], a["c_prefer"]), (expert_no[:], a["c_expert_no"]),
                  (fulls[:], a["c_fulls"]), (earlier[:], a["c_earlier"]), (more_no[:], a["c_more_no"]),
                  (token_ids[:], a["c_token_ids"])]
        block = st.open()

        @block.sync
        def _(sp):
            with nc.allow_non_contiguous_dma("the routers' few columns"):
                for to, of in consts:
                    sp.dma_start(to, of).then_inc(const, 16)
            sp.wait_ge(cleared, 1)
            sp.dma_start(slot_token.rearrange("(p b) a -> p (b a)", p=P), no_token[:]).then_inc(cleared_ready, 16)

        @block.tensor
        def _(pe):
            pe.wait_ge(const, 16 * len(consts))
            width = GROUPS + EXPERTS
            for t in range(TT):
                for k in range(KT):
                    last = pe.matmul(bank[0][:, t * width:(t + 1) * width], feat[:, k, t * P:(t + 1) * P], w[:, k, :],
                                     start=(k == 0), stop=(k == KT - 1))
            last.then_inc(logits_made, 1)
            pe.wait_ge(hot_ready, 1)
            every = both[:].rearrange("p t e -> p (t e)")
            pe.matmul(bank[1][:, 0:TT * EXPERTS], strict[:], every, start=True, stop=True)
            pe.matmul(bank[2][:, 0:TT * EXPERTS], ones[:], every, start=True, stop=True).then_inc(ranked, 1)

        @block.scalar
        def _(act):
            act.wait_ge(g_shifted, 1)
            act.activation(g_shift[:], g_shift[:], ACT.Exp).then_inc(g_exp_ready, 1)
            act.wait_ge(gap_ready, 1)
            act.activation(e_gap[:], gap[:], ACT.Exp).then_inc(gap_exp_ready, 1)

        @block.gpsimd
        def _(pool):
            pool.wait_ge(cleared_ready, 16)
            pool.wait_ge(slots_ready, 1)
            for c in range(2):
                for t in range(TT):
                    pool.indirect_dma_start(
                        out=slot_token, out_offset=bass.IndirectOffsetOnAxis(ap=slot_index[:, c, t:t + 1], axis=0),
                        in_=token_ids[:, t:t + 1], in_offset=None).then_inc(scattered, 16)
            pool.wait_ge(scattered, 16 * 2 * TT)

        @block.vector
        def _(v):
            steps = [0]

            def link(ins):
                steps[0] += 1
                ins.then_inc(dve_order, 1)
                v.wait_ge(dve_order, steps[0])

            def first_of(hot_out, values, top, n):
                link(v.tensor_tensor(eq[:, :, 0:n], values, per_row(top, n), ALU.is_equal))
                link(v.tensor_tensor(eq[:, :, 0:n], eq[:, :, 0:n], per_block(prefer[:, 0:n], TT), ALU.mult))
                link(v.tensor_reduce(pick[:], eq[:, :, 0:n], AX_X, ALU.max))
                link(v.tensor_tensor(hot_out, eq[:, :, 0:n], per_row(pick[:], n), ALU.is_equal))

            def of_chosen(to, values):
                for c in range(2):
                    link(v.tensor_tensor(weighed[:], hot[c][:], values, ALU.mult))
                    link(v.tensor_reduce(to[:, c, :], weighed[:], AX_X, ALU.add))

            link(v.memset(ones[:], 1.0))
            v.memset(no_token[:], 0).then_inc(cleared, 1)
            v.wait_ge(const, 16 * len(consts))
            v.wait_ge(logits_made, 1)
            link(v.tensor_tensor(logit[:], three(bank[0][:, 0:TT * (GROUPS + EXPERTS)], TT), per_block(bias[:], TT), ALU.add))
            g_logit = logit[:, :, 0:GROUPS]
            link(v.tensor_reduce(g_max[:], g_logit, AX_X, ALU.max))
            v.tensor_tensor(g_shift[:], g_logit, per_row(g_max[:], GROUPS), ALU.subtract).then_inc(g_shifted, 1)
            first_of(g_hot[:], g_logit, g_max[:], GROUPS)
            v.wait_ge(g_exp_ready, 1)
            link(v.tensor_reduce(g_sum[:], g_shift[:], AX_X, ALU.add))
            link(v.reciprocal(g_prob[:], g_sum[:]))
            e_logit = logit[:, :, GROUPS:].rearrange("p t (g e) -> p t g e", g=GROUPS)
            g_wide = g_hot[:].unsqueeze(3).to_broadcast([P, TT, GROUPS, PER_GROUP])
            link(v.tensor_tensor(spread[:], e_logit, g_wide, ALU.mult))
            link(v.tensor_reduce(inside[:], spread[:].rearrange("p t g e -> p t e g"), AX_X, ALU.add))
            link(v.tensor_reduce(top1[:], inside[:], AX_X, ALU.max))
            first_of(e_hot1[:], inside[:], top1[:], PER_GROUP)
            link(v.scalar_tensor_tensor(out=left[:], in0=e_hot1[:], scalar=-FAR, in1=inside[:], op0=ALU.mult, op1=ALU.add))
            link(v.tensor_reduce(top2[:], left[:], AX_X, ALU.max))
            first_of(e_hot2[:], left[:], top2[:], PER_GROUP)
            v.tensor_tensor(gap[:], top2[:], top1[:], ALU.subtract).then_inc(gap_ready, 1)
            for c, e_hot in enumerate((e_hot1, e_hot2)):
                link(v.tensor_tensor(hot[c][:].rearrange("p t (g e) -> p t g e", g=GROUPS), g_wide,
                                     e_hot[:].unsqueeze(2).to_broadcast([P, TT, GROUPS, PER_GROUP]), ALU.mult))
            v.tensor_tensor(both[:], hot[0][:], hot[1][:], ALU.add).then_inc(hot_ready, 1)
            v.wait_ge(gap_exp_ready, 1)
            link(v.tensor_scalar(denom[:], e_gap[:], 1.0, None, ALU.add))
            link(v.reciprocal(denom[:], denom[:]))
            link(v.tensor_tensor(slot_weight[:, 0, :], denom[:], g_prob[:], ALU.mult))
            link(v.tensor_tensor(slot_weight[:, 1, :], slot_weight[:, 0, :], e_gap[:], ALU.mult))
            v.wait_ge(ranked, 1)
            link(v.memset(carry[:, 0, :], 0.0))
            for t in range(TT):
                link(v.tensor_tensor(carry[:, t + 1, :], carry[:, t, :], bank[2][:, t * EXPERTS:(t + 1) * EXPERTS], ALU.add))
            link(v.tensor_tensor(rank[:], three(bank[1][:, 0:TT * EXPERTS], TT), carry[:, 0:TT, :], ALU.add))
            count = carry[:, TT, :]
            link(v.tensor_tensor(over[:], per_row(count, FULL_STEPS), per_block(fulls[:], EXPERTS), ALU.is_gt))
            link(v.tensor_reduce(blocks[:], over[:], AX_X, ALU.add))
            link(v.tensor_tensor(ahead[:], earlier[:], per_block(blocks[:], EXPERTS), ALU.mult))
            link(v.tensor_reduce(first[:], ahead[:], AX_X, ALU.add))
            link(v.tensor_tensor(last_of[:], first[:], blocks[:], ALU.add))
            of_chosen(place, rank[:])
            of_chosen(own, per_block(expert_no[:], TT))
            of_chosen(start, per_block(first[:], TT))
            places = place[:].rearrange("p c t -> p (c t)")
            link(v.tensor_tensor(past[:], per_row(places, FULL_STEPS), per_block(fulls[:], 2 * TT), ALU.is_ge))
            link(v.tensor_reduce(full[:].rearrange("p c t -> p (c t)"), past[:], AX_X, ALU.add))
            link(v.tensor_scalar(far[:], full[:], 1.0, None, ALU.min))
            link(v.tensor_tensor(shift[:], start[:], full[:], ALU.add))
            link(v.scalar_tensor_tensor(out=shift[:], in0=shift[:], scalar=float(EXPERTS - 1), in1=own[:], op0=ALU.add,
                                        op1=ALU.subtract))
            link(v.tensor_tensor(shift[:], shift[:], far[:], ALU.mult))
            link(v.tensor_tensor(shift[:], shift[:], own[:], ALU.add))
            link(v.tensor_tensor(shift[:], shift[:], full[:], ALU.subtract))
            link(v.scalar_tensor_tensor(out=where[:], in0=shift[:], scalar=float(SLOT_BLOCK), in1=place[:], op0=ALU.mult,
                                        op1=ALU.add))
            v.tensor_copy(slot_index[:], where[:]).then_inc(slots_ready, 1)
            link(v.tensor_tensor(passed[:], per_block(last_of[0:1, :], MORE_BLOCKS), per_row(more_no[:], EXPERTS), ALU.is_le))
            link(v.tensor_reduce(more_f[:, 0, :], passed[:], AX_X, ALU.add))
            link(v.tensor_scalar(more_f[:, 0, :], more_f[:, 0, :], float(EXPERTS - 1), None, ALU.min))
            link(v.tensor_reduce(used[:], blocks[0:1, :], AX_X, ALU.add))
            link(v.tensor_scalar(more_f[:, 1, :], more_no[:], used[0:1, 0:1], None, ALU.is_lt))
            link(v.tensor_copy(more[:], more_f[:]))


HIDDEN = 512
FT = HIDDEN // P


def expert_stage(nc, bank, ident, a, more, slot_token, h_rows, y_rows):
    with Stage(nc, "expert") as st:
        w_gate, w_up = ([st.sb(f"{n}{u}", [P, KT, HIDDEN]) for u in range(2)] for n in ("w_gate", "w_up"))
        w_down = [st.sb(f"w_down{u}", [P, FT, D]) for u in range(2)]
        gain = st.sb("gain", [P, KT])
        ids = st.sb("ids", [P, SLOT_BLOCKS], I32)
        pick = [st.sb(f"pick{u}", [P, 1], I32) for u in range(2)]
        rows_in = [st.sb(f"rows_in{u}", [P, D]) for u in range(2)]
        x_t = [st.sb(f"x_t{u}", [P, KT, P]) for u in range(2)]
        silu, hidden = st.sb("silu", [P, HIDDEN]), st.sb("hidden", [P, HIDDEN])
        hidden_t = st.sb("hidden_t", [P, FT, P])
        y = [st.sb(f"y{u}", [P, D]) for u in range(2)]
        ids_loaded, gain_loaded = st.sem("ids_loaded"), st.sem("gain_loaded")
        up_loaded, down_loaded, picked, gathered, stored, up_used, down_used = (
            [st.sem(f"{n}{u}") for u in range(2)]
            for n in ("up_loaded", "down_loaded", "picked", "gathered", "stored", "up_used", "down_used"))
        passed = st.sem("passed")
        x_turned, low_out, high_out = st.sem("x_turned"), st.sem("low_out"), st.sem("high_out")
        lifted, silu_ready, hidden_ready, hidden_turned, hidden_t_ready, made, y_low, y_high = (
            st.sem(n) for n in ("lifted", "silu_ready", "hidden_ready", "hidden_turned", "hidden_t_ready", "made", "y_low", "y_high"))
        block = st.open()
        half = EXPERTS // 2
        BOTH = 32

        def load_up(sp, gate_of, up_of, u):
            sp.dma_start(w_gate[u][:], gate_of.rearrange("(k p) f -> p k f", p=P)).then_inc(up_loaded[u], 16)
            sp.dma_start(w_up[u][:], up_of.rearrange("(k p) f -> p k f", p=P)).then_inc(up_loaded[u], 16)

        def load_down(sp, down_of, u):
            sp.dma_start(w_down[u][:], down_of.rearrange("(k p) n -> p k n", p=P)).then_inc(down_loaded[u], 16)

        def turn_x(pe, n, u, per_u):
            pe.wait_ge(gathered[u], per_u * 16 + 16)
            pe.wait_ge(low_out, n)
            pe.wait_ge(high_out, n)
            for k in range(KT):
                last = pe.transpose(bank[k // 4][:, (k % 4) * P:(k % 4 + 1) * P], rows_in[u][:, k * P:(k + 1) * P], ident[:])
            last.then_inc(x_turned, 1)

        def lift(pe, n, u, per_u):
            pe.wait_ge(up_loaded[u], per_u * BOTH + BOTH)
            pe.wait_ge(low_out, n + 1)
            pe.wait_ge(high_out, n + 1)
            pe.wait_ge(hidden_ready, n)
            for b, w in ((2, w_gate), (3, w_up)):
                for k in range(KT):
                    last = pe.matmul(bank[b][:], x_t[u][:, k, :], w[u][:, k, :], start=(k == 0), stop=(k == KT - 1))
                if b == 3:
                    last.then_inc(up_used[u], 1)
                else:
                    last.then_inc(lifted, 1)

        def lower(pe, n, u, per_u):
            pe.wait_ge(hidden_ready, n + 1)
            for k in range(FT):
                last = pe.transpose(bank[4][:, k * P:(k + 1) * P], hidden[:, k * P:(k + 1) * P], ident[:])
            last.then_inc(hidden_turned, 1)
            pe.wait_ge(down_loaded[u], per_u * 16 + 16)
            pe.wait_ge(hidden_t_ready, n + 1)
            pe.wait_ge(y_low, n)
            pe.wait_ge(y_high, n)
            for b in range(2):
                for k in range(FT):
                    last = pe.matmul(bank[5 + b][:], hidden_t[:, k, :], w_down[u][:, k, b * BANK:(b + 1) * BANK],
                                     start=(k == 0), stop=(k == FT - 1))
                last.then_inc((made, down_used[u])[b], 1)

        def x_high(act, n, u):
            act.wait_ge(x_turned, n + 1)
            for k in range(4, 8):
                last = act.activation(x_t[u][:, k, :], bank[1][:, (k - 4) * P:(k - 3) * P], ACT.Copy, scale=gain[:, k:k + 1])
            last.then_inc(high_out, 1)

        def gate_and_out(act, n, u, per_u, y_to):
            act.wait_ge(lifted, n + 1)
            act.wait_ge(hidden_ready, n)
            act.activation(silu[:], bank[2][:], ACT.Silu).then_inc(silu_ready, 1)
            act.wait_ge(hidden_turned, n + 1)
            act.activation(hidden_t[:], three(bank[4][:], FT), ACT.Copy).then_inc(hidden_t_ready, 1)

        def out_low(act, n, u, per_u, y_to):
            act.wait_ge(made, n + 1)
            act.wait_ge(stored[u], per_u * 16)
            act.activation(y[u][:, 0:BANK], bank[5][:], ACT.Copy).then_inc(y_low, 1)
            act.wait_ge(y_low, n + 1)
            act.wait_ge(y_high, n + 1)
            act.dma_start(y_to, y[u][:]).then_inc(stored[u], 16)

        def x_low(v, n, u):
            v.wait_ge(x_turned, n + 1)
            v.tensor_tensor(x_t[u][:, 0:4, :], three(bank[0][:], 4), per_row(gain[:, 0:4], P), ALU.mult).then_inc(low_out, 1)

        def hide(v, n, u, per_u):
            v.wait_ge(silu_ready, n + 1)
            v.wait_ge(up_used[u], per_u + 1)
            v.wait_ge(hidden_turned, n)
            v.tensor_tensor(hidden[:], silu[:], bank[3][:], ALU.mult).then_inc(hidden_ready, 1)

        def out_high(v, n, u, per_u):
            v.wait_ge(down_used[u], per_u + 1)
            v.wait_ge(stored[u], per_u * 16)
            v.tensor_copy(y[u][:, BANK:D], bank[6][:]).then_inc(y_high, 1)

        def if_used(eng, i):
            return eng.If(eng.value_load(more[0:1, 1, ds(i, 1)], min_val=0, max_val=1))

        @block.sync
        def _(sp):
            with nc.allow_non_contiguous_dma("a slot's token for each partition"):
                sp.dma_start(ids[:], slot_token.rearrange("(b p) a -> p (b a)", p=P)).then_inc(ids_loaded, 16)
                sp.dma_start(gain[:], a["norm2_gain"].rearrange("(k p) -> p k", p=P)).then_inc(gain_loaded, 16)
            with sp.Fori(0, half) as j:
                for u in range(2):
                    e = j * 2 + u
                    sp.wait_ge(up_used[u], j)
                    load_up(sp, a["w_gate"][ds(e, 1)].rearrange("a d f -> (a d) f"),
                            a["w_up"][ds(e, 1)].rearrange("a d f -> (a d) f"), u)
                    sp.wait_ge(down_used[u], j)
                    load_down(sp, a["w_down"][ds(e, 1)].rearrange("a f d -> (a f) d"), u)
            with sp.Fori(0, MORE_BLOCKS) as i:
                with if_used(sp, i):
                    e = sp.value_load(more[0:1, 0, ds(i, 1)], min_val=0, max_val=EXPERTS - 1)
                    sp.wait_ge(up_used[0], half + i)
                    load_up(sp, a["w_gate"][ds(e, 1)].rearrange("a d f -> (a d) f"),
                            a["w_up"][ds(e, 1)].rearrange("a d f -> (a d) f"), 0)
                    sp.wait_ge(down_used[0], half + i)
                    load_down(sp, a["w_down"][ds(e, 1)].rearrange("a f d -> (a f) d"), 0)

        @block.gpsimd
        def _(pool):
            def fetch(at, u, per_u):
                pool.tensor_copy(pick[u][:], ids[:, at]).then_inc(picked[u], 1)
                pool.wait_ge(picked[u], per_u + 1)
                pool.sem_inc(passed, 1)
                pool.indirect_dma_start(out=rows_in[u][:], out_offset=None, in_=h_rows,
                                        in_offset=bass.IndirectOffsetOnAxis(ap=pick[u][:, 0:1], axis=0)).then_inc(gathered[u], 16)

            pool.wait_ge(ids_loaded, 16)
            with pool.Fori(0, half) as j:
                for u in range(2):
                    pool.wait_ge(x_turned, j * 2)
                    pool.wait_ge(gathered[u], j * 16)
                    fetch(ds(j * 2 + u, 1), u, j)
            with pool.Fori(0, MORE_BLOCKS) as i:
                with if_used(pool, i):
                    pool.wait_ge(x_turned, i + EXPERTS)
                    pool.wait_ge(gathered[0], (i + half) * 16)
                    fetch(ds(i + EXPERTS, 1), 0, i + half)

        @block.tensor
        def _(pe):
            turn_x(pe, 0, 0, 0)
            with pe.Fori(0, half - 1) as j:
                lift(pe, j * 2, 0, j)
                turn_x(pe, j * 2 + 1, 1, j)
                lower(pe, j * 2, 0, j)
                lift(pe, j * 2 + 1, 1, j)
                turn_x(pe, j * 2 + 2, 0, j + 1)
                lower(pe, j * 2 + 1, 1, j)
            n, j = EXPERTS - 2, half - 1
            lift(pe, n, 0, j)
            turn_x(pe, n + 1, 1, j)
            lower(pe, n, 0, j)
            lift(pe, n + 1, 1, j)
            lower(pe, n + 1, 1, j)
            with pe.Fori(0, MORE_BLOCKS) as i:
                with if_used(pe, i):
                    turn_x(pe, i + EXPERTS, 0, i + half)
                    lift(pe, i + EXPERTS, 0, i + half)
                    lower(pe, i + EXPERTS, 0, i + half)

        @block.scalar
        def _(act):
            def to(n):
                return y_rows[ds(n * P, P), :]

            act.wait_ge(gain_loaded, 16)
            x_high(act, 0, 0)
            with act.Fori(0, half - 1) as j:
                for u in range(2):
                    n = j * 2 + u
                    gate_and_out(act, n, u, j, None)
                    x_high(act, n + 1, 1 - u)
                    out_low(act, n, u, j, to(n))
            n, j = EXPERTS - 2, half - 1
            gate_and_out(act, n, 0, j, None)
            x_high(act, n + 1, 1)
            out_low(act, n, 0, j, to(n))
            gate_and_out(act, n + 1, 1, j, None)
            out_low(act, n + 1, 1, j, to(n + 1))
            act.wait_ge(stored[1], 16 * half)
            act.wait_ge(stored[0], 16 * half)
            with act.Fori(0, MORE_BLOCKS) as i:
                with if_used(act, i):
                    n = i + EXPERTS
                    x_high(act, n, 0)
                    gate_and_out(act, n, 0, i + half, None)
                    out_low(act, n, 0, i + half, to(n))
                    act.wait_ge(stored[0], (i + half) * 16 + 16)
                    act.sem_inc(passed, 1)

        @block.vector
        def _(v):
            v.wait_ge(gain_loaded, 16)
            x_low(v, 0, 0)
            with v.Fori(0, half - 1) as j:
                for u in range(2):
                    n = j * 2 + u
                    hide(v, n, u, j)
                    x_low(v, n + 1, 1 - u)
                    out_high(v, n, u, j)
            n, j = EXPERTS - 2, half - 1
            hide(v, n, 0, j)
            x_low(v, n + 1, 1)
            out_high(v, n, 0, j)
            hide(v, n + 1, 1, j)
            out_high(v, n + 1, 1, j)
            with v.Fori(0, MORE_BLOCKS) as i:
                with if_used(v, i):
                    n = i + EXPERTS
                    x_low(v, n, 0)
                    hide(v, n, 0, i + half)
                    out_high(v, n, 0, i + half)


def combine_stage(nc, x, y_rows, slot_index, slot_weight, gain_dram, x_dram):
    with Stage(nc, "combine") as st:
        gain = st.sb("gain", [P, D])
        got = [[st.sb(f"got{c}{u}", [P, D]) for u in range(2)] for c in range(2)]
        pick = [[st.sb(f"pick{c}{u}", [P, 1], I32) for u in range(2)] for c in range(2)]
        junk = [st.sb(f"junk{u}", [P, D]) for u in range(2)]
        square, mean, root, rstd = ([st.sb(f"{n}{u}", [P, 1]) for u in range(2)] for n in ("square", "mean", "root", "rstd"))
        gain_loaded, passed, stored = st.sem("gain_loaded"), st.sem("passed"), st.sem("stored")
        gathered, picked, added, squared, mean_ready, root_ready, rstd_ready, normed = (
            [st.sem(f"{n}{u}") for u in range(2)]
            for n in ("gathered", "picked", "added", "squared", "mean_ready", "root_ready", "rstd_ready", "normed"))
        block = st.open()

        @block.sync
        def _(sp):
            sp.dma_start(gain[:], rows(gain_dram, D)).then_inc(gain_loaded, 16)
            with sp.Fori(0, TT // 2) as j:
                for u in range(2):
                    t = j * 2 + u
                    sp.wait_ge(normed[u], j + 1)
                    sp.dma_start(x_dram[ds(t * P, P), :], x[:, ds(t, 1), :].rearrange("p a d -> p (a d)"))\
                        .then_inc(stored, 16)
            sp.wait_ge(stored, 16 * TT)

        @block.gpsimd
        def _(pool):
            with pool.Fori(0, TT // 2) as j:
                for u in range(2):
                    pool.wait_ge(gathered[u], j * 32)
                    pool.wait_ge(added[u], j * 2)
                    for c in range(2):
                        pool.tensor_copy(pick[c][u][:], slot_index[:, c, ds(j * 2 + u, 1)]).then_inc(picked[u], 1)
                    pool.wait_ge(picked[u], j * 2 + 2)
                    pool.sem_inc(passed, 1)
                    for c in range(2):
                        pool.indirect_dma_start(out=got[c][u][:], out_offset=None, in_=y_rows,
                                                in_offset=bass.IndirectOffsetOnAxis(ap=pick[c][u][:, 0:1], axis=0))\
                            .then_inc(gathered[u], 16)

        @block.vector
        def _(v):
            v.wait_ge(gain_loaded, 16)
            with v.Fori(0, TT // 2) as j:
                for u in range(2):
                    t = j * 2 + u
                    row = x[:, ds(t, 1), :].rearrange("p a d -> p (a d)")
                    v.wait_ge(gathered[u], j * 32 + 32)
                    for c in range(2):
                        v.scalar_tensor_tensor(out=row, in0=got[c][u][:], scalar=slot_weight[:, c, ds(t, 1)], in1=row,
                                               op0=ALU.mult, op1=ALU.add).then_inc(added[u], 1)
                        v.wait_ge(added[u], j * 2 + c + 1)
                    v.wait_ge(squared[u], j + 1)
                    v.tensor_scalar(mean[u][:], square[u][:], 1.0 / D, EPS, ALU.mult, ALU.add).then_inc(mean_ready[u], 1)
                    v.wait_ge(root_ready[u], j + 1)
                    v.reciprocal(rstd[u][:], root[u][:]).then_inc(rstd_ready[u], 1)
                    v.wait_ge(rstd_ready[u], j + 1)
                    v.scalar_tensor_tensor(out=row, in0=row, scalar=rstd[u][:, 0:1], in1=gain[:], op0=ALU.mult,
                                           op1=ALU.mult).then_inc(normed[u], 1)
                    v.wait_ge(normed[u], j + 1)

        @block.scalar
        def _(act):
            with act.Fori(0, TT // 2) as j:
                for u in range(2):
                    act.wait_ge(added[u], j * 2 + 2)
                    act.wait_ge(mean_ready[u], j)
                    act.activation(junk[u][:], x[:, ds(j * 2 + u, 1), :].rearrange("p a d -> p (a d)"), ACT.Square,
                                   accum_out=square[u][:]).then_inc(squared[u], 1)
                    act.wait_ge(mean_ready[u], j + 1)
                    act.wait_ge(rstd_ready[u], j)
                    act.activation(root[u][:], mean[u][:], ACT.Sqrt).then_inc(root_ready[u], 1)


MLA_HEADS, Q_LORA, KV_LORA, NOPE, ROPE, V_DIM = 8, 256, 128, 64, 32, 64
QK = NOPE + ROPE
SC, SC_TAPS = 256, 3
SSD_HEADS, SSD_HD, SSD_GROUPS, SSD_STATE, SSD_TAPS = 4, 64, 2, 128, 4
SSD = SSD_HEADS * SSD_HD
XBC = SSD + 2 * SSD_GROUPS * SSD_STATE
LATENT = Q_LORA + KV_LORA + ROPE
SC_AT = LATENT
Z_AT = SC_AT + 3 * SC
XBC_AT = Z_AT + SSD
DT_AT = XBC_AT + XBC
TM_COLS = LATENT + SSD + SSD_HEADS
SC_T, XBC_T = 3 * SC // P, XBC // P
MLA_T = MLA_HEADS * V_DIM // P


def wide(psum, b, n):
    return psum[:, b:b + n, :].rearrange("p a b -> p (a b)")


def project2_stage(nc, psum, bank, feat, a, rows2, xbc):
    with Stage(nc, "project2") as st:
        w_tm = st.sb("w_tm", [P, KT, TM_COLS])
        w_fm = [st.sb(f"w_fm{u}", [P, KT, P]) for u in range(2)]
        sc = st.sb("sc", [P, SC_T, S])
        acc = st.sb("acc", [P, S])
        taps, bias = st.sb("taps", [P, XBC_T, SSD_TAPS]), st.sb("bias", [P, XBC_T])
        sc_taps = st.sb("sc_taps", [P, SC // P, SC_TAPS])
        const, tm_loaded = st.sem("const"), st.sem("tm_loaded")
        fm_loaded = [st.sem(f"fm_loaded{u}") for u in range(2)]
        made = [st.sem(f"made{u}") for u in range(2)]
        product, latent_out, z_out, sc_out, scaled, tapped, xbc_out = (
            st.sem(n) for n in ("product", "latent_out", "z_out", "sc_out", "scaled", "tapped", "xbc_out"))
        gated, sc_scaled, sc_order = st.sem("gated"), st.sem("sc_scaled"), st.sem("sc_order")
        block = st.open()
        cols = lambda w, at, n: w[:, at:at + n].rearrange("(k p) n -> p k n", p=P)
        w_dram = a["w_in_2"]

        @block.sync
        def _(sp):
            sp.dma_start(w_tm[:, :, 0:LATENT], cols(w_dram, 0, LATENT)).then_inc(tm_loaded, 16)
            sp.dma_start(w_tm[:, :, LATENT:LATENT + SSD], cols(w_dram, Z_AT, SSD)).then_inc(tm_loaded, 16)
            with nc.allow_non_contiguous_dma("a few taps for each channel"):
                sp.dma_start(w_tm[:, :, LATENT + SSD:], cols(w_dram, DT_AT, SSD_HEADS)).then_inc(tm_loaded, 16)
                for i in range(SSD_TAPS):
                    sp.dma_start(taps[:, :, i], a["ssd_conv_w_2"][i, :].rearrange("(c p) -> p c", p=P)).then_inc(const, 16)
                sp.dma_start(bias[:], a["ssd_conv_b_2"].rearrange("(c p) -> p c", p=P)).then_inc(const, 16)
                for i in range(SC_TAPS):
                    sp.dma_start(sc_taps[:, :, i], a["sc_conv_w_2"][i, :].rearrange("(c p) -> p c", p=P)).then_inc(const, 16)
            with sp.Fori(0, SC_T) as j:
                for u, at in enumerate((SC_AT, XBC_AT)):
                    sp.wait_ge(made[u], j)
                    sp.dma_start(w_fm[u][:], w_dram[:, ds(j * P + at, P)].rearrange("(k p) n -> p k n", p=P))\
                        .then_inc(fm_loaded[u], 16)

        @block.tensor
        def _(pe):
            pe.wait_ge(tm_loaded, 48)
            for t in range(TT):
                if t >= 4:
                    pe.wait_ge(latent_out, t - 3)
                    pe.wait_ge(z_out, t - 3)
                for n, (lo_, hi) in enumerate(((0, LATENT), (LATENT, TM_COLS))):
                    for k in range(KT):
                        last = pe.matmul(bank[2 * (t % 4) + n][:, 0:hi - lo_], feat[:, k, t * P:(t + 1) * P],
                                         w_tm[:, k, lo_:hi], start=(k == 0), stop=(k == KT - 1))
                    last.then_inc(product, 1)
            pe.wait_ge(latent_out, TT)
            pe.wait_ge(z_out, TT)
            with pe.Fori(0, SC_T) as j:
                for u in range(2):
                    pe.wait_ge(fm_loaded[u], j * 16 + 16)
                    pe.wait_ge((sc_out, tapped)[u], j * (1, 3)[u])
                    for n in range(2):
                        for k in range(KT):
                            last = pe.matmul(bank[2 * u + n][:], w_fm[u][:, k, :], feat[:, k, n * BANK:(n + 1) * BANK],
                                             start=(k == 0), stop=(k == KT - 1))
                    last.then_inc(made[u], 1)

        @block.scalar
        def _(act):
            for t in range(TT):
                act.wait_ge(product, 2 * t + 1)
                act.activation(rows2[:, t, 0:LATENT], bank[2 * (t % 4)][:, 0:LATENT], ACT.Copy).then_inc(latent_out, 1)
            act.wait_ge(const, 16 * (SSD_TAPS + 1 + SC_TAPS))
            with act.Fori(0, SC_T) as j:
                act.wait_ge(made[0], j + 1)
                act.activation(sc[:, ds(j, 1), :].rearrange("p a s -> p (a s)"), wide(psum, 0, 2), ACT.Copy).then_inc(sc_out, 1)
                act.wait_ge(made[1], j + 1)
                act.wait_ge(xbc_out, j)
                act.activation(acc[:], wide(psum, 2, 2), ACT.Identity, scale=taps[:, ds(j, 1), SSD_TAPS - 1],
                               bias=bias[:, ds(j, 1)]).then_inc(scaled, 1)
                act.wait_ge(tapped, j * 3 + 3)
                act.activation(xbc[:, ds(j, 1), :].rearrange("p a s -> p (a s)"), acc[:], ACT.Silu).then_inc(xbc_out, 1)
            for i in range(SC // P):
                act.wait_ge(gated, i + 1)
                act.activation(sc[:, i + 4, :], sc[:, i + 2, :], ACT.Copy, scale=sc_taps[:, i, SC_TAPS - 1:SC_TAPS])\
                    .then_inc(sc_scaled, 1)

        @block.vector
        def _(v):
            for t in range(TT):
                v.wait_ge(product, 2 * t + 2)
                v.tensor_copy(rows2[:, t, LATENT:], bank[2 * (t % 4) + 1][:, 0:SSD + SSD_HEADS]).then_inc(z_out, 1)
            v.wait_ge(const, 16 * (SSD_TAPS + 1 + SC_TAPS))
            with v.Fori(0, XBC_T) as j:
                v.wait_ge(scaled, j + 1)
                for i in range(1, SSD_TAPS):
                    if i > 1:
                        v.wait_ge(tapped, j * 3 + i - 1)
                    v.scalar_tensor_tensor(out=acc[:, i:], in0=wide(psum, 2, 2)[:, 0:S - i],
                                           scalar=taps[:, ds(j, 1), SSD_TAPS - 1 - i], in1=acc[:, i:],
                                           op0=ALU.mult, op1=ALU.add).then_inc(tapped, 1)
            v.wait_ge(sc_out, SC_T)
            v.wait_ge(made[1], XBC_T)
            for i in range(2):
                v.tensor_tensor(sc[:, i + 2, :], sc[:, i + 2, :], sc[:, i + 4, :], ALU.mult).then_inc(gated, 1)
            for i in range(2):
                v.wait_ge(sc_scaled, i + 1)
                for n in range(1, SC_TAPS):
                    v.scalar_tensor_tensor(out=sc[:, i + 4, n:], in0=sc[:, i + 2, 0:S - n],
                                           scalar=sc_taps[:, i, SC_TAPS - 1 - n:SC_TAPS - n], in1=sc[:, i + 4, n:],
                                           op0=ALU.mult, op1=ALU.add).then_inc(sc_order, 1)
                    v.wait_ge(sc_order, 3 * i + n)
                v.tensor_tensor(feat[:, MLA_T + i, :], sc[:, i + 4, :], sc[:, i, :], ALU.mult).then_inc(sc_order, 1)


def mixers2_stage(nc, bank, ident, a, rows2, xbc, feat, q_t, k_t, values):
    R2 = ROPE // 2
    with Stage(nc, "mixers2") as st:
        w_q, w_kv = st.sb("w_q", [P, Q_LORA // P, MLA_HEADS * QK]), st.sb("w_kv", [P, MLA_HEADS * (NOPE + V_DIM)])
        gains = st.sb("gains", [P, 3])
        incl = st.sb("incl", [P, P])
        inv_freq = st.sb("inv_freq", [P, R2])
        pos_i, pos = st.sb("pos_i", [P, TT], I32), st.sb("pos", [P, TT])
        angle, turns, wrap = (st.sb(n, [P, TT, R2]) for n in ("angle", "turns", "wrap"))
        turns_i = st.sb("turns_i", [P, TT, R2], I32)
        cos, sin = st.sb("cos", [P, TT, R2]), st.sb("sin", [P, TT, R2])
        dt_bias, a_log, d_skip = (st.sb(n, [P, SSD_HEADS]) for n in ("dt_bias", "a_log", "d_skip"))
        dt, dt_raw, soft, a_dt = (st.sb(n, [P, TT, SSD_HEADS]) for n in ("dt", "dt_raw", "soft", "a_dt"))
        ssd_gain = st.sb("ssd_gain", [P, SSD // P])
        junk = st.sb("junk", [P, Q_LORA])
        stats = st.sb("stats", [P, 4, 2])
        latent = st.sb("latent", [P, Q_LORA + KV_LORA])
        latent_t = st.sb("latent_t", [P, 3, P])
        q_row = st.sb("q_row", [P, MLA_HEADS + 1, QK])
        k_row = st.sb("k_row", [P, MLA_HEADS, QK])
        rot = st.sb("rot", [P, 4, MLA_HEADS + 1, R2])
        cur = st.sb("cur", [P, XBC_T, P])
        row = st.sb("row", [P, BANK])
        a_wide, decay, pt = (st.sb(n, [P, SSD_HEADS, P]) for n in ("a_wide", "decay", "pt"))
        run, to_end, run_exp, tile_exp, end_gap = (st.sb(n, [P, SSD_HEADS]) for n in ("run", "to_end", "run_exp", "tile_exp", "end_gap"))
        xdt, xdt_end, state, y, part, silu_z = (st.sb(n, [P, SSD]) for n in ("xdt", "xdt_end", "state", "y", "part", "silu_z"))
        y_stats = st.sb("y_stats", [P, 4])
        names = ("const angle_ready wrapped trig_ready soft_asked soft_ready a_asked rates_ready dve_order pool_order turn_done "
                 "squared mean_ready root_ready latent_ready latent_turned latent_t_ready lifted q_ready k_ready v_ready "
                 "q_rotated k_full heads_turned heads_even heads_odd copied row_turned row_ready a_wide_ready run_made "
                 "run_ready scored gap_ready decay_ready gaps_ready pt_ready xdt_ready y_made state_made silu_ready "
                 "y_mean y_root y_ready y_turned y_out pool_passed").split()
        s = {n: st.sem(n) for n in names}
        block = st.open()
        with_const = [
            (w_q[:], a["mla_w_q_up_2"].rearrange("(k p) n -> p k n", p=P)), (w_kv[:], a["mla_w_kv_up_2"]),
            (gains[:, 0:2], a["mla_q_norm_2"].rearrange("(k p) -> p k", p=P)),
            (gains[:, 2:3], a["mla_kv_norm_2"].rearrange("(k p) -> p k", p=P)),
            (ssd_gain[:], a["ssd_norm_2"].rearrange("(k p) -> p k", p=P)),
            (incl[:], a["c_incl"]), (inv_freq[:], a["c_inv_freq"]),
            (pos_i[:], a["positions_2"].rearrange("(t p) -> p t", p=P)),
            (dt_bias[:], rows(a["ssd_dt_bias_2"], SSD_HEADS)), (a_log[:], rows(a["ssd_a_log_2"], SSD_HEADS)),
            (d_skip[:], rows(a["ssd_d_2"], SSD_HEADS))]

        @block.sync
        def _(sp):
            with nc.allow_non_contiguous_dma("gains and positions, one to a partition"):
                for to, of in with_const:
                    sp.dma_start(to, of).then_inc(s["const"], 16)

        @block.gpsimd
        def _(pool):
            pool.wait_ge(s["trig_ready"], 2)
            with pool.Fori(0, TT) as t:
                steps = [0]

                def link(ins):
                    steps[0] += 1
                    ins.then_inc(s["pool_order"], 1)
                    pool.wait_ge(s["pool_order"], t * 7 + steps[0])
                    pool.sem_inc(s["pool_passed"], 1)

                pool.wait_ge(s["turn_done"], t * 4)
                pool.sem_inc(s["pool_passed"], 1)
                pool.tensor_copy(cur[:], xbc[:, :, ds(t * P, P)]).then_inc(s["copied"], 1)
                link(pool.tensor_copy(q_row[:, MLA_HEADS, NOPE:QK],
                                      rows2[:, ds(t, 1), Q_LORA + KV_LORA:LATENT].rearrange("p a d -> p (a d)")))
                pool.wait_ge(s["q_ready"], t * 2 + 2)
                pool.sem_inc(s["pool_passed"], 1)
                first, second = q_row[:, :, NOPE:NOPE + R2], q_row[:, :, NOPE + R2:QK]
                c, n = (x[:, ds(t, 1), :].to_broadcast([P, MLA_HEADS + 1, R2]) for x in (cos, sin))
                link(pool.tensor_tensor(rot[:, 0], first, c, ALU.mult))
                link(pool.tensor_tensor(rot[:, 1], second, n, ALU.mult))
                link(pool.tensor_tensor(rot[:, 2], second, c, ALU.mult))
                link(pool.tensor_tensor(rot[:, 3], first, n, ALU.mult))
                link(pool.tensor_tensor(first, rot[:, 0], rot[:, 1], ALU.subtract))
                link(pool.tensor_tensor(second, rot[:, 2], rot[:, 3], ALU.add))
                pool.tensor_copy(k_row[:, :, NOPE:QK], q_row[:, MLA_HEADS:MLA_HEADS + 1, NOPE:QK]
                                 .to_broadcast([P, MLA_HEADS, ROPE])).then_inc(s["q_rotated"], 1)
                pool.wait_ge(s["q_rotated"], t + 1)
                pool.wait_ge(s["copied"], t + 1)
                pool.sem_inc(s["turn_done"], 1)

        @block.scalar
        def _(act):
            act.wait_ge(s["const"], 16 * len(with_const))
            act.wait_ge(s["soft_asked"], 1)
            act.activation(soft[:], soft[:], ACT.Exp, scale=-1.0).then_inc(s["soft_ready"], 1)
            act.activation(a_log[:], a_log[:], ACT.Exp).then_inc(s["rates_ready"], 1)
            act.wait_ge(s["soft_ready"], 1)
            act.activation(soft[:], soft[:], ACT.Ln, bias=1.0).then_inc(s["soft_ready"], 1)
            for n, to in enumerate((sin, cos)):
                act.wait_ge(s["angle_ready"], n + 1)
                act.activation(to[:], wrap[:] if n else angle[:], ACT.Sin).then_inc(s["trig_ready"], 1)
            with act.Fori(0, TT) as t:
                act.wait_ge(s["turn_done"], t * 4)
                lat = rows2[:, ds(t, 1), :].rearrange("p a d -> p (a d)")
                act.activation(junk[:], lat[:, 0:Q_LORA], ACT.Square, accum_out=stats[:, 0, 0:1]).then_inc(s["squared"], 1)
                act.wait_ge(s["squared"], t * 2 + 1)
                act.activation(junk[:, 0:KV_LORA], lat[:, Q_LORA:Q_LORA + KV_LORA], ACT.Square,
                               accum_out=stats[:, 0, 1:2]).then_inc(s["squared"], 1)
                act.wait_ge(s["mean_ready"], t * 2 + 2)
                act.activation(stats[:, 2, :], stats[:, 1, :], ACT.Sqrt).then_inc(s["root_ready"], 1)
                act.activation(silu_z[:], lat[:, LATENT:LATENT + SSD], ACT.Silu).then_inc(s["silu_ready"], 1)
                act.wait_ge(s["row_turned"], t + 1)
                act.activation(row[:], bank[5][:], ACT.Copy).then_inc(s["row_ready"], 1)
                act.wait_ge(s["gap_ready"], t + 1)
                act.activation(decay[:], decay[:], ACT.Exp).then_inc(s["decay_ready"], 1)
                act.wait_ge(s["gaps_ready"], t + 1)
                act.activation(to_end[:], end_gap[:], ACT.Exp).then_inc(s["decay_ready"], 1)
                act.activation(run_exp[:], run[:], ACT.Exp).then_inc(s["decay_ready"], 1)
                act.activation(tile_exp[:], three(bank[6][:], SSD_HEADS)[:, :, P - 1], ACT.Exp).then_inc(s["decay_ready"], 1)
                for n in range(2):
                    act.wait_ge(s["lifted"], t * 4 + n + 1)
                    act.activation(q_row[:, 4 * n:4 * n + 4, :], three(bank[1 + n][:, 0:4 * QK], 4), ACT.Copy).then_inc(s["q_ready"], 1)
                for n in range(2):
                    act.wait_ge(s["k_ready"], t * 2 + n + 1)
                    act.activation(values[:, ds(t, 1), 4 * V_DIM * n:4 * V_DIM * (n + 1)].rearrange("p a (h d) -> p (a h) d", d=V_DIM),
                                   three(bank[3 + n][:], 4)[:, :, NOPE:], ACT.Copy).then_inc(s["v_ready"], 1)
                for n, to in enumerate((q_t, k_t)):
                    act.wait_ge(s["heads_turned"], t * 4 + 2 * n + 1)
                    act.activation(to[:, 0:4, ds(t * P, P)], three(bank[1 + 2 * n][0:QK, :], 4), ACT.Copy).then_inc(s["heads_even"], 1)
                act.wait_ge(s["y_mean"], t + 1)
                act.activation(y_stats[:, 2:3], y_stats[:, 1:2], ACT.Sqrt).then_inc(s["y_root"], 1)
                act.wait_ge(s["y_turned"], t + 1)
                for i in range(2):
                    act.activation(feat[:, KT - 2 + i, ds(t * P, P)], bank[7][:, i * P:(i + 1) * P], ACT.Copy,
                                   scale=ssd_gain[:, i:i + 1]).then_inc(s["y_out"], 1)
                act.wait_ge(s["y_out"], t * 2 + 2)
                act.wait_ge(s["heads_even"], t * 2 + 2)
                act.sem_inc(s["turn_done"], 1)

        @block.tensor
        def _(pe):
            pe.wait_ge(s["const"], 16 * len(with_const))
            with pe.Fori(0, TT) as t:
                pe.wait_ge(s["turn_done"], t * 4)
                pe.wait_ge(s["copied"], t + 1)
                for i in range(4):
                    last = pe.transpose(bank[5][:, i * P:(i + 1) * P], cur[:, i, :], ident[:])
                last.then_inc(s["row_turned"], 1)
                for gr in range(SSD_GROUPS):
                    last = pe.matmul(bank[7][:, gr * P:(gr + 1) * P], cur[:, 2 + gr, :], cur[:, 4 + gr, :], start=True, stop=True)
                last.then_inc(s["scored"], 1)
                pe.wait_ge(s["a_wide_ready"], t + 1)
                for h in range(SSD_HEADS):
                    pe.matmul(bank[6][:, h * P:(h + 1) * P], a_wide[:, h, :], incl[:], start=True, stop=True)
                pe.matmul(bank[7][:, 2 * P:2 * P + SSD_HEADS], incl[:], a_dt[:, ds(t, 1), :].rearrange("p a h -> p (a h)"),
                          start=True, stop=True).then_inc(s["run_made"], 1)
                pe.wait_ge(s["latent_ready"], t * 2 + 2)
                for i in range(3):
                    last = pe.transpose(bank[0][:, i * P:(i + 1) * P], latent[:, i * P:(i + 1) * P], ident[:])
                last.then_inc(s["latent_turned"], 1)
                pe.wait_ge(s["latent_t_ready"], t + 1)
                for n in range(2):
                    for k in range(2):
                        last = pe.matmul(bank[1 + n][:, 0:4 * QK], latent_t[:, k, :], w_q[:, k, 4 * QK * n:4 * QK * (n + 1)],
                                         start=(k == 0), stop=(k == 1))
                    last.then_inc(s["lifted"], 1)
                for n in range(2):
                    pe.matmul(bank[3 + n][:], latent_t[:, 2, :], w_kv[:, n * BANK:(n + 1) * BANK], start=True, stop=True)\
                        .then_inc(s["lifted"], 1)
                pe.wait_ge(s["row_ready"], t + 1)
                pe.wait_ge(s["xdt_ready"], t * 2 + 2)
                pe.wait_ge(s["pt_ready"], t + 1)
                for gr in range(SSD_GROUPS):
                    pe.matmul(bank[5][:, gr * P:(gr + 1) * P], cur[:, 4 + gr, :], state[:, gr * P:(gr + 1) * P], start=True, stop=True)
                for h in range(SSD_HEADS):
                    at = h * SSD_HD
                    last = pe.matmul(bank[5][:, SSD + at:SSD + at + SSD_HD], pt[:, h, :], xdt[:, at:at + SSD_HD], start=True, stop=True)
                last.then_inc(s["y_made"], 1)
                pe.wait_ge(s["decay_ready"], t * 4 + 4)
                for gr in range(SSD_GROUPS):
                    last = pe.matmul(bank[6][:, gr * P:(gr + 1) * P], row[:, SSD + gr * P:SSD + (gr + 1) * P],
                                     xdt_end[:, gr * P:(gr + 1) * P], start=True, stop=True)
                last.then_inc(s["state_made"], 1)
                pe.wait_ge(s["q_rotated"], t + 1)
                pe.wait_ge(s["k_ready"], t * 2 + 2)
                pe.wait_ge(s["v_ready"], t * 2 + 2)
                for n in range(4):
                    of = (q_row, k_row)[n // 2]
                    for h in range(4):
                        last = pe.transpose(bank[1 + n][0:QK, h * P:(h + 1) * P], of[:, 4 * (n % 2) + h, :], ident[:])
                    last.then_inc(s["heads_turned"], 1)
                pe.wait_ge(s["y_ready"], t + 1)
                for i in range(2):
                    last = pe.transpose(bank[7][:, i * P:(i + 1) * P], y[:, i * P:(i + 1) * P], ident[:])
                last.then_inc(s["y_turned"], 1)
                pe.wait_ge(s["y_out"], t * 2 + 2)
                pe.sem_inc(s["turn_done"], 1)

        @block.vector
        def _(v):
            BEFORE, PER = 21, 14
            steps = [0]
            base = [0]

            def link(ins):
                steps[0] += 1
                ins.then_inc(s["dve_order"], 1)
                v.wait_ge(s["dve_order"], base[0] + steps[0])

            v.wait_ge(s["const"], 16 * len(with_const))
            link(v.memset(state[:], 0.0))
            link(v.tensor_tensor(dt_raw[:], rows2[:, :, LATENT + SSD:], per_block(dt_bias[:], TT), ALU.add))
            v.scalar_tensor_tensor(out=soft[:], in0=dt_raw[:], scalar=-1.0, in1=dt_raw[:], op0=ALU.mult, op1=ALU.max)\
                .then_inc(s["soft_asked"], 1)
            link(v.tensor_copy(pos[:], pos_i[:]))
            link(v.tensor_tensor(angle[:], per_row(pos[:], R2), per_block(inv_freq[:], TT), ALU.mult))
            link(v.tensor_scalar(turns[:], angle[:], float(1 / (2 * np.pi)), None, ALU.mult))
            link(v.tensor_copy(turns_i[:], turns[:]))
            link(v.tensor_copy(turns[:], turns_i[:]))
            two_pi = 2 * np.pi
            high = float(np.float32(6.28125))
            middle = float(np.float32(np.round((two_pi - high) * 2 ** 21) / 2 ** 21))
            for part_of in (high, middle, float(np.float32(two_pi - high - middle))):
                link(v.scalar_tensor_tensor(out=angle[:], in0=turns[:], scalar=-part_of, in1=angle[:], op0=ALU.mult, op1=ALU.add))

            def keep_within(x):
                link(v.tensor_scalar(turns[:], x, float(np.pi), -two_pi, ALU.is_gt, ALU.mult))
                link(v.tensor_tensor(x, x, turns[:], ALU.add))
                link(v.tensor_scalar(turns[:], x, -float(np.pi), two_pi, ALU.is_lt, ALU.mult))
                link(v.tensor_tensor(x, x, turns[:], ALU.add))
                limit = float(np.nextafter(np.float32(np.pi), np.float32(0)))
                return v.tensor_scalar(x, x, limit, -limit, ALU.min, ALU.max)

            keep_within(angle[:]).then_inc(s["angle_ready"], 1)
            v.wait_ge(s["angle_ready"], 1)
            link(v.tensor_scalar(wrap[:], angle[:], float(np.pi / 2), None, ALU.add))
            keep_within(wrap[:]).then_inc(s["angle_ready"], 1)
            v.wait_ge(s["soft_ready"], 2)
            v.wait_ge(s["rates_ready"], 1)
            link(v.scalar_tensor_tensor(out=dt[:], in0=dt_raw[:], scalar=0.0, in1=soft[:], op0=ALU.max, op1=ALU.add))
            link(v.scalar_tensor_tensor(out=a_dt[:], in0=dt[:], scalar=-1.0, in1=per_block(a_log[:], TT), op0=ALU.mult, op1=ALU.mult))
            assert steps[0] == BEFORE, steps
            with v.Fori(0, TT) as t:
                steps[0] = 0
                base[0] = t * PER + BEFORE
                v.wait_ge(s["turn_done"], t * 4)
                lat = rows2[:, ds(t, 1), :].rearrange("p a d -> p (a d)")
                dt_now = dt[:, ds(t, 1), :].rearrange("p a h -> p (a h)")
                v.tensor_copy(a_wide[:], per_row(a_dt[:, ds(t, 1), :].rearrange("p a h -> p (a h)"), P)).then_inc(s["a_wide_ready"], 1)
                v.wait_ge(s["squared"], t * 2 + 2)
                for i, n in enumerate((Q_LORA, KV_LORA)):
                    v.tensor_scalar(stats[:, 1, i:i + 1], stats[:, 0, i:i + 1], 1.0 / n, EPS, ALU.mult, ALU.add).then_inc(s["mean_ready"], 1)
                v.wait_ge(s["root_ready"], t + 1)
                link(v.reciprocal(stats[:, 3, :], stats[:, 2, :]))
                for i, (lo_, hi) in enumerate(((0, Q_LORA), (Q_LORA, Q_LORA + KV_LORA))):
                    v.tensor_scalar(latent[:, lo_:hi], lat[:, lo_:hi], stats[:, 3, i:i + 1], None, ALU.mult).then_inc(s["latent_ready"], 1)
                v.wait_ge(s["run_made"], t + 1)
                link(v.tensor_copy(run[:], bank[7][:, 2 * P:2 * P + SSD_HEADS]))
                link(v.tensor_tensor(decay[:], three(bank[6][:], SSD_HEADS), per_row(run[:], P), ALU.subtract))
                v.tensor_scalar(decay[:], decay[:], 0.0, None, ALU.min).then_inc(s["gap_ready"], 1)
                v.tensor_tensor(end_gap[:], three(bank[6][:], SSD_HEADS)[:, :, P - 1], run[:], ALU.subtract).then_inc(s["gaps_ready"], 1)
                v.wait_ge(s["latent_turned"], t + 1)
                v.tensor_tensor(latent_t[:], three(bank[0][:, 0:3 * P], 3), per_row(gains[:], P), ALU.mult).then_inc(s["latent_t_ready"], 1)
                v.wait_ge(s["row_ready"], t + 1)
                v.tensor_tensor(three(xdt[:], SSD_HEADS), three(row[:, 0:SSD], SSD_HEADS), per_row(dt_now, SSD_HD), ALU.mult)\
                    .then_inc(s["xdt_ready"], 1)
                v.wait_ge(s["decay_ready"], t * 4 + 4)
                v.wait_ge(s["xdt_ready"], t * 2 + 1)
                v.tensor_tensor(three(xdt_end[:], SSD_HEADS), three(xdt[:], SSD_HEADS), per_row(to_end[:], SSD_HD), ALU.mult)\
                    .then_inc(s["xdt_ready"], 1)
                link(v.tensor_tensor(decay[:], decay[:], per_block(incl[:], SSD_HEADS), ALU.mult))
                for gr in range(SSD_GROUPS):
                    each = SSD_HEADS // SSD_GROUPS
                    ins = v.tensor_tensor(pt[:, gr * each:(gr + 1) * each, :], decay[:, gr * each:(gr + 1) * each, :],
                                          per_block(bank[7][:, gr * P:(gr + 1) * P], each), ALU.mult)
                ins.then_inc(s["pt_ready"], 1)
                for n in range(2):
                    v.wait_ge(s["lifted"], t * 4 + 2 + n + 1)
                    v.tensor_copy(k_row[:, 4 * n:4 * n + 4, 0:NOPE], three(bank[3 + n][:], 4)[:, :, 0:NOPE]).then_inc(s["k_ready"], 1)
                v.wait_ge(s["y_made"], t + 1)
                link(v.tensor_tensor(three(y[:], SSD_HEADS), three(bank[5][:, 0:SSD], SSD_HEADS), per_row(run_exp[:], SSD_HD), ALU.mult))
                link(v.tensor_tensor(y[:], y[:], bank[5][:, SSD:2 * SSD], ALU.add))
                link(v.tensor_tensor(three(part[:], SSD_HEADS), three(row[:, 0:SSD], SSD_HEADS), per_row(d_skip[:], SSD_HD), ALU.mult))
                link(v.tensor_tensor(y[:], y[:], part[:], ALU.add))
                v.wait_ge(s["silu_ready"], t + 1)
                link(v.tensor_tensor(y[:], y[:], silu_z[:], ALU.mult))
                v.wait_ge(s["state_made"], t + 1)
                link(v.tensor_tensor(three(state[:], SSD_HEADS), three(state[:], SSD_HEADS), per_row(tile_exp[:], SSD_HD), ALU.mult))
                link(v.tensor_tensor(state[:], state[:], bank[6][:, 0:SSD], ALU.add))
                link(v.tensor_tensor(part[:], y[:], y[:], ALU.mult))
                link(v.tensor_reduce(y_stats[:, 0:1], part[:], AX_X, ALU.add))
                v.tensor_scalar(y_stats[:, 1:2], y_stats[:, 0:1], 1.0 / SSD, EPS, ALU.mult, ALU.add).then_inc(s["y_mean"], 1)
                v.wait_ge(s["y_root"], t + 1)
                link(v.reciprocal(y_stats[:, 3:4], y_stats[:, 2:3]))
                v.tensor_scalar(y[:], y[:], y_stats[:, 3:4], None, ALU.mult).then_inc(s["y_ready"], 1)
                for n, to in enumerate((q_t, k_t)):
                    v.wait_ge(s["heads_turned"], t * 4 + 2 * n + 2)
                    v.tensor_copy(to[:, 4:8, ds(t * P, P)], three(bank[2 + 2 * n][0:QK, :], 4)).then_inc(s["heads_odd"], 1)
                v.wait_ge(s["heads_odd"], t * 2 + 2)
                v.wait_ge(s["y_ready"], t + 1)
                assert steps[0] == PER, steps
                v.sem_inc(s["turn_done"], 1)


def attention_stage(nc, psum, bank, ident, a, q_t, k_t, values, feat):
    scale = QK ** -0.5
    TURNS = MLA_HEADS // 2
    N = 2 * TT
    with Stage(nc, "attention") as st:
        q_now = [st.sb(f"q_now{u}", [QK, S]) for u in range(2)]
        future = st.sb("future", [P, P])
        p = [st.sb(f"p{b}", [P, S]) for b in range(2)]
        p_t = [st.sb(f"p_t{b}", [P, TT, P]) for b in range(2)]
        most, bias, total, share = ([st.sb(f"{n}{b}", [P, 1]) for b in range(2)] for n in ("most", "bias", "total", "share"))
        out = st.sb("out", [P, TT, MLA_HEADS * V_DIM])
        const = st.sem("const")
        q_copied, scored = ([st.sem(f"{n}{u}") for u in range(2)] for n in ("q_copied", "scored"))
        pool_passed = st.sem("pool_passed")
        masked, most_ready, bias_ready, exp_ready, turned, low_ready, high_ready, made, share_ready, out_ready = (
            st.sem(n) for n in ("masked", "most_ready", "bias_ready", "exp_ready", "turned", "low_ready",
                                "high_ready", "made", "share_ready", "out_ready"))
        out_turned, even_out, odd_out = st.sem("out_turned"), st.sem("even_out"), st.sem("odd_out")
        block = st.open()

        @block.sync
        def _(sp):
            sp.dma_start(future[:], a["c_future"]).then_inc(const, 16)

        @block.gpsimd
        def _(pool):
            with pool.Fori(0, TURNS) as j:
                for u in range(2):
                    pool.wait_ge(scored[u], j * TT)
                    pool.sem_inc(pool_passed, 1)
                    pool.tensor_copy(q_now[u][:], q_t[:, ds(j * 2 + u, 1), :].rearrange("p a s -> p (a s)")).then_inc(q_copied[u], 1)

        @block.tensor
        def _(pe):
            def scores(j, m):
                u, i = m // TT, m % TT
                if i == 0:
                    pe.wait_ge(q_copied[u], j + 1)
                pe.wait_ge(exp_ready, j * N + max(m - 1, 0))
                for n in range(i // 4 + 1):
                    width = min(BANK, (i + 1) * P - n * BANK)
                    last = pe.matmul(bank[2 * (m % 2) + n][:, 0:width], q_now[u][:, i * P:(i + 1) * P],
                                     k_t[:, ds(j * 2 + u, 1), n * BANK:n * BANK + width].rearrange("p a s -> p (a s)"),
                                     start=True, stop=True)
                last.then_inc(scored[u], 1)

            def turn(j, m):
                pe.wait_ge(exp_ready, j * N + m + 1)
                pe.wait_ge(low_ready, j * N + m)
                pe.wait_ge(high_ready, j * N + m)
                i = m % TT
                for b in range(i + 1):
                    last = pe.transpose(bank[4 + b // 4][:, (b % 4) * P:(b % 4 + 1) * P], p[m % 2][:, b * P:(b + 1) * P], ident[:])
                last.then_inc(turned, 1)

            def weigh(j, m):
                u, i = m // TT, m % TT
                pe.wait_ge(low_ready, j * N + m + 1)
                pe.wait_ge(high_ready, j * N + m + 1)
                pe.wait_ge(out_ready, j * N + max(m - 1, 0))
                for b in range(i + 1):
                    last = pe.matmul(bank[6 + m % 2][:, 0:V_DIM], p_t[m % 2][:, b, :],
                                     values[:, b, ds((j * 2 + u) * V_DIM, V_DIM)], start=(b == 0), stop=(b == i))
                last.then_inc(made, 1)

            with pe.Fori(0, TURNS) as j:
                scores(j, 0)
                for m in range(N):
                    if m + 1 < N:
                        scores(j, m + 1)
                    turn(j, m)
                    if m >= 1:
                        weigh(j, m - 1)
                weigh(j, N - 1)
            pe.wait_ge(out_ready, TURNS * N)
            for t in range(TT):
                for k in range(MLA_T):
                    last = pe.transpose(bank[t][:, k * P:(k + 1) * P], out[:, t, k * P:(k + 1) * P], ident[:])
                last.then_inc(out_turned, 1)

        @block.scalar
        def _(act):
            with act.Fori(0, TURNS) as j:
                for m in range(N):
                    i, b = m % TT, m % 2
                    act.wait_ge(bias_ready, j * N + m + 1)
                    act.wait_ge(turned, j * N + max(m - 1, 0))
                    act.wait_ge(share_ready, j * N + max(m - 1, 0))
                    act.activation(p[b][:, 0:(i + 1) * P], wide(psum, 2 * b, 2)[:, 0:(i + 1) * P], ACT.Exp, bias=bias[b][:, 0:1],
                                   scale=scale, accum_out=total[b][:]).then_inc(exp_ready, 1)
                    act.wait_ge(turned, j * N + m + 1)
                    act.wait_ge(made, j * N + max(m - 1, 0))
                    low = min(i + 1, 4)
                    act.activation(p_t[b][:, 0:low, :], three(bank[4][:, 0:low * P], low), ACT.Copy).then_inc(low_ready, 1)
            for t in range(0, TT, 2):
                act.wait_ge(out_turned, t + 1)
                act.activation(feat[:, 0:MLA_T, t * P:(t + 1) * P], three(bank[t][:], MLA_T), ACT.Copy).then_inc(even_out, 1)
            act.wait_ge(even_out, TT // 2)

        @block.vector
        def _(v):
            def bound(j, m):
                i, b = m % TT, m % 2
                at = wide(psum, 2 * b, 2)
                v.wait_ge(scored[m // TT], j * TT + i + 1)
                v.tensor_tensor(at[:, i * P:(i + 1) * P], at[:, i * P:(i + 1) * P], future[:], ALU.add).then_inc(masked, 1)
                v.wait_ge(masked, j * N + m + 1)
                v.wait_ge(bias_ready, j * N + max(m - 1, 0))
                v.tensor_reduce(most[b][:], at[:, 0:(i + 1) * P], AX_X, ALU.max).then_inc(most_ready, 1)
                v.wait_ge(most_ready, j * N + m + 1)
                v.wait_ge(exp_ready, j * N + max(m - 1, 0))
                v.tensor_scalar(bias[b][:], most[b][:], -scale, None, ALU.mult).then_inc(bias_ready, 1)

            def high(j, m):
                i, b = m % TT, m % 2
                v.wait_ge(turned, j * N + m + 1)
                v.wait_ge(made, j * N + max(m - 1, 0))
                if i >= 4:
                    v.tensor_copy(p_t[b][:, 4:i + 1, :], three(bank[5][:, 0:(i - 3) * P], i - 3)).then_inc(high_ready, 1)
                else:
                    v.sem_inc(high_ready, 1)

            def finish(j, m):
                u, i, b = m // TT, m % TT, m % 2
                v.wait_ge(exp_ready, j * N + m + 1)
                v.wait_ge(out_ready, j * N + max(m - 1, 0))
                v.reciprocal(share[b][:], total[b][:]).then_inc(share_ready, 1)
                v.wait_ge(share_ready, j * N + m + 1)
                v.wait_ge(made, j * N + m + 1)
                v.tensor_scalar(out[:, i, ds((j * 2 + u) * V_DIM, V_DIM)], bank[6 + b][:, 0:V_DIM], share[b][:, 0:1], None,
                                ALU.mult).then_inc(out_ready, 1)

            v.wait_ge(const, 16)
            with v.Fori(0, TURNS) as j:
                bound(j, 0)
                for m in range(N):
                    if m + 1 < N:
                        bound(j, m + 1)
                    high(j, m)
                    if m >= 1:
                        finish(j, m - 1)
                finish(j, N - 1)
            for t in range(1, TT, 2):
                v.wait_ge(out_turned, t + 1)
                v.tensor_copy(feat[:, 0:MLA_T, t * P:(t + 1) * P], three(bank[t][:], MLA_T)).then_inc(odd_out, 1)
            v.wait_ge(odd_out, TT // 2)


FFN = 2816
FFN_T = FFN // P
FFN_TAPS = 3


def ffn_up_stage(nc, psum, bank, ident, a, feat, hidden):
    with Stage(nc, "ffn_up") as st:
        tap_rows = st.sb("tap_rows", [2 * FFN_T, FFN_TAPS + 1, P])
        taps = st.sb("taps", [P, FFN_TAPS + 1, 2 * FFN_T])
        w = [[st.sb(f"w{c}{u}", [P, KT, P]) for u in range(2)] for c in range(2)]
        acc = [[st.sb(f"acc{c}{u}", [P, S]) for u in range(2)] for c in range(2)]
        taps_loaded, taps_turned, taps_ready = st.sem("taps_loaded"), st.sem("taps_turned"), st.sem("taps_ready")
        loaded, made, scaled, tapped = ([[st.sem(f"{n}{c}{u}") for u in range(2)] for c in range(2)]
                                        for n in ("loaded", "made", "scaled", "tapped"))
        silu_ready, hidden_ready = ([st.sem(f"{n}{u}") for u in range(2)] for n in ("silu_ready", "hidden_ready"))
        block = st.open()
        last_tap = FFN_TAPS - 1

        @block.sync
        def _(sp):
            sp.dma_start(tap_rows[:, 0:FFN_TAPS, :], a["ffn_conv_w_2"].rearrange("i (c p) -> c i p", p=P)).then_inc(taps_loaded, 16)
            sp.dma_start(tap_rows[:, FFN_TAPS, :], a["ffn_conv_b_2"].rearrange("(c p) -> c p", p=P)).then_inc(taps_loaded, 16)
            with sp.Fori(0, FFN_T // 2) as j:
                for u in range(2):
                    for c in range(2):
                        sp.wait_ge(made[c][u], j)
                        sp.dma_start(w[c][u][:], a["ffn_w_up_2"][:, ds((j * 2 + u) * P + c * FFN, P)]
                                     .rearrange("(k p) n -> p k n", p=P)).then_inc(loaded[c][u], 16)

        @block.tensor
        def _(pe):
            pe.wait_ge(taps_loaded, 32)
            n = 2 * FFN_T
            for i in range(FFN_TAPS + 1):
                last = pe.transpose(bank[0][:, i * n:(i + 1) * n], tap_rows[:, i, :], ident[0:n, 0:n])
            last.then_inc(taps_turned, 1)
            pe.wait_ge(taps_ready, 1)
            with pe.Fori(0, FFN_T // 2) as j:
                for u in range(2):
                    for c in range(2):
                        pe.wait_ge(loaded[c][u], j * 16 + 16)
                        pe.wait_ge(tapped[c][u], j * last_tap)
                        for h in range(2):
                            for k in range(KT):
                                last = pe.matmul(bank[4 * u + 2 * c + h][:], w[c][u][:, k, :], feat[:, k, h * BANK:(h + 1) * BANK],
                                                 start=(k == 0), stop=(k == KT - 1))
                        last.then_inc(made[c][u], 1)

        @block.scalar
        def _(act):
            act.wait_ge(taps_turned, 1)
            act.activation(taps[:], three(bank[0][:, 0:(FFN_TAPS + 1) * 2 * FFN_T], FFN_TAPS + 1), ACT.Copy).then_inc(taps_ready, 1)
            act.wait_ge(taps_ready, 1)
            with act.Fori(0, FFN_T // 2) as j:
                for u in range(2):
                    for c in range(2):
                        at = j * 2 + u + c * FFN_T
                        act.wait_ge(made[c][u], j + 1)
                        act.wait_ge(hidden_ready[u], j)
                        act.activation(acc[c][u][:], wide(psum, 4 * u + 2 * c, 2), ACT.Identity, scale=taps[:, last_tap, ds(at, 1)],
                                       bias=taps[:, FFN_TAPS, ds(at, 1)]).then_inc(scaled[c][u], 1)
                    act.wait_ge(tapped[0][u], j * last_tap + last_tap)
                    act.activation(acc[0][u][:], acc[0][u][:], ACT.Silu).then_inc(silu_ready[u], 1)

        @block.vector
        def _(v):
            v.wait_ge(taps_ready, 1)
            with v.Fori(0, FFN_T // 2) as j:
                for u in range(2):
                    for c in range(2):
                        at = j * 2 + u + c * FFN_T
                        v.wait_ge(scaled[c][u], j + 1)
                        for i in range(1, FFN_TAPS):
                            v.wait_ge(tapped[c][u], j * last_tap + i - 1)
                            v.scalar_tensor_tensor(out=acc[c][u][:, i:], in0=wide(psum, 4 * u + 2 * c, 2)[:, 0:S - i],
                                                   scalar=taps[:, last_tap - i, ds(at, 1)], in1=acc[c][u][:, i:],
                                                   op0=ALU.mult, op1=ALU.add).then_inc(tapped[c][u], 1)
                    v.wait_ge(silu_ready[u], j + 1)
                    v.wait_ge(tapped[1][u], j * last_tap + last_tap)
                    v.tensor_tensor(hidden[:, ds(j * 2 + u, 1), :].rearrange("p a s -> p (a s)"), acc[0][u][:], acc[1][u][:],
                                    ALU.mult).then_inc(hidden_ready[u], 1)


def ffn_down_stage(nc, bank, a, hidden, y):
    width = D // 4
    with Stage(nc, "ffn_down") as st:
        w = [st.sb(f"w{u}", [P, FFN_T, width]) for u in range(2)]
        loaded = [st.sem(f"loaded{u}") for u in range(2)]
        product, even_out, odd_out = st.sem("product"), st.sem("even_out"), st.sem("odd_out")
        block = st.open()

        @block.sync
        def _(sp):
            with sp.Fori(0, 2) as j:
                for u in range(2):
                    sp.wait_ge(odd_out, j * 8 + u * 4)
                    sp.dma_start(w[u][:], a["ffn_w_down_2"][:, ds((j * 2 + u) * width, width)]
                                 .rearrange("(k p) n -> p k n", p=P)).then_inc(loaded[u], 16)

        @block.tensor
        def _(pe):
            with pe.Fori(0, 2) as j:
                for u in range(2):
                    b = j * 2 + u
                    pe.wait_ge(loaded[u], j * 16 + 16)
                    for t in range(TT):
                        pe.wait_ge((even_out, odd_out)[t % 2], b * 4 + t // 2 + 1)
                        for k in range(FFN_T):
                            last = pe.matmul(bank[t][:, 0:width], hidden[:, k, t * P:(t + 1) * P], w[u][:, k, :],
                                             start=(k == 0), stop=(k == FFN_T - 1))
                        last.then_inc(product, 1)

        @block.scalar
        def _(act):
            act.sem_inc(even_out, 4)
            with act.Fori(0, 4) as b:
                for t in range(0, TT, 2):
                    act.wait_ge(product, b * TT + t + 1)
                    act.activation(y[:, t, ds(b * width, width)], bank[t][:, 0:width], ACT.Copy).then_inc(even_out, 1)

        @block.vector
        def _(v):
            v.sem_inc(odd_out, 4)
            with v.Fori(0, 4) as b:
                for t in range(1, TT, 2):
                    v.wait_ge(product, b * TT + t + 1)
                    v.tensor_copy(y[:, t, ds(b * width, width)], bank[t][:, 0:width]).then_inc(odd_out, 1)


def finish_stage(nc, x, y, gain_dram, out):
    with Stage(nc, "finish") as st:
        gain = st.sb("gain", [P, D])
        junk = [st.sb(f"junk{u}", [P, D]) for u in range(2)]
        square, mean, root, rstd = ([st.sb(f"{n}{u}", [P, 1]) for u in range(2)] for n in ("square", "mean", "root", "rstd"))
        gain_loaded, stored = st.sem("gain_loaded"), st.sem("stored")
        squared, mean_ready, root_ready, rstd_ready, scaled, added = (
            [st.sem(f"{n}{u}") for u in range(2)] for n in ("squared", "mean_ready", "root_ready", "rstd_ready", "scaled", "added"))
        block = st.open()

        def tile(ap, t):
            return ap[:, ds(t, 1), :].rearrange("p a d -> p (a d)")

        @block.sync
        def _(sp):
            sp.dma_start(gain[:], rows(gain_dram, D)).then_inc(gain_loaded, 16)
            with sp.Fori(0, TT // 2) as j:
                for u in range(2):
                    sp.wait_ge(added[u], j + 1)
                    sp.dma_start(out[ds((j * 2 + u) * P, P), :], tile(x, j * 2 + u)).then_inc(stored, 16)
            sp.wait_ge(stored, 16 * TT)

        @block.scalar
        def _(act):
            with act.Fori(0, TT // 2) as j:
                for u in range(2):
                    act.wait_ge(mean_ready[u], j)
                    act.activation(junk[u][:], tile(y, j * 2 + u), ACT.Square, accum_out=square[u][:]).then_inc(squared[u], 1)
                for u in range(2):
                    act.wait_ge(mean_ready[u], j + 1)
                    act.wait_ge(rstd_ready[u], j)
                    act.activation(root[u][:], mean[u][:], ACT.Sqrt).then_inc(root_ready[u], 1)

        @block.vector
        def _(v):
            v.wait_ge(gain_loaded, 16)
            with v.Fori(0, TT // 2) as j:
                for u in range(2):
                    v.wait_ge(squared[u], j + 1)
                    v.wait_ge(root_ready[u], j)
                    v.tensor_scalar(mean[u][:], square[u][:], 1.0 / D, EPS, ALU.mult, ALU.add).then_inc(mean_ready[u], 1)
                for u in range(2):
                    t = j * 2 + u
                    v.wait_ge(root_ready[u], j + 1)
                    v.wait_ge(scaled[u], j)
                    v.reciprocal(rstd[u][:], root[u][:]).then_inc(rstd_ready[u], 1)
                    v.wait_ge(rstd_ready[u], j + 1)
                    v.scalar_tensor_tensor(out=tile(y, t), in0=tile(y, t), scalar=rstd[u][:, 0:1], in1=gain[:], op0=ALU.mult,
                                           op1=ALU.mult).then_inc(scaled[u], 1)
                    v.wait_ge(scaled[u], j + 1)
                    v.tensor_tensor(tile(x, t), tile(x, t), tile(y, t), ALU.add).then_inc(added[u], 1)


def program(nc, a, out):
    with ExitStack() as ctx:
        def sb(name, shape, dt=F32):
            return ctx.enter_context(nc.sbuf_tensor(name, shape, dt))

        psum = ctx.enter_context(nc.psum_tensor("psum", [P, 8, BANK], F32))
        bank = [psum[:, i, :] for i in range(8)]
        ident = sb("ident", [P, P])
        proj = nc.dram_tensor("proj", [S + 1, IN_COLS], F32).ap()
        h_rows = nc.dram_tensor("h_rows", [S, D], F32).ap()
        y_rows = nc.dram_tensor("y_rows", [SLOT_BLOCKS * P, D], F32).ap()
        feat = sb("feat", [P, KT, S])
        with nc.sbuf_tensor("x_rows", [P, TT, D], F32) as x:
            load_stage(nc, x, ident, a["x"], a["c_ident"], proj[0:1, :])
            norm_stage(nc, "norm1", bank, ident, x, a["norm1_gain"], feat)
        project_stage(nc, "project", bank, feat, a["w_in"], 480, IN_COLS // 480, proj[1:S + 1, :], y_rows[EXPERTS * P:, :])
        mix_stage(nc, bank, ident, a, proj, feat)
        x2_dram = nc.dram_tensor("x2_rows", [S, D], F32).ap()
        with ExitStack() as first:
            def sb1(name, shape, dt=F32):
                return first.enter_context(nc.sbuf_tensor(name, shape, dt))

            x = sb1("h", [P, TT, D])
            add_product_stage(nc, "out1", bank, feat, a["w_out"], x, x_dram=a["x"])
            token_ids = sb1("token_ids", [P, TT], I32)
            slot_weight = sb1("slot_weight", [P, 2, TT])
            slot_index = sb1("slot_index", [P, 2, TT], I32)
            more = sb1("more", [1, 2, MORE_BLOCKS], I32)
            slot_token = nc.dram_tensor("slot_token", [SLOT_BLOCKS * P, 1], I32).ap()
            norm_stage(nc, "norm2", bank, ident, x, a["norm2_gain"], feat, h_rows)
            route_stage(nc, bank, a, feat, token_ids, slot_weight, slot_index, more, slot_token)
            expert_stage(nc, bank, ident, a, more, slot_token, h_rows, y_rows)
            combine_stage(nc, x, y_rows, slot_index, slot_weight, a["final_norm_gain"], x2_dram)
            norm_stage(nc, "norm3", bank, ident, x, a["norm_mix_pre_2"], feat)
        second_block(nc, a, out, psum, bank, ident, feat, x2_dram)


def second_block(nc, a, out, psum, bank, ident, feat, x2_dram):
    with ExitStack() as ctx:
        def sb(name, shape, dt=F32):
            return ctx.enter_context(nc.sbuf_tensor(name, shape, dt))

        rows2, xbc = sb("rows2", [P, TT, TM_COLS]), sb("xbc", [P, XBC_T, S])
        project2_stage(nc, psum, bank, feat, a, rows2, xbc)
        q_t, k_t = sb("q_t", [QK, MLA_HEADS, S]), sb("k_t", [QK, MLA_HEADS, S])
        values = sb("values", [P, TT, MLA_HEADS * V_DIM])
        mixers2_stage(nc, bank, ident, a, rows2, xbc, feat, q_t, k_t, values)
        attention_stage(nc, psum, bank, ident, a, q_t, k_t, values, feat)
    with ExitStack() as ctx:
        x = ctx.enter_context(nc.sbuf_tensor("x2", [P, TT, D], F32))
        add_product_stage(nc, "out2", bank, feat, a["w_out_2"], x, x2_dram, a["norm_mix_post_2"])
        norm_stage(nc, "norm4", bank, ident, x, a["norm_ffn_pre_2"], feat)
        hidden = ctx.enter_context(nc.sbuf_tensor("hidden", [P, FFN_T, S], F32))
        ffn_up_stage(nc, psum, bank, ident, a, feat, hidden)
        ffn_down_stage(nc, bank, a, hidden, feat)
        finish_stage(nc, x, feat, a["norm_ffn_post_2"], out)


def kernel(**inputs):
    import concourse.bacc as bacc
    from concourse import mybir as types
    from concourse.bass_utils import run_bass_kernel_spmd

    nc = bacc.Bacc("TRN2", target_bir_lowering=False, num_devices=1)
    arrays, args = {}, {}
    for name, value in lay_out(inputs).items():
        arrays[f"in_{name}_dram"] = value
        args[name] = nc.dram_tensor(f"in_{name}_dram", value.shape, types.dt.from_np(value.dtype), kind="ExternalInput").ap()
    out = nc.dram_tensor("out_0_dram", [S, D], types.dt.float32, kind="ExternalOutput").ap()
    program(nc, args, out)
    r = run_bass_kernel_spmd(nc, [arrays], core_ids=[0])
    return r.results[0]["out_0_dram"].reshape(1, S, D)
```

```python
from contextlib import ExitStack

import concourse.bass as bass
import numpy as np
from concourse import mybir

F32 = mybir.dt.float32
F32R = mybir.dt.float32r
I32 = mybir.dt.int32
U32 = mybir.dt.uint32
ALU = mybir.AluOpType
ACT = mybir.ActivationFunctionType
AX_X = mybir.AxisListType.X
ds = bass.ds

P = 128
D = 1024
S = 1024
KT = D // P
TT = S // P
BANK = 512
EPS = 1e-6

RET_W = 512
RET_HEADS = 4
RET_D = RET_W // RET_HEADS
RET_CHUNK = 64
RW_W = 512
RW_HEADS = 8
RW_N = RW_W // RW_HEADS
LORA = 64
RW_COLS = 3 * RW_W + 2 * LORA + 128
IN_COLS = 4 * RET_W + RW_COLS
RET_GN_EPS = 1e-5
RW_GN_EPS = 64e-5
DECAY = -float(np.exp(-0.5))
SOLVE_STEPS = (2, 4, 8, 16, 32, 64)


def overlay(nc, *tensors):
    with ExitStack() as ctx:
        return [ctx.enter_context(nc.sbuf_tensor(name, shape, dt)) for name, shape, dt in tensors]


class Stage:

    def __init__(self, nc, name):
        self.nc, self.name, self.sems, self.ctx = nc, name, [], ExitStack()

    def __enter__(self):
        self.block_ctx = self.nc.Block()
        self.block = None
        return self

    def open(self):
        self.block = self.block_ctx.__enter__()
        return self.block

    def sem(self, name):
        s = self.nc.alloc_semaphore(name=f"{self.name}_{name}")
        self.sems.append(s)
        return s

    def sb(self, name, shape, dt=F32):
        return self.ctx.enter_context(self.nc.sbuf_tensor(f"{self.name}_{name}", shape, dt))

    def twin(self, name, shape):
        plain, = overlay(self.nc, (f"{self.name}_{name}", shape, F32))
        return plain, self.sb(f"{name}_low", shape, F32R)

    def __exit__(self, *error):
        if error[0] is None:
            self.block_ctx.__exit__(None, None, None)
            self.nc.clear_and_free_semaphores(self.sems)
            self.nc.all_engine_barrier()
        self.ctx.close()


def rows(dram, cols):
    return dram.rearrange("(a n) -> a n", a=1)[:, 0:cols].partition_broadcast(P)


def flat(ap):
    return ap.rearrange("p a b -> p (a b)")


def three(ap, a):
    return ap.rearrange("p (a b) -> p a b", a=a)


def per_row(ap, n):
    return ap.unsqueeze(2).to_broadcast([ap.shape[0], ap.shape[1], n])


def per_block(ap, n):
    return ap.unsqueeze(1).to_broadcast([ap.shape[0], n, ap.shape[1]])


def split_high(act, high, x):
    return act.activation(high, x, ACT.Copy)


def split_low(v, low, x, high):
    return v.tensor_tensor(low, x, high, ALU.subtract)


def three_passes(pe, out, left, right, start, stop):
    pe.matmul(out, left[0], right[0], start=start, stop=False)
    pe.matmul(out, left[0], right[1], start=False, stop=False)
    return pe.matmul(out, left[1], right[0], start=False, stop=stop)


def load_stage(nc, x, ident, x_dram, ident_dram, zero_row_of):
    with Stage(nc, "load") as st:
        zeros = st.sb("zeros", [1, IN_COLS])
        loaded, zeroed, cleared = st.sem("loaded"), st.sem("zeroed"), st.sem("cleared")
        block = st.open()

        @block.sync
        def _(sp):
            sp.dma_start(x[:], x_dram.rearrange("(t p) d -> p t d", p=P)).then_inc(loaded, 16)
            sp.dma_start(ident[:], ident_dram).then_inc(loaded, 16)
            sp.wait_ge(zeroed, 1)
            sp.dma_start(zero_row_of, zeros[0:1, 0:zero_row_of.shape[1]]).then_inc(cleared, 16)
            sp.wait_ge(cleared, 16)
            sp.wait_ge(loaded, 32)

        @block.vector
        def _(v):
            v.memset(zeros[:], 0.0).then_inc(zeroed, 1)


def norm_stage(nc, name, bank, ident, x, gain_dram, out, rows_dram=None, low=None):
    with Stage(nc, name) as st:
        gain = st.sb("gain", [P, KT])
        junk = [st.sb(f"junk{u}", [P, D]) for u in range(2)]
        square = [st.sb(f"square{u}", [P, 1]) for u in range(2)]
        mean = [st.sb(f"mean{u}", [P, 1]) for u in range(2)]
        rstd = [st.sb(f"rstd{u}", [P, 1]) for u in range(2)]
        root = [st.sb(f"root{u}", [P, 1]) for u in range(2)]
        xs = [st.sb(f"xs{u}", [P, D]) for u in range(2)]
        gain_loaded = st.sem("gain_loaded")
        squared = [st.sem(f"squared{u}") for u in range(2)]
        mean_ready = [st.sem(f"mean_ready{u}") for u in range(2)]
        root_ready = [st.sem(f"root_ready{u}") for u in range(2)]
        rstd_ready = [st.sem(f"rstd_ready{u}") for u in range(2)]
        xs_ready = [st.sem(f"xs_ready{u}") for u in range(2)]
        turned = [st.sem(f"turned{u}") for u in range(2)]
        low_out = [st.sem(f"low_out{u}") for u in range(2)]
        high_out = [st.sem(f"high_out{u}") for u in range(2)]
        first_out = [st.sem(f"first_out{u}") for u in range(2)]
        stored = [st.sem(f"stored{u}") for u in range(2)]
        block = st.open()

        @block.sync
        def _(sp):
            sp.dma_start(gain[:], gain_dram.rearrange("(k p) -> p k", p=P),
                         allow_slow_non_contiguous=True).then_inc(gain_loaded, 16)
            if rows_dram is not None:
                with sp.Fori(0, TT // 2) as j:
                    for u in range(2):
                        sp.wait_ge(xs_ready[u], j + 1)
                        sp.dma_start(rows_dram[ds((j * 2 + u) * P, P), :], xs[u][:]).then_inc(stored[u], 16)
                for u in range(2):
                    sp.wait_ge(stored[u], 16 * (TT // 2))

        @block.scalar
        def _(act):
            act.wait_ge(gain_loaded, 16)
            with act.Fori(0, TT // 2) as j:
                for u in range(2):
                    t = j * 2 + u
                    act.wait_ge(mean_ready[u], j)
                    act.activation(junk[u][:], x[:, ds(t, 1), :].rearrange("p a d -> p (a d)"), ACT.Square,
                                   accum_out=square[u][:]).then_inc(squared[u], 1)
                for u in range(2):
                    act.wait_ge(mean_ready[u], j + 1)
                    act.wait_ge(xs_ready[u], j)
                    act.activation(root[u][:], mean[u][:], ACT.Sqrt).then_inc(root_ready[u], 1)
                for u in range(2):
                    t = j * 2 + u
                    act.wait_ge(turned[u], j + 1)
                    for k in range(0 if low is not None else 4, 8):
                        to = out[:, k, ds(t * P, P)]
                        last = act.activation(to, bank[2 * u + k // 4][:, (k % 4) * P:(k % 4 + 1) * P],
                                              ACT.Copy, scale=gain[:, k:k + 1])
                        if k == 3:
                            last.then_inc(first_out[u], 1)
                    last.then_inc(high_out[u], 1)

        @block.vector
        def _(v):
            v.wait_ge(gain_loaded, 16)
            with v.Fori(0, TT // 2) as j:
                for u in range(2):
                    t = j * 2 + u
                    v.wait_ge(squared[u], j + 1)
                    v.wait_ge(root_ready[u], j)
                    v.tensor_scalar(mean[u][:], square[u][:], 1.0 / D, EPS, ALU.mult, ALU.add).then_inc(mean_ready[u], 1)
                    v.wait_ge(root_ready[u], j + 1)
                    v.reciprocal(rstd[u][:], root[u][:]).then_inc(rstd_ready[u], 1)
                    v.wait_ge(rstd_ready[u], j + 1)
                    v.wait_ge(turned[u], j)
                    if rows_dram is not None:
                        v.wait_ge(stored[u], j * 16)
                    v.tensor_scalar(xs[u][:], x[:, ds(t, 1), :].rearrange("p a d -> p (a d)"), rstd[u][:, 0:1], None,
                                    ALU.mult).then_inc(xs_ready[u], 1)
                for u in range(2):
                    t = j * 2 + u
                    if low is not None:
                        for k in range(KT):
                            if k % 4 == 0:
                                v.wait_ge((first_out, high_out)[k // 4][u], j + 1)
                            last = v.scalar_tensor_tensor(
                                out=low[:, k, ds(t * P, P)], in0=bank[2 * u + k // 4][:, (k % 4) * P:(k % 4 + 1) * P],
                                scalar=gain[:, k:k + 1], in1=out[:, k, ds(t * P, P)], op0=ALU.mult, op1=ALU.subtract)
                        last.then_inc(low_out[u], 1)
                        continue
                    v.wait_ge(turned[u], j + 1)
                    v.tensor_tensor(out[:, 0:4, ds(t * P, P)], three(bank[2 * u][:], 4), per_row(gain[:, 0:4], P),
                                    ALU.mult).then_inc(low_out[u], 1)

        @block.tensor
        def _(pe):
            with pe.Fori(0, TT // 2) as j:
                for u in range(2):
                    pe.wait_ge(xs_ready[u], j + 1)
                    pe.wait_ge(low_out[u], j)
                    pe.wait_ge(high_out[u], j)
                    for k in range(KT):
                        last = pe.transpose(bank[2 * u + k // 4][:, (k % 4) * P:(k % 4 + 1) * P],
                                            xs[u][:, k * P:(k + 1) * P], ident[:])
                    last.then_inc(turned[u], 1)


def project_stage(nc, name, bank, feat, low, w_dram, width, blocks, out_dram, idle_rows):
    half = blocks // 2
    with Stage(nc, name) as st:
        w, w_low = zip(*(st.twin(f"w{u}", [P, KT, width]) for u in range(2)))
        w_high = [st.sb(f"w_high{u}", [P, KT, width], F32R) for u in range(2)]
        out = [st.sb(f"out{u}", [P, TT, width]) for u in range(2)]
        w_loaded = [st.sem(f"w_loaded{u}") for u in range(2)]
        high_ready = [st.sem(f"high_ready{u}") for u in range(2)]
        low_ready = [st.sem(f"low_ready{u}") for u in range(2)]
        stored = [st.sem(f"stored{u}") for u in range(2)]
        product = st.sem("product")
        even_out, odd_out = st.sem("even_out"), st.sem("odd_out")
        zeros = st.sb("zeros", [P, D])
        zeroed, cleared = st.sem("zeroed"), st.sem("cleared")
        block = st.open()

        @block.gpsimd
        def _(pool):
            pool.memset(zeros[:], 0.0).then_inc(zeroed, 1)
            pool.wait_ge(zeroed, 1)
            pool.dma_start(idle_rows.rearrange("(b p) d -> p b d", p=P),
                           per_block(zeros[:], idle_rows.shape[0] // P)).then_inc(cleared, 16)

        @block.sync
        def _(sp):
            with sp.Fori(0, half) as j:
                for u in range(2):
                    sp.wait_ge(odd_out, j * 8 + u * 4)
                    sp.dma_start(w[u][:], w_dram[:, ds((j * 2 + u) * width, width)]
                                 .rearrange("(k p) n -> p k n", p=P)).then_inc(w_loaded[u], 16)
            sp.wait_ge(cleared, 16)

        @block.tensor
        def _(pe):
            with pe.Fori(0, half) as j:
                for u in range(2):
                    b = j * 2 + u
                    pe.wait_ge(low_ready[u], j + 1)
                    for t in range(TT):
                        tile = slice(t * P, (t + 1) * P)
                        if t % 2 == 0:
                            pe.wait_ge(even_out, b * 4 + t // 2 + 1)
                        else:
                            pe.wait_ge(odd_out, b * 4 + t // 2 + 1)
                        for k in range(KT):
                            last = three_passes(pe, bank[t][:, 0:width], (feat[:, k, tile], low[:, k, tile]),
                                                (w_high[u][:, k, :], w_low[u][:, k, :]), start=(k == 0), stop=(k == KT - 1))
                        last.then_inc(product, 1)

        @block.scalar
        def _(act):
            def split(j, u):
                act.wait_ge(w_loaded[u], j * 16 + 16)
                split_high(act, w_high[u][:], w[u][:]).then_inc(high_ready[u], 1)

            def take(j, u):
                b = j * 2 + u
                act.wait_ge(stored[u], j * 16)
                for t in range(0, TT, 2):
                    act.wait_ge(product, b * TT + t + 1)
                    act.activation(out[u][:, t, :], bank[t][:, 0:width], ACT.Copy).then_inc(even_out, 1)
                act.wait_ge(even_out, b * 4 + 8)
                act.wait_ge(odd_out, b * 4 + 8)
                act.dma_start(out_dram[:, ds(b * width, width)].rearrange("(t p) n -> p t n", p=P),
                              out[u][:]).then_inc(stored[u], 16)

            act.sem_inc(even_out, 4)
            split(0, 0)
            with act.Fori(0, half - 1) as j:
                split(j, 1)
                take(j, 0)
                split(j + 1, 0)
                take(j, 1)
            split(half - 1, 1)
            take(half - 1, 0)
            take(half - 1, 1)
            for u in range(2):
                act.wait_ge(stored[u], 16 * half)

        @block.vector
        def _(v):
            def split(j, u):
                v.wait_ge(high_ready[u], j + 1)
                split_low(v, w_low[u][:], w[u][:], w_high[u][:]).then_inc(low_ready[u], 1)

            def take(j, u):
                v.wait_ge(stored[u], j * 16)
                for t in range(1, TT, 2):
                    v.wait_ge(product, (j * 2 + u) * TT + t + 1)
                    v.tensor_copy(out[u][:, t, :], bank[t][:, 0:width]).then_inc(odd_out, 1)

            v.sem_inc(odd_out, 4)
            split(0, 0)
            with v.Fori(0, half - 1) as j:
                split(j, 1)
                take(j, 0)
                split(j + 1, 0)
                take(j, 1)
            split(half - 1, 1)
            take(half - 1, 0)
            take(half - 1, 1)


def norm_spread(v, link, y, scratch, stats, heads, width, eps, out, spread_ready):
    total, mean, var, spread = (stats[:, i, 0:heads] for i in range(4))
    link(v.tensor_reduce(total, three(y, heads), AX_X, ALU.add))
    link(v.tensor_scalar(mean, total, 1.0 / width, None, ALU.mult))
    link(v.tensor_tensor(three(out, heads), three(y, heads), per_row(mean, width), ALU.subtract))
    link(v.tensor_tensor(scratch, out, out, ALU.mult))
    link(v.tensor_reduce(var, three(scratch, heads), AX_X, ALU.add))
    v.tensor_scalar(spread, var, 1.0 / width, eps, ALU.mult, ALU.add).then_inc(spread_ready, 1)


def norm_divide(v, link, stats, heads, width, out, normed):
    link(v.reciprocal(stats[:, 5, 0:heads], stats[:, 4, 0:heads]))
    v.tensor_tensor(three(out, heads), three(out, heads), per_row(stats[:, 5, 0:heads], width), ALU.mult).then_inc(normed, 1)


def mix_stage(nc, bank, ident, a, proj, mixed):
    HG = 4
    with Stage(nc, "mix") as st:
        mu = st.sb("mu", [P, RW_COLS])
        w0, a0, k_k, k_a, r_k, rw_gain, ret_gain = (st.sb(n, [P, 512]) for n in
                                                    ("w0", "a0", "k_k", "k_a", "r_k", "rw_gain", "ret_gain"))
        lora_up = st.sb("lora_up", [P, RW_W])
        g_up = st.sb("g_up", [P, RW_W])
        incl, strict, incl_mid, strict_mid = (st.sb(n, [P, P]) for n in ("incl", "strict", "incl_mid", "strict_mid"))
        pair_mask = [st.sb(f"pair_mask{i}", [P, P]) for i in range(1 + len(SOLVE_STEPS))]
        ends = st.sb("ends", [P, 2])
        intra = st.sb("intra", [P, RET_HEADS, P])
        q_decay = st.sb("q_decay", [P, RET_HEADS, P])
        k_decay = st.sb("k_decay", [P, RET_HEADS])
        tile_decay = st.sb("tile_decay", [P, RET_HEADS])

        def pair(name, shape):
            return [st.sb(f"{name}{u}", shape) for u in range(2)]

        feat, ret_in = pair("feat", [P, RW_COLS]), pair("ret_in", [P, 4 * RET_W])
        prev = st.sb("prev", [P, RW_COLS])
        rope = pair("rope", [P, 2, RET_D // 2])
        lo, lo_t = st.sb("lo", [P, 256]), st.sb("lo_t", [P, 256])
        sg, ag, p_t, p_inv, k2 = (st.sb(n, [P, RW_W]) for n in ("sg", "ag", "p_t", "p_inv", "k2"))
        p_ex = ag
        g, bonus_v = pair("g", [P, RW_W]), pair("bonus_v", [P, RW_W])
        tilde_r, tilde_a = sg, p_ex
        tilde_b, tilde_k = pair("tilde_b", [P, RW_W]), pair("tilde_k", [P, RW_W])
        tilde_t = [st.sb(f"tilde_t_{n}", [RW_N, RW_HEADS, P]) for n in "bkra"]
        kk_stats = st.sb("kk_stats", [P, 3, RW_HEADS])
        rw_stats, ret_stats = st.sb("rw_stats", [P, 6, RW_HEADS]), st.sb("ret_stats", [P, 6, RET_HEADS])
        bonus = st.sb("bonus", [P, RW_HEADS])
        reach = pair("reach", [RW_N, RW_HEADS, 2])
        m, m0 = st.sb("m", [RW_N, RW_W]), st.sb("m0", [RW_N, RW_W])
        ab, ak, rb, rk = ([st.sb(f"{n}{i}", [P, HG, P]) for i in range(2)] for n in ("ab", "ak", "rb", "rk"))
        ab_step = [[st.sb(f"ab_step{i}_{s}", [P, HG, P]) for s in range(3)] for i in range(2)]
        x_t, x_n, zs = ([st.sb(f"{n}{i}", [P, HG, P]) for i in range(2)] for n in ("x_t", "x_n", "zs"))
        q1, u_ = st.sb("q1", [P, RW_W]), st.sb("u", [P, RW_W])
        rot = st.sb("rot", [P, 4, 512])
        qk = st.sb("qk", [P, 2 * RET_W])
        kd = rot[:, 0, :]
        q_t, k_t, qd_t, pt = (st.sb(n, [P, RET_HEADS, P]) for n in ("q_t", "k_t", "qd_t", "pt"))
        state, gate = st.sb("state", [P, RET_W]), st.sb("gate", [P, RET_W])
        out_t = st.sb("out_t", [P, KT, P])
        y_raw, y, ry_raw, ry, scratch = (st.sb(n, [P, 512]) for n in ("y_raw", "y", "ry_raw", "ry", "scratch"))

        names = ("const shift_order kk_order b_order bonus_order rw_order ret_order state_order m_order pool_order "
                 "shifted lo_ready lo_turned lo_t_ready lifted w_added a_added sg_ready a_ready g_ready run_ready exp_ready "
                 "reach_ready tilde_ready tilde_turned fm_even fm_odd kk_squared kk_root bonus_ready "
                 "scored masked ab_split x_ready x_turned x_n_ready z_made z_ready x_step "
                 "m0_ready q1_made q1_ready u_made u_ready y_made m_made m_ready y_copied rw_spread rw_root rw_normed rw_ready "
                 "rw_turned rw_mixed rotated q_turned k_turned q_t_ready k_t_ready qd_ready ret_scored pt_ready ret_made "
                 "state_ready ret_copied gate_ready ret_spread ret_root ret_normed ret_ready ret_out_turned ret_mixed "
                 "pe_passed prev_ready stored zeroed").split()
        sem = {n: st.sem(n) for n in names}
        (const, shift_order, kk_order, b_order, bonus_order, rw_order, ret_order, state_order, m_order, pool_order,
         shifted, lo_ready, lo_turned, lo_t_ready, lifted, w_added, a_added, sg_ready, a_ready, g_ready, run_ready, exp_ready,
         reach_ready, tilde_ready, tilde_turned, fm_even, fm_odd, kk_squared, kk_root, bonus_ready,
         scored, masked, ab_split, x_ready, x_turned, x_n_ready, z_made, z_ready, x_step,
         m0_ready, q1_made, q1_ready, u_made, u_ready, y_made, m_made, m_ready, y_copied, rw_spread, rw_root, rw_normed, rw_ready,
         rw_turned, rw_mixed, rotated, q_turned, k_turned, q_t_ready, k_t_ready, qd_ready, ret_scored, pt_ready, ret_made,
         state_ready, ret_copied, gate_ready, ret_spread, ret_root, ret_normed, ret_ready, ret_out_turned, ret_mixed,
         pe_passed, prev_ready, stored, zeroed) = (sem[n] for n in names)
        in_ready = [st.sem(f"in_ready{u}") for u in range(2)]
        NS = len(SOLVE_STEPS)
        PAIRS = TT // 2
        LAST = TT - 1

        def r_(u):
            return feat[u][:, 0:512]

        def k_(u):
            return feat[u][:, 512:1024]

        def v_(u):
            return feat[u][:, 1024:1536]

        k_scaled, b_, kk = (prev[:, i * RW_W:(i + 1) * RW_W] for i in range(3))

        def head(ap, h, n):
            return ap[:, h * n:(h + 1) * n]

        def each_turn(eng, turn):
            for u in range(2):
                turn(0, u, u == 0, False)
            with eng.Fori(1, PAIRS - 1) as j:
                for u in range(2):
                    turn(j, u, False, False)
            for u in range(2):
                turn(PAIRS - 1, u, False, u == 1)

        consts = [
            (mu[:], rows(a["rwkv_mu"], RW_COLS)), (w0[:], rows(a["rwkv_w0"], 512)), (a0[:], rows(a["rwkv_a0"], 512)),
            (k_k[:], rows(a["rwkv_k_k"], 512)), (k_a[:], rows(a["rwkv_k_a"], 512)),
            (r_k[:], rows(a["rwkv_r_k"].rearrange("h n -> (h n)"), 512)),
            (rw_gain[:], rows(a["rwkv_gn_gain"], 512)), (ret_gain[:], rows(a["ret_gn_gain"], 512)),
            (lora_up[0:LORA, :], a["rwkv_w_up"]), (lora_up[LORA:2 * LORA, :], a["rwkv_a_up"]), (g_up[:], a["rwkv_g_up"]),
            (incl[:], a["c_incl"]), (strict[:], a["c_strict"]), (incl_mid[:], a["c_incl_mid"]),
            (strict_mid[:], a["c_strict_mid"]), (ends[:], a["c_ends"]),
            (intra[:], a["c_ret_intra"]), (q_decay[:], a["c_ret_q"]), (k_decay[:], a["c_ret_k"]),
            (tile_decay[:], a["c_ret_tile"]),
        ] + [(pair_mask[i][:], a["c_pairs"][i]) for i in range(1 + NS)]
        block = st.open()

        @block.sync
        def _(sp):
            def load(j, u):
                t = 2 * j + u
                sp.dma_start(feat[u][:], proj[ds(t * P + 1, P), 4 * RET_W:IN_COLS]).then_inc(in_ready[u], 16)
                sp.dma_start(ret_in[u][:], proj[ds(t * P + 1, P), 0:4 * RET_W]).then_inc(in_ready[u], 16)
                sp.dma_start(rope[u][:], a["c_rope"][ds(t * P, P), :].rearrange("p (a d) -> p a d", a=2)).then_inc(in_ready[u], 16)

            def load_prev(t):
                sp.dma_start(prev[:], proj[ds(t * P, P), 4 * RET_W:IN_COLS]).then_inc(prev_ready, 16)

            load(0, 0)
            load_prev(0)
            load(0, 1)
            for to, of in consts:
                sp.dma_start(to, of).then_inc(const, 16)
            sp.wait_ge(tilde_ready, 4)
            load_prev(1)
            with sp.Fori(1, PAIRS) as j:
                for u in range(2):
                    t = 2 * j + u
                    sp.wait_ge(tilde_ready, t * 4)
                    load_prev(t)
                    sp.wait_ge(bonus_ready, t - 1)
                    sp.wait_ge(y_made, t - 1)
                    sp.wait_ge(ret_made, t - 1)
                    sp.wait_ge(gate_ready, t - 1)
                    load(j, u)

        @block.vector
        def _(v):
            def chain(order, t, per):
                steps = [0]

                def link(ins):
                    steps[0] += 1
                    assert steps[0] <= per
                    ins.then_inc(order, 1)
                    v.wait_ge(order, t * per + steps[0])

                return link

            def shift(j, u):
                link = chain(shift_order, 2 * j + u, 2)
                v.wait_ge(in_ready[u], j * 48 + 48)
                v.wait_ge(prev_ready, (2 * j + u) * 16 + 16)
                link(v.tensor_tensor(prev[:], prev[:], feat[u][:], ALU.subtract))
                link(v.tensor_tensor(prev[:], prev[:], mu[:], ALU.mult))

            def shift_end(j, u):
                t = 2 * j + u
                link = chain(kk_order, t, 5)
                v.tensor_tensor(feat[u][:], feat[u][:], prev[:], ALU.add).then_inc(shifted, 1)
                v.wait_ge(shifted, t + 1)
                link(v.tensor_tensor(k_scaled, k_(u), k_k[:], ALU.mult))
                link(v.tensor_tensor(b_, k_scaled, k_scaled, ALU.mult))
                v.tensor_reduce(kk_stats[:, 0, :], three(b_, RW_HEADS), AX_X, ALU.add).then_inc(kk_squared, 1)
                return link

            def unit_kk(j, u, link):
                v.wait_ge(kk_root, 2 * j + u + 1)
                link(v.tensor_scalar(kk_stats[:, 1, :], kk_stats[:, 1, :], 1e-12, None, ALU.max))
                link(v.reciprocal(kk_stats[:, 2, :], kk_stats[:, 1, :]))
                link(v.tensor_tensor(three(kk, RW_HEADS), three(k_scaled, RW_HEADS), per_row(kk_stats[:, 2, :], RW_N),
                                     ALU.mult))

            def sigmoid_args(j, u):
                v.wait_ge(lifted, 2 * j + u + 1)
                v.tensor_tensor(p_t[:], bank[2][:], w0[:], ALU.add).then_inc(w_added, 1)
                v.tensor_tensor(p_inv[:], bank[3][:], a0[:], ALU.add).then_inc(a_added, 1)

            def rated(j, u):
                t = 2 * j + u
                link = chain(b_order, t, 3)
                v.wait_ge(a_ready, t + 1)
                link(v.scalar_tensor_tensor(out=k_scaled, in0=ag[:], scalar=-1.0, in1=k_a[:], op0=ALU.add, op1=ALU.mult))
                link(v.scalar_tensor_tensor(out=k2[:], in0=k_scaled, scalar=1.0, in1=k_(u), op0=ALU.add, op1=ALU.mult))
                link(v.tensor_tensor(b_, kk, ag[:], ALU.mult))

            def tildes(j, u):
                v.wait_ge(exp_ready, (2 * j + u) * 3 + 3)
                v.tensor_tensor(tilde_b[u][:], b_, p_inv[:], ALU.mult).then_inc(tilde_ready, 1)
                v.tensor_tensor(tilde_k[u][:], k2[:], p_inv[:], ALU.mult).then_inc(tilde_ready, 1)
                v.tensor_tensor(tilde_r[:], r_(u), p_t[:], ALU.mult).then_inc(tilde_ready, 1)
                v.scalar_tensor_tensor(out=tilde_a[:], in0=kk, scalar=-1.0, in1=p_ex[:], op0=ALU.mult,
                                       op1=ALU.mult).then_inc(tilde_ready, 1)

            def score(j, u, first):
                t = 2 * j + u
                v.wait_ge(reach_ready, t + 1)
                if not first:
                    v.wait_ge(y_made, t)
                v.tensor_tensor(three(m0[:], RW_HEADS), three(m[:], RW_HEADS), per_row(reach[u][:, :, 0], RW_N),
                                ALU.mult).then_inc(m0_ready, 1)
                for n in range(1, 8, 2):
                    v.wait_ge(tilde_turned, t * 8 + n + 1)
                    v.tensor_copy(tilde_t[n // 2][:, 4 * (n % 2):4 * (n % 2) + 4, :],
                                  three(bank[n][0:RW_N, :], HG)).then_inc(fm_odd, 1)
                link = chain(bonus_order, t, 3)
                v.wait_ge(tilde_ready, t * 4 + 4)
                link(v.tensor_tensor(scratch[:], r_(u), k2[:], ALU.mult))
                link(v.tensor_tensor(scratch[:], scratch[:], r_k[:], ALU.mult))
                link(v.tensor_reduce(bonus[:], three(scratch[:], RW_HEADS), AX_X, ALU.add))
                v.tensor_tensor(three(bonus_v[u][:], RW_HEADS), three(v_(u), RW_HEADS), per_row(bonus[:], RW_N), ALU.mult)\
                    .then_inc(bonus_ready, 1)
                for gr in range(2):
                    for n, (to, mask) in enumerate(((ab, strict), (rb, incl), (ak, strict), (rk, incl))):
                        v.wait_ge(scored, t * 8 + 4 * gr + n + 1)
                        v.tensor_tensor(to[gr][:], three(bank[4 * gr + n][:], HG), per_block(mask[:], HG),
                                        ALU.mult).then_inc(masked, 1)

            def rw_norm(t):
                if not isinstance(t, int) or t:
                    v.wait_ge(rw_turned, t)
                v.wait_ge(y_copied, t + 1)
                link = chain(rw_order, t, 6)
                norm_spread(v, link, y_raw[:], scratch[:], rw_stats, RW_HEADS, RW_N, RW_GN_EPS, y[:], rw_spread)
                return link

            def rw_divide(t, link):
                v.wait_ge(rw_root, t + 1)
                norm_divide(v, link, rw_stats, RW_HEADS, RW_N, y[:], rw_normed)

            def ret_norm(t):
                if not isinstance(t, int) or t:
                    v.wait_ge(ret_out_turned, t)
                v.wait_ge(ret_copied, t + 1)
                link = chain(ret_order, t, 6)
                norm_spread(v, link, ry_raw[:], scratch[:], ret_stats, RET_HEADS, RET_D, RET_GN_EPS, ry[:], ret_spread)
                return link

            def ret_divide(t, link):
                v.wait_ge(ret_root, t + 1)
                norm_divide(v, link, ret_stats, RET_HEADS, RET_D, ry[:], ret_normed)

            def turn(j, u, first, last):
                t = 2 * j + u
                after = (j + u, 1 - u)
                score(j, u, first)
                for gr in range(2):
                    v.wait_ge(ab_split, t * 2 * (NS + 1) + gr + 1)
                    v.tensor_tensor(x_t[gr][:], ab_step[gr][0][:], per_block(ident[:], HG), ALU.add).then_inc(x_ready, 1)
                for s in range(NS):
                    if s == 0 and not first:
                        rw_link = rw_norm(t - 1)
                    elif s == 1 and not last:
                        shift(*after)
                    elif s == 2:
                        if not last:
                            kk_link = shift_end(*after)
                        if not first:
                            rw_divide(t - 1, rw_link)
                    elif s == 3:
                        if not last:
                            unit_kk(*after, kk_link)
                        if not first:
                            ret_link = ret_norm(t - 1)
                    elif s == 4:
                        if not last:
                            sigmoid_args(*after)
                        if not first:
                            ret_divide(t - 1, ret_link)
                    elif s == 5 and not last:
                        rated(*after)
                    for gr in range(2):
                        v.wait_ge(x_step, t * 2 * NS + 2 * s + gr + 1)
                        v.wait_ge(x_ready, t * 2 * (NS + 1) + 2 * s + gr + 1)
                        v.tensor_tensor(x_t[gr][:], x_t[gr][:], three(bank[4 * gr][:], HG), ALU.add).then_inc(x_ready, 1)
                v.wait_ge(ret_scored, t + 1)
                v.tensor_tensor(pt[:], three(bank[6][:], RET_HEADS), intra[:], ALU.mult).then_inc(pt_ready, 1)
                if not last:
                    tildes(*after)
                link = chain(m_order, t, 1)
                v.wait_ge(m_made, t + 1)
                link(v.tensor_tensor(m[:], m0[:], bank[4][0:RW_N, :], ALU.add))
                v.tensor_tensor(three(m[:], RW_HEADS), three(m[:], RW_HEADS), per_row(reach[u][:, :, 1], RW_N), ALU.mult)\
                    .then_inc(m_ready, 1)
                v.wait_ge(m_ready, t + 1)
                link = chain(state_order, t, 1)
                v.wait_ge(ret_made, t + 1)
                link(v.tensor_tensor(three(state[:], RET_HEADS), three(state[:], RET_HEADS),
                                     per_row(tile_decay[:], RET_D), ALU.mult))
                v.tensor_tensor(state[:], state[:], bank[6][:], ALU.add).then_inc(state_ready, 1)
                v.wait_ge(state_ready, t + 1)

            v.wait_ge(const, 16 * len(consts))
            shift(0, 0)
            link = shift_end(0, 0)
            unit_kk(0, 0, link)
            sigmoid_args(0, 0)
            rated(0, 0)
            tildes(0, 0)
            v.memset(m[:], 0.0).then_inc(zeroed, 1)
            v.memset(state[:], 0.0).then_inc(zeroed, 1)
            v.wait_ge(zeroed, 2)
            each_turn(v, turn)
            link = rw_norm(LAST)
            rw_divide(LAST, link)
            link = ret_norm(LAST)
            ret_divide(LAST, link)

        @block.gpsimd
        def _(pool):
            half = RET_D // 2

            def link(ins, count):
                ins.then_inc(pool_order, 1)
                pool.wait_ge(pool_order, count)

            def rotate(j, u, first):
                t = 2 * j + u
                pool.wait_ge(in_ready[u], j * 48 + 48)
                if not first:
                    pool.wait_ge(ret_made, t)
                both = ret_in[u][:, 0:2 * RET_W].rearrange("p (h c d) -> p h c d", c=2, d=half)
                to = qk[:].rearrange("p (h c d) -> p h c d", c=2, d=half)
                cos, sin = (per_block(rope[u][:, i, :], 2 * RET_HEADS) for i in range(2))
                parts = [three(rot[:, i, :], 2 * RET_HEADS) for i in range(4)]
                link(pool.tensor_tensor(parts[0], both[:, :, 0, :], cos, ALU.mult), t * 6 + 1)
                link(pool.tensor_tensor(parts[1], both[:, :, 1, :], sin, ALU.mult), t * 6 + 2)
                link(pool.tensor_tensor(parts[2], both[:, :, 0, :], sin, ALU.mult), t * 6 + 3)
                link(pool.tensor_tensor(parts[3], both[:, :, 1, :], cos, ALU.mult), t * 6 + 4)
                link(pool.tensor_tensor(to[:, :, 0, :], parts[0], parts[1], ALU.subtract), t * 6 + 5)
                link(pool.tensor_tensor(to[:, :, 1, :], parts[2], parts[3], ALU.add), t * 6 + 6)
                pool.tensor_tensor(three(kd, RET_HEADS), three(qk[:, RET_W:2 * RET_W], RET_HEADS),
                                   per_row(k_decay[:], RET_D), ALU.mult).then_inc(rotated, 1)

            def rw_leave(t, u):
                pool.wait_ge(rw_normed, t * 3 + 1)
                pool.tensor_tensor(y[:], y[:], rw_gain[:], ALU.mult).then_inc(rw_normed, 1)
                pool.wait_ge(rw_normed, t * 3 + 2)
                pool.tensor_tensor(y[:], y[:], bonus_v[u][:], ALU.add).then_inc(rw_normed, 1)
                pool.wait_ge(rw_normed, t * 3 + 3)
                pool.wait_ge(g_ready, t + 1)
                pool.tensor_tensor(y[:], y[:], g[u][:], ALU.mult).then_inc(rw_ready, 1)

            def ret_leave(t):
                pool.wait_ge(ret_normed, t * 2 + 1)
                pool.tensor_tensor(ry[:], ry[:], ret_gain[:], ALU.mult).then_inc(ret_normed, 1)
                pool.wait_ge(ret_normed, t * 2 + 2)
                pool.wait_ge(gate_ready, t + 1)
                pool.tensor_tensor(ry[:], ry[:], gate[:], ALU.mult).then_inc(ret_ready, 1)

            def turn(j, u, first, last):
                t = 2 * j + u
                rotate(j, u, first)
                for s in range(NS + 1):
                    for gr in range(2):
                        if s == 0:
                            pool.wait_ge(masked, t * 8 + gr * 4 + 1)
                        elif s == 3:
                            pool.wait_ge(x_ready, t * 2 * (NS + 1) + gr + 1)
                        elif s > 3:
                            pool.wait_ge(z_made, t * 2 * NS + 2 * (s - 4) + gr + 1)
                        pool.tensor_tensor(ab_step[gr][s % 3][:], ab[gr][:], per_block(pair_mask[s][:], HG),
                                           ALU.mult).then_inc(ab_split, 1)
                if not first:
                    rw_leave(t - 1, 1 - u)
                    ret_leave(t - 1)
                pool.wait_ge(q_t_ready, t + 1)
                pool.tensor_tensor(qd_t[:], q_t[:], q_decay[:], ALU.mult).then_inc(qd_ready, 1)

            pool.wait_ge(const, 16 * len(consts))
            each_turn(pool, turn)
            rw_leave(LAST, LAST % 2)
            ret_leave(LAST)

        @block.scalar
        def _(act):
            def squash(j, u):
                t = 2 * j + u
                f = feat[u]
                act.wait_ge(shifted, t + 1)
                act.activation(lo[:, 0:LORA], f[:, 1536:1536 + LORA], ACT.Tanh).then_inc(lo_ready, 1)
                act.activation(lo[:, LORA:2 * LORA], f[:, 1536 + LORA:1536 + 2 * LORA], ACT.Copy).then_inc(lo_ready, 1)
                act.activation(lo[:, 2 * LORA:256], f[:, 1536 + 2 * LORA:RW_COLS], ACT.Sigmoid).then_inc(lo_ready, 1)
                act.wait_ge(kk_squared, t + 1)
                act.activation(kk_stats[:, 1, :], kk_stats[:, 0, :], ACT.Sqrt).then_inc(kk_root, 1)

            def take_lo(j, u):
                act.wait_ge(lo_turned, 2 * j + u + 1)
                act.activation(lo_t[:], bank[6][:, 0:256], ACT.Copy).then_inc(lo_t_ready, 1)

            def sigmoids(j, u, first):
                t = 2 * j + u
                act.wait_ge(w_added, t + 1)
                act.activation(sg[:], p_t[:], ACT.Sigmoid).then_inc(sg_ready, 1)
                act.wait_ge(a_added, t + 1)
                act.activation(ag[:], p_inv[:], ACT.Sigmoid).then_inc(a_ready, 1)
                if not first:
                    act.wait_ge(rw_ready, t - 1)
                act.activation(g[u][:], bank[7][:], ACT.Copy).then_inc(g_ready, 1)

            def decays(j, u):
                t = 2 * j + u
                act.wait_ge(a_ready, t + 1)
                act.wait_ge(sg_ready, t + 1)
                act.wait_ge(run_ready, t + 1)
                act.wait_ge(b_order, t * 3 + 3)
                act.activation(p_t[:], bank[2][:], ACT.Exp, scale=DECAY).then_inc(exp_ready, 1)
                act.activation(p_inv[:], bank[2][:], ACT.Exp, scale=-DECAY).then_inc(exp_ready, 1)
                act.activation(p_ex[:], bank[3][:], ACT.Exp, scale=DECAY).then_inc(exp_ready, 1)
                act.activation(reach[u][:], three(bank[7][0:RW_N, 0:2 * RW_HEADS], RW_HEADS), ACT.Exp,
                               scale=DECAY).then_inc(reach_ready, 1)

            def rw_deviation(t):
                act.wait_ge(rw_spread, t + 1)
                act.activation(rw_stats[:, 4, :], rw_stats[:, 3, :], ACT.Sqrt).then_inc(rw_root, 1)

            def ret_deviation(t):
                act.wait_ge(ret_spread, t + 1)
                act.activation(ret_stats[:, 4, :], ret_stats[:, 3, :], ACT.Sqrt).then_inc(ret_root, 1)

            def leave(t):
                if not isinstance(t, int) or t:
                    act.wait_ge(stored, t * 16)
                act.wait_ge(rw_turned, t + 1)
                act.activation(out_t[:, 4:8, :], three(bank[7][:], 4), ACT.Copy).then_inc(rw_mixed, 1)
                act.wait_ge(ret_out_turned, t + 1)
                act.activation(out_t[:, 0:4, :], three(bank[3][:], 4), ACT.Copy).then_inc(ret_mixed, 1)
                act.wait_ge(rw_mixed, t + 1)
                act.wait_ge(ret_mixed, t + 1)
                act.dma_start(mixed[ds(t, 1)].rearrange("a p f -> (a p) f"), flat(out_t[:])).then_inc(stored, 16)

            def turn(j, u, first, last):
                t = 2 * j + u
                after = (j + u, 1 - u)
                for n in range(0, 8, 2):
                    act.wait_ge(tilde_turned, t * 8 + n + 1)
                    act.activation(tilde_t[n // 2][:, 0:4, :], three(bank[n][0:RW_N, :], HG), ACT.Copy).then_inc(fm_even, 1)
                for s in range(NS):
                    for gr in range(2):
                        act.wait_ge(x_turned, t * 2 * NS + 2 * s + gr + 1)
                        act.activation(x_n[gr][:], three(bank[4 * gr][:], HG), ACT.Copy).then_inc(x_n_ready, 1)
                    for gr in range(2):
                        act.wait_ge(z_made, t * 2 * NS + 2 * s + gr + 1)
                        act.activation(zs[gr][:], three(bank[4 * gr + 1][:], HG), ACT.Copy).then_inc(z_ready, 1)
                    if s == 1 and not first:
                        rw_deviation(t - 1)
                    elif s == 2 and not last:
                        squash(*after)
                    elif s == 3:
                        if not last:
                            take_lo(*after)
                        if not first:
                            ret_deviation(t - 1)
                    elif s == 4 and not last:
                        sigmoids(*after, first)
                act.wait_ge(q1_made, t + 1)
                act.activation(q1[:], bank[1][:], ACT.Copy).then_inc(q1_ready, 1)
                act.wait_ge(q_turned, t + 1)
                act.activation(q_t[:], three(bank[6][:], RET_HEADS), ACT.Copy).then_inc(q_t_ready, 1)
                act.wait_ge(k_turned, t + 1)
                act.activation(k_t[:], three(bank[5][:], RET_HEADS), ACT.Copy).then_inc(k_t_ready, 1)
                act.wait_ge(u_made, t + 1)
                act.activation(u_[:], bank[1][:], ACT.Copy).then_inc(u_ready, 1)
                if not last:
                    decays(*after)
                act.wait_ge(y_made, t + 1)
                act.activation(y_raw[:], bank[0][:], ACT.Copy).then_inc(y_copied, 1)
                act.wait_ge(ret_made, t + 1)
                act.activation(ry_raw[:], bank[5][:], ACT.Copy).then_inc(ret_copied, 1)
                if not first:
                    leave(t - 1)
                    act.wait_ge(ret_ready, t)
                act.activation(gate[:], ret_in[u][:, 3 * RET_W:4 * RET_W], ACT.Silu).then_inc(gate_ready, 1)

            act.wait_ge(const, 16 * len(consts))
            squash(0, 0)
            take_lo(0, 0)
            sigmoids(0, 0, True)
            decays(0, 0)
            each_turn(act, turn)
            rw_deviation(LAST)
            ret_deviation(LAST)
            leave(LAST)
            act.wait_ge(stored, 16 * TT)

        @block.tensor
        def _(pe):
            def turn_lo(j, u):
                pe.wait_ge(lo_ready, (2 * j + u) * 3 + 3)
                pe.transpose(bank[6][:, 0:P], lo[:, 0:P], ident[:])
                pe.transpose(bank[6][:, P:2 * P], lo[:, P:2 * P], ident[:]).then_inc(lo_turned, 1)

            def lift(j, u):
                pe.wait_ge(lo_t_ready, 2 * j + u + 1)
                pe.matmul(bank[2][:], lo_t[0:LORA, 0:P], lora_up[0:LORA, :], start=True, stop=True)
                pe.matmul(bank[3][:], lo_t[LORA:2 * LORA, 0:P], lora_up[LORA:2 * LORA, :], start=True, stop=True)
                pe.matmul(bank[7][:], lo_t[:, P:2 * P], g_up[:], start=True, stop=True).then_inc(lifted, 1)

            def run_sums(j, u):
                t = 2 * j + u
                pe.wait_ge(sg_ready, t + 1)
                pe.wait_ge(a_added, t + 1)
                pe.wait_ge(g_ready, t + 1)
                pe.matmul(bank[2][:], incl_mid[:], sg[:], start=True, stop=True)
                pe.matmul(bank[3][:], strict_mid[:], sg[:], start=True, stop=True)
                for h in range(RW_HEADS):
                    last = pe.matmul(bank[7][0:RW_N, 2 * h:2 * h + 2], head(sg, h, RW_N), ends[:], start=True, stop=True)
                last.then_inc(run_ready, 1)

            def score(j, u, first):
                t = 2 * j + u
                pe.wait_ge(exp_ready, t * 3 + 3)
                pe.wait_ge(reach_ready, t + 1)
                if not first:
                    pe.wait_ge(y_copied, t)
                    pe.wait_ge(m_ready, t)
                    pe.wait_ge(ret_copied, t)
                    pe.wait_ge(state_ready, t)
                    if not isinstance(t, int) or t > 1:
                        pe.wait_ge(rw_mixed, t - 1)
                        pe.wait_ge(ret_mixed, t - 1)
                for n in range(8):
                    pe.wait_ge(tilde_ready, t * 4 + n // 2 + 1)
                    pe.sem_inc(pe_passed, 1)
                    of = (tilde_b[u], tilde_k[u], tilde_r, tilde_a)[n // 2]
                    for h in range(HG):
                        last = pe.transpose(bank[n][0:RW_N, h * P:(h + 1) * P], head(of, HG * (n % 2) + h, RW_N), ident[:])
                    last.then_inc(tilde_turned, 1)
                b_t, kt_t, r_t, a_t = tilde_t
                pe.wait_ge(fm_even, t * 4 + 4)
                pe.wait_ge(fm_odd, t * 4 + 4)
                for gr in range(2):
                    for left, at in ((b_t, 0), (kt_t, 2)):
                        for n, right in enumerate((a_t, r_t)):
                            for h in range(HG):
                                hh = HG * gr + h
                                last = pe.matmul(bank[4 * gr + at + n][:, h * P:(h + 1) * P], left[:, hh, :],
                                                 right[:, hh, :], start=True, stop=True)
                            last.then_inc(scored, 1)

            def double(t, s):
                for gr in range(2):
                    pe.wait_ge(x_ready, t * 2 * (NS + 1) + 2 * s + gr + 1)
                    for h in range(HG):
                        last = pe.transpose(bank[4 * gr][:, h * P:(h + 1) * P], x_t[gr][:, h, :], ident[:])
                    last.then_inc(x_turned, 1)
                for gr in range(2):
                    pe.wait_ge(x_n_ready, t * 2 * NS + 2 * s + gr + 1)
                    pe.wait_ge(ab_split, t * 2 * (NS + 1) + 2 * (s + 1) + gr + 1)
                    for h in range(HG):
                        last = pe.matmul(bank[4 * gr + 1][:, h * P:(h + 1) * P], ab_step[gr][(1 + s) % 3][:, h, :],
                                         x_n[gr][:, h, :], start=True, stop=True)
                    last.then_inc(z_made, 1)
                for gr in range(2):
                    pe.wait_ge(z_ready, t * 2 * NS + 2 * s + gr + 1)
                    for h in range(HG):
                        last = pe.matmul(bank[4 * gr][:, h * P:(h + 1) * P], zs[gr][:, h, :], x_t[gr][:, h, :],
                                         start=True, stop=True)
                    last.then_inc(x_step, 1)

            def turn_ret(t, n, done):
                for h in range(RET_HEADS):
                    last = pe.transpose(bank[(6, 5)[n]][:, h * P:(h + 1) * P],
                                        head(qk[:, n * RET_W:(n + 1) * RET_W], h, RET_D), ident[:])
                last.then_inc(done, 1)

            def leave(t):
                pe.wait_ge(rw_ready, t + 1)
                for n in range(4):
                    last = pe.transpose(bank[7][:, n * P:(n + 1) * P], y[:, n * P:(n + 1) * P], ident[:])
                last.then_inc(rw_turned, 1)
                pe.wait_ge(ret_ready, t + 1)
                for n in range(4):
                    last = pe.transpose(bank[3][:, n * P:(n + 1) * P], ry[:, n * P:(n + 1) * P], ident[:])
                last.then_inc(ret_out_turned, 1)

            def turn(j, u, first, last_turn):
                t = 2 * j + u
                after = (j + u, 1 - u)
                b_t, kt_t, r_t, a_t = tilde_t
                score(j, u, first)
                pe.wait_ge(masked, t * 8 + 8)
                for s in range(NS):
                    double(t, s)
                    if not last_turn and s in (2, 3, 5):
                        (turn_lo, lift, None, run_sums)[s - 2](*after)
                pe.wait_ge(rotated, t + 1)
                turn_ret(t, 0, q_turned)
                pe.wait_ge(m0_ready, t + 1)
                for h in range(RW_HEADS):
                    to = head(bank[1], h, RW_N)
                    pe.matmul(to, a_t[:, h, :], head(m0, h, RW_N), start=True, stop=False)
                    last = pe.matmul(to, ak[h // HG][:, h % HG, :], head(v_(u), h, RW_N), start=False, stop=True)
                last.then_inc(q1_made, 1)
                turn_ret(t, 1, k_turned)
                pe.wait_ge(q1_ready, t + 1)
                pe.wait_ge(x_ready, t * 2 * (NS + 1) + 2 * (NS + 1))
                for h in range(RW_HEADS):
                    last = pe.matmul(head(bank[1], h, RW_N), x_t[h // HG][:, h % HG, :], head(q1, h, RW_N),
                                     start=True, stop=True)
                last.then_inc(u_made, 1)
                pe.wait_ge(q_t_ready, t + 1)
                pe.wait_ge(k_t_ready, t + 1)
                for h in range(RET_HEADS):
                    last = pe.matmul(bank[6][:, h * P:(h + 1) * P], k_t[:, h, :], q_t[:, h, :], start=True, stop=True)
                last.then_inc(ret_scored, 1)
                pe.wait_ge(u_ready, t + 1)
                for h in range(RW_HEADS):
                    to = head(bank[4], h, RW_N)[0:RW_N, :]
                    pe.matmul(to, head(tilde_b[u], h, RW_N), head(u_, h, RW_N), start=True, stop=False)
                    last = pe.matmul(to, head(tilde_k[u], h, RW_N), head(v_(u), h, RW_N), start=False, stop=True)
                last.then_inc(m_made, 1)
                for h in range(RW_HEADS):
                    to = head(bank[0], h, RW_N)
                    pe.matmul(to, r_t[:, h, :], head(m0, h, RW_N), start=True, stop=False)
                    pe.matmul(to, rb[h // HG][:, h % HG, :], head(u_, h, RW_N), start=False, stop=False)
                    last = pe.matmul(to, rk[h // HG][:, h % HG, :], head(v_(u), h, RW_N), start=False, stop=True)
                last.then_inc(y_made, 1)
                pe.wait_ge(pt_ready, t + 1)
                pe.wait_ge(qd_ready, t + 1)
                ret_v = ret_in[u][:, 2 * RET_W:3 * RET_W]
                for h in range(RET_HEADS):
                    to = head(bank[5], h, RET_D)
                    pe.matmul(to, pt[:, h, :], head(ret_v, h, RET_D), start=True, stop=False)
                    pe.matmul(to, qd_t[:, h, :], head(state, h, RET_D), start=False, stop=True)
                for h in range(RET_HEADS):
                    last = pe.matmul(head(bank[6], h, RET_D), head(kd, h, RET_D), head(ret_v, h, RET_D), start=True, stop=True)
                last.then_inc(ret_made, 1)
                if not first:
                    if not last_turn:
                        pe.wait_ge(exp_ready, t * 3 + 6)
                        pe.wait_ge(reach_ready, t + 2)
                    leave(t - 1)

            pe.wait_ge(const, 16 * len(consts))
            turn_lo(0, 0)
            lift(0, 0)
            run_sums(0, 0)
            each_turn(pe, turn)
            leave(LAST)


def constants():
    i = np.arange(P)
    incl = (i[:, None] <= i[None, :]).astype(np.float32)
    strict = (i[:, None] < i[None, :]).astype(np.float32)
    first = (i < P // 2).astype(np.float32)[:, None]
    pairs = [((i[:, None] // (2 * s) == i[None, :] // (2 * s)) & (i[:, None] % (2 * s) < s) & (i[None, :] % (2 * s) >= s))
             for s in (1,) + SOLVE_STEPS]
    log_g = np.log(1.0 - np.exp2(-5.0 - np.arange(RET_HEADS)))
    gap = i[None, :] - i[:, None]
    chunk = i // RET_CHUNK
    seen = chunk[None, :] >= chunk[:, None]
    intra = np.exp(log_g[:, None, None] * np.abs(gap)) * seen * RET_D ** -0.5
    half = RET_D // 2
    angle = np.arange(S, dtype=np.float32)[:, None] * (np.float32(10000.0) ** (-np.arange(half, dtype=np.float32) / np.float32(half)))[None, :]
    angle = angle.astype(np.float32).astype(np.float64)
    out = {
        "c_ident": np.eye(P), "c_incl": incl, "c_strict": strict,
        "c_incl_mid": incl - first, "c_strict_mid": strict - first,
        "c_ends": np.concatenate([first, 1.0 - first], axis=1),
        "c_pairs": np.stack(pairs), "c_ret_intra": intra.transpose(1, 0, 2),
        "c_ret_q": np.broadcast_to(np.exp(log_g[:, None] * (i + 1.0)), (P, RET_HEADS, P)),
        "c_ret_k": (np.exp(log_g[None, :] * (P - 1.0 - i)[:, None]) * RET_D ** -0.5),
        "c_ret_tile": np.broadcast_to(np.exp(log_g * P), (P, RET_HEADS)),
        "c_prefer": np.broadcast_to(8.0 - np.arange(8), (P, 8)),
        "c_expert_no": np.broadcast_to(np.arange(EXPERTS), (P, EXPERTS)),
        "c_fulls": np.broadcast_to(SLOT_BLOCK * np.arange(1, FULL_STEPS + 1), (P, FULL_STEPS)),
        "c_earlier": np.broadcast_to(np.tril(np.ones((EXPERTS, EXPERTS)), -1), (P, EXPERTS, EXPERTS)),
        "c_more_no": np.arange(MORE_BLOCKS)[None, :],
        "c_future": np.where(i[None, :] > i[:, None], -FAR, 0.0),
        "c_inv_freq": np.broadcast_to(1.0 / (np.float32(10000.0) ** (np.arange(0, ROPE, 2, dtype=np.float32) / np.float32(ROPE))),
                                      (P, ROPE // 2)),
        "c_rope": np.concatenate([np.cos(angle), np.sin(angle)], axis=1),
    }
    out = {k: np.ascontiguousarray(v, dtype=np.float32) for k, v in out.items()}
    out["c_token_ids"] = (np.arange(TT)[None, :] * P + i[:, None]).astype(np.int32)
    return out


def lay_out(inputs):
    out = {}
    for name, value in inputs.items():
        value = np.ascontiguousarray(value)
        out[name] = value[0] if value.ndim > 1 else value
    out.update(constants())
    return out


def add_product_stage(nc, name, bank, feat, feat_low, w_dram, x, x_dram=None, post_gain=None, store_dram=None, weights=None, feat_dram=None):
    halves = D // BANK
    with Stage(nc, name) as st:
        w, w_low, w_high = weights or (*st.twin("w", [P, KT, D]), st.sb("w_high", [P, KT, D], F32R))
        feat_high = st.sb("feat_high", [P, KT, S], F32R)
        gain = st.sb("gain", [P, D])
        junk = [st.sb(f"junk{i}", [P, D]) for i in range(2)]
        scaled = [st.sb(f"scaled{i}", [P, D]) for i in range(2)]
        stats = st.sb("stats", [P, TT, 6])
        w_loaded = [st.sem(f"w_loaded{n}") for n in range(halves)]
        feat_loaded = [st.sem(f"feat_loaded{t}") for t in range(TT)]
        x_loaded, gain_loaded, stored = st.sem("x_loaded"), st.sem("gain_loaded"), st.sem("stored")
        w_high_ready, w_low_ready, feat_high_ready, feat_low_ready = (
            st.sem(n) for n in ("w_high_ready", "w_low_ready", "feat_high_ready", "feat_low_ready"))
        product, squared, mean_ready, root_ready, dve_order, added = (
            st.sem(n) for n in ("product", "squared", "mean_ready", "root_ready", "dve_order", "added"))
        block = st.open()

        def half(ap, n):
            return ap[:, :, n * BANK:(n + 1) * BANK]

        def tile(ap, t):
            return ap[:, :, t * P:(t + 1) * P]

        @block.sync
        def _(sp):
            if feat_dram is not None:
                for t in range(TT):
                    sp.dma_start(tile(feat, t), three(feat_dram[t], KT)).then_inc(feat_loaded[t], 16)
            for n in range(halves):
                sp.dma_start(half(w, n), w_dram[:, n * BANK:(n + 1) * BANK].rearrange("(k p) n -> p k n", p=P))\
                    .then_inc(w_loaded[n], 16)
            if x_dram is not None:
                sp.dma_start(x[:], x_dram.rearrange("(t p) d -> p t d", p=P)).then_inc(x_loaded, 16)
            if post_gain is not None:
                sp.dma_start(gain[:], rows(post_gain, D)).then_inc(gain_loaded, 16)
            if store_dram is not None:
                for t in range(TT):
                    sp.wait_ge(added, t + 1)
                    sp.dma_start(store_dram[t * P:(t + 1) * P, :], x[:, t, :]).then_inc(stored, 16)
                sp.wait_ge(stored, 16 * TT)

        @block.tensor
        def _(pe):
            for t in range(TT):
                pe.wait_ge(feat_low_ready, t + 1)
                for n in range(halves):
                    pe.wait_ge(w_low_ready, n + 1)
                    if t >= 4:
                        pe.wait_ge(added, t - 3)
                    for k in range(KT):
                        last = three_passes(pe, bank[2 * (t % 4) + n][:],
                                            (tile(feat_high, t)[:, k, :], tile(feat_low, t)[:, k, :]),
                                            (half(w_high, n)[:, k, :], half(w_low, n)[:, k, :]),
                                            start=(k == 0), stop=(k == KT - 1))
                    last.then_inc(product, 1)

        @block.scalar
        def _(act):
            for t in range(TT):
                if feat_dram is not None:
                    act.wait_ge(feat_loaded[t], 16)
                split_high(act, tile(feat_high, t), tile(feat, t)).then_inc(feat_high_ready, 1)
            for n in range(halves):
                act.wait_ge(w_loaded[n], 16)
                split_high(act, half(w_high, n), half(w, n)).then_inc(w_high_ready, 1)
            if post_gain is not None:
                for t in range(TT):
                    for n in range(halves):
                        act.wait_ge(product, 2 * t + n + 1)
                        if t >= 2:
                            act.wait_ge(squared, 2 * t - 2)
                        act.activation(junk[t % 2][:, n * BANK:(n + 1) * BANK], bank[2 * (t % 4) + n][:], ACT.Square,
                                       accum_out=stats[:, t, n:n + 1]).then_inc(squared, 1)
                    act.wait_ge(mean_ready, t + 1)
                    act.activation(stats[:, t, 4:5], stats[:, t, 3:4], ACT.Sqrt).then_inc(root_ready, 1)

        @block.vector
        def _(v):
            steps = [0]

            def link(ins):
                steps[0] += 1
                ins.then_inc(dve_order, 1)
                v.wait_ge(dve_order, steps[0])

            for t in range(TT):
                v.wait_ge(feat_high_ready, t + 1)
                split_low(v, tile(feat_low, t), tile(feat, t), tile(feat_high, t)).then_inc(feat_low_ready, 1)
            for n in range(halves):
                v.wait_ge(w_high_ready, n + 1)
                split_low(v, half(w_low, n), half(w, n), half(w_high, n)).then_inc(w_low_ready, 1)
            if x_dram is not None:
                v.wait_ge(x_loaded, 16)
            if post_gain is not None:
                v.wait_ge(gain_loaded, 16)
            for t in range(TT):
                if post_gain is not None:
                    v.wait_ge(squared, 2 * t + 2)
                    link(v.tensor_tensor(stats[:, t, 2:3], stats[:, t, 0:1], stats[:, t, 1:2], ALU.add))
                    v.tensor_scalar(stats[:, t, 3:4], stats[:, t, 2:3], 1.0 / D, EPS, ALU.mult, ALU.add).then_inc(mean_ready, 1)
                    v.wait_ge(root_ready, t + 1)
                    link(v.reciprocal(stats[:, t, 5:6], stats[:, t, 4:5]))
                for n in range(halves):
                    cols = slice(n * BANK, (n + 1) * BANK)
                    v.wait_ge(product, 2 * t + n + 1)
                    if post_gain is None:
                        link(v.tensor_tensor(x[:, t, cols], x[:, t, cols], bank[2 * (t % 4) + n][:], ALU.add))
                    else:
                        link(v.scalar_tensor_tensor(out=scaled[t % 2][:, cols], in0=bank[2 * (t % 4) + n][:],
                                                    scalar=stats[:, t, 5:6], in1=gain[:, cols], op0=ALU.mult, op1=ALU.mult))
                        link(v.tensor_tensor(x[:, t, cols], x[:, t, cols], scaled[t % 2][:, cols], ALU.add))
                v.sem_inc(added, 1)


GROUPS, PER_GROUP = 4, 8
EXPERTS = GROUPS * PER_GROUP
SLOT_BLOCK = 128
MORE_BLOCKS = 2 * S // SLOT_BLOCK - 1
SLOT_BLOCKS = EXPERTS + MORE_BLOCKS
FULL_STEPS = S // SLOT_BLOCK - 1
FAR = 1e30


def route_stage(nc, bank, a, feat, token_ids, slot_weight, slot_index, more, slot_token):
    with Stage(nc, "route") as st:
        w = st.sb("w", [P, KT, GROUPS + EXPERTS])
        bias = st.sb("bias", [P, GROUPS + EXPERTS])
        strict, ones = st.sb("strict", [P, P]), st.sb("ones", [P, P])
        prefer, expert_no = st.sb("prefer", [P, PER_GROUP]), st.sb("expert_no", [P, EXPERTS])
        fulls = st.sb("fulls", [P, FULL_STEPS])
        earlier = st.sb("earlier", [P, EXPERTS, EXPERTS])
        more_no = st.sb("more_no", [1, MORE_BLOCKS])
        logit = st.sb("logit", [P, TT, GROUPS + EXPERTS])
        g_shift, g_hot = st.sb("g_shift", [P, TT, GROUPS]), st.sb("g_hot", [P, TT, GROUPS])
        spread = st.sb("spread", [P, TT, GROUPS, PER_GROUP])
        inside, left, e_hot1, e_hot2, eq = (st.sb(n, [P, TT, PER_GROUP]) for n in ("inside", "left", "e_hot1", "e_hot2", "eq"))
        hot = [st.sb(f"hot{i}", [P, TT, EXPERTS]) for i in range(2)]
        both, rank, weighed = (st.sb(n, [P, TT, EXPERTS]) for n in ("both", "rank", "weighed"))
        carry = st.sb("carry", [P, TT + 1, EXPERTS])
        g_max, g_sum, g_prob, top1, top2, pick, gap, e_gap, denom = (
            st.sb(n, [P, TT]) for n in ("g_max", "g_sum", "g_prob", "top1", "top2", "pick", "gap", "e_gap", "denom"))
        over = st.sb("over", [P, EXPERTS, FULL_STEPS])
        blocks, first, last_of = (st.sb(n, [P, EXPERTS]) for n in ("blocks", "first", "last_of"))
        ahead = st.sb("ahead", [P, EXPERTS, EXPERTS])
        own, place, full, far, shift, where = (st.sb(n, [P, 2, TT]) for n in ("own", "place", "full", "far", "shift", "where"))
        start = st.sb("start", [P, 2, TT])
        past = st.sb("past", [P, 2 * TT, FULL_STEPS])
        passed = st.sb("passed", [1, MORE_BLOCKS, EXPERTS])
        more_f = st.sb("more_f", [1, 2, MORE_BLOCKS])
        used = st.sb("used", [1, 1])
        no_token = st.sb("no_token", [P, SLOT_BLOCKS], I32)
        (const, gate_const, logits_made, dve_order, g_shifted, g_exp_ready, gap_ready, gap_exp_ready, hot_ready, ranked,
         slots_ready, cleared, cleared_ready, scattered) = (st.sem(n) for n in (
             "const", "gate_const", "logits_made", "dve_order", "g_shifted", "g_exp_ready", "gap_ready", "gap_exp_ready",
             "hot_ready", "ranked", "slots_ready", "cleared", "cleared_ready", "scattered"))
        consts = [(w[:, :, 0:GROUPS], a["w_route_group"].rearrange("(k p) n -> p k n", p=P)),
                  (w[:, :, GROUPS:], a["w_route_expert"].rearrange("(k p) n -> p k n", p=P)),
                  (bias[:, 0:GROUPS], rows(a["b_route_group"], GROUPS)), (bias[:, GROUPS:], rows(a["b_route_expert"], EXPERTS)),
                  (strict[:], a["c_strict"]), (prefer[:], a["c_prefer"]), (expert_no[:], a["c_expert_no"]),
                  (fulls[:], a["c_fulls"]), (earlier[:], a["c_earlier"]), (more_no[:], a["c_more_no"]),
                  (token_ids[:], a["c_token_ids"])]
        block = st.open()

        @block.sync
        def _(sp):
            with nc.allow_non_contiguous_dma("the routers' few columns"):
                for to, of in consts:
                    sp.dma_start(to, of).then_inc(const, 16)
            sp.wait_ge(cleared, 1)
            sp.dma_start(slot_token.rearrange("(p b) a -> p (b a)", p=P), no_token[:]).then_inc(cleared_ready, 16)

        @block.tensor
        def _(pe):
            pe.wait_ge(const, 16 * len(consts))
            width = GROUPS + EXPERTS
            for t in range(TT):
                for k in range(KT):
                    last = pe.matmul(bank[0][:, t * width:(t + 1) * width], feat[:, k, t * P:(t + 1) * P], w[:, k, :],
                                     start=(k == 0), stop=(k == KT - 1))
            last.then_inc(logits_made, 1)
            pe.wait_ge(hot_ready, 1)
            every = both[:].rearrange("p t e -> p (t e)")
            pe.matmul(bank[1][:, 0:TT * EXPERTS], strict[:], every, start=True, stop=True)
            pe.matmul(bank[2][:, 0:TT * EXPERTS], ones[:], every, start=True, stop=True).then_inc(ranked, 1)

        @block.scalar
        def _(act):
            act.wait_ge(g_shifted, 1)
            act.activation(g_shift[:], g_shift[:], ACT.Exp).then_inc(g_exp_ready, 1)
            act.wait_ge(gap_ready, 1)
            act.activation(e_gap[:], gap[:], ACT.Exp).then_inc(gap_exp_ready, 1)

        @block.gpsimd
        def _(pool):
            pool.wait_ge(cleared_ready, 16)
            pool.wait_ge(slots_ready, 1)
            for c in range(2):
                for t in range(TT):
                    pool.indirect_dma_start(
                        out=slot_token, out_offset=bass.IndirectOffsetOnAxis(ap=slot_index[:, c, t:t + 1], axis=0),
                        in_=token_ids[:, t:t + 1], in_offset=None).then_inc(scattered, 16)
            pool.wait_ge(scattered, 16 * 2 * TT)

        @block.vector
        def _(v):
            steps = [0]

            def link(ins):
                steps[0] += 1
                ins.then_inc(dve_order, 1)
                v.wait_ge(dve_order, steps[0])

            def first_of(hot_out, values, top, n):
                link(v.tensor_tensor(eq[:, :, 0:n], values, per_row(top, n), ALU.is_equal))
                link(v.tensor_tensor(eq[:, :, 0:n], eq[:, :, 0:n], per_block(prefer[:, 0:n], TT), ALU.mult))
                link(v.tensor_reduce(pick[:], eq[:, :, 0:n], AX_X, ALU.max))
                link(v.tensor_tensor(hot_out, eq[:, :, 0:n], per_row(pick[:], n), ALU.is_equal))

            def of_chosen(to, values):
                for c in range(2):
                    link(v.tensor_tensor(weighed[:], hot[c][:], values, ALU.mult))
                    link(v.tensor_reduce(to[:, c, :], weighed[:], AX_X, ALU.add))

            link(v.memset(ones[:], 1.0))
            v.memset(no_token[:], 0).then_inc(cleared, 1)
            v.wait_ge(const, 16 * len(consts))
            v.wait_ge(logits_made, 1)
            link(v.tensor_tensor(logit[:], three(bank[0][:, 0:TT * (GROUPS + EXPERTS)], TT), per_block(bias[:], TT), ALU.add))
            g_logit = logit[:, :, 0:GROUPS]
            link(v.tensor_reduce(g_max[:], g_logit, AX_X, ALU.max))
            v.tensor_tensor(g_shift[:], g_logit, per_row(g_max[:], GROUPS), ALU.subtract).then_inc(g_shifted, 1)
            first_of(g_hot[:], g_logit, g_max[:], GROUPS)
            v.wait_ge(g_exp_ready, 1)
            link(v.tensor_reduce(g_sum[:], g_shift[:], AX_X, ALU.add))
            link(v.reciprocal(g_prob[:], g_sum[:]))
            e_logit = logit[:, :, GROUPS:].rearrange("p t (g e) -> p t g e", g=GROUPS)
            g_wide = g_hot[:].unsqueeze(3).to_broadcast([P, TT, GROUPS, PER_GROUP])
            link(v.tensor_tensor(spread[:], e_logit, g_wide, ALU.mult))
            link(v.tensor_reduce(inside[:], spread[:].rearrange("p t g e -> p t e g"), AX_X, ALU.add))
            link(v.tensor_reduce(top1[:], inside[:], AX_X, ALU.max))
            first_of(e_hot1[:], inside[:], top1[:], PER_GROUP)
            link(v.scalar_tensor_tensor(out=left[:], in0=e_hot1[:], scalar=-FAR, in1=inside[:], op0=ALU.mult, op1=ALU.add))
            link(v.tensor_reduce(top2[:], left[:], AX_X, ALU.max))
            first_of(e_hot2[:], left[:], top2[:], PER_GROUP)
            v.tensor_tensor(gap[:], top2[:], top1[:], ALU.subtract).then_inc(gap_ready, 1)
            for c, e_hot in enumerate((e_hot1, e_hot2)):
                link(v.tensor_tensor(hot[c][:].rearrange("p t (g e) -> p t g e", g=GROUPS), g_wide,
                                     e_hot[:].unsqueeze(2).to_broadcast([P, TT, GROUPS, PER_GROUP]), ALU.mult))
            v.tensor_tensor(both[:], hot[0][:], hot[1][:], ALU.add).then_inc(hot_ready, 1)
            v.wait_ge(gap_exp_ready, 1)
            link(v.tensor_scalar(denom[:], e_gap[:], 1.0, None, ALU.add))
            link(v.reciprocal(denom[:], denom[:]))
            link(v.tensor_tensor(slot_weight[:, 0, :], denom[:], g_prob[:], ALU.mult))
            link(v.tensor_tensor(slot_weight[:, 1, :], slot_weight[:, 0, :], e_gap[:], ALU.mult))
            v.wait_ge(ranked, 1)
            link(v.memset(carry[:, 0, :], 0.0))
            for t in range(TT):
                link(v.tensor_tensor(carry[:, t + 1, :], carry[:, t, :], bank[2][:, t * EXPERTS:(t + 1) * EXPERTS], ALU.add))
            link(v.tensor_tensor(rank[:], three(bank[1][:, 0:TT * EXPERTS], TT), carry[:, 0:TT, :], ALU.add))
            count = carry[:, TT, :]
            link(v.tensor_tensor(over[:], per_row(count, FULL_STEPS), per_block(fulls[:], EXPERTS), ALU.is_gt))
            link(v.tensor_reduce(blocks[:], over[:], AX_X, ALU.add))
            link(v.tensor_tensor(ahead[:], earlier[:], per_block(blocks[:], EXPERTS), ALU.mult))
            link(v.tensor_reduce(first[:], ahead[:], AX_X, ALU.add))
            link(v.tensor_tensor(last_of[:], first[:], blocks[:], ALU.add))
            of_chosen(place, rank[:])
            of_chosen(own, per_block(expert_no[:], TT))
            of_chosen(start, per_block(first[:], TT))
            places = place[:].rearrange("p c t -> p (c t)")
            link(v.tensor_tensor(past[:], per_row(places, FULL_STEPS), per_block(fulls[:], 2 * TT), ALU.is_ge))
            link(v.tensor_reduce(full[:].rearrange("p c t -> p (c t)"), past[:], AX_X, ALU.add))
            link(v.tensor_scalar(far[:], full[:], 1.0, None, ALU.min))
            link(v.tensor_tensor(shift[:], start[:], full[:], ALU.add))
            link(v.scalar_tensor_tensor(out=shift[:], in0=shift[:], scalar=float(EXPERTS - 1), in1=own[:], op0=ALU.add,
                                        op1=ALU.subtract))
            link(v.tensor_tensor(shift[:], shift[:], far[:], ALU.mult))
            link(v.tensor_tensor(shift[:], shift[:], own[:], ALU.add))
            link(v.tensor_tensor(shift[:], shift[:], full[:], ALU.subtract))
            link(v.scalar_tensor_tensor(out=where[:], in0=shift[:], scalar=float(SLOT_BLOCK), in1=place[:], op0=ALU.mult,
                                        op1=ALU.add))
            v.tensor_copy(slot_index[:], where[:]).then_inc(slots_ready, 1)
            link(v.tensor_tensor(passed[:], per_block(last_of[0:1, :], MORE_BLOCKS), per_row(more_no[:], EXPERTS), ALU.is_le))
            link(v.tensor_reduce(more_f[:, 0, :], passed[:], AX_X, ALU.add))
            link(v.tensor_scalar(more_f[:, 0, :], more_f[:, 0, :], float(EXPERTS - 1), None, ALU.min))
            link(v.tensor_reduce(used[:], blocks[0:1, :], AX_X, ALU.add))
            link(v.tensor_scalar(more_f[:, 1, :], more_no[:], used[0:1, 0:1], None, ALU.is_lt))
            link(v.tensor_copy(more[:], more_f[:]))


HIDDEN = 512
FT = HIDDEN // P


def expert_stage(nc, bank, ident, a, more, slot_token, h_rows, y_rows):
    with Stage(nc, "expert") as st:
        w_gate, w_up = ([st.sb(f"{n}{u}", [P, KT, HIDDEN]) for u in range(2)] for n in ("w_gate", "w_up"))
        w_down = [st.sb(f"w_down{u}", [P, FT, D]) for u in range(2)]
        gain = st.sb("gain", [P, KT])
        ids = st.sb("ids", [P, SLOT_BLOCKS], I32)
        pick = [st.sb(f"pick{u}", [P, 1], I32) for u in range(2)]
        rows_in = [st.sb(f"rows_in{u}", [P, D]) for u in range(2)]
        x_t = [st.sb(f"x_t{u}", [P, KT, P]) for u in range(2)]
        silu, hidden = st.sb("silu", [P, HIDDEN]), st.sb("hidden", [P, HIDDEN])
        hidden_t = st.sb("hidden_t", [P, FT, P])
        y = [st.sb(f"y{u}", [P, D]) for u in range(2)]
        ids_loaded, gain_loaded = st.sem("ids_loaded"), st.sem("gain_loaded")
        up_loaded, down_loaded, picked, gathered, stored, up_used, down_used = (
            [st.sem(f"{n}{u}") for u in range(2)]
            for n in ("up_loaded", "down_loaded", "picked", "gathered", "stored", "up_used", "down_used"))
        passed = st.sem("passed")
        x_turned, low_out, high_out = st.sem("x_turned"), st.sem("low_out"), st.sem("high_out")
        lifted, silu_ready, hidden_ready, hidden_turned, hidden_t_ready, made, y_low, y_high = (
            st.sem(n) for n in ("lifted", "silu_ready", "hidden_ready", "hidden_turned", "hidden_t_ready", "made", "y_low", "y_high"))
        block = st.open()
        half = EXPERTS // 2
        BOTH = 32

        def load_up(sp, gate_of, up_of, u):
            sp.dma_start(w_gate[u][:], gate_of.rearrange("(k p) f -> p k f", p=P)).then_inc(up_loaded[u], 16)
            sp.dma_start(w_up[u][:], up_of.rearrange("(k p) f -> p k f", p=P)).then_inc(up_loaded[u], 16)

        def load_down(sp, down_of, u):
            sp.dma_start(w_down[u][:], down_of.rearrange("(k p) n -> p k n", p=P)).then_inc(down_loaded[u], 16)

        def turn_x(pe, n, u, per_u):
            pe.wait_ge(gathered[u], per_u * 16 + 16)
            pe.wait_ge(low_out, n)
            pe.wait_ge(high_out, n)
            for k in range(KT):
                last = pe.transpose(bank[k // 4][:, (k % 4) * P:(k % 4 + 1) * P], rows_in[u][:, k * P:(k + 1) * P], ident[:])
            last.then_inc(x_turned, 1)

        def lift(pe, n, u, per_u):
            pe.wait_ge(up_loaded[u], per_u * BOTH + BOTH)
            pe.wait_ge(low_out, n + 1)
            pe.wait_ge(high_out, n + 1)
            pe.wait_ge(hidden_ready, n)
            for b, w in ((2, w_gate), (3, w_up)):
                for k in range(KT):
                    last = pe.matmul(bank[b][:], x_t[u][:, k, :], w[u][:, k, :], start=(k == 0), stop=(k == KT - 1))
                if b == 3:
                    last.then_inc(up_used[u], 1)
                else:
                    last.then_inc(lifted, 1)

        def lower(pe, n, u, per_u):
            pe.wait_ge(hidden_ready, n + 1)
            for k in range(FT):
                last = pe.transpose(bank[4][:, k * P:(k + 1) * P], hidden[:, k * P:(k + 1) * P], ident[:])
            last.then_inc(hidden_turned, 1)
            pe.wait_ge(down_loaded[u], per_u * 16 + 16)
            pe.wait_ge(hidden_t_ready, n + 1)
            pe.wait_ge(y_low, n)
            pe.wait_ge(y_high, n)
            for b in range(2):
                for k in range(FT):
                    last = pe.matmul(bank[5 + b][:], hidden_t[:, k, :], w_down[u][:, k, b * BANK:(b + 1) * BANK],
                                     start=(k == 0), stop=(k == FT - 1))
                last.then_inc((made, down_used[u])[b], 1)

        def x_high(act, n, u):
            act.wait_ge(x_turned, n + 1)
            for k in range(4, 8):
                last = act.activation(x_t[u][:, k, :], bank[1][:, (k - 4) * P:(k - 3) * P], ACT.Copy, scale=gain[:, k:k + 1])
            last.then_inc(high_out, 1)

        def gate_and_out(act, n, u, per_u, y_to):
            act.wait_ge(lifted, n + 1)
            act.wait_ge(hidden_ready, n)
            act.activation(silu[:], bank[2][:], ACT.Silu).then_inc(silu_ready, 1)
            act.wait_ge(hidden_turned, n + 1)
            act.activation(hidden_t[:], three(bank[4][:], FT), ACT.Copy).then_inc(hidden_t_ready, 1)

        def out_low(act, n, u, per_u, y_to):
            act.wait_ge(made, n + 1)
            act.wait_ge(stored[u], per_u * 16)
            act.activation(y[u][:, 0:BANK], bank[5][:], ACT.Copy).then_inc(y_low, 1)
            act.wait_ge(y_low, n + 1)
            act.wait_ge(y_high, n + 1)
            act.dma_start(y_to, y[u][:]).then_inc(stored[u], 16)

        def x_low(v, n, u):
            v.wait_ge(x_turned, n + 1)
            v.tensor_tensor(x_t[u][:, 0:4, :], three(bank[0][:], 4), per_row(gain[:, 0:4], P), ALU.mult).then_inc(low_out, 1)

        def hide(v, n, u, per_u):
            v.wait_ge(silu_ready, n + 1)
            v.wait_ge(up_used[u], per_u + 1)
            v.wait_ge(hidden_turned, n)
            v.tensor_tensor(hidden[:], silu[:], bank[3][:], ALU.mult).then_inc(hidden_ready, 1)

        def out_high(v, n, u, per_u):
            v.wait_ge(down_used[u], per_u + 1)
            v.wait_ge(stored[u], per_u * 16)
            v.tensor_copy(y[u][:, BANK:D], bank[6][:]).then_inc(y_high, 1)

        def if_used(eng, i):
            return eng.If(eng.value_load(more[0:1, 1, ds(i, 1)], min_val=0, max_val=1))

        @block.sync
        def _(sp):
            with nc.allow_non_contiguous_dma("a slot's token for each partition"):
                sp.dma_start(ids[:], slot_token.rearrange("(b p) a -> p (b a)", p=P)).then_inc(ids_loaded, 16)
                sp.dma_start(gain[:], a["norm2_gain"].rearrange("(k p) -> p k", p=P)).then_inc(gain_loaded, 16)
            with sp.Fori(0, half) as j:
                for u in range(2):
                    e = j * 2 + u
                    sp.wait_ge(up_used[u], j)
                    load_up(sp, a["w_gate"][ds(e, 1)].rearrange("a d f -> (a d) f"),
                            a["w_up"][ds(e, 1)].rearrange("a d f -> (a d) f"), u)
                    sp.wait_ge(down_used[u], j)
                    load_down(sp, a["w_down"][ds(e, 1)].rearrange("a f d -> (a f) d"), u)
            with sp.Fori(0, MORE_BLOCKS) as i:
                with if_used(sp, i):
                    e = sp.value_load(more[0:1, 0, ds(i, 1)], min_val=0, max_val=EXPERTS - 1)
                    sp.wait_ge(up_used[0], half + i)
                    load_up(sp, a["w_gate"][ds(e, 1)].rearrange("a d f -> (a d) f"),
                            a["w_up"][ds(e, 1)].rearrange("a d f -> (a d) f"), 0)
                    sp.wait_ge(down_used[0], half + i)
                    load_down(sp, a["w_down"][ds(e, 1)].rearrange("a f d -> (a f) d"), 0)

        @block.gpsimd
        def _(pool):
            def fetch(at, u, per_u):
                pool.tensor_copy(pick[u][:], ids[:, at]).then_inc(picked[u], 1)
                pool.wait_ge(picked[u], per_u + 1)
                pool.sem_inc(passed, 1)
                pool.indirect_dma_start(out=rows_in[u][:], out_offset=None, in_=h_rows,
                                        in_offset=bass.IndirectOffsetOnAxis(ap=pick[u][:, 0:1], axis=0)).then_inc(gathered[u], 16)

            pool.wait_ge(ids_loaded, 16)
            with pool.Fori(0, half) as j:
                for u in range(2):
                    pool.wait_ge(x_turned, j * 2)
                    pool.wait_ge(gathered[u], j * 16)
                    fetch(ds(j * 2 + u, 1), u, j)
            with pool.Fori(0, MORE_BLOCKS) as i:
                with if_used(pool, i):
                    pool.wait_ge(x_turned, i + EXPERTS)
                    pool.wait_ge(gathered[0], (i + half) * 16)
                    fetch(ds(i + EXPERTS, 1), 0, i + half)

        @block.tensor
        def _(pe):
            turn_x(pe, 0, 0, 0)
            with pe.Fori(0, half - 1) as j:
                lift(pe, j * 2, 0, j)
                turn_x(pe, j * 2 + 1, 1, j)
                lower(pe, j * 2, 0, j)
                lift(pe, j * 2 + 1, 1, j)
                turn_x(pe, j * 2 + 2, 0, j + 1)
                lower(pe, j * 2 + 1, 1, j)
            n, j = EXPERTS - 2, half - 1
            lift(pe, n, 0, j)
            turn_x(pe, n + 1, 1, j)
            lower(pe, n, 0, j)
            lift(pe, n + 1, 1, j)
            lower(pe, n + 1, 1, j)
            with pe.Fori(0, MORE_BLOCKS) as i:
                with if_used(pe, i):
                    turn_x(pe, i + EXPERTS, 0, i + half)
                    lift(pe, i + EXPERTS, 0, i + half)
                    lower(pe, i + EXPERTS, 0, i + half)

        @block.scalar
        def _(act):
            def to(n):
                return y_rows[ds(n * P, P), :]

            act.wait_ge(gain_loaded, 16)
            x_high(act, 0, 0)
            with act.Fori(0, half - 1) as j:
                for u in range(2):
                    n = j * 2 + u
                    gate_and_out(act, n, u, j, None)
                    x_high(act, n + 1, 1 - u)
                    out_low(act, n, u, j, to(n))
            n, j = EXPERTS - 2, half - 1
            gate_and_out(act, n, 0, j, None)
            x_high(act, n + 1, 1)
            out_low(act, n, 0, j, to(n))
            gate_and_out(act, n + 1, 1, j, None)
            out_low(act, n + 1, 1, j, to(n + 1))
            act.wait_ge(stored[1], 16 * half)
            act.wait_ge(stored[0], 16 * half)
            with act.Fori(0, MORE_BLOCKS) as i:
                with if_used(act, i):
                    n = i + EXPERTS
                    x_high(act, n, 0)
                    gate_and_out(act, n, 0, i + half, None)
                    out_low(act, n, 0, i + half, to(n))
                    act.wait_ge(stored[0], (i + half) * 16 + 16)
                    act.sem_inc(passed, 1)

        @block.vector
        def _(v):
            v.wait_ge(gain_loaded, 16)
            x_low(v, 0, 0)
            with v.Fori(0, half - 1) as j:
                for u in range(2):
                    n = j * 2 + u
                    hide(v, n, u, j)
                    x_low(v, n + 1, 1 - u)
                    out_high(v, n, u, j)
            n, j = EXPERTS - 2, half - 1
            hide(v, n, 0, j)
            x_low(v, n + 1, 1)
            out_high(v, n, 0, j)
            hide(v, n + 1, 1, j)
            out_high(v, n + 1, 1, j)
            with v.Fori(0, MORE_BLOCKS) as i:
                with if_used(v, i):
                    n = i + EXPERTS
                    x_low(v, n, 0)
                    hide(v, n, 0, i + half)
                    out_high(v, n, 0, i + half)


def combine_stage(nc, x, y_rows, slot_index, slot_weight, gain_dram, x_dram):
    with Stage(nc, "combine") as st:
        gain = st.sb("gain", [P, D])
        got = [[st.sb(f"got{c}{u}", [P, D]) for u in range(2)] for c in range(2)]
        pick = [[st.sb(f"pick{c}{u}", [P, 1], I32) for u in range(2)] for c in range(2)]
        junk = [st.sb(f"junk{u}", [P, D]) for u in range(2)]
        square, mean, root, rstd = ([st.sb(f"{n}{u}", [P, 1]) for u in range(2)] for n in ("square", "mean", "root", "rstd"))
        gain_loaded, passed, stored = st.sem("gain_loaded"), st.sem("passed"), st.sem("stored")
        gathered, picked, added, squared, mean_ready, root_ready, rstd_ready, normed = (
            [st.sem(f"{n}{u}") for u in range(2)]
            for n in ("gathered", "picked", "added", "squared", "mean_ready", "root_ready", "rstd_ready", "normed"))
        block = st.open()

        @block.sync
        def _(sp):
            sp.dma_start(gain[:], rows(gain_dram, D)).then_inc(gain_loaded, 16)
            with sp.Fori(0, TT // 2) as j:
                for u in range(2):
                    t = j * 2 + u
                    sp.wait_ge(normed[u], j + 1)
                    sp.dma_start(x_dram[ds(t * P, P), :], x[:, ds(t, 1), :].rearrange("p a d -> p (a d)"))\
                        .then_inc(stored, 16)
            sp.wait_ge(stored, 16 * TT)

        @block.gpsimd
        def _(pool):
            with pool.Fori(0, TT // 2) as j:
                for u in range(2):
                    pool.wait_ge(gathered[u], j * 32)
                    pool.wait_ge(added[u], j * 2)
                    for c in range(2):
                        pool.tensor_copy(pick[c][u][:], slot_index[:, c, ds(j * 2 + u, 1)]).then_inc(picked[u], 1)
                    pool.wait_ge(picked[u], j * 2 + 2)
                    pool.sem_inc(passed, 1)
                    for c in range(2):
                        pool.indirect_dma_start(out=got[c][u][:], out_offset=None, in_=y_rows,
                                                in_offset=bass.IndirectOffsetOnAxis(ap=pick[c][u][:, 0:1], axis=0))\
                            .then_inc(gathered[u], 16)

        @block.vector
        def _(v):
            v.wait_ge(gain_loaded, 16)
            with v.Fori(0, TT // 2) as j:
                for u in range(2):
                    t = j * 2 + u
                    row = x[:, ds(t, 1), :].rearrange("p a d -> p (a d)")
                    v.wait_ge(gathered[u], j * 32 + 32)
                    for c in range(2):
                        v.scalar_tensor_tensor(out=row, in0=got[c][u][:], scalar=slot_weight[:, c, ds(t, 1)], in1=row,
                                               op0=ALU.mult, op1=ALU.add).then_inc(added[u], 1)
                        v.wait_ge(added[u], j * 2 + c + 1)
                    v.wait_ge(squared[u], j + 1)
                    v.tensor_scalar(mean[u][:], square[u][:], 1.0 / D, EPS, ALU.mult, ALU.add).then_inc(mean_ready[u], 1)
                    v.wait_ge(root_ready[u], j + 1)
                    v.reciprocal(rstd[u][:], root[u][:]).then_inc(rstd_ready[u], 1)
                    v.wait_ge(rstd_ready[u], j + 1)
                    v.scalar_tensor_tensor(out=row, in0=row, scalar=rstd[u][:, 0:1], in1=gain[:], op0=ALU.mult,
                                           op1=ALU.mult).then_inc(normed[u], 1)
                    v.wait_ge(normed[u], j + 1)

        @block.scalar
        def _(act):
            with act.Fori(0, TT // 2) as j:
                for u in range(2):
                    act.wait_ge(added[u], j * 2 + 2)
                    act.wait_ge(mean_ready[u], j)
                    act.activation(junk[u][:], x[:, ds(j * 2 + u, 1), :].rearrange("p a d -> p (a d)"), ACT.Square,
                                   accum_out=square[u][:]).then_inc(squared[u], 1)
                    act.wait_ge(mean_ready[u], j + 1)
                    act.wait_ge(rstd_ready[u], j)
                    act.activation(root[u][:], mean[u][:], ACT.Sqrt).then_inc(root_ready[u], 1)


MLA_HEADS, Q_LORA, KV_LORA, NOPE, ROPE, V_DIM = 8, 256, 128, 64, 32, 64
QK = NOPE + ROPE
SC, SC_TAPS = 256, 3
SSD_HEADS, SSD_HD, SSD_GROUPS, SSD_STATE, SSD_TAPS = 4, 64, 2, 128, 4
SSD = SSD_HEADS * SSD_HD
XBC = SSD + 2 * SSD_GROUPS * SSD_STATE
LATENT = Q_LORA + KV_LORA + ROPE
SC_AT = LATENT
Z_AT = SC_AT + 3 * SC
XBC_AT = Z_AT + SSD
DT_AT = XBC_AT + XBC
TM_COLS = LATENT + SSD + SSD_HEADS
SC_T, XBC_T = 3 * SC // P, XBC // P
MLA_T = MLA_HEADS * V_DIM // P


def wide(psum, b, n):
    return psum[:, b:b + n, :].rearrange("p a b -> p (a b)")


def project2_stage(nc, psum, bank, high, low, feat, a, rows2, xbc):
    with Stage(nc, "project2") as st:
        w_tm, w_tm_low = st.twin("w_tm", [P, KT, TM_COLS])
        w_fm, w_fm_low = zip(*(st.twin(f"w_fm{u}", [P, KT, P]) for u in range(2)))
        w_tm_high = st.sb("w_tm_high", [P, KT, TM_COLS], F32R)
        w_fm_high = [st.sb(f"w_fm_high{u}", [P, KT, P], F32R) for u in range(2)]
        sc = st.sb("sc", [P, SC_T, S])
        acc = st.sb("acc", [P, S])
        taps, bias = st.sb("taps", [P, XBC_T, SSD_TAPS]), st.sb("bias", [P, XBC_T])
        sc_taps = st.sb("sc_taps", [P, SC // P, SC_TAPS])
        const, tm_loaded = st.sem("const"), st.sem("tm_loaded")
        fm_loaded = [st.sem(f"fm_loaded{u}") for u in range(2)]
        made = [st.sem(f"made{u}") for u in range(2)]
        tm_high_ready, tm_low_ready = st.sem("tm_high_ready"), st.sem("tm_low_ready")
        fm_high_ready, fm_low_ready = ([st.sem(f"{n}{u}") for u in range(2)] for n in ("fm_high_ready", "fm_low_ready"))
        product, latent_out, z_out, sc_out, scaled, tapped, xbc_out = (
            st.sem(n) for n in ("product", "latent_out", "z_out", "sc_out", "scaled", "tapped", "xbc_out"))
        gated, sc_scaled, sc_order = st.sem("gated"), st.sem("sc_scaled"), st.sem("sc_order")
        block = st.open()

        def cols(w, at, n):
            return w[:, at:at + n].rearrange("(k p) n -> p k n", p=P)

        w_dram = a["w_in_2"]

        @block.sync
        def _(sp):
            sp.dma_start(w_tm[:, :, 0:LATENT], cols(w_dram, 0, LATENT)).then_inc(tm_loaded, 16)
            sp.dma_start(w_tm[:, :, LATENT:LATENT + SSD], cols(w_dram, Z_AT, SSD)).then_inc(tm_loaded, 16)
            with nc.allow_non_contiguous_dma("a few taps for each channel"):
                sp.dma_start(w_tm[:, :, LATENT + SSD:], cols(w_dram, DT_AT, SSD_HEADS)).then_inc(tm_loaded, 16)
                for i in range(SSD_TAPS):
                    sp.dma_start(taps[:, :, i], a["ssd_conv_w_2"][i, :].rearrange("(c p) -> p c", p=P)).then_inc(const, 16)
                sp.dma_start(bias[:], a["ssd_conv_b_2"].rearrange("(c p) -> p c", p=P)).then_inc(const, 16)
                for i in range(SC_TAPS):
                    sp.dma_start(sc_taps[:, :, i], a["sc_conv_w_2"][i, :].rearrange("(c p) -> p c", p=P)).then_inc(const, 16)
            with sp.Fori(0, SC_T) as j:
                for u, at in enumerate((SC_AT, XBC_AT)):
                    sp.wait_ge(made[u], j)
                    sp.dma_start(w_fm[u][:], w_dram[:, ds(j * P + at, P)].rearrange("(k p) n -> p k n", p=P))\
                        .then_inc(fm_loaded[u], 16)

        @block.tensor
        def _(pe):
            pe.wait_ge(tm_low_ready, 1)
            for t in range(TT):
                tile = slice(t * P, (t + 1) * P)
                if t >= 4:
                    pe.wait_ge(latent_out, t - 3)
                    pe.wait_ge(z_out, t - 3)
                for n, (lo_, hi) in enumerate(((0, LATENT), (LATENT, TM_COLS))):
                    for k in range(KT):
                        last = three_passes(pe, bank[2 * (t % 4) + n][:, 0:hi - lo_], (high[:, k, tile], low[:, k, tile]),
                                            (w_tm_high[:, k, lo_:hi], w_tm_low[:, k, lo_:hi]), start=(k == 0), stop=(k == KT - 1))
                    last.then_inc(product, 1)
            pe.wait_ge(latent_out, TT)
            pe.wait_ge(z_out, TT)
            with pe.Fori(0, SC_T) as j:
                for u in range(2):
                    pe.wait_ge(fm_low_ready[u], j + 1)
                    pe.wait_ge((sc_out, tapped)[u], j * (1, 3)[u])
                    for n in range(2):
                        half = slice(n * BANK, (n + 1) * BANK)
                        for k in range(KT):
                            last = three_passes(pe, bank[2 * u + n][:], (w_fm_high[u][:, k, :], w_fm_low[u][:, k, :]),
                                                (high[:, k, half], low[:, k, half]), start=(k == 0), stop=(k == KT - 1))
                    last.then_inc(made[u], 1)

        @block.scalar
        def _(act):
            def split(j, u):
                act.wait_ge(fm_loaded[u], j * 16 + 16)
                split_high(act, w_fm_high[u][:], w_fm[u][:]).then_inc(fm_high_ready[u], 1)

            def take_sc(j):
                act.wait_ge(made[0], j + 1)
                act.activation(sc[:, ds(j, 1), :].rearrange("p a s -> p (a s)"), wide(psum, 0, 2), ACT.Copy).then_inc(sc_out, 1)

            def convolve(j):
                act.wait_ge(made[1], j + 1)
                act.wait_ge(xbc_out, j)
                act.activation(acc[:], wide(psum, 2, 2), ACT.Identity, scale=taps[:, ds(j, 1), SSD_TAPS - 1],
                               bias=bias[:, ds(j, 1)]).then_inc(scaled, 1)
                act.wait_ge(tapped, j * 3 + 3)
                act.activation(xbc[:, ds(j, 1), :].rearrange("p a s -> p (a s)"), acc[:], ACT.Silu).then_inc(xbc_out, 1)

            act.wait_ge(tm_loaded, 48)
            split_high(act, w_tm_high[:], w_tm[:]).then_inc(tm_high_ready, 1)
            for u in range(2):
                split(0, u)
            for t in range(TT):
                act.wait_ge(product, 2 * t + 1)
                act.activation(rows2[:, t, 0:LATENT], bank[2 * (t % 4)][:, 0:LATENT], ACT.Copy).then_inc(latent_out, 1)
            act.wait_ge(const, 16 * (SSD_TAPS + 1 + SC_TAPS))
            with act.Fori(0, SC_T - 1) as j:
                take_sc(j)
                split(j + 1, 0)
                convolve(j)
                split(j + 1, 1)
            take_sc(SC_T - 1)
            convolve(SC_T - 1)
            for i in range(SC // P):
                act.wait_ge(gated, i + 1)
                act.activation(sc[:, i + 4, :], sc[:, i + 2, :], ACT.Copy, scale=sc_taps[:, i, SC_TAPS - 1:SC_TAPS])\
                    .then_inc(sc_scaled, 1)

        @block.vector
        def _(v):
            def split(j, u):
                v.wait_ge(fm_high_ready[u], j + 1)
                split_low(v, w_fm_low[u][:], w_fm[u][:], w_fm_high[u][:]).then_inc(fm_low_ready[u], 1)

            def convolve(j):
                v.wait_ge(scaled, j + 1)
                for i in range(1, SSD_TAPS):
                    if i > 1:
                        v.wait_ge(tapped, j * 3 + i - 1)
                    v.scalar_tensor_tensor(out=acc[:, i:], in0=wide(psum, 2, 2)[:, 0:S - i],
                                           scalar=taps[:, ds(j, 1), SSD_TAPS - 1 - i], in1=acc[:, i:],
                                           op0=ALU.mult, op1=ALU.add).then_inc(tapped, 1)

            v.wait_ge(tm_high_ready, 1)
            split_low(v, w_tm_low[:], w_tm[:], w_tm_high[:]).then_inc(tm_low_ready, 1)
            for u in range(2):
                split(0, u)
            for t in range(TT):
                v.wait_ge(product, 2 * t + 2)
                v.tensor_copy(rows2[:, t, LATENT:], bank[2 * (t % 4) + 1][:, 0:SSD + SSD_HEADS]).then_inc(z_out, 1)
            v.wait_ge(const, 16 * (SSD_TAPS + 1 + SC_TAPS))
            with v.Fori(0, XBC_T - 1) as j:
                split(j + 1, 0)
                convolve(j)
                split(j + 1, 1)
            convolve(XBC_T - 1)
            v.wait_ge(sc_out, SC_T)
            v.wait_ge(made[1], XBC_T)
            for i in range(2):
                v.tensor_tensor(sc[:, i + 2, :], sc[:, i + 2, :], sc[:, i + 4, :], ALU.mult).then_inc(gated, 1)
            for i in range(2):
                v.wait_ge(sc_scaled, i + 1)
                for n in range(1, SC_TAPS):
                    v.scalar_tensor_tensor(out=sc[:, i + 4, n:], in0=sc[:, i + 2, 0:S - n],
                                           scalar=sc_taps[:, i, SC_TAPS - 1 - n:SC_TAPS - n], in1=sc[:, i + 4, n:],
                                           op0=ALU.mult, op1=ALU.add).then_inc(sc_order, 1)
                    v.wait_ge(sc_order, 3 * i + n)
                v.tensor_tensor(feat[:, MLA_T + i, :], sc[:, i + 4, :], sc[:, i, :], ALU.mult).then_inc(sc_order, 1)


def mixers2_stage(nc, bank, ident, a, rows2, xbc, feat, q_t, k_t, values, spare):
    R2 = ROPE // 2
    with Stage(nc, "mixers2") as st:
        q_cols, kv_cols = MLA_HEADS * QK, MLA_HEADS * (NOPE + V_DIM)
        w_q = three(spare[:, 0:Q_LORA // P * q_cols], Q_LORA // P)
        w_kv = spare[:, Q_LORA // P * q_cols:Q_LORA // P * q_cols + kv_cols]
        gains = st.sb("gains", [P, 3])
        incl = st.sb("incl", [P, P])
        inv_freq = st.sb("inv_freq", [P, R2])
        pos_i, pos = st.sb("pos_i", [P, TT], I32), st.sb("pos", [P, TT])
        angle, turns, wrap = (st.sb(n, [P, TT, R2]) for n in ("angle", "turns", "wrap"))
        turns_i = st.sb("turns_i", [P, TT, R2], I32)
        cos, sin = st.sb("cos", [P, TT, R2]), st.sb("sin", [P, TT, R2])
        dt_bias, a_log, d_skip = (st.sb(n, [P, SSD_HEADS]) for n in ("dt_bias", "a_log", "d_skip"))
        dt, dt_raw, soft, a_dt = (st.sb(n, [P, TT, SSD_HEADS]) for n in ("dt", "dt_raw", "soft", "a_dt"))
        ssd_gain = st.sb("ssd_gain", [P, SSD // P])
        junk = st.sb("junk", [P, Q_LORA])
        stats = st.sb("stats", [P, 4, 2])
        latent = st.sb("latent", [P, Q_LORA + KV_LORA])
        latent_t = st.sb("latent_t", [P, 3, P])
        q_row = st.sb("q_row", [P, MLA_HEADS + 1, QK])
        k_row = st.sb("k_row", [P, MLA_HEADS, QK])
        rot = st.sb("rot", [P, 4, MLA_HEADS + 1, R2])
        cur = st.sb("cur", [P, XBC_T, P])
        row = st.sb("row", [P, BANK])
        a_wide, decay, pt = (st.sb(n, [P, SSD_HEADS, P]) for n in ("a_wide", "decay", "pt"))
        run, to_end, run_exp, tile_exp, end_gap = (st.sb(n, [P, SSD_HEADS]) for n in ("run", "to_end", "run_exp", "tile_exp", "end_gap"))
        xdt, xdt_end, state, y, part, silu_z = (st.sb(n, [P, SSD]) for n in ("xdt", "xdt_end", "state", "y", "part", "silu_z"))
        y_stats = st.sb("y_stats", [P, 4])
        names = ("const angle_ready wrapped trig_ready soft_asked soft_ready a_asked rates_ready dve_order pool_order turn_done "
                 "squared mean_ready root_ready latent_ready latent_turned latent_t_ready lifted q_ready k_ready v_ready "
                 "q_rotated k_full heads_turned heads_even heads_odd copied row_turned row_ready a_wide_ready run_made "
                 "run_ready scored gap_ready decay_ready gaps_ready pt_ready xdt_ready y_made state_made silu_ready "
                 "y_mean y_root y_ready y_turned y_out pool_passed").split()
        s = {n: st.sem(n) for n in names}
        block = st.open()
        with_const = [
            (w_q, a["mla_w_q_up_2"].rearrange("(k p) n -> p k n", p=P)), (w_kv, a["mla_w_kv_up_2"]),
            (gains[:, 0:2], a["mla_q_norm_2"].rearrange("(k p) -> p k", p=P)),
            (gains[:, 2:3], a["mla_kv_norm_2"].rearrange("(k p) -> p k", p=P)),
            (ssd_gain[:], a["ssd_norm_2"].rearrange("(k p) -> p k", p=P)),
            (incl[:], a["c_incl"]), (inv_freq[:], a["c_inv_freq"]),
            (pos_i[:], a["positions_2"].rearrange("(t p) -> p t", p=P)),
            (dt_bias[:], rows(a["ssd_dt_bias_2"], SSD_HEADS)), (a_log[:], rows(a["ssd_a_log_2"], SSD_HEADS)),
            (d_skip[:], rows(a["ssd_d_2"], SSD_HEADS))]

        @block.sync
        def _(sp):
            with nc.allow_non_contiguous_dma("gains and positions, one to a partition"):
                for to, of in with_const:
                    sp.dma_start(to, of).then_inc(s["const"], 16)

        @block.gpsimd
        def _(pool):
            pool.wait_ge(s["trig_ready"], 2)
            with pool.Fori(0, TT) as t:
                steps = [0]

                def link(ins):
                    steps[0] += 1
                    ins.then_inc(s["pool_order"], 1)
                    pool.wait_ge(s["pool_order"], t * 7 + steps[0])
                    pool.sem_inc(s["pool_passed"], 1)

                pool.wait_ge(s["turn_done"], t * 4)
                pool.sem_inc(s["pool_passed"], 1)
                pool.tensor_copy(cur[:], xbc[:, :, ds(t * P, P)]).then_inc(s["copied"], 1)
                link(pool.tensor_copy(q_row[:, MLA_HEADS, NOPE:QK],
                                      rows2[:, ds(t, 1), Q_LORA + KV_LORA:LATENT].rearrange("p a d -> p (a d)")))
                pool.wait_ge(s["q_ready"], t * 2 + 2)
                pool.sem_inc(s["pool_passed"], 1)
                first, second = q_row[:, :, NOPE:NOPE + R2], q_row[:, :, NOPE + R2:QK]
                c, n = (x[:, ds(t, 1), :].to_broadcast([P, MLA_HEADS + 1, R2]) for x in (cos, sin))
                link(pool.tensor_tensor(rot[:, 0], first, c, ALU.mult))
                link(pool.tensor_tensor(rot[:, 1], second, n, ALU.mult))
                link(pool.tensor_tensor(rot[:, 2], second, c, ALU.mult))
                link(pool.tensor_tensor(rot[:, 3], first, n, ALU.mult))
                link(pool.tensor_tensor(first, rot[:, 0], rot[:, 1], ALU.subtract))
                link(pool.tensor_tensor(second, rot[:, 2], rot[:, 3], ALU.add))
                pool.tensor_copy(k_row[:, :, NOPE:QK], q_row[:, MLA_HEADS:MLA_HEADS + 1, NOPE:QK]
                                 .to_broadcast([P, MLA_HEADS, ROPE])).then_inc(s["q_rotated"], 1)
                pool.wait_ge(s["q_rotated"], t + 1)
                pool.wait_ge(s["copied"], t + 1)
                pool.sem_inc(s["turn_done"], 1)

        @block.scalar
        def _(act):
            act.wait_ge(s["const"], 16 * len(with_const))
            act.wait_ge(s["soft_asked"], 1)
            act.activation(soft[:], soft[:], ACT.Exp, scale=-1.0).then_inc(s["soft_ready"], 1)
            act.activation(a_log[:], a_log[:], ACT.Exp).then_inc(s["rates_ready"], 1)
            act.wait_ge(s["soft_ready"], 1)
            act.activation(soft[:], soft[:], ACT.Ln, bias=1.0).then_inc(s["soft_ready"], 1)
            for n, to in enumerate((sin, cos)):
                act.wait_ge(s["angle_ready"], n + 1)
                act.activation(to[:], wrap[:] if n else angle[:], ACT.Sin).then_inc(s["trig_ready"], 1)
            with act.Fori(0, TT) as t:
                act.wait_ge(s["turn_done"], t * 4)
                lat = rows2[:, ds(t, 1), :].rearrange("p a d -> p (a d)")
                act.activation(junk[:], lat[:, 0:Q_LORA], ACT.Square, accum_out=stats[:, 0, 0:1]).then_inc(s["squared"], 1)
                act.wait_ge(s["squared"], t * 2 + 1)
                act.activation(junk[:, 0:KV_LORA], lat[:, Q_LORA:Q_LORA + KV_LORA], ACT.Square,
                               accum_out=stats[:, 0, 1:2]).then_inc(s["squared"], 1)
                act.wait_ge(s["mean_ready"], t * 2 + 2)
                act.activation(stats[:, 2, :], stats[:, 1, :], ACT.Sqrt).then_inc(s["root_ready"], 1)
                act.activation(silu_z[:], lat[:, LATENT:LATENT + SSD], ACT.Silu).then_inc(s["silu_ready"], 1)
                act.wait_ge(s["row_turned"], t + 1)
                act.activation(row[:], bank[5][:], ACT.Copy).then_inc(s["row_ready"], 1)
                act.wait_ge(s["gap_ready"], t + 1)
                act.activation(decay[:], decay[:], ACT.Exp).then_inc(s["decay_ready"], 1)
                act.wait_ge(s["gaps_ready"], t + 1)
                act.activation(to_end[:], end_gap[:], ACT.Exp).then_inc(s["decay_ready"], 1)
                act.activation(run_exp[:], run[:], ACT.Exp).then_inc(s["decay_ready"], 1)
                act.activation(tile_exp[:], three(bank[6][:], SSD_HEADS)[:, :, P - 1], ACT.Exp).then_inc(s["decay_ready"], 1)
                for n in range(2):
                    act.wait_ge(s["lifted"], t * 4 + n + 1)
                    act.activation(q_row[:, 4 * n:4 * n + 4, :], three(bank[1 + n][:, 0:4 * QK], 4), ACT.Copy).then_inc(s["q_ready"], 1)
                for n in range(2):
                    act.wait_ge(s["k_ready"], t * 2 + n + 1)
                    act.activation(values[:, ds(t, 1), 4 * V_DIM * n:4 * V_DIM * (n + 1)].rearrange("p a (h d) -> p (a h) d", d=V_DIM),
                                   three(bank[3 + n][:], 4)[:, :, NOPE:], ACT.Copy).then_inc(s["v_ready"], 1)
                for n, to in enumerate((q_t, k_t)):
                    act.wait_ge(s["heads_turned"], t * 4 + 2 * n + 1)
                    act.activation(to[:, 0:4, ds(t * P, P)], three(bank[1 + 2 * n][0:QK, :], 4), ACT.Copy).then_inc(s["heads_even"], 1)
                act.wait_ge(s["y_mean"], t + 1)
                act.activation(y_stats[:, 2:3], y_stats[:, 1:2], ACT.Sqrt).then_inc(s["y_root"], 1)
                act.wait_ge(s["y_turned"], t + 1)
                for i in range(2):
                    act.activation(feat[:, KT - 2 + i, ds(t * P, P)], bank[7][:, i * P:(i + 1) * P], ACT.Copy,
                                   scale=ssd_gain[:, i:i + 1]).then_inc(s["y_out"], 1)
                act.wait_ge(s["y_out"], t * 2 + 2)
                act.wait_ge(s["heads_even"], t * 2 + 2)
                act.sem_inc(s["turn_done"], 1)

        @block.tensor
        def _(pe):
            pe.wait_ge(s["const"], 16 * len(with_const))
            with pe.Fori(0, TT) as t:
                pe.wait_ge(s["turn_done"], t * 4)
                pe.wait_ge(s["copied"], t + 1)
                for i in range(4):
                    last = pe.transpose(bank[5][:, i * P:(i + 1) * P], cur[:, i, :], ident[:])
                last.then_inc(s["row_turned"], 1)
                for gr in range(SSD_GROUPS):
                    last = pe.matmul(bank[7][:, gr * P:(gr + 1) * P], cur[:, 2 + gr, :], cur[:, 4 + gr, :], start=True, stop=True)
                last.then_inc(s["scored"], 1)
                pe.wait_ge(s["a_wide_ready"], t + 1)
                for h in range(SSD_HEADS):
                    pe.matmul(bank[6][:, h * P:(h + 1) * P], a_wide[:, h, :], incl[:], start=True, stop=True)
                pe.matmul(bank[7][:, 2 * P:2 * P + SSD_HEADS], incl[:], a_dt[:, ds(t, 1), :].rearrange("p a h -> p (a h)"),
                          start=True, stop=True).then_inc(s["run_made"], 1)
                pe.wait_ge(s["latent_ready"], t * 2 + 2)
                for i in range(3):
                    last = pe.transpose(bank[0][:, i * P:(i + 1) * P], latent[:, i * P:(i + 1) * P], ident[:])
                last.then_inc(s["latent_turned"], 1)
                pe.wait_ge(s["latent_t_ready"], t + 1)
                for n in range(2):
                    for k in range(2):
                        last = pe.matmul(bank[1 + n][:, 0:4 * QK], latent_t[:, k, :], w_q[:, k, 4 * QK * n:4 * QK * (n + 1)],
                                         start=(k == 0), stop=(k == 1))
                    last.then_inc(s["lifted"], 1)
                for n in range(2):
                    pe.matmul(bank[3 + n][:], latent_t[:, 2, :], w_kv[:, n * BANK:(n + 1) * BANK], start=True, stop=True)\
                        .then_inc(s["lifted"], 1)
                pe.wait_ge(s["row_ready"], t + 1)
                pe.wait_ge(s["xdt_ready"], t * 2 + 2)
                pe.wait_ge(s["pt_ready"], t + 1)
                for gr in range(SSD_GROUPS):
                    pe.matmul(bank[5][:, gr * P:(gr + 1) * P], cur[:, 4 + gr, :], state[:, gr * P:(gr + 1) * P], start=True, stop=True)
                for h in range(SSD_HEADS):
                    at = h * SSD_HD
                    last = pe.matmul(bank[5][:, SSD + at:SSD + at + SSD_HD], pt[:, h, :], xdt[:, at:at + SSD_HD], start=True, stop=True)
                last.then_inc(s["y_made"], 1)
                pe.wait_ge(s["decay_ready"], t * 4 + 4)
                for gr in range(SSD_GROUPS):
                    last = pe.matmul(bank[6][:, gr * P:(gr + 1) * P], row[:, SSD + gr * P:SSD + (gr + 1) * P],
                                     xdt_end[:, gr * P:(gr + 1) * P], start=True, stop=True)
                last.then_inc(s["state_made"], 1)
                pe.wait_ge(s["q_rotated"], t + 1)
                pe.wait_ge(s["k_ready"], t * 2 + 2)
                pe.wait_ge(s["v_ready"], t * 2 + 2)
                for n in range(4):
                    of = (q_row, k_row)[n // 2]
                    for h in range(4):
                        last = pe.transpose(bank[1 + n][0:QK, h * P:(h + 1) * P], of[:, 4 * (n % 2) + h, :], ident[:])
                    last.then_inc(s["heads_turned"], 1)
                pe.wait_ge(s["y_ready"], t + 1)
                for i in range(2):
                    last = pe.transpose(bank[7][:, i * P:(i + 1) * P], y[:, i * P:(i + 1) * P], ident[:])
                last.then_inc(s["y_turned"], 1)
                pe.wait_ge(s["y_out"], t * 2 + 2)
                pe.sem_inc(s["turn_done"], 1)

        @block.vector
        def _(v):
            BEFORE, PER = 21, 14
            steps = [0]
            base = [0]

            def link(ins):
                steps[0] += 1
                ins.then_inc(s["dve_order"], 1)
                v.wait_ge(s["dve_order"], base[0] + steps[0])

            v.wait_ge(s["const"], 16 * len(with_const))
            link(v.memset(state[:], 0.0))
            link(v.tensor_tensor(dt_raw[:], rows2[:, :, LATENT + SSD:], per_block(dt_bias[:], TT), ALU.add))
            v.scalar_tensor_tensor(out=soft[:], in0=dt_raw[:], scalar=-1.0, in1=dt_raw[:], op0=ALU.mult, op1=ALU.max)\
                .then_inc(s["soft_asked"], 1)
            link(v.tensor_copy(pos[:], pos_i[:]))
            link(v.tensor_tensor(angle[:], per_row(pos[:], R2), per_block(inv_freq[:], TT), ALU.mult))
            link(v.tensor_scalar(turns[:], angle[:], float(1 / (2 * np.pi)), None, ALU.mult))
            link(v.tensor_copy(turns_i[:], turns[:]))
            link(v.tensor_copy(turns[:], turns_i[:]))
            two_pi = 2 * np.pi
            high = float(np.float32(6.28125))
            middle = float(np.float32(np.round((two_pi - high) * 2 ** 21) / 2 ** 21))
            for part_of in (high, middle, float(np.float32(two_pi - high - middle))):
                link(v.scalar_tensor_tensor(out=angle[:], in0=turns[:], scalar=-part_of, in1=angle[:], op0=ALU.mult, op1=ALU.add))

            def keep_within(x):
                link(v.tensor_scalar(turns[:], x, float(np.pi), -two_pi, ALU.is_gt, ALU.mult))
                link(v.tensor_tensor(x, x, turns[:], ALU.add))
                link(v.tensor_scalar(turns[:], x, -float(np.pi), two_pi, ALU.is_lt, ALU.mult))
                link(v.tensor_tensor(x, x, turns[:], ALU.add))
                limit = float(np.nextafter(np.float32(np.pi), np.float32(0)))
                return v.tensor_scalar(x, x, limit, -limit, ALU.min, ALU.max)

            keep_within(angle[:]).then_inc(s["angle_ready"], 1)
            v.wait_ge(s["angle_ready"], 1)
            link(v.tensor_scalar(wrap[:], angle[:], float(np.pi / 2), None, ALU.add))
            keep_within(wrap[:]).then_inc(s["angle_ready"], 1)
            v.wait_ge(s["soft_ready"], 2)
            v.wait_ge(s["rates_ready"], 1)
            link(v.scalar_tensor_tensor(out=dt[:], in0=dt_raw[:], scalar=0.0, in1=soft[:], op0=ALU.max, op1=ALU.add))
            link(v.scalar_tensor_tensor(out=a_dt[:], in0=dt[:], scalar=-1.0, in1=per_block(a_log[:], TT), op0=ALU.mult, op1=ALU.mult))
            assert steps[0] == BEFORE, steps
            with v.Fori(0, TT) as t:
                steps[0] = 0
                base[0] = t * PER + BEFORE
                v.wait_ge(s["turn_done"], t * 4)
                lat = rows2[:, ds(t, 1), :].rearrange("p a d -> p (a d)")
                dt_now = dt[:, ds(t, 1), :].rearrange("p a h -> p (a h)")
                v.tensor_copy(a_wide[:], per_row(a_dt[:, ds(t, 1), :].rearrange("p a h -> p (a h)"), P)).then_inc(s["a_wide_ready"], 1)
                v.wait_ge(s["squared"], t * 2 + 2)
                for i, n in enumerate((Q_LORA, KV_LORA)):
                    v.tensor_scalar(stats[:, 1, i:i + 1], stats[:, 0, i:i + 1], 1.0 / n, EPS, ALU.mult, ALU.add).then_inc(s["mean_ready"], 1)
                v.wait_ge(s["root_ready"], t + 1)
                link(v.reciprocal(stats[:, 3, :], stats[:, 2, :]))
                for i, (lo_, hi) in enumerate(((0, Q_LORA), (Q_LORA, Q_LORA + KV_LORA))):
                    v.tensor_scalar(latent[:, lo_:hi], lat[:, lo_:hi], stats[:, 3, i:i + 1], None, ALU.mult).then_inc(s["latent_ready"], 1)
                v.wait_ge(s["run_made"], t + 1)
                link(v.tensor_copy(run[:], bank[7][:, 2 * P:2 * P + SSD_HEADS]))
                link(v.tensor_tensor(decay[:], three(bank[6][:], SSD_HEADS), per_row(run[:], P), ALU.subtract))
                v.tensor_scalar(decay[:], decay[:], 0.0, None, ALU.min).then_inc(s["gap_ready"], 1)
                v.tensor_tensor(end_gap[:], three(bank[6][:], SSD_HEADS)[:, :, P - 1], run[:], ALU.subtract).then_inc(s["gaps_ready"], 1)
                v.wait_ge(s["latent_turned"], t + 1)
                v.tensor_tensor(latent_t[:], three(bank[0][:, 0:3 * P], 3), per_row(gains[:], P), ALU.mult).then_inc(s["latent_t_ready"], 1)
                v.wait_ge(s["row_ready"], t + 1)
                v.tensor_tensor(three(xdt[:], SSD_HEADS), three(row[:, 0:SSD], SSD_HEADS), per_row(dt_now, SSD_HD), ALU.mult)\
                    .then_inc(s["xdt_ready"], 1)
                v.wait_ge(s["decay_ready"], t * 4 + 4)
                v.wait_ge(s["xdt_ready"], t * 2 + 1)
                v.tensor_tensor(three(xdt_end[:], SSD_HEADS), three(xdt[:], SSD_HEADS), per_row(to_end[:], SSD_HD), ALU.mult)\
                    .then_inc(s["xdt_ready"], 1)
                link(v.tensor_tensor(decay[:], decay[:], per_block(incl[:], SSD_HEADS), ALU.mult))
                for gr in range(SSD_GROUPS):
                    each = SSD_HEADS // SSD_GROUPS
                    ins = v.tensor_tensor(pt[:, gr * each:(gr + 1) * each, :], decay[:, gr * each:(gr + 1) * each, :],
                                          per_block(bank[7][:, gr * P:(gr + 1) * P], each), ALU.mult)
                ins.then_inc(s["pt_ready"], 1)
                for n in range(2):
                    v.wait_ge(s["lifted"], t * 4 + 2 + n + 1)
                    v.tensor_copy(k_row[:, 4 * n:4 * n + 4, 0:NOPE], three(bank[3 + n][:], 4)[:, :, 0:NOPE]).then_inc(s["k_ready"], 1)
                v.wait_ge(s["y_made"], t + 1)
                link(v.tensor_tensor(three(y[:], SSD_HEADS), three(bank[5][:, 0:SSD], SSD_HEADS), per_row(run_exp[:], SSD_HD), ALU.mult))
                link(v.tensor_tensor(y[:], y[:], bank[5][:, SSD:2 * SSD], ALU.add))
                link(v.tensor_tensor(three(part[:], SSD_HEADS), three(row[:, 0:SSD], SSD_HEADS), per_row(d_skip[:], SSD_HD), ALU.mult))
                link(v.tensor_tensor(y[:], y[:], part[:], ALU.add))
                v.wait_ge(s["silu_ready"], t + 1)
                link(v.tensor_tensor(y[:], y[:], silu_z[:], ALU.mult))
                v.wait_ge(s["state_made"], t + 1)
                link(v.tensor_tensor(three(state[:], SSD_HEADS), three(state[:], SSD_HEADS), per_row(tile_exp[:], SSD_HD), ALU.mult))
                link(v.tensor_tensor(state[:], state[:], bank[6][:, 0:SSD], ALU.add))
                link(v.tensor_tensor(part[:], y[:], y[:], ALU.mult))
                link(v.tensor_reduce(y_stats[:, 0:1], part[:], AX_X, ALU.add))
                v.tensor_scalar(y_stats[:, 1:2], y_stats[:, 0:1], 1.0 / SSD, EPS, ALU.mult, ALU.add).then_inc(s["y_mean"], 1)
                v.wait_ge(s["y_root"], t + 1)
                link(v.reciprocal(y_stats[:, 3:4], y_stats[:, 2:3]))
                v.tensor_scalar(y[:], y[:], y_stats[:, 3:4], None, ALU.mult).then_inc(s["y_ready"], 1)
                for n, to in enumerate((q_t, k_t)):
                    v.wait_ge(s["heads_turned"], t * 4 + 2 * n + 2)
                    v.tensor_copy(to[:, 4:8, ds(t * P, P)], three(bank[2 + 2 * n][0:QK, :], 4)).then_inc(s["heads_odd"], 1)
                v.wait_ge(s["heads_odd"], t * 2 + 2)
                v.wait_ge(s["y_ready"], t + 1)
                assert steps[0] == PER, steps
                v.sem_inc(s["turn_done"], 1)


def attention_stage(nc, psum, bank, ident, a, q_t, k_t, values, feat, room):
    scale = QK ** -0.5
    TURNS = MLA_HEADS // 2
    N = 2 * TT
    with Stage(nc, "attention") as st:
        q_now = [st.sb(f"q_now{u}", [QK, S]) for u in range(2)]
        future = st.sb("future", [P, P])
        p = [st.sb(f"p{b}", [P, S]) for b in range(2)]
        p_t = [st.sb(f"p_t{b}", [P, TT, P]) for b in range(2)]
        most, bias, total, share = ([st.sb(f"{n}{b}", [P, 1]) for b in range(2)] for n in ("most", "bias", "total", "share"))
        out = three(room[:, 0:TT * MLA_HEADS * V_DIM], TT)
        const = st.sem("const")
        q_copied, scored = ([st.sem(f"{n}{u}") for u in range(2)] for n in ("q_copied", "scored"))
        pool_passed = st.sem("pool_passed")
        masked, most_ready, bias_ready, exp_ready, turned, low_ready, high_ready, made, share_ready, out_ready = (
            st.sem(n) for n in ("masked", "most_ready", "bias_ready", "exp_ready", "turned", "low_ready",
                                "high_ready", "made", "share_ready", "out_ready"))
        out_turned, even_out, odd_out = st.sem("out_turned"), st.sem("even_out"), st.sem("odd_out")
        block = st.open()

        @block.sync
        def _(sp):
            sp.dma_start(future[:], a["c_future"]).then_inc(const, 16)

        @block.gpsimd
        def _(pool):
            with pool.Fori(0, TURNS) as j:
                for u in range(2):
                    pool.wait_ge(scored[u], j * TT)
                    pool.sem_inc(pool_passed, 1)
                    pool.tensor_copy(q_now[u][:], q_t[:, ds(j * 2 + u, 1), :].rearrange("p a s -> p (a s)")).then_inc(q_copied[u], 1)

        @block.tensor
        def _(pe):
            def scores(j, m):
                u, i = m // TT, m % TT
                if i == 0:
                    pe.wait_ge(q_copied[u], j + 1)
                pe.wait_ge(exp_ready, j * N + max(m - 1, 0))
                for n in range(i // 4 + 1):
                    width = min(BANK, (i + 1) * P - n * BANK)
                    last = pe.matmul(bank[2 * (m % 2) + n][:, 0:width], q_now[u][:, i * P:(i + 1) * P],
                                     k_t[:, ds(j * 2 + u, 1), n * BANK:n * BANK + width].rearrange("p a s -> p (a s)"),
                                     start=True, stop=True)
                last.then_inc(scored[u], 1)

            def turn(j, m):
                pe.wait_ge(exp_ready, j * N + m + 1)
                pe.wait_ge(low_ready, j * N + m)
                pe.wait_ge(high_ready, j * N + m)
                i = m % TT
                for b in range(i + 1):
                    last = pe.transpose(bank[4 + b // 4][:, (b % 4) * P:(b % 4 + 1) * P], p[m % 2][:, b * P:(b + 1) * P], ident[:])
                last.then_inc(turned, 1)

            def weigh(j, m):
                u, i = m // TT, m % TT
                pe.wait_ge(low_ready, j * N + m + 1)
                pe.wait_ge(high_ready, j * N + m + 1)
                pe.wait_ge(out_ready, j * N + max(m - 1, 0))
                for b in range(i + 1):
                    last = pe.matmul(bank[6 + m % 2][:, 0:V_DIM], p_t[m % 2][:, b, :],
                                     values[:, b, ds((j * 2 + u) * V_DIM, V_DIM)], start=(b == 0), stop=(b == i))
                last.then_inc(made, 1)

            with pe.Fori(0, TURNS) as j:
                scores(j, 0)
                for m in range(N):
                    if m + 1 < N:
                        scores(j, m + 1)
                    turn(j, m)
                    if m >= 1:
                        weigh(j, m - 1)
                weigh(j, N - 1)
            pe.wait_ge(out_ready, TURNS * N)
            for t in range(TT):
                for k in range(MLA_T):
                    last = pe.transpose(bank[t][:, k * P:(k + 1) * P], out[:, t, k * P:(k + 1) * P], ident[:])
                last.then_inc(out_turned, 1)

        @block.scalar
        def _(act):
            with act.Fori(0, TURNS) as j:
                for m in range(N):
                    i, b = m % TT, m % 2
                    act.wait_ge(bias_ready, j * N + m + 1)
                    act.wait_ge(turned, j * N + max(m - 1, 0))
                    act.wait_ge(share_ready, j * N + max(m - 1, 0))
                    act.activation(p[b][:, 0:(i + 1) * P], wide(psum, 2 * b, 2)[:, 0:(i + 1) * P], ACT.Exp, bias=bias[b][:, 0:1],
                                   scale=scale, accum_out=total[b][:]).then_inc(exp_ready, 1)
                    act.wait_ge(turned, j * N + m + 1)
                    act.wait_ge(made, j * N + max(m - 1, 0))
                    low = min(i + 1, 4)
                    act.activation(p_t[b][:, 0:low, :], three(bank[4][:, 0:low * P], low), ACT.Copy).then_inc(low_ready, 1)
            for t in range(0, TT, 2):
                act.wait_ge(out_turned, t + 1)
                act.activation(feat[:, 0:MLA_T, t * P:(t + 1) * P], three(bank[t][:], MLA_T), ACT.Copy).then_inc(even_out, 1)
            act.wait_ge(even_out, TT // 2)

        @block.vector
        def _(v):
            def bound(j, m):
                i, b = m % TT, m % 2
                at = wide(psum, 2 * b, 2)
                v.wait_ge(scored[m // TT], j * TT + i + 1)
                v.tensor_tensor(at[:, i * P:(i + 1) * P], at[:, i * P:(i + 1) * P], future[:], ALU.add).then_inc(masked, 1)
                v.wait_ge(masked, j * N + m + 1)
                v.wait_ge(bias_ready, j * N + max(m - 1, 0))
                v.tensor_reduce(most[b][:], at[:, 0:(i + 1) * P], AX_X, ALU.max).then_inc(most_ready, 1)
                v.wait_ge(most_ready, j * N + m + 1)
                v.wait_ge(exp_ready, j * N + max(m - 1, 0))
                v.tensor_scalar(bias[b][:], most[b][:], -scale, None, ALU.mult).then_inc(bias_ready, 1)

            def high(j, m):
                i, b = m % TT, m % 2
                v.wait_ge(turned, j * N + m + 1)
                v.wait_ge(made, j * N + max(m - 1, 0))
                if i >= 4:
                    v.tensor_copy(p_t[b][:, 4:i + 1, :], three(bank[5][:, 0:(i - 3) * P], i - 3)).then_inc(high_ready, 1)
                else:
                    v.sem_inc(high_ready, 1)

            def finish(j, m):
                u, i, b = m // TT, m % TT, m % 2
                v.wait_ge(exp_ready, j * N + m + 1)
                v.wait_ge(out_ready, j * N + max(m - 1, 0))
                v.reciprocal(share[b][:], total[b][:]).then_inc(share_ready, 1)
                v.wait_ge(share_ready, j * N + m + 1)
                v.wait_ge(made, j * N + m + 1)
                v.tensor_scalar(out[:, i, ds((j * 2 + u) * V_DIM, V_DIM)], bank[6 + b][:, 0:V_DIM], share[b][:, 0:1], None,
                                ALU.mult).then_inc(out_ready, 1)

            v.wait_ge(const, 16)
            with v.Fori(0, TURNS) as j:
                bound(j, 0)
                for m in range(N):
                    if m + 1 < N:
                        bound(j, m + 1)
                    high(j, m)
                    if m >= 1:
                        finish(j, m - 1)
                finish(j, N - 1)
            for t in range(1, TT, 2):
                v.wait_ge(out_turned, t + 1)
                v.tensor_copy(feat[:, 0:MLA_T, t * P:(t + 1) * P], three(bank[t][:], MLA_T)).then_inc(odd_out, 1)
            v.wait_ge(odd_out, TT // 2)


FFN = 2816
FFN_T = FFN // P
FFN_TAPS = 3


def ffn_up_stage(nc, psum, bank, ident, a, high, low, hidden):
    with Stage(nc, "ffn_up") as st:
        tap_rows = st.sb("tap_rows", [2 * FFN_T, FFN_TAPS + 1, P])
        taps = st.sb("taps", [P, FFN_TAPS + 1, 2 * FFN_T])
        w, w_low = zip(*(zip(*(st.twin(f"w{c}{u}", [P, KT, P]) for u in range(2))) for c in range(2)))
        w_high = [[st.sb(f"w_high{c}{u}", [P, KT, P], F32R) for u in range(2)] for c in range(2)]
        acc = [[st.sb(f"acc{c}{u}", [P, S]) for u in range(2)] for c in range(2)]
        taps_loaded, taps_turned, taps_ready = st.sem("taps_loaded"), st.sem("taps_turned"), st.sem("taps_ready")
        loaded, high_ready, low_ready, made, scaled, tapped = (
            [[st.sem(f"{n}{c}{u}") for u in range(2)] for c in range(2)]
            for n in ("loaded", "high_ready", "low_ready", "made", "scaled", "tapped"))
        silu_ready, hidden_ready = ([st.sem(f"{n}{u}") for u in range(2)] for n in ("silu_ready", "hidden_ready"))
        block = st.open()
        last_tap = FFN_TAPS - 1
        TURNS = FFN_T // 2

        @block.sync
        def _(sp):
            sp.dma_start(tap_rows[:, 0:FFN_TAPS, :], a["ffn_conv_w_2"].rearrange("i (c p) -> c i p", p=P)).then_inc(taps_loaded, 16)
            sp.dma_start(tap_rows[:, FFN_TAPS, :], a["ffn_conv_b_2"].rearrange("(c p) -> c p", p=P)).then_inc(taps_loaded, 16)
            with sp.Fori(0, TURNS) as j:
                for u in range(2):
                    for c in range(2):
                        sp.wait_ge(made[c][u], j)
                        sp.dma_start(w[c][u][:], a["ffn_w_up_2"][:, ds((j * 2 + u) * P + c * FFN, P)]
                                     .rearrange("(k p) n -> p k n", p=P)).then_inc(loaded[c][u], 16)

        @block.tensor
        def _(pe):
            pe.wait_ge(taps_loaded, 32)
            n = 2 * FFN_T
            for i in range(FFN_TAPS + 1):
                last = pe.transpose(bank[0][:, i * n:(i + 1) * n], tap_rows[:, i, :], ident[0:n, 0:n])
            last.then_inc(taps_turned, 1)
            pe.wait_ge(taps_ready, 1)
            with pe.Fori(0, TURNS) as j:
                for u in range(2):
                    for c in range(2):
                        pe.wait_ge(low_ready[c][u], j + 1)
                        pe.wait_ge(tapped[c][u], j * last_tap)
                        for h in range(2):
                            half = slice(h * BANK, (h + 1) * BANK)
                            for k in range(KT):
                                last = three_passes(pe, bank[4 * u + 2 * c + h][:], (w_high[c][u][:, k, :], w_low[c][u][:, k, :]),
                                                    (high[:, k, half], low[:, k, half]), start=(k == 0), stop=(k == KT - 1))
                        last.then_inc(made[c][u], 1)

        @block.scalar
        def _(act):
            def split(j, u, c):
                act.wait_ge(loaded[c][u], j * 16 + 16)
                split_high(act, w_high[c][u][:], w[c][u][:]).then_inc(high_ready[c][u], 1)

            def scale(j, u, c):
                at = j * 2 + u + c * FFN_T
                act.wait_ge(made[c][u], j + 1)
                act.wait_ge(hidden_ready[u], j)
                act.activation(acc[c][u][:], wide(psum, 4 * u + 2 * c, 2), ACT.Identity, scale=taps[:, last_tap, ds(at, 1)],
                               bias=taps[:, FFN_TAPS, ds(at, 1)]).then_inc(scaled[c][u], 1)

            def gate(j, u):
                act.wait_ge(tapped[0][u], j * last_tap + last_tap)
                act.activation(acc[0][u][:], acc[0][u][:], ACT.Silu).then_inc(silu_ready[u], 1)

            act.wait_ge(taps_turned, 1)
            act.activation(taps[:], three(bank[0][:, 0:(FFN_TAPS + 1) * 2 * FFN_T], FFN_TAPS + 1), ACT.Copy).then_inc(taps_ready, 1)
            split(0, 0, 0)
            split(0, 0, 1)
            act.wait_ge(taps_ready, 1)

            def turn(j, last):
                for u in range(2):
                    for c in range(2):
                        if u == 0 or not last:
                            split(j + u, 1 - u, c)
                        scale(j, u, c)
                    gate(j, u)

            with act.Fori(0, TURNS - 1) as j:
                turn(j, False)
            turn(TURNS - 1, True)

        @block.vector
        def _(v):
            def split(j, u, c):
                v.wait_ge(high_ready[c][u], j + 1)
                split_low(v, w_low[c][u][:], w[c][u][:], w_high[c][u][:]).then_inc(low_ready[c][u], 1)

            def convolve(j, u, c):
                at = j * 2 + u + c * FFN_T
                v.wait_ge(scaled[c][u], j + 1)
                for i in range(1, FFN_TAPS):
                    v.wait_ge(tapped[c][u], j * last_tap + i - 1)
                    v.scalar_tensor_tensor(out=acc[c][u][:, i:], in0=wide(psum, 4 * u + 2 * c, 2)[:, 0:S - i],
                                           scalar=taps[:, last_tap - i, ds(at, 1)], in1=acc[c][u][:, i:],
                                           op0=ALU.mult, op1=ALU.add).then_inc(tapped[c][u], 1)

            def hide(j, u):
                v.wait_ge(silu_ready[u], j + 1)
                v.wait_ge(tapped[1][u], j * last_tap + last_tap)
                v.tensor_tensor(hidden[:, ds(j * 2 + u, 1), :].rearrange("p a s -> p (a s)"), acc[0][u][:], acc[1][u][:],
                                ALU.mult).then_inc(hidden_ready[u], 1)

            def turn(j, last):
                for u in range(2):
                    for c in range(2):
                        if u == 0 or not last:
                            split(j + u, 1 - u, c)
                        convolve(j, u, c)
                    hide(j, u)

            split(0, 0, 0)
            split(0, 0, 1)
            v.wait_ge(taps_ready, 1)
            with v.Fori(0, TURNS - 1) as j:
                turn(j, False)
            turn(TURNS - 1, True)


def ffn_down_stage(nc, psum, bank, a, hidden, hidden_low, high_parts, x, gain, x_dram, gain_dram, out):
    RING = 3
    with Stage(nc, "ffn_down") as st:
        beyond = st.sb("beyond", [P, FFN_T - 2 * KT, S], F32R)
        hidden_high = [part[:, k, :] for part in (*high_parts, beyond) for k in range(part.shape[1])]
        w, w_low = zip(*(st.twin(f"w{i}", [P, BANK]) for i in range(RING)))
        w_high = [st.sb(f"w_high{i}", [P, BANK], F32R) for i in range(RING)]
        y = st.sb("y", [P, TT, BANK])
        square = st.sb("square", [P, 2, TT])
        mean, root, rstd = (st.sb(n, [P, TT]) for n in ("mean", "root", "rstd"))
        scaled, junk = hidden[:, 0:TT, :], hidden[:, TT, :]
        loaded, w_high_ready, w_low_ready, used = (
            [st.sem(f"{n}{i}") for i in range(RING)] for n in ("loaded", "w_high_ready", "w_low_ready", "used"))
        hidden_high_ready, hidden_low_ready, made, even_out, odd_out, squared, summed, mean_ready, root_ready, rstd_ready = (
            st.sem(n) for n in ("hidden_high_ready", "hidden_low_ready", "made", "even_out", "odd_out", "squared", "summed",
                                "mean_ready", "root_ready", "rstd_ready"))
        x_loaded, gain_loaded, scaled_ready, added, stored = (
            st.sem(n) for n in ("x_loaded", "gain_loaded", "scaled_ready", "added", "stored"))
        block = st.open()

        def uses(k):
            return len(range(k % RING, FFN_T, RING))

        def count(n, k):
            return n * uses(k) + k // RING

        @block.sync
        def _(sp):
            for n in range(2):
                for k in range(FFN_T):
                    i = k % RING
                    if n or k >= RING:
                        sp.wait_ge(used[i], count(n, k))
                    sp.dma_start(w[i][:], a["ffn_w_down_2"][k * P:(k + 1) * P, n * BANK:(n + 1) * BANK]).then_inc(loaded[i], 16)
            for i in range(RING):
                k = (TT // RING) * RING + i
                sp.wait_ge(used[i], count(1, k) + 1)
            sp.dma_start(x, x_dram.rearrange("(t p) d -> p t d", p=P)).then_inc(x_loaded, 16)
            sp.dma_start(gain, rows(gain_dram, D)).then_inc(gain_loaded, 16)
            for t in range(TT):
                sp.wait_ge(added, t + 1)
                sp.dma_start(out[t * P:(t + 1) * P, :], x[:, t, :]).then_inc(stored, 16)
            sp.wait_ge(stored, 16 * TT)

        @block.tensor
        def _(pe):
            for n in range(2):
                for k in range(FFN_T):
                    i = k % RING
                    pe.wait_ge(w_low_ready[i], count(n, k) + 1)
                    if n == 0:
                        pe.wait_ge(hidden_low_ready, k + 1)
                    for t in range(TT):
                        if n and k == 0:
                            pe.wait_ge((even_out, odd_out)[t % 2], t // 2 + 1)
                        tile = slice(t * P, (t + 1) * P)
                        last = three_passes(pe, bank[t][:], (hidden_high[k][:, tile], hidden_low[:, k, tile]),
                                            (w_high[i][:], w_low[i][:]), start=(k == 0), stop=(k == FFN_T - 1))
                        if k == FFN_T - 1:
                            last.then_inc((made, used[i])[t == TT - 1], 1)
                    if k < FFN_T - 1:
                        last.then_inc(used[i], 1)

        def wait_made(eng, n, t):
            if t == TT - 1:
                eng.wait_ge(used[(FFN_T - 1) % RING], count(n, FFN_T - 1) + 1)
            else:
                eng.wait_ge(made, n * (TT - 1) + t + 1)

        @block.scalar
        def _(act):
            def square_of(n, t):
                if n * TT + t:
                    act.wait_ge(squared, n * TT + t)
                act.activation(junk[:, 0:BANK], (y[:, t, :], bank[t][:])[n], ACT.Square, accum_out=square[:, n, t:t + 1])\
                    .then_inc(squared, 1)

            for n in range(2):
                for k in range(FFN_T):
                    i = k % RING
                    if n == 0:
                        split_high(act, hidden_high[k], hidden[:, k, :]).then_inc(hidden_high_ready, 1)
                    act.wait_ge(loaded[i], 16 * (count(n, k) + 1))
                    split_high(act, w_high[i][:], w[i][:]).then_inc(w_high_ready[i], 1)
                if n == 0:
                    for t in range(0, TT, 2):
                        wait_made(act, 0, t)
                        act.activation(y[:, t, :], bank[t][:], ACT.Copy).then_inc(even_out, 1)
            act.wait_ge(used[TT % RING], count(1, TT) + 1)
            act.wait_ge(even_out, TT // 2)
            act.wait_ge(odd_out, TT // 2)
            for t in range(TT):
                square_of(0, t)
            for t in range(TT):
                wait_made(act, 1, t)
                square_of(1, t)
            act.wait_ge(mean_ready, 1)
            act.activation(root[:], mean[:], ACT.Sqrt).then_inc(root_ready, 1)

        @block.vector
        def _(v):
            for n in range(2):
                for k in range(FFN_T):
                    i = k % RING
                    if n == 0:
                        v.wait_ge(hidden_high_ready, k + 1)
                        split_low(v, hidden_low[:, k, :], hidden[:, k, :], hidden_high[k]).then_inc(hidden_low_ready, 1)
                    v.wait_ge(w_high_ready[i], count(n, k) + 1)
                    split_low(v, w_low[i][:], w[i][:], w_high[i][:]).then_inc(w_low_ready[i], 1)
                if n == 0:
                    for t in range(1, TT, 2):
                        wait_made(v, 0, t)
                        v.tensor_copy(y[:, t, :], bank[t][:]).then_inc(odd_out, 1)
            v.wait_ge(squared, 2 * TT)
            v.tensor_tensor(mean[:], square[:, 0, :], square[:, 1, :], ALU.add).then_inc(summed, 1)
            v.wait_ge(summed, 1)
            v.tensor_scalar(mean[:], mean[:], 1.0 / D, EPS, ALU.mult, ALU.add).then_inc(mean_ready, 1)
            v.wait_ge(root_ready, 1)
            v.reciprocal(rstd[:], root[:]).then_inc(rstd_ready, 1)
            v.wait_ge(rstd_ready, 1)
            v.wait_ge(gain_loaded, 16)
            for t in range(TT):
                for n in range(2):
                    cols = slice(n * BANK, (n + 1) * BANK)
                    v.scalar_tensor_tensor(out=scaled[:, t, cols], in0=(y[:, t, :], bank[t][:])[n], scalar=rstd[:, t:t + 1],
                                           in1=gain[:, cols], op0=ALU.mult, op1=ALU.mult).then_inc(scaled_ready, 1)

        @block.gpsimd
        def _(pool):
            pool.wait_ge(x_loaded, 16)
            for t in range(TT):
                pool.wait_ge(scaled_ready, 2 * t + 2)
                pool.tensor_tensor(x[:, t, :], x[:, t, :], scaled[:, t, :], ALU.add).then_inc(added, 1)


def program(nc, a, out):
    with ExitStack() as ctx:
        def sb(name, shape, dt=F32):
            return ctx.enter_context(nc.sbuf_tensor(name, shape, dt))

        psum = ctx.enter_context(nc.psum_tensor("psum", [P, 8, BANK], F32))
        bank = [psum[:, i, :] for i in range(8)]
        ident = sb("ident", [P, P])
        proj = nc.dram_tensor("proj", [S + 1, IN_COLS], F32).ap()
        h_rows = nc.dram_tensor("h_rows", [S, D], F32).ap()
        y_rows = nc.dram_tensor("y_rows", [SLOT_BLOCKS * P, D], F32).ap()
        with nc.sbuf_tensor("high1", [P, KT, S], F32R) as high, nc.sbuf_tensor("low1", [P, KT, S], F32R) as low:
            with nc.sbuf_tensor("x_rows", [P, TT, D], F32) as x:
                load_stage(nc, x, ident, a["x"], a["c_ident"], proj[0:1, :])
                norm_stage(nc, "norm1", bank, ident, x, a["norm1_gain"], high, low=low)
            project_stage(nc, "project", bank, high, low, a["w_in"], 480, IN_COLS // 480, proj[1:S + 1, :],
                          y_rows[EXPERTS * P:, :])
        mixed = nc.dram_tensor("mixed", [TT, P, KT * P], F32).ap()
        mix_stage(nc, bank, ident, a, proj, mixed)
        feat, = overlay(nc, ("feat", [P, KT, S], F32))
        part = sb("part", [P, KT, S], F32R)
        x2_dram = nc.dram_tensor("x2_rows", [S, D], F32).ap()
        with nc.sbuf_tensor("h", [P, TT, D], F32) as x:
            with ExitStack() as routed:
                def sb1(name, shape, dt=F32):
                    return routed.enter_context(nc.sbuf_tensor(name, shape, dt))

                add_product_stage(nc, "out1", bank, feat, part, a["w_out"], x, x_dram=a["x"], feat_dram=mixed)
                token_ids = sb1("token_ids", [P, TT], I32)
                slot_weight = sb1("slot_weight", [P, 2, TT])
                slot_index = sb1("slot_index", [P, 2, TT], I32)
                more = sb1("more", [1, 2, MORE_BLOCKS], I32)
                slot_token = nc.dram_tensor("slot_token", [SLOT_BLOCKS * P, 1], I32).ap()
                norm_stage(nc, "norm2", bank, ident, x, a["norm2_gain"], feat, h_rows)
                route_stage(nc, bank, a, feat, token_ids, slot_weight, slot_index, more, slot_token)
                expert_stage(nc, bank, ident, a, more, slot_token, h_rows, y_rows)
                combine_stage(nc, x, y_rows, slot_index, slot_weight, a["final_norm_gain"], x2_dram)
            mixers2(nc, a, psum, bank, ident, feat, part, x)
        second_half(nc, a, out, psum, bank, ident, feat, part, x2_dram)


def mixers2(nc, a, psum, bank, ident, feat, part, x):
    with ExitStack() as ctx:
        def sb(name, shape, dt=F32):
            return ctx.enter_context(nc.sbuf_tensor(name, shape, dt))

        xbc = sb("xbc", [P, XBC_T, S])
        room = flat(x)
        rows2, spare = three(room[:, 0:TT * TM_COLS], TT), room[:, TT * TM_COLS:]
        with nc.sbuf_tensor("low3", [P, KT, S], F32R) as low:
            norm_stage(nc, "norm3", bank, ident, x, a["norm_mix_pre_2"], part, low=low)
            project2_stage(nc, psum, bank, part, low, feat, a, rows2, xbc)
        q_t, k_t = sb("q_t", [QK, MLA_HEADS, S]), sb("k_t", [QK, MLA_HEADS, S])
        values = sb("values", [P, TT, MLA_HEADS * V_DIM])
        mixers2_stage(nc, bank, ident, a, rows2, xbc, feat, q_t, k_t, values, spare)
        attention_stage(nc, psum, bank, ident, a, q_t, k_t, values, feat, room)


def second_half(nc, a, out, psum, bank, ident, feat, part, x2_dram):
    x3_dram = nc.dram_tensor("x3_rows", [S, D], F32).ap()
    x, w = overlay(nc, ("x2", [P, TT, D], F32), ("w_out2", [P, KT, D], F32))
    _, w_low, w_high = overlay(nc, ("x2_place", [P, TT, D], F32), ("w_out2_low", [P, KT, D], F32R),
                               ("w_out2_high", [P, KT, D], F32R))
    hidden, low_plain = overlay(nc, ("hidden", [P, FFN_T, S], F32), ("low4_plain", [P, KT, S], F32))
    with nc.sbuf_tensor("hidden_low", [P, FFN_T, S], F32R) as hidden_low, nc.sbuf_tensor("low4", [P, KT, S], F32R) as low:
        add_product_stage(nc, "out2", bank, feat, part, a["w_out_2"], x, x2_dram, a["norm_mix_post_2"], x3_dram,
                          weights=(w, w_low, w_high))
        norm_stage(nc, "norm4", bank, ident, x, a["norm_ffn_pre_2"], part, low=low)
        ffn_up_stage(nc, psum, bank, ident, a, part, low, hidden)
        ffn_down_stage(nc, psum, bank, a, hidden, hidden_low, (part, low), feat[:], low_plain[:, 0, :], x3_dram,
                       a["norm_ffn_post_2"], out)


def kernel(**inputs):
    import concourse.bacc as bacc
    from concourse import mybir as types
    from concourse.bass_utils import run_bass_kernel_spmd

    nc = bacc.Bacc("TRN2", target_bir_lowering=False, num_devices=1)
    arrays, args = {}, {}
    for name, value in lay_out(inputs).items():
        arrays[f"in_{name}_dram"] = value
        args[name] = nc.dram_tensor(f"in_{name}_dram", value.shape, types.dt.from_np(value.dtype), kind="ExternalInput").ap()
    out = nc.dram_tensor("out_0_dram", [S, D], types.dt.float32, kind="ExternalOutput").ap()
    program(nc, args, out)
    r = run_bass_kernel_spmd(nc, [arrays], core_ids=[0])
    return r.results[0]["out_0_dram"].reshape(1, S, D)
```

```python
from contextlib import ExitStack

import concourse.bass as bass
import numpy as np
from concourse import mybir

F32 = mybir.dt.float32
F32R = mybir.dt.float32r
I32 = mybir.dt.int32
U32 = mybir.dt.uint32
ALU = mybir.AluOpType
ACT = mybir.ActivationFunctionType
AX_X = mybir.AxisListType.X
ds = bass.ds

P = 128
D = 1024
S = 1024
KT = D // P
TT = S // P
BANK = 512
EPS = 1e-6

RET_W = 512
RET_HEADS = 4
RET_D = RET_W // RET_HEADS
RET_CHUNK = 64
RW_W = 512
RW_HEADS = 8
RW_N = RW_W // RW_HEADS
LORA = 64
RW_COLS = 3 * RW_W + 2 * LORA + 128
IN_COLS = 4 * RET_W + RW_COLS
RET_GN_EPS = 1e-5
RW_GN_EPS = 64e-5
DECAY = -float(np.exp(-0.5))
SOLVE_STEPS = (2, 4, 8, 16, 32, 64)


def overlay(nc, *tensors):
    with ExitStack() as ctx:
        return [ctx.enter_context(nc.sbuf_tensor(name, shape, dt)) for name, shape, dt in tensors]


def twin(nc, ctx, name, shape):
    plain, = overlay(nc, (name, shape, F32))
    return plain, ctx.enter_context(nc.sbuf_tensor(f"{name}_low", shape, F32R))


class Stage:

    def __init__(self, nc, name):
        self.nc, self.name, self.sems, self.ctx = nc, name, [], ExitStack()

    def __enter__(self):
        self.block_ctx = self.nc.Block()
        self.block = None
        return self

    def open(self):
        self.block = self.block_ctx.__enter__()
        return self.block

    def sem(self, name):
        s = self.nc.alloc_semaphore(name=f"{self.name}_{name}")
        self.sems.append(s)
        return s

    def sb(self, name, shape, dt=F32):
        return self.ctx.enter_context(self.nc.sbuf_tensor(f"{self.name}_{name}", shape, dt))

    def twin(self, name, shape):
        return twin(self.nc, self.ctx, f"{self.name}_{name}", shape)

    def adopt(self, sems):
        self.sems += sems

    def __exit__(self, *error):
        if error[0] is None:
            self.block_ctx.__exit__(None, None, None)
            self.nc.clear_and_free_semaphores(self.sems)
            self.nc.all_engine_barrier()
        self.ctx.close()


def rows(dram, cols):
    return dram.rearrange("(a n) -> a n", a=1)[:, 0:cols].partition_broadcast(P)


def flat(ap):
    return ap.rearrange("p a b -> p (a b)")


def three(ap, a):
    return ap.rearrange("p (a b) -> p a b", a=a)


def per_row(ap, n):
    return ap.unsqueeze(2).to_broadcast([ap.shape[0], ap.shape[1], n])


def per_block(ap, n):
    return ap.unsqueeze(1).to_broadcast([ap.shape[0], n, ap.shape[1]])


def split_high(act, high, x):
    return act.activation(high, x, ACT.Copy)


def split_low(v, low, x, high):
    return v.tensor_tensor(low, x, high, ALU.subtract)


def three_passes(pe, out, left, right, start, stop):
    pe.matmul(out, left[0], right[0], start=start, stop=False)
    pe.matmul(out, left[0], right[1], start=False, stop=False)
    return pe.matmul(out, left[1], right[0], start=False, stop=stop)


def square_rows(act, x, t, junk, squares, done):
    if t >= 2:
        act.wait_ge(done, t - 1)
    act.activation(junk[t % 2][:], x[:, t, :], ACT.Square, accum_out=squares[:, t:t + 1]).then_inc(done, 1)


def load_stage(nc, x, squares, ident, x_dram, ident_dram, zero_row_of):
    with Stage(nc, "load") as st:
        zeros = st.sb("zeros", [1, IN_COLS])
        junk = [st.sb(f"junk{u}", [P, D]) for u in range(2)]
        x_loaded = [st.sem(f"x_loaded{t}") for t in range(TT)]
        loaded, zeroed, cleared, squared = (st.sem(n) for n in ("loaded", "zeroed", "cleared", "squared"))
        block = st.open()

        @block.sync
        def _(sp):
            for t in range(TT):
                sp.dma_start(x[:, t, :], x_dram[t * P:(t + 1) * P, :]).then_inc(x_loaded[t], 16)
            sp.dma_start(ident[:], ident_dram).then_inc(loaded, 16)
            sp.wait_ge(zeroed, 1)
            sp.dma_start(zero_row_of, zeros[0:1, 0:zero_row_of.shape[1]]).then_inc(cleared, 16)
            sp.wait_ge(cleared, 16)
            sp.wait_ge(loaded, 16)

        @block.scalar
        def _(act):
            for t in range(TT):
                act.wait_ge(x_loaded[t], 16)
                square_rows(act, x, t, junk, squares, squared)

        @block.vector
        def _(v):
            v.memset(zeros[:], 0.0).then_inc(zeroed, 1)


def norm_stage(nc, name, bank, ident, x, squares, gain_dram, out, rows_dram=None, low=None):
    with Stage(nc, name) as st:
        gain = st.sb("gain", [P, KT])
        mean, root, rstd = (st.sb(n, [P, TT]) for n in ("mean", "root", "rstd"))
        xs = [st.sb(f"xs{u}", [P, D]) for u in range(2)]
        gain_loaded, mean_ready, root_ready, rstd_ready = (
            st.sem(n) for n in ("gain_loaded", "mean_ready", "root_ready", "rstd_ready"))
        xs_ready, turned, first_out, high_out, low_out, stored = (
            [st.sem(f"{n}{u}") for u in range(2)] for n in ("xs_ready", "turned", "first_out", "high_out", "low_out", "stored"))
        block = st.open()
        TURNS = TT // 2

        @block.sync
        def _(sp):
            sp.dma_start(gain[:], gain_dram.rearrange("(k p) -> p k", p=P),
                         allow_slow_non_contiguous=True).then_inc(gain_loaded, 16)
            if rows_dram is not None:
                with sp.Fori(0, TURNS) as j:
                    for u in range(2):
                        sp.wait_ge(xs_ready[u], j + 1)
                        sp.dma_start(rows_dram[ds((j * 2 + u) * P, P), :], xs[u][:]).then_inc(stored[u], 16)
                for u in range(2):
                    sp.wait_ge(stored[u], 16 * TURNS)

        @block.scalar
        def _(act):
            act.wait_ge(mean_ready, 1)
            act.activation(root[:], mean[:], ACT.Sqrt).then_inc(root_ready, 1)
            act.wait_ge(gain_loaded, 16)
            with act.Fori(0, TURNS) as j:
                for u in range(2):
                    t = j * 2 + u
                    act.wait_ge(turned[u], j + 1)
                    for k in range(0 if low is not None else 4, 8):
                        last = act.activation(out[:, k, ds(t * P, P)], bank[2 * u + k // 4][:, (k % 4) * P:(k % 4 + 1) * P],
                                              ACT.Copy, scale=gain[:, k:k + 1])
                        if k == 3:
                            last.then_inc(first_out[u], 1)
                    last.then_inc(high_out[u], 1)

        @block.vector
        def _(v):
            def scale(j, u):
                if not isinstance(j, int) or j:
                    v.wait_ge(turned[u], j)
                    if rows_dram is not None:
                        v.wait_ge(stored[u], j * 16)
                t = j * 2 + u
                v.tensor_scalar(xs[u][:], x[:, ds(t, 1), :].rearrange("p a d -> p (a d)"), rstd[:, ds(t, 1)], None,
                                ALU.mult).then_inc(xs_ready[u], 1)

            def take(j, u):
                t = j * 2 + u
                if low is not None:
                    for k in range(KT):
                        if k % 4 == 0:
                            v.wait_ge((first_out, high_out)[k // 4][u], j + 1)
                        last = v.scalar_tensor_tensor(
                            out=low[:, k, ds(t * P, P)], in0=bank[2 * u + k // 4][:, (k % 4) * P:(k % 4 + 1) * P],
                            scalar=gain[:, k:k + 1], in1=out[:, k, ds(t * P, P)], op0=ALU.mult, op1=ALU.subtract)
                    last.then_inc(low_out[u], 1)
                else:
                    v.wait_ge(turned[u], j + 1)
                    v.tensor_tensor(out[:, 0:4, ds(t * P, P)], three(bank[2 * u][:], 4), per_row(gain[:, 0:4], P),
                                    ALU.mult).then_inc(low_out[u], 1)

            v.tensor_scalar(mean[:], squares[:], 1.0 / D, EPS, ALU.mult, ALU.add).then_inc(mean_ready, 1)
            v.wait_ge(root_ready, 1)
            v.reciprocal(rstd[:], root[:]).then_inc(rstd_ready, 1)
            v.wait_ge(rstd_ready, 1)
            scale(0, 0)
            scale(0, 1)
            v.wait_ge(gain_loaded, 16)
            with v.Fori(0, TURNS - 1) as j:
                for u in range(2):
                    take(j, u)
                    scale(j + 1, u)
            for u in range(2):
                take(TURNS - 1, u)

        @block.tensor
        def _(pe):
            with pe.Fori(0, TURNS) as j:
                for u in range(2):
                    pe.wait_ge(xs_ready[u], j + 1)
                    pe.wait_ge(low_out[u], j)
                    pe.wait_ge(high_out[u], j)
                    for k in range(KT):
                        last = pe.transpose(bank[2 * u + k // 4][:, (k % 4) * P:(k % 4 + 1) * P],
                                            xs[u][:, k * P:(k + 1) * P], ident[:])
                    last.then_inc(turned[u], 1)


def project_stage(nc, name, bank, feat, low, w_dram, width, blocks, out_dram, idle_rows):
    half = blocks // 2
    PIECES = 4
    with Stage(nc, name) as st:
        w, w_low = zip(*(st.twin(f"w{u}", [P, KT, width]) for u in range(2)))
        w_high = [st.sb(f"w_high{u}", [P, KT, width], F32R) for u in range(2)]
        out = [st.sb(f"out{u}", [P, TT, width]) for u in range(2)]
        piece_loaded = [st.sem(f"piece_loaded{c}") for c in range(PIECES)]
        w_loaded = [st.sem(f"w_loaded{u}") for u in range(2)]
        high_ready = [st.sem(f"high_ready{u}") for u in range(2)]
        low_ready = [st.sem(f"low_ready{u}") for u in range(2)]
        stored = [st.sem(f"stored{u}") for u in range(2)]
        product = st.sem("product")
        even_out, odd_out = st.sem("even_out"), st.sem("odd_out")
        zeros = st.sb("zeros", [P, D])
        zeroed, cleared = st.sem("zeroed"), st.sem("cleared")
        block = st.open()

        def piece(ap, c):
            return ap[:, c * KT // PIECES:(c + 1) * KT // PIECES, :]

        def splits(j, u):
            return j + 1 if u else j + PIECES

        @block.gpsimd
        def _(pool):
            pool.memset(zeros[:], 0.0).then_inc(zeroed, 1)
            pool.wait_ge(zeroed, 1)
            pool.dma_start(idle_rows.rearrange("(b p) d -> p b d", p=P),
                           per_block(zeros[:], idle_rows.shape[0] // P)).then_inc(cleared, 16)

        @block.sync
        def _(sp):
            def load(j, u):
                sp.dma_start(w[u][:], w_dram[:, ds((j * 2 + u) * width, width)]
                             .rearrange("(k p) n -> p k n", p=P)).then_inc(w_loaded[u], 16)

            for c in range(PIECES):
                sp.dma_start(piece(w[0], c), w_dram[c * D // PIECES:(c + 1) * D // PIECES, 0:width]
                             .rearrange("(k p) n -> p k n", p=P)).then_inc(piece_loaded[c], 16)
            load(0, 1)
            with sp.Fori(1, half) as j:
                for u in range(2):
                    sp.wait_ge(odd_out, j * 8 + u * 4)
                    load(j, u)
            sp.wait_ge(cleared, 16)

        @block.tensor
        def _(pe):
            def multiply(j, u, first):
                b = j * 2 + u
                if not first:
                    pe.wait_ge(low_ready[u], splits(j, u))
                for t in range(TT):
                    tile = slice(t * P, (t + 1) * P)
                    if t % 2 == 0:
                        pe.wait_ge(even_out, b * 4 + t // 2 + 1)
                    else:
                        pe.wait_ge(odd_out, b * 4 + t // 2 + 1)
                    for k in range(KT):
                        if first and t == 0 and k % (KT // PIECES) == 0:
                            pe.wait_ge(low_ready[0], k * PIECES // KT + 1)
                        last = three_passes(pe, bank[t][:, 0:width], (feat[:, k, tile], low[:, k, tile]),
                                            (w_high[u][:, k, :], w_low[u][:, k, :]), start=(k == 0), stop=(k == KT - 1))
                    last.then_inc(product, 1)

            multiply(0, 0, True)
            multiply(0, 1, False)
            with pe.Fori(1, half) as j:
                for u in range(2):
                    multiply(j, u, False)

        @block.scalar
        def _(act):
            def split(j, u):
                act.wait_ge(w_loaded[u], (j if u == 0 else j + 1) * 16)
                split_high(act, w_high[u][:], w[u][:]).then_inc(high_ready[u], 1)

            def take(j, u):
                b = j * 2 + u
                act.wait_ge(stored[u], j * 16)
                for t in range(0, TT, 2):
                    act.wait_ge(product, b * TT + t + 1)
                    act.activation(out[u][:, t, :], bank[t][:, 0:width], ACT.Copy).then_inc(even_out, 1)
                act.wait_ge(even_out, b * 4 + 8)
                act.wait_ge(odd_out, b * 4 + 8)
                act.dma_start(out_dram[:, ds(b * width, width)].rearrange("(t p) n -> p t n", p=P),
                              out[u][:]).then_inc(stored[u], 16)

            act.sem_inc(even_out, 4)
            for c in range(PIECES):
                act.wait_ge(piece_loaded[c], 16)
                split_high(act, piece(w_high[0], c), piece(w[0], c)).then_inc(high_ready[0], 1)
            with act.Fori(0, half - 1) as j:
                split(j, 1)
                take(j, 0)
                split(j + 1, 0)
                take(j, 1)
            split(half - 1, 1)
            take(half - 1, 0)
            take(half - 1, 1)
            for u in range(2):
                act.wait_ge(stored[u], 16 * half)

        @block.vector
        def _(v):
            def split(j, u):
                v.wait_ge(high_ready[u], splits(j, u))
                split_low(v, w_low[u][:], w[u][:], w_high[u][:]).then_inc(low_ready[u], 1)

            def take(j, u):
                v.wait_ge(stored[u], j * 16)
                for t in range(1, TT, 2):
                    v.wait_ge(product, (j * 2 + u) * TT + t + 1)
                    v.tensor_copy(out[u][:, t, :], bank[t][:, 0:width]).then_inc(odd_out, 1)

            v.sem_inc(odd_out, 4)
            for c in range(PIECES):
                v.wait_ge(high_ready[0], c + 1)
                split_low(v, piece(w_low[0], c), piece(w[0], c), piece(w_high[0], c)).then_inc(low_ready[0], 1)
            with v.Fori(0, half - 1) as j:
                split(j, 1)
                take(j, 0)
                split(j + 1, 0)
                take(j, 1)
            split(half - 1, 1)
            take(half - 1, 0)
            take(half - 1, 1)


def norm_spread(v, link, y, scratch, stats, heads, width, eps, out, spread_ready):
    total, mean, var, spread = (stats[:, i, 0:heads] for i in range(4))
    link(v.tensor_reduce(total, three(y, heads), AX_X, ALU.add))
    link(v.tensor_scalar(mean, total, 1.0 / width, None, ALU.mult))
    link(v.tensor_tensor(three(out, heads), three(y, heads), per_row(mean, width), ALU.subtract))
    link(v.tensor_tensor(scratch, out, out, ALU.mult))
    link(v.tensor_reduce(var, three(scratch, heads), AX_X, ALU.add))
    v.tensor_scalar(spread, var, 1.0 / width, eps, ALU.mult, ALU.add).then_inc(spread_ready, 1)


def norm_divide(v, link, stats, heads, width, out, normed):
    link(v.reciprocal(stats[:, 5, 0:heads], stats[:, 4, 0:heads]))
    v.tensor_tensor(three(out, heads), three(out, heads), per_row(stats[:, 5, 0:heads], width), ALU.mult).then_inc(normed, 1)


def mix_stage(nc, bank, ident, a, proj, mixed):
    HG = 4
    with Stage(nc, "mix") as st:
        mu = st.sb("mu", [P, RW_COLS])
        w0, a0, k_k, k_a, r_k, rw_gain, ret_gain = (st.sb(n, [P, 512]) for n in
                                                    ("w0", "a0", "k_k", "k_a", "r_k", "rw_gain", "ret_gain"))
        lora_up = st.sb("lora_up", [P, RW_W])
        g_up = st.sb("g_up", [P, RW_W])
        incl, strict, incl_mid, strict_mid = (st.sb(n, [P, P]) for n in ("incl", "strict", "incl_mid", "strict_mid"))
        pair_mask = [st.sb(f"pair_mask{i}", [P, P]) for i in range(1 + len(SOLVE_STEPS))]
        ends = st.sb("ends", [P, 2])
        intra = st.sb("intra", [P, RET_HEADS, P])
        q_decay = st.sb("q_decay", [P, RET_HEADS, P])
        k_decay = st.sb("k_decay", [P, RET_HEADS])
        tile_decay = st.sb("tile_decay", [P, RET_HEADS])

        def pair(name, shape):
            return [st.sb(f"{name}{u}", shape) for u in range(2)]

        feat, ret_in = pair("feat", [P, RW_COLS]), pair("ret_in", [P, 4 * RET_W])
        prev = st.sb("prev", [P, RW_COLS])
        rope = pair("rope", [P, 2, RET_D // 2])
        lo, lo_t = st.sb("lo", [P, 256]), st.sb("lo_t", [P, 256])
        sg, ag, p_t, p_inv, k2 = (st.sb(n, [P, RW_W]) for n in ("sg", "ag", "p_t", "p_inv", "k2"))
        p_ex = ag
        g, bonus_v = pair("g", [P, RW_W]), pair("bonus_v", [P, RW_W])
        tilde_r, tilde_a = sg, p_ex
        tilde_b, tilde_k = pair("tilde_b", [P, RW_W]), pair("tilde_k", [P, RW_W])
        tilde_t = [st.sb(f"tilde_t_{n}", [RW_N, RW_HEADS, P]) for n in "bark"]
        kk_stats = st.sb("kk_stats", [P, 3, RW_HEADS])
        rw_stats, ret_stats = st.sb("rw_stats", [P, 6, RW_HEADS]), st.sb("ret_stats", [P, 6, RET_HEADS])
        bonus = st.sb("bonus", [P, RW_HEADS])
        reach = pair("reach", [RW_N, RW_HEADS, 2])
        m, m0 = st.sb("m", [RW_N, RW_W]), st.sb("m0", [RW_N, RW_W])
        ab, ak, rb, rk = ([st.sb(f"{n}{i}", [P, HG, P]) for i in range(2)] for n in ("ab", "ak", "rb", "rk"))
        ab_step = [[st.sb(f"ab_step{i}_{s}", [P, HG, P]) for s in range(3)] for i in range(2)]
        x_t, x_n, zs = ([st.sb(f"{n}{i}", [P, HG, P]) for i in range(2)] for n in ("x_t", "x_n", "zs"))
        q1, u_ = st.sb("q1", [P, RW_W]), st.sb("u", [P, RW_W])
        rot = st.sb("rot", [P, 4, 512])
        qk = st.sb("qk", [P, 2 * RET_W])
        kd = rot[:, 0, :]
        q_t, k_t, qd_t, pt = (st.sb(n, [P, RET_HEADS, P]) for n in ("q_t", "k_t", "qd_t", "pt"))
        state, gate = st.sb("state", [P, RET_W]), st.sb("gate", [P, RET_W])
        out_t = st.sb("out_t", [P, KT, P])
        y_raw, y, ry_raw, ry, scratch = (st.sb(n, [P, 512]) for n in ("y_raw", "y", "ry_raw", "ry", "scratch"))

        names = ("const shift_order kk_order b_order bonus_order rw_order ret_order state_order m_order pool_order "
                 "shifted lo_ready lo_turned lo_t_ready lifted w_added a_added sg_ready a_ready g_ready run_ready exp_ready "
                 "reach_ready tilde_ready tilde_turned fm_even fm_odd kk_squared kk_root bonus_ready "
                 "scored masked ab_ready ab_split x_started x_ready x_turned x_n_ready x_n_by_vector z_made z_ready x_step "
                 "m0_ready q1_made q1_ready u_made u_ready y_made m_made m_ready y_copied rw_spread rw_root rw_normed rw_ready "
                 "rw_turned rw_mixed rotated q_turned k_turned q_t_ready k_t_ready qd_ready ret_scored pt_ready ret_made "
                 "state_ready ret_copied gate_ready ret_spread ret_root ret_normed ret_ready ret_out_turned ret_mixed "
                 "pe_passed prev_ready stored zeroed").split()
        sem = {n: st.sem(n) for n in names}
        (const, shift_order, kk_order, b_order, bonus_order, rw_order, ret_order, state_order, m_order, pool_order,
         shifted, lo_ready, lo_turned, lo_t_ready, lifted, w_added, a_added, sg_ready, a_ready, g_ready, run_ready, exp_ready,
         reach_ready, tilde_ready, tilde_turned, fm_even, fm_odd, kk_squared, kk_root, bonus_ready,
         scored, masked, ab_ready, ab_split, x_started, x_ready, x_turned, x_n_ready, x_n_by_vector, z_made, z_ready, x_step,
         m0_ready, q1_made, q1_ready, u_made, u_ready, y_made, m_made, m_ready, y_copied, rw_spread, rw_root, rw_normed, rw_ready,
         rw_turned, rw_mixed, rotated, q_turned, k_turned, q_t_ready, k_t_ready, qd_ready, ret_scored, pt_ready, ret_made,
         state_ready, ret_copied, gate_ready, ret_spread, ret_root, ret_normed, ret_ready, ret_out_turned, ret_mixed,
         pe_passed, prev_ready, stored, zeroed) = (sem[n] for n in names)
        feat_ready, ret_in_ready = ([st.sem(f"{n}{u}") for u in range(2)] for n in ("feat_ready", "ret_in_ready"))
        mu_ready = st.sem("mu_ready")
        NS = len(SOLVE_STEPS)
        PAIRS = TT // 2
        LAST = TT - 1

        def r_(u):
            return feat[u][:, 0:512]

        def k_(u):
            return feat[u][:, 512:1024]

        def v_(u):
            return feat[u][:, 1024:1536]

        k_scaled, b_, kk = (prev[:, i * RW_W:(i + 1) * RW_W] for i in range(3))

        def head(ap, h, n):
            return ap[:, h * n:(h + 1) * n]

        def each_turn(eng, turn):
            for u in range(2):
                turn(0, u, u == 0, False)
            with eng.Fori(1, PAIRS - 1) as j:
                for u in range(2):
                    turn(j, u, False, False)
            for u in range(2):
                turn(PAIRS - 1, u, False, u == 1)

        consts = [
            (w0[:], rows(a["rwkv_w0"], 512)), (a0[:], rows(a["rwkv_a0"], 512)),
            (k_k[:], rows(a["rwkv_k_k"], 512)), (k_a[:], rows(a["rwkv_k_a"], 512)),
            (r_k[:], rows(a["rwkv_r_k"].rearrange("h n -> (h n)"), 512)),
            (rw_gain[:], rows(a["rwkv_gn_gain"], 512)), (ret_gain[:], rows(a["ret_gn_gain"], 512)),
            (lora_up[0:LORA, :], a["rwkv_w_up"]), (lora_up[LORA:2 * LORA, :], a["rwkv_a_up"]), (g_up[:], a["rwkv_g_up"]),
            (incl[:], a["c_incl"]), (strict[:], a["c_strict"]), (incl_mid[:], a["c_incl_mid"]),
            (strict_mid[:], a["c_strict_mid"]), (ends[:], a["c_ends"]),
            (intra[:], a["c_ret_intra"]), (q_decay[:], a["c_ret_q"]), (k_decay[:], a["c_ret_k"]),
            (tile_decay[:], a["c_ret_tile"]),
        ] + [(pair_mask[i][:], a["c_pairs"][i]) for i in range(1 + NS)]
        block = st.open()

        @block.sync
        def _(sp):
            def load_feat(j, u):
                sp.dma_start(feat[u][:], proj[ds((2 * j + u) * P + 1, P), 4 * RET_W:IN_COLS]).then_inc(feat_ready[u], 16)

            def load_ret(j, u):
                t = 2 * j + u
                sp.dma_start(ret_in[u][:], proj[ds(t * P + 1, P), 0:4 * RET_W]).then_inc(ret_in_ready[u], 16)
                sp.dma_start(rope[u][:], a["c_rope"][ds(t * P, P), :].rearrange("p (a d) -> p a d", a=2)).then_inc(ret_in_ready[u], 16)

            def load_prev(t):
                sp.dma_start(prev[:], proj[ds(t * P, P), 4 * RET_W:IN_COLS]).then_inc(prev_ready, 16)

            load_feat(0, 0)
            load_prev(0)
            sp.dma_start(mu[:], rows(a["rwkv_mu"], RW_COLS)).then_inc(mu_ready, 16)
            for to, of in consts:
                sp.dma_start(to, of).then_inc(const, 16)
            load_ret(0, 0)
            load_feat(0, 1)
            load_ret(0, 1)
            sp.wait_ge(tilde_ready, 4)
            load_prev(1)
            with sp.Fori(1, PAIRS) as j:
                for u in range(2):
                    t = 2 * j + u
                    sp.wait_ge(tilde_ready, t * 4)
                    load_prev(t)
                    sp.wait_ge(bonus_ready, t - 1)
                    sp.wait_ge(y_made, t - 1)
                    sp.wait_ge(ret_made, t - 1)
                    sp.wait_ge(gate_ready, t - 1)
                    load_feat(j, u)
                    load_ret(j, u)

        @block.vector
        def _(v):
            def chain(order, t, per):
                steps = [0]

                def link(ins):
                    steps[0] += 1
                    assert steps[0] <= per
                    ins.then_inc(order, 1)
                    v.wait_ge(order, t * per + steps[0])

                return link

            def shift_end(j, u):
                t = 2 * j + u
                link = chain(kk_order, t, 5)
                v.wait_ge(shift_order, t * 2 + 2)
                v.tensor_tensor(feat[u][:], feat[u][:], prev[:], ALU.add).then_inc(shifted, 1)
                v.wait_ge(shifted, t + 1)
                link(v.tensor_tensor(k_scaled, k_(u), k_k[:], ALU.mult))
                link(v.tensor_tensor(b_, k_scaled, k_scaled, ALU.mult))
                v.tensor_reduce(kk_stats[:, 0, :], three(b_, RW_HEADS), AX_X, ALU.add).then_inc(kk_squared, 1)
                return link

            def unit_kk(j, u, link):
                v.wait_ge(kk_root, 2 * j + u + 1)
                link(v.tensor_scalar(kk_stats[:, 1, :], kk_stats[:, 1, :], 1e-12, None, ALU.max))
                link(v.reciprocal(kk_stats[:, 2, :], kk_stats[:, 1, :]))
                link(v.tensor_tensor(three(kk, RW_HEADS), three(k_scaled, RW_HEADS), per_row(kk_stats[:, 2, :], RW_N),
                                     ALU.mult))

            def sigmoid_args(j, u):
                v.wait_ge(lifted, (2 * j + u) * 3 + 1)
                v.tensor_tensor(p_t[:], bank[2][:], w0[:], ALU.add).then_inc(w_added, 1)
                v.wait_ge(lifted, (2 * j + u) * 3 + 2)
                v.tensor_tensor(p_inv[:], bank[3][:], a0[:], ALU.add).then_inc(a_added, 1)

            def rated(j, u):
                t = 2 * j + u
                link = chain(b_order, t, 3)
                v.wait_ge(a_ready, t + 1)
                link(v.scalar_tensor_tensor(out=k_scaled, in0=ag[:], scalar=-1.0, in1=k_a[:], op0=ALU.add, op1=ALU.mult))
                link(v.scalar_tensor_tensor(out=k2[:], in0=k_scaled, scalar=1.0, in1=k_(u), op0=ALU.add, op1=ALU.mult))
                link(v.tensor_tensor(b_, kk, ag[:], ALU.mult))

            def tildes(j, u):
                v.wait_ge(exp_ready, (2 * j + u) * 3 + 3)
                v.tensor_tensor(tilde_b[u][:], b_, p_inv[:], ALU.mult).then_inc(tilde_ready, 1)
                v.scalar_tensor_tensor(out=tilde_a[:], in0=kk, scalar=-1.0, in1=p_ex[:], op0=ALU.mult,
                                       op1=ALU.mult).then_inc(tilde_ready, 1)
                v.tensor_tensor(tilde_r[:], r_(u), p_t[:], ALU.mult).then_inc(tilde_ready, 1)
                v.tensor_tensor(tilde_k[u][:], k2[:], p_inv[:], ALU.mult).then_inc(tilde_ready, 1)

            def add_bonus(j, u, first):
                t = 2 * j + u
                link = chain(bonus_order, t, 3)
                if not first:
                    v.wait_ge(rw_ready, t - 1)
                link(v.tensor_tensor(scratch[:], r_(u), k2[:], ALU.mult))
                link(v.tensor_tensor(scratch[:], scratch[:], r_k[:], ALU.mult))
                link(v.tensor_reduce(bonus[:], three(scratch[:], RW_HEADS), AX_X, ALU.add))
                v.tensor_tensor(three(bonus_v[u][:], RW_HEADS), three(v_(u), RW_HEADS), per_row(bonus[:], RW_N), ALU.mult)\
                    .then_inc(bonus_ready, 1)

            def score(j, u, first):
                t = 2 * j + u
                for n in range(1, 8, 2):
                    v.wait_ge(tilde_turned, t * 8 + n + 1)
                    v.tensor_copy(tilde_t[n // 2][:, 4 * (n % 2):4 * (n % 2) + 4, :],
                                  three(bank[n][0:RW_N, :], HG)).then_inc(fm_odd, 1)
                for gr in range(2):
                    v.wait_ge(ab_ready, t * 2 + gr + 1)
                    v.tensor_tensor(x_t[gr][:], ab[gr][:], per_block(pair_mask[0][:], HG), ALU.mult).then_inc(x_started, 1)
                for gr in range(2):
                    v.wait_ge(x_started, t * 2 + gr + 1)
                    v.tensor_tensor(x_t[gr][:], x_t[gr][:], per_block(ident[:], HG), ALU.add).then_inc(x_ready, 1)
                mask_scores(t, 1, rb, incl)
                mask_scores(t, 2, ak, strict)

            def mask_scores(t, n, to, mask):
                for gr in range(2):
                    v.wait_ge(scored, t * 8 + 2 * n + gr + 1)
                    v.tensor_tensor(to[gr][:], three(bank[4 * gr + n][:], HG), per_block(mask[:], HG),
                                    ALU.mult).then_inc(masked, 1)

            def scale_state(t, u, first):
                v.wait_ge(reach_ready, t + 1)
                if not first:
                    v.wait_ge(y_made, t)
                v.tensor_tensor(three(m0[:], RW_HEADS), three(m[:], RW_HEADS), per_row(reach[u][:, :, 0], RW_N),
                                ALU.mult).then_inc(m0_ready, 1)

            def rw_norm(t):
                if not isinstance(t, int) or t:
                    v.wait_ge(rw_turned, t)
                v.wait_ge(y_copied, t + 1)
                link = chain(rw_order, t, 6)
                norm_spread(v, link, y_raw[:], scratch[:], rw_stats, RW_HEADS, RW_N, RW_GN_EPS, y[:], rw_spread)
                return link

            def rw_divide(t, link):
                v.wait_ge(rw_root, t + 1)
                norm_divide(v, link, rw_stats, RW_HEADS, RW_N, y[:], rw_normed)

            def ret_norm(t):
                if not isinstance(t, int) or t:
                    v.wait_ge(ret_out_turned, t)
                v.wait_ge(ret_copied, t + 1)
                link = chain(ret_order, t, 6)
                norm_spread(v, link, ry_raw[:], scratch[:], ret_stats, RET_HEADS, RET_D, RET_GN_EPS, ry[:], ret_spread)
                return link

            def ret_divide(t, link):
                v.wait_ge(ret_root, t + 1)
                norm_divide(v, link, ret_stats, RET_HEADS, RET_D, ry[:], ret_normed)

            def turn(j, u, first, last):
                t = 2 * j + u
                after = (j + u, 1 - u)
                score(j, u, first)
                for s in range(NS):
                    if s == 1:
                        mask_scores(t, 3, rk, incl)
                        scale_state(t, u, first)
                        if not first:
                            rw_link = rw_norm(t - 1)
                    elif s == 2:
                        if not last:
                            kk_link = shift_end(*after)
                        if not first:
                            rw_divide(t - 1, rw_link)
                    elif s == 3:
                        for gr in range(2):
                            v.wait_ge(x_turned, t * 2 * NS + 2 * s + gr + 1)
                            v.tensor_copy(x_n[gr][:], three(bank[4 * gr][:], HG)).then_inc(x_n_by_vector, 1)
                        if not last:
                            unit_kk(*after, kk_link)
                    elif s == 4:
                        if not first:
                            ret_link = ret_norm(t - 1)
                        if not last:
                            sigmoid_args(*after)
                        if not first:
                            ret_divide(t - 1, ret_link)
                    elif s == 5 and not last:
                        rated(*after)
                    for gr in range(2):
                        v.wait_ge(x_step, t * 2 * NS + 2 * s + gr + 1)
                        v.wait_ge(x_ready, t * 2 * (NS + 1) + 2 * s + gr + 1)
                        v.tensor_tensor(x_t[gr][:], x_t[gr][:], three(bank[4 * gr][:], HG), ALU.add).then_inc(x_ready, 1)
                v.wait_ge(ret_scored, t + 1)
                v.tensor_tensor(pt[:], three(bank[6][:], RET_HEADS), intra[:], ALU.mult).then_inc(pt_ready, 1)
                if not last:
                    tildes(*after)
                link = chain(m_order, t, 1)
                v.wait_ge(m_made, t + 1)
                link(v.tensor_tensor(m[:], m0[:], bank[4][0:RW_N, :], ALU.add))
                v.tensor_tensor(three(m[:], RW_HEADS), three(m[:], RW_HEADS), per_row(reach[u][:, :, 1], RW_N), ALU.mult)\
                    .then_inc(m_ready, 1)
                v.wait_ge(m_ready, t + 1)
                if not last:
                    add_bonus(*after, first)
                link = chain(state_order, t, 1)
                v.wait_ge(ret_made, t + 1)
                link(v.tensor_tensor(three(state[:], RET_HEADS), three(state[:], RET_HEADS),
                                     per_row(tile_decay[:], RET_D), ALU.mult))
                v.tensor_tensor(state[:], state[:], bank[6][:], ALU.add).then_inc(state_ready, 1)
                v.wait_ge(state_ready, t + 1)

            v.wait_ge(const, 16 * len(consts))
            link = shift_end(0, 0)
            unit_kk(0, 0, link)
            sigmoid_args(0, 0)
            rated(0, 0)
            tildes(0, 0)
            add_bonus(0, 0, True)
            v.memset(m[:], 0.0).then_inc(zeroed, 1)
            v.memset(state[:], 0.0).then_inc(zeroed, 1)
            v.wait_ge(zeroed, 2)
            each_turn(v, turn)
            link = rw_norm(LAST)
            rw_divide(LAST, link)
            link = ret_norm(LAST)
            ret_divide(LAST, link)

        @block.gpsimd
        def _(pool):
            half = RET_D // 2

            def link(ins, count):
                ins.then_inc(pool_order, 1)
                pool.wait_ge(pool_order, count)

            def shift(j, u):
                t = 2 * j + u
                pool.wait_ge(feat_ready[u], j * 16 + 16)
                pool.wait_ge(prev_ready, t * 16 + 16)
                pool.tensor_tensor(prev[:], prev[:], feat[u][:], ALU.subtract).then_inc(shift_order, 1)
                pool.wait_ge(shift_order, t * 2 + 1)
                pool.tensor_tensor(prev[:], prev[:], mu[:], ALU.mult).then_inc(shift_order, 1)

            def rotate(j, u, first):
                t = 2 * j + u
                pool.wait_ge(ret_in_ready[u], j * 32 + 32)
                if not first:
                    pool.wait_ge(ret_made, t)
                both = ret_in[u][:, 0:2 * RET_W].rearrange("p (h c d) -> p h c d", c=2, d=half)
                to = qk[:].rearrange("p (h c d) -> p h c d", c=2, d=half)
                cos, sin = (per_block(rope[u][:, i, :], 2 * RET_HEADS) for i in range(2))
                parts = [three(rot[:, i, :], 2 * RET_HEADS) for i in range(4)]
                link(pool.tensor_tensor(parts[0], both[:, :, 0, :], cos, ALU.mult), t * 6 + 1)
                link(pool.tensor_tensor(parts[1], both[:, :, 1, :], sin, ALU.mult), t * 6 + 2)
                link(pool.tensor_tensor(parts[2], both[:, :, 0, :], sin, ALU.mult), t * 6 + 3)
                link(pool.tensor_tensor(parts[3], both[:, :, 1, :], cos, ALU.mult), t * 6 + 4)
                link(pool.tensor_tensor(to[:, :, 0, :], parts[0], parts[1], ALU.subtract), t * 6 + 5)
                link(pool.tensor_tensor(to[:, :, 1, :], parts[2], parts[3], ALU.add), t * 6 + 6)
                pool.tensor_tensor(three(kd, RET_HEADS), three(qk[:, RET_W:2 * RET_W], RET_HEADS),
                                   per_row(k_decay[:], RET_D), ALU.mult).then_inc(rotated, 1)

            def rw_leave(t, u):
                pool.wait_ge(rw_normed, t * 3 + 1)
                pool.tensor_tensor(y[:], y[:], rw_gain[:], ALU.mult).then_inc(rw_normed, 1)
                pool.wait_ge(rw_normed, t * 3 + 2)
                pool.tensor_tensor(y[:], y[:], bonus_v[u][:], ALU.add).then_inc(rw_normed, 1)
                pool.wait_ge(rw_normed, t * 3 + 3)
                pool.wait_ge(g_ready, t + 1)
                pool.tensor_tensor(y[:], y[:], g[u][:], ALU.mult).then_inc(rw_ready, 1)

            def ret_leave(t):
                pool.wait_ge(ret_normed, t * 2 + 1)
                pool.tensor_tensor(ry[:], ry[:], ret_gain[:], ALU.mult).then_inc(ret_normed, 1)
                pool.wait_ge(ret_normed, t * 2 + 2)
                pool.wait_ge(gate_ready, t + 1)
                pool.tensor_tensor(ry[:], ry[:], gate[:], ALU.mult).then_inc(ret_ready, 1)

            def turn(j, u, first, last):
                t = 2 * j + u
                rotate(j, u, first)
                for s in range(NS):
                    for gr in range(2):
                        if s == 0:
                            pool.wait_ge(ab_ready, t * 2 + gr + 1)
                        elif s >= 3:
                            pool.wait_ge(z_made, t * 2 * NS + 2 * (s - 3) + gr + 1)
                        pool.tensor_tensor(ab_step[gr][s % 3][:], ab[gr][:], per_block(pair_mask[s + 1][:], HG),
                                           ALU.mult).then_inc(ab_split, 1)
                    if s == 1 and not last:
                        shift(j + u, 1 - u)
                if not first:
                    rw_leave(t - 1, 1 - u)
                    ret_leave(t - 1)
                pool.wait_ge(q_t_ready, t + 1)
                pool.tensor_tensor(qd_t[:], q_t[:], q_decay[:], ALU.mult).then_inc(qd_ready, 1)

            pool.wait_ge(mu_ready, 16)
            shift(0, 0)
            pool.wait_ge(const, 16 * len(consts))
            each_turn(pool, turn)
            rw_leave(LAST, LAST % 2)
            ret_leave(LAST)

        @block.scalar
        def _(act):
            def squash(j, u):
                t = 2 * j + u
                f = feat[u]
                act.wait_ge(shifted, t + 1)
                act.activation(lo[:, 0:LORA], f[:, 1536:1536 + LORA], ACT.Tanh).then_inc(lo_ready, 1)
                act.activation(lo[:, LORA:2 * LORA], f[:, 1536 + LORA:1536 + 2 * LORA], ACT.Copy).then_inc(lo_ready, 1)
                act.activation(lo[:, 2 * LORA:256], f[:, 1536 + 2 * LORA:RW_COLS], ACT.Sigmoid).then_inc(lo_ready, 1)
                act.wait_ge(kk_squared, t + 1)
                act.activation(kk_stats[:, 1, :], kk_stats[:, 0, :], ACT.Sqrt).then_inc(kk_root, 1)

            def take_lo(j, u):
                act.wait_ge(lo_turned, 2 * j + u + 1)
                act.activation(lo_t[:], bank[6][:, 0:256], ACT.Copy).then_inc(lo_t_ready, 1)

            def sigmoids(j, u, first):
                t = 2 * j + u
                act.wait_ge(w_added, t + 1)
                act.activation(sg[:], p_t[:], ACT.Sigmoid).then_inc(sg_ready, 1)
                act.wait_ge(a_added, t + 1)
                act.activation(ag[:], p_inv[:], ACT.Sigmoid).then_inc(a_ready, 1)
                if not first:
                    act.wait_ge(rw_ready, t - 1)
                act.wait_ge(lifted, t * 3 + 3)
                act.activation(g[u][:], bank[7][:], ACT.Copy).then_inc(g_ready, 1)

            def decays(j, u):
                t = 2 * j + u
                act.wait_ge(a_ready, t + 1)
                act.wait_ge(sg_ready, t + 1)
                act.wait_ge(run_ready, t + 1)
                act.wait_ge(b_order, t * 3 + 3)
                act.activation(p_t[:], bank[2][:], ACT.Exp, scale=DECAY).then_inc(exp_ready, 1)
                act.activation(p_inv[:], bank[2][:], ACT.Exp, scale=-DECAY).then_inc(exp_ready, 1)
                act.activation(p_ex[:], bank[3][:], ACT.Exp, scale=DECAY).then_inc(exp_ready, 1)
                act.activation(reach[u][:], three(bank[7][0:RW_N, 0:2 * RW_HEADS], RW_HEADS), ACT.Exp,
                               scale=DECAY).then_inc(reach_ready, 1)

            def rw_deviation(t):
                act.wait_ge(rw_spread, t + 1)
                act.activation(rw_stats[:, 4, :], rw_stats[:, 3, :], ACT.Sqrt).then_inc(rw_root, 1)

            def ret_deviation(t):
                act.wait_ge(ret_spread, t + 1)
                act.activation(ret_stats[:, 4, :], ret_stats[:, 3, :], ACT.Sqrt).then_inc(ret_root, 1)

            def leave(t):
                if not isinstance(t, int) or t:
                    act.wait_ge(stored, t * 16)
                act.wait_ge(rw_turned, t + 1)
                act.activation(out_t[:, 4:8, :], three(bank[7][:], 4), ACT.Copy).then_inc(rw_mixed, 1)
                act.wait_ge(ret_out_turned, t + 1)
                act.activation(out_t[:, 0:4, :], three(bank[3][:], 4), ACT.Copy).then_inc(ret_mixed, 1)
                act.wait_ge(rw_mixed, t + 1)
                act.wait_ge(ret_mixed, t + 1)
                act.dma_start(mixed[ds(t, 1)].rearrange("a p f -> (a p) f"), flat(out_t[:])).then_inc(stored, 16)

            def turn(j, u, first, last):
                t = 2 * j + u
                after = (j + u, 1 - u)
                for n in range(0, 8, 2):
                    act.wait_ge(tilde_turned, t * 8 + n + 1)
                    act.activation(tilde_t[n // 2][:, 0:4, :], three(bank[n][0:RW_N, :], HG), ACT.Copy).then_inc(fm_even, 1)
                for gr in range(2):
                    act.wait_ge(scored, t * 8 + gr + 1)
                    act.activation(ab[gr][:], three(bank[4 * gr][:], HG), ACT.Copy).then_inc(ab_ready, 1)
                for s in range(NS):
                    for gr in range(2 if s != 3 else 0):
                        act.wait_ge(x_turned, t * 2 * NS + 2 * s + gr + 1)
                        act.activation(x_n[gr][:], three(bank[4 * gr][:], HG), ACT.Copy).then_inc(x_n_ready, 1)
                    for gr in range(2):
                        act.wait_ge(z_made, t * 2 * NS + 2 * s + gr + 1)
                        act.activation(zs[gr][:], three(bank[4 * gr + 1][:], HG), ACT.Copy).then_inc(z_ready, 1)
                    if s == 1 and not first:
                        rw_deviation(t - 1)
                    elif s == 2:
                        if not last:
                            squash(*after)
                    elif s == 3:
                        act.wait_ge(q1_made, t + 1)
                        act.activation(q1[:], bank[2][:], ACT.Copy).then_inc(q1_ready, 1)
                        if not last:
                            take_lo(*after)
                    elif s == 4:
                        if not first:
                            ret_deviation(t - 1)
                        if not last:
                            sigmoids(*after, first)
                if not first:
                    act.wait_ge(ret_ready, t)
                act.wait_ge(ret_in_ready[u], j * 32 + 32)
                act.activation(gate[:], ret_in[u][:, 3 * RET_W:4 * RET_W], ACT.Silu).then_inc(gate_ready, 1)
                act.wait_ge(q_turned, t + 1)
                act.activation(q_t[:], three(bank[6][:], RET_HEADS), ACT.Copy).then_inc(q_t_ready, 1)
                act.wait_ge(k_turned, t + 1)
                act.activation(k_t[:], three(bank[5][:], RET_HEADS), ACT.Copy).then_inc(k_t_ready, 1)
                act.wait_ge(u_made, t + 1)
                act.activation(u_[:], bank[1][:], ACT.Copy).then_inc(u_ready, 1)
                if not last:
                    decays(*after)
                act.wait_ge(y_made, t + 1)
                act.activation(y_raw[:], bank[0][:], ACT.Copy).then_inc(y_copied, 1)
                act.wait_ge(ret_made, t + 1)
                act.activation(ry_raw[:], bank[5][:], ACT.Copy).then_inc(ret_copied, 1)
                if not first:
                    leave(t - 1)

            act.wait_ge(const, 16 * len(consts))
            squash(0, 0)
            take_lo(0, 0)
            sigmoids(0, 0, True)
            decays(0, 0)
            each_turn(act, turn)
            rw_deviation(LAST)
            ret_deviation(LAST)
            leave(LAST)
            act.wait_ge(stored, 16 * TT)

        @block.tensor
        def _(pe):
            def turn_lo(j, u):
                pe.wait_ge(lo_ready, (2 * j + u) * 3 + 3)
                pe.transpose(bank[6][:, 0:P], lo[:, 0:P], ident[:])
                pe.transpose(bank[6][:, P:2 * P], lo[:, P:2 * P], ident[:]).then_inc(lo_turned, 1)

            def lift(n, j, u):
                pe.wait_ge(lo_t_ready, 2 * j + u + 1)
                if n == 0:
                    pe.matmul(bank[2][:], lo_t[0:LORA, 0:P], lora_up[0:LORA, :], start=True, stop=True).then_inc(lifted, 1)
                elif n == 1:
                    pe.matmul(bank[3][:], lo_t[LORA:2 * LORA, 0:P], lora_up[LORA:2 * LORA, :], start=True, stop=True)\
                        .then_inc(lifted, 1)
                else:
                    pe.matmul(bank[7][:], lo_t[:, P:2 * P], g_up[:], start=True, stop=True).then_inc(lifted, 1)

            def run_sums(n, j, u):
                t = 2 * j + u
                pe.wait_ge(sg_ready, t + 1)
                if n == 0:
                    pe.matmul(bank[2][:], incl_mid[:], sg[:], start=True, stop=True)
                else:
                    pe.wait_ge(a_added, t + 1)
                    pe.matmul(bank[3][:], strict_mid[:], sg[:], start=True, stop=True)

            def run_spans(j, u):
                pe.wait_ge(g_ready, 2 * j + u + 1)
                for h in range(RW_HEADS):
                    last = pe.matmul(bank[7][0:RW_N, 2 * h:2 * h + 2], head(sg, h, RW_N), ends[:], start=True, stop=True)
                last.then_inc(run_ready, 1)

            def score(j, u, first):
                t = 2 * j + u
                pe.wait_ge(exp_ready, t * 3 + 3)
                pe.wait_ge(reach_ready, t + 1)
                for n in range(8):
                    if not first:
                        if n == 0:
                            pe.wait_ge(y_copied, t)
                        elif n == 3 and (not isinstance(t, int) or t > 1):
                            pe.wait_ge(ret_mixed, t - 1)
                        elif n == 4:
                            pe.wait_ge(m_ready, t)
                        elif n == 5:
                            pe.wait_ge(ret_copied, t)
                        elif n == 6:
                            pe.wait_ge(state_ready, t)
                        elif n == 7 and (not isinstance(t, int) or t > 1):
                            pe.wait_ge(rw_mixed, t - 1)
                    pe.wait_ge(tilde_ready, t * 4 + n // 2 + 1)
                    pe.sem_inc(pe_passed, 1)
                    of = (tilde_b[u], tilde_a, tilde_r, tilde_k[u])[n // 2]
                    for h in range(HG):
                        last = pe.transpose(bank[n][0:RW_N, h * P:(h + 1) * P], head(of, HG * (n % 2) + h, RW_N), ident[:])
                    last.then_inc(tilde_turned, 1)

            def product(t, gr, at, left, right):
                pe.wait_ge(fm_even, t * 4 + (2 + gr, 3, 4, 4)[at])
                pe.wait_ge(fm_odd, t * 4 + (2, 3, 4, 4)[at])
                for h in range(HG):
                    hh = HG * gr + h
                    last = pe.matmul(bank[4 * gr + at][:, h * P:(h + 1) * P], left[:, hh, :], right[:, hh, :],
                                     start=True, stop=True)
                last.then_inc(scored, 1)

            def double(t, s, fill):
                fill(s, 0)
                for gr in range(2):
                    pe.wait_ge(x_ready, t * 2 * (NS + 1) + 2 * s + gr + 1)
                    for h in range(HG):
                        last = pe.transpose(bank[4 * gr][:, h * P:(h + 1) * P], x_t[gr][:, h, :], ident[:])
                    last.then_inc(x_turned, 1)
                fill(s, 1)
                for gr in range(2):
                    if s == 0:
                        pe.wait_ge(masked, t * 6 + gr + 1)
                    if s == 3:
                        pe.wait_ge(x_n_by_vector, t * 2 + gr + 1)
                    else:
                        pe.wait_ge(x_n_ready, t * 2 * (NS - 1) + 2 * (s - (s > 3)) + gr + 1)
                    pe.wait_ge(ab_split, t * 2 * NS + 2 * s + gr + 1)
                    for h in range(HG):
                        last = pe.matmul(bank[4 * gr + 1][:, h * P:(h + 1) * P], ab_step[gr][s % 3][:, h, :],
                                         x_n[gr][:, h, :], start=True, stop=True)
                    last.then_inc(z_made, 1)
                fill(s, 2)
                for gr in range(2):
                    pe.wait_ge(z_ready, t * 2 * NS + 2 * s + gr + 1)
                    for h in range(HG):
                        last = pe.matmul(bank[4 * gr][:, h * P:(h + 1) * P], zs[gr][:, h, :], x_t[gr][:, h, :],
                                         start=True, stop=True)
                    last.then_inc(x_step, 1)

            def turn_ret(t, n, done):
                for h in range(RET_HEADS):
                    last = pe.transpose(bank[(6, 5)[n]][:, h * P:(h + 1) * P],
                                        head(qk[:, n * RET_W:(n + 1) * RET_W], h, RET_D), ident[:])
                last.then_inc(done, 1)

            def leave(t):
                pe.wait_ge(rw_ready, t + 1)
                for n in range(4):
                    last = pe.transpose(bank[7][:, n * P:(n + 1) * P], y[:, n * P:(n + 1) * P], ident[:])
                last.then_inc(rw_turned, 1)
                pe.wait_ge(ret_ready, t + 1)
                for n in range(4):
                    last = pe.transpose(bank[3][:, n * P:(n + 1) * P], ry[:, n * P:(n + 1) * P], ident[:])
                last.then_inc(ret_out_turned, 1)

            def turn(j, u, first, last_turn):
                t = 2 * j + u
                after = (j + u, 1 - u)
                b_t, a_t, r_t, kt_t = tilde_t

                def right_hand_side(n):
                    if n == 0:
                        pe.wait_ge(masked, t * 6 + 6)
                        pe.wait_ge(m0_ready, t + 1)
                    for h in (2 * n, 2 * n + 1):
                        to = head(bank[2], h, RW_N)
                        pe.matmul(to, a_t[:, h, :], head(m0, h, RW_N), start=True, stop=False)
                        last = pe.matmul(to, ak[h // HG][:, h % HG, :], head(v_(u), h, RW_N), start=False, stop=True)
                    if n == 3:
                        last.then_inc(q1_made, 1)

                def fill(s, n):
                    if (s, n) == (0, 1):
                        for gr in range(2):
                            product(t, gr, 2, kt_t, a_t)
                    elif s == 1 and n < 2:
                        product(t, n, 3, kt_t, r_t)
                    elif s in (2, 3) and n < 2:
                        right_hand_side(2 * (s - 2) + n)
                    elif last_turn:
                        return
                    elif (s, n) == (3, 2):
                        turn_lo(*after)
                    elif s == 4:
                        if n == 0:
                            pe.wait_ge(q1_ready, t + 1)
                        lift(n, *after)
                    elif s == 5 and n:
                        run_sums(n - 1, *after)

                score(j, u, first)
                for at, right in ((0, a_t), (1, r_t)):
                    for gr in range(2):
                        product(t, gr, at, b_t, right)
                for s in range(NS):
                    double(t, s, fill)
                if not last_turn:
                    run_spans(*after)
                pe.wait_ge(rotated, t + 1)
                turn_ret(t, 0, q_turned)
                turn_ret(t, 1, k_turned)
                pe.wait_ge(q1_ready, t + 1)
                pe.wait_ge(x_ready, t * 2 * (NS + 1) + 2 * (NS + 1))
                for h in range(RW_HEADS):
                    last = pe.matmul(head(bank[1], h, RW_N), x_t[h // HG][:, h % HG, :], head(q1, h, RW_N),
                                     start=True, stop=True)
                last.then_inc(u_made, 1)
                pe.wait_ge(q_t_ready, t + 1)
                pe.wait_ge(k_t_ready, t + 1)
                for h in range(RET_HEADS):
                    last = pe.matmul(bank[6][:, h * P:(h + 1) * P], k_t[:, h, :], q_t[:, h, :], start=True, stop=True)
                last.then_inc(ret_scored, 1)
                pe.wait_ge(u_ready, t + 1)
                for h in range(RW_HEADS):
                    to = head(bank[4], h, RW_N)[0:RW_N, :]
                    pe.matmul(to, head(tilde_b[u], h, RW_N), head(u_, h, RW_N), start=True, stop=False)
                    last = pe.matmul(to, head(tilde_k[u], h, RW_N), head(v_(u), h, RW_N), start=False, stop=True)
                last.then_inc(m_made, 1)
                for h in range(RW_HEADS):
                    to = head(bank[0], h, RW_N)
                    pe.matmul(to, r_t[:, h, :], head(m0, h, RW_N), start=True, stop=False)
                    pe.matmul(to, rb[h // HG][:, h % HG, :], head(u_, h, RW_N), start=False, stop=False)
                    last = pe.matmul(to, rk[h // HG][:, h % HG, :], head(v_(u), h, RW_N), start=False, stop=True)
                last.then_inc(y_made, 1)
                pe.wait_ge(pt_ready, t + 1)
                pe.wait_ge(qd_ready, t + 1)
                ret_v = ret_in[u][:, 2 * RET_W:3 * RET_W]
                for h in range(RET_HEADS):
                    to = head(bank[5], h, RET_D)
                    pe.matmul(to, pt[:, h, :], head(ret_v, h, RET_D), start=True, stop=False)
                    pe.matmul(to, qd_t[:, h, :], head(state, h, RET_D), start=False, stop=True)
                for h in range(RET_HEADS):
                    last = pe.matmul(head(bank[6], h, RET_D), head(kd, h, RET_D), head(ret_v, h, RET_D), start=True, stop=True)
                last.then_inc(ret_made, 1)
                if not first:
                    if not last_turn:
                        pe.wait_ge(exp_ready, t * 3 + 6)
                        pe.wait_ge(reach_ready, t + 2)
                    leave(t - 1)

            pe.wait_ge(const, 16 * len(consts))
            turn_lo(0, 0)
            for n in range(3):
                lift(n, 0, 0)
            for n in range(2):
                run_sums(n, 0, 0)
            run_spans(0, 0)
            each_turn(pe, turn)
            leave(LAST)


def constants():
    i = np.arange(P)
    incl = (i[:, None] <= i[None, :]).astype(np.float32)
    strict = (i[:, None] < i[None, :]).astype(np.float32)
    first = (i < P // 2).astype(np.float32)[:, None]
    pairs = [((i[:, None] // (2 * s) == i[None, :] // (2 * s)) & (i[:, None] % (2 * s) < s) & (i[None, :] % (2 * s) >= s))
             for s in (1,) + SOLVE_STEPS]
    log_g = np.log(1.0 - np.exp2(-5.0 - np.arange(RET_HEADS)))
    gap = i[None, :] - i[:, None]
    chunk = i // RET_CHUNK
    seen = chunk[None, :] >= chunk[:, None]
    intra = np.exp(log_g[:, None, None] * np.abs(gap)) * seen * RET_D ** -0.5
    half = RET_D // 2
    angle = np.arange(S, dtype=np.float32)[:, None] * (np.float32(10000.0) ** (-np.arange(half, dtype=np.float32) / np.float32(half)))[None, :]
    angle = angle.astype(np.float32).astype(np.float64)
    out = {
        "c_ident": np.eye(P), "c_incl": incl, "c_strict": strict,
        "c_incl_mid": incl - first, "c_strict_mid": strict - first,
        "c_ends": np.concatenate([first, 1.0 - first], axis=1),
        "c_pairs": np.stack(pairs), "c_ret_intra": intra.transpose(1, 0, 2),
        "c_ret_q": np.broadcast_to(np.exp(log_g[:, None] * (i + 1.0)), (P, RET_HEADS, P)),
        "c_ret_k": (np.exp(log_g[None, :] * (P - 1.0 - i)[:, None]) * RET_D ** -0.5),
        "c_ret_tile": np.broadcast_to(np.exp(log_g * P), (P, RET_HEADS)),
        "c_prefer": np.broadcast_to(8.0 - np.arange(8), (P, 8)),
        "c_expert_no": np.broadcast_to(np.arange(EXPERTS), (P, EXPERTS)),
        "c_fulls": np.broadcast_to(SLOT_BLOCK * np.arange(1, FULL_STEPS + 1), (P, FULL_STEPS)),
        "c_earlier": np.broadcast_to(np.tril(np.ones((EXPERTS, EXPERTS)), -1), (P, EXPERTS, EXPERTS)),
        "c_more_no": np.arange(MORE_BLOCKS)[None, :],
        "c_future": np.where(i[None, :] > i[:, None], -FAR, 0.0),
        "c_inv_freq": np.broadcast_to(1.0 / (np.float32(10000.0) ** (np.arange(0, ROPE, 2, dtype=np.float32) / np.float32(ROPE))),
                                      (P, ROPE // 2)),
        "c_rope": np.concatenate([np.cos(angle), np.sin(angle)], axis=1),
    }
    out = {k: np.ascontiguousarray(v, dtype=np.float32) for k, v in out.items()}
    out["c_token_ids"] = (np.arange(TT)[None, :] * P + i[:, None]).astype(np.int32)
    return out


def lay_out(inputs):
    out = {}
    for name, value in inputs.items():
        value = np.ascontiguousarray(value)
        out[name] = value[0] if value.ndim > 1 else value
    out.update(constants())
    return out


def add_product_stage(nc, name, bank, feat, feat_low, w_dram, x, squares, x_dram=None, post_gain=None, store_dram=None, weights=None, feat_dram=None):
    halves = D // BANK
    with Stage(nc, name) as st:
        w, w_low, w_high = weights or (*st.twin("w", [P, KT, D]), st.sb("w_high", [P, KT, D], F32R))
        feat_high = st.sb("feat_high", [P, KT, S], F32R)
        gain = st.sb("gain", [P, D])
        junk, scaled = ([st.sb(f"{name}{n}", [P, BANK]) for n in range(halves)] for name in ("junk", "scaled"))
        stats = st.sb("stats", [P, TT, 6])
        w_loaded = [st.sem(f"w_loaded{n}") for n in range(2 * halves)]
        feat_loaded = [st.sem(f"feat_loaded{t}") for t in range(TT)]
        x_loaded, gain_loaded, stored = st.sem("x_loaded"), st.sem("gain_loaded"), st.sem("stored")
        w_high_ready, w_low_ready, feat_high_ready, feat_low_ready = (
            st.sem(n) for n in ("w_high_ready", "w_low_ready", "feat_high_ready", "feat_low_ready"))
        x_junk = [st.sb(f"x_junk{i}", [P, D]) for i in range(2)]
        product, squared, mean_ready, root_ready, dve_order, added, x_squared = (
            st.sem(n) for n in ("product", "squared", "mean_ready", "root_ready", "dve_order", "added", "x_squared"))
        block = st.open()

        def half(ap, n):
            return ap[:, :, n * BANK:(n + 1) * BANK]

        def quarter(ap, n):
            return half(ap[:, n % 2 * KT // 2:(n % 2 + 1) * KT // 2, :], n // 2)

        def tile(ap, t):
            return ap[:, :, t * P:(t + 1) * P]

        @block.sync
        def _(sp):
            def load_feat(t):
                if feat_dram is not None:
                    sp.dma_start(tile(feat, t), three(feat_dram[t], KT)).then_inc(feat_loaded[t], 16)

            load_feat(0)
            for n in range(2 * halves):
                sp.dma_start(quarter(w, n), w_dram[n % 2 * D // 2:(n % 2 + 1) * D // 2, n // 2 * BANK:(n // 2 + 1) * BANK]
                             .rearrange("(k p) n -> p k n", p=P)).then_inc(w_loaded[n], 16)
            for t in range(1, TT):
                load_feat(t)
            if x_dram is not None:
                sp.dma_start(x[:], x_dram.rearrange("(t p) d -> p t d", p=P)).then_inc(x_loaded, 16)
            if post_gain is not None:
                sp.dma_start(gain[:], rows(post_gain, D)).then_inc(gain_loaded, 16)
            if store_dram is not None:
                for t in range(TT):
                    sp.wait_ge(added, t + 1)
                    sp.dma_start(store_dram[t * P:(t + 1) * P, :], x[:, t, :]).then_inc(stored, 16)
                sp.wait_ge(stored, 16 * TT)

        @block.tensor
        def _(pe):
            for t in range(TT):
                pe.wait_ge(feat_low_ready, t + 1)
                for n in range(halves):
                    if t >= 4:
                        pe.wait_ge(added, t - 3)
                    for k in range(KT):
                        if t == 0 and k % (KT // 2) == 0:
                            pe.wait_ge(w_low_ready, 2 * n + 2 * k // KT + 1)
                        last = three_passes(pe, bank[2 * (t % 4) + n][:],
                                            (tile(feat_high, t)[:, k, :], tile(feat_low, t)[:, k, :]),
                                            (half(w_high, n)[:, k, :], half(w_low, n)[:, k, :]),
                                            start=(k == 0), stop=(k == KT - 1))
                    last.then_inc(product, 1)

        @block.scalar
        def _(act):
            def split_feat(t):
                if feat_dram is not None:
                    act.wait_ge(feat_loaded[t], 16)
                split_high(act, tile(feat_high, t), tile(feat, t)).then_inc(feat_high_ready, 1)

            split_feat(0)
            for n in range(2 * halves):
                act.wait_ge(w_loaded[n], 16)
                split_high(act, quarter(w_high, n), quarter(w, n)).then_inc(w_high_ready, 1)
            for t in range(1, TT):
                split_feat(t)
            for t in range(TT):
                if post_gain is not None:
                    for n in range(halves):
                        act.wait_ge(product, 2 * t + n + 1)
                        if t:
                            act.wait_ge(squared, 2 * t + n - 1)
                        act.activation(junk[n][:], bank[2 * (t % 4) + n][:], ACT.Square,
                                       accum_out=stats[:, t, n:n + 1]).then_inc(squared, 1)
                    act.wait_ge(mean_ready, t + 1)
                    act.activation(stats[:, t, 4:5], stats[:, t, 3:4], ACT.Sqrt).then_inc(root_ready, 1)
                if t:
                    act.wait_ge(added, t)
                    square_rows(act, x, t - 1, x_junk, squares, x_squared)
            act.wait_ge(added, TT)
            square_rows(act, x, TT - 1, x_junk, squares, x_squared)

        @block.vector
        def _(v):
            steps = [0]

            def link(ins):
                steps[0] += 1
                ins.then_inc(dve_order, 1)
                v.wait_ge(dve_order, steps[0])

            def split_feat(t):
                v.wait_ge(feat_high_ready, t + 1)
                split_low(v, tile(feat_low, t), tile(feat, t), tile(feat_high, t)).then_inc(feat_low_ready, 1)

            split_feat(0)
            for n in range(2 * halves):
                v.wait_ge(w_high_ready, n + 1)
                split_low(v, quarter(w_low, n), quarter(w, n), quarter(w_high, n)).then_inc(w_low_ready, 1)
            for t in range(1, TT):
                split_feat(t)
            if x_dram is not None:
                v.wait_ge(x_loaded, 16)
            if post_gain is not None:
                v.wait_ge(gain_loaded, 16)
            for t in range(TT):
                if post_gain is not None:
                    v.wait_ge(squared, 2 * t + 2)
                    link(v.tensor_tensor(stats[:, t, 2:3], stats[:, t, 0:1], stats[:, t, 1:2], ALU.add))
                    v.tensor_scalar(stats[:, t, 3:4], stats[:, t, 2:3], 1.0 / D, EPS, ALU.mult, ALU.add).then_inc(mean_ready, 1)
                    v.wait_ge(root_ready, t + 1)
                    link(v.reciprocal(stats[:, t, 5:6], stats[:, t, 4:5]))
                for n in range(halves):
                    cols = slice(n * BANK, (n + 1) * BANK)
                    v.wait_ge(product, 2 * t + n + 1)
                    if post_gain is None:
                        link(v.tensor_tensor(x[:, t, cols], x[:, t, cols], bank[2 * (t % 4) + n][:], ALU.add))
                    else:
                        link(v.scalar_tensor_tensor(out=scaled[n][:], in0=bank[2 * (t % 4) + n][:],
                                                    scalar=stats[:, t, 5:6], in1=gain[:, cols], op0=ALU.mult, op1=ALU.mult))
                        link(v.tensor_tensor(x[:, t, cols], x[:, t, cols], scaled[n][:], ALU.add))
                v.sem_inc(added, 1)


GROUPS, PER_GROUP = 4, 8
EXPERTS = GROUPS * PER_GROUP
SLOT_BLOCK = 128
MORE_BLOCKS = 2 * S // SLOT_BLOCK - 1
SLOT_BLOCKS = EXPERTS + MORE_BLOCKS
FULL_STEPS = S // SLOT_BLOCK - 1
FAR = 1e30


def route_stage(nc, bank, ident, a, feat, token_ids, slot_weight, slot_index, more, slot_token, load_ahead):
    with Stage(nc, "route") as st:
        w = st.sb("w", [P, KT, GROUPS + EXPERTS])
        bias = st.sb("bias", [P, GROUPS + EXPERTS])
        strict, ones = st.sb("strict", [P, P]), st.sb("ones", [P, P])
        prefer, expert_no = st.sb("prefer", [P, PER_GROUP]), st.sb("expert_no", [P, EXPERTS])
        fulls = st.sb("fulls", [P, FULL_STEPS])
        earlier = st.sb("earlier", [P, EXPERTS, EXPERTS])
        more_no = st.sb("more_no", [1, MORE_BLOCKS])
        logit = st.sb("logit", [P, TT, GROUPS + EXPERTS])
        g_shift, g_hot = st.sb("g_shift", [P, TT, GROUPS]), st.sb("g_hot", [P, TT, GROUPS])
        spread = st.sb("spread", [P, TT, GROUPS, PER_GROUP])
        inside, left, e_hot1, e_hot2, eq = (st.sb(n, [P, TT, PER_GROUP]) for n in ("inside", "left", "e_hot1", "e_hot2", "eq"))
        hot = [st.sb(f"hot{i}", [P, TT, EXPERTS]) for i in range(2)]
        both, rank, weighed = (st.sb(n, [P, TT, EXPERTS]) for n in ("both", "rank", "weighed"))
        carry = st.sb("carry", [P, TT + 1, EXPERTS])
        g_max, g_sum, g_prob, top1, top2, pick, gap, e_gap, denom = (
            st.sb(n, [P, TT]) for n in ("g_max", "g_sum", "g_prob", "top1", "top2", "pick", "gap", "e_gap", "denom"))
        over = st.sb("over", [P, EXPERTS, FULL_STEPS])
        blocks, first, last_of = (st.sb(n, [P, EXPERTS]) for n in ("blocks", "first", "last_of"))
        ahead = st.sb("ahead", [P, EXPERTS, EXPERTS])
        own, place, full, far, shift, where = (st.sb(n, [P, 2, TT]) for n in ("own", "place", "full", "far", "shift", "where"))
        start = st.sb("start", [P, 2, TT])
        past = st.sb("past", [P, 2 * TT, FULL_STEPS])
        passed = st.sb("passed", [1, MORE_BLOCKS, EXPERTS])
        more_f = st.sb("more_f", [1, 2, MORE_BLOCKS])
        used = st.sb("used", [1, 1])
        no_token = st.sb("no_token", [P, SLOT_BLOCKS], I32)
        (const, logits_made, dve_order, g_shifted, g_exp_ready, gap_ready, gap_exp_ready, hot_ready, ranked,
         slots_ready, cleared, cleared_ready, scattered) = (st.sem(n) for n in (
             "const", "logits_made", "dve_order", "g_shifted", "g_exp_ready", "gap_ready", "gap_exp_ready",
             "hot_ready", "ranked", "slots_ready", "cleared", "cleared_ready", "scattered"))
        logit_t = st.sb("logit_t", [GROUPS + EXPERTS, S])
        w_loaded, logits_t_made, first_out, second_out = (
            st.sem(n) for n in ("w_loaded", "logits_t_made", "first_out", "second_out"))
        consts = [(bias[:, 0:GROUPS], rows(a["b_route_group"], GROUPS)), (bias[:, GROUPS:], rows(a["b_route_expert"], EXPERTS)),
                  (strict[:], a["c_strict"]), (prefer[:], a["c_prefer"]), (expert_no[:], a["c_expert_no"]),
                  (fulls[:], a["c_fulls"]), (earlier[:], a["c_earlier"]), (more_no[:], a["c_more_no"]),
                  (token_ids[:], a["c_token_ids"])]
        block = st.open()

        @block.sync
        def _(sp):
            with nc.allow_non_contiguous_dma("the routers' few columns"):
                sp.dma_start(w[:, :, 0:GROUPS], a["w_route_group"].rearrange("(k p) n -> p k n", p=P)).then_inc(w_loaded, 16)
                sp.dma_start(w[:, :, GROUPS:], a["w_route_expert"].rearrange("(k p) n -> p k n", p=P)).then_inc(w_loaded, 16)
                for to, of in consts:
                    sp.dma_start(to, of).then_inc(const, 16)
            sp.wait_ge(cleared, 1)
            sp.dma_start(slot_token.rearrange("(p b) a -> p (b a)", p=P), no_token[:]).then_inc(cleared_ready, 16)
            load_ahead(sp)

        @block.tensor
        def _(pe):
            pe.wait_ge(w_loaded, 32)
            width = GROUPS + EXPERTS
            for n in range(S // BANK):
                for k in range(KT):
                    last = pe.matmul(bank[3 + n][0:width, :], w[:, k, :], feat[:, k, n * BANK:(n + 1) * BANK],
                                     start=(k == 0), stop=(k == KT - 1))
                last.then_inc(logits_t_made, 1)
            pe.wait_ge(first_out, 1)
            pe.wait_ge(second_out, 1)
            for t in range(TT):
                last = pe.transpose(bank[0][:, t * width:(t + 1) * width], logit_t[:, t * P:(t + 1) * P], ident[0:width, 0:width])
            last.then_inc(logits_made, 1)
            pe.wait_ge(const, 16 * len(consts))
            pe.wait_ge(hot_ready, 1)
            every = both[:].rearrange("p t e -> p (t e)")
            pe.matmul(bank[1][:, 0:TT * EXPERTS], strict[:], every, start=True, stop=True)
            pe.matmul(bank[2][:, 0:TT * EXPERTS], ones[:], every, start=True, stop=True).then_inc(ranked, 1)

        @block.scalar
        def _(act):
            act.wait_ge(logits_t_made, 1)
            act.activation(logit_t[:, 0:BANK], bank[3][0:GROUPS + EXPERTS, :], ACT.Copy).then_inc(first_out, 1)
            act.wait_ge(g_shifted, 1)
            act.activation(g_shift[:], g_shift[:], ACT.Exp).then_inc(g_exp_ready, 1)
            act.wait_ge(gap_ready, 1)
            act.activation(e_gap[:], gap[:], ACT.Exp).then_inc(gap_exp_ready, 1)

        @block.gpsimd
        def _(pool):
            pool.wait_ge(cleared_ready, 16)
            pool.wait_ge(slots_ready, 1)
            for c in range(2):
                for t in range(TT):
                    pool.indirect_dma_start(
                        out=slot_token, out_offset=bass.IndirectOffsetOnAxis(ap=slot_index[:, c, t:t + 1], axis=0),
                        in_=token_ids[:, t:t + 1], in_offset=None).then_inc(scattered, 16)
            pool.wait_ge(scattered, 16 * 2 * TT)

        @block.vector
        def _(v):
            steps = [0]

            def link(ins):
                steps[0] += 1
                ins.then_inc(dve_order, 1)
                v.wait_ge(dve_order, steps[0])

            def first_of(hot_out, values, top, n):
                link(v.tensor_tensor(eq[:, :, 0:n], values, per_row(top, n), ALU.is_equal))
                link(v.tensor_tensor(eq[:, :, 0:n], eq[:, :, 0:n], per_block(prefer[:, 0:n], TT), ALU.mult))
                link(v.tensor_reduce(pick[:], eq[:, :, 0:n], AX_X, ALU.max))
                link(v.tensor_tensor(hot_out, eq[:, :, 0:n], per_row(pick[:], n), ALU.is_equal))

            def of_chosen(to, values):
                for c in range(2):
                    link(v.tensor_tensor(weighed[:], hot[c][:], values, ALU.mult))
                    link(v.tensor_reduce(to[:, c, :], weighed[:], AX_X, ALU.add))

            link(v.memset(ones[:], 1.0))
            v.memset(no_token[:], 0).then_inc(cleared, 1)
            v.wait_ge(logits_t_made, 2)
            v.tensor_copy(logit_t[:, BANK:2 * BANK], bank[4][0:GROUPS + EXPERTS, :]).then_inc(second_out, 1)
            v.wait_ge(const, 16 * len(consts))
            v.wait_ge(logits_made, 1)
            link(v.tensor_tensor(logit[:], three(bank[0][:, 0:TT * (GROUPS + EXPERTS)], TT), per_block(bias[:], TT), ALU.add))
            g_logit = logit[:, :, 0:GROUPS]
            link(v.tensor_reduce(g_max[:], g_logit, AX_X, ALU.max))
            v.tensor_tensor(g_shift[:], g_logit, per_row(g_max[:], GROUPS), ALU.subtract).then_inc(g_shifted, 1)
            first_of(g_hot[:], g_logit, g_max[:], GROUPS)
            v.wait_ge(g_exp_ready, 1)
            link(v.tensor_reduce(g_sum[:], g_shift[:], AX_X, ALU.add))
            link(v.reciprocal(g_prob[:], g_sum[:]))
            e_logit = logit[:, :, GROUPS:].rearrange("p t (g e) -> p t g e", g=GROUPS)
            g_wide = g_hot[:].unsqueeze(3).to_broadcast([P, TT, GROUPS, PER_GROUP])
            link(v.tensor_tensor(spread[:], e_logit, g_wide, ALU.mult))
            link(v.tensor_reduce(inside[:], spread[:].rearrange("p t g e -> p t e g"), AX_X, ALU.add))
            link(v.tensor_reduce(top1[:], inside[:], AX_X, ALU.max))
            first_of(e_hot1[:], inside[:], top1[:], PER_GROUP)
            link(v.scalar_tensor_tensor(out=left[:], in0=e_hot1[:], scalar=-FAR, in1=inside[:], op0=ALU.mult, op1=ALU.add))
            link(v.tensor_reduce(top2[:], left[:], AX_X, ALU.max))
            first_of(e_hot2[:], left[:], top2[:], PER_GROUP)
            v.tensor_tensor(gap[:], top2[:], top1[:], ALU.subtract).then_inc(gap_ready, 1)
            for c, e_hot in enumerate((e_hot1, e_hot2)):
                link(v.tensor_tensor(hot[c][:].rearrange("p t (g e) -> p t g e", g=GROUPS), g_wide,
                                     e_hot[:].unsqueeze(2).to_broadcast([P, TT, GROUPS, PER_GROUP]), ALU.mult))
            v.tensor_tensor(both[:], hot[0][:], hot[1][:], ALU.add).then_inc(hot_ready, 1)
            v.wait_ge(gap_exp_ready, 1)
            link(v.tensor_scalar(denom[:], e_gap[:], 1.0, None, ALU.add))
            link(v.reciprocal(denom[:], denom[:]))
            link(v.tensor_tensor(slot_weight[:, 0, :], denom[:], g_prob[:], ALU.mult))
            link(v.tensor_tensor(slot_weight[:, 1, :], slot_weight[:, 0, :], e_gap[:], ALU.mult))
            v.wait_ge(ranked, 1)
            link(v.memset(carry[:, 0, :], 0.0))
            for t in range(TT):
                link(v.tensor_tensor(carry[:, t + 1, :], carry[:, t, :], bank[2][:, t * EXPERTS:(t + 1) * EXPERTS], ALU.add))
            link(v.tensor_tensor(rank[:], three(bank[1][:, 0:TT * EXPERTS], TT), carry[:, 0:TT, :], ALU.add))
            count = carry[:, TT, :]
            link(v.tensor_tensor(over[:], per_row(count, FULL_STEPS), per_block(fulls[:], EXPERTS), ALU.is_gt))
            link(v.tensor_reduce(blocks[:], over[:], AX_X, ALU.add))
            link(v.tensor_tensor(ahead[:], earlier[:], per_block(blocks[:], EXPERTS), ALU.mult))
            link(v.tensor_reduce(first[:], ahead[:], AX_X, ALU.add))
            link(v.tensor_tensor(last_of[:], first[:], blocks[:], ALU.add))
            of_chosen(place, rank[:])
            of_chosen(own, per_block(expert_no[:], TT))
            of_chosen(start, per_block(first[:], TT))
            places = place[:].rearrange("p c t -> p (c t)")
            link(v.tensor_tensor(past[:], per_row(places, FULL_STEPS), per_block(fulls[:], 2 * TT), ALU.is_ge))
            link(v.tensor_reduce(full[:].rearrange("p c t -> p (c t)"), past[:], AX_X, ALU.add))
            link(v.tensor_scalar(far[:], full[:], 1.0, None, ALU.min))
            link(v.tensor_tensor(shift[:], start[:], full[:], ALU.add))
            link(v.scalar_tensor_tensor(out=shift[:], in0=shift[:], scalar=float(EXPERTS - 1), in1=own[:], op0=ALU.add,
                                        op1=ALU.subtract))
            link(v.tensor_tensor(shift[:], shift[:], far[:], ALU.mult))
            link(v.tensor_tensor(shift[:], shift[:], own[:], ALU.add))
            link(v.tensor_tensor(shift[:], shift[:], full[:], ALU.subtract))
            link(v.scalar_tensor_tensor(out=where[:], in0=shift[:], scalar=float(SLOT_BLOCK), in1=place[:], op0=ALU.mult,
                                        op1=ALU.add))
            v.tensor_copy(slot_index[:], where[:]).then_inc(slots_ready, 1)
            link(v.tensor_tensor(passed[:], per_block(last_of[0:1, :], MORE_BLOCKS), per_row(more_no[:], EXPERTS), ALU.is_le))
            link(v.tensor_reduce(more_f[:, 0, :], passed[:], AX_X, ALU.add))
            link(v.tensor_scalar(more_f[:, 0, :], more_f[:, 0, :], float(EXPERTS - 1), None, ALU.min))
            link(v.tensor_reduce(used[:], blocks[0:1, :], AX_X, ALU.add))
            link(v.tensor_scalar(more_f[:, 1, :], more_no[:], used[0:1, 0:1], None, ALU.is_lt))
            link(v.tensor_copy(more[:], more_f[:]))


HIDDEN = 512
FT = HIDDEN // P


class ExpertWeights:

    def __init__(self, nc, ctx, a):
        self.gate, self.gate_low = zip(*(twin(nc, ctx, f"expert_gate{u}", [P, KT, HIDDEN]) for u in range(2)))
        self.up, self.up_low = zip(*(twin(nc, ctx, f"expert_up{u}", [P, KT, HIDDEN]) for u in range(2)))
        self.down = [ctx.enter_context(nc.sbuf_tensor(f"expert_down{u}", [P, FT, D], F32)) for u in range(2)]
        self.gate_loaded, self.up_loaded, self.down_loaded = (
            [nc.alloc_semaphore(name=f"expert_{n}_loaded{u}") for u in range(2)] for n in ("gate", "up", "down"))
        self.a = a

    def sems(self):
        return self.gate_loaded + self.up_loaded + self.down_loaded

    def of(self, name, e):
        return self.a[name][ds(e, 1)].rearrange("a d f -> (a d) f").rearrange("(k p) f -> p k f", p=P)

    def load_gate(self, sp, e, u):
        sp.dma_start(self.gate[u][:], self.of("w_gate", e)).then_inc(self.gate_loaded[u], 16)

    def load_up(self, sp, e, u):
        sp.dma_start(self.up[u][:], self.of("w_up", e)).then_inc(self.up_loaded[u], 16)

    def load_down(self, sp, e, u):
        sp.dma_start(self.down[u][:], self.of("w_down", e)).then_inc(self.down_loaded[u], 16)

    def load_first(self, sp):
        for u in range(2):
            self.load_gate(sp, u, u)
            self.load_up(sp, u, u)
            self.load_down(sp, u, u)


def expert_stage(nc, bank, ident, a, w, part, more, slot_token, h_rows, y_rows):
    with Stage(nc, "expert") as st:
        st.adopt(w.sems())
        gate_high, up_high = part[:, :, 0:HIDDEN], part[:, :, HIDDEN:]
        gain = st.sb("gain", [P, KT])
        ids = st.sb("ids", [P, SLOT_BLOCKS], I32)
        pick = [st.sb(f"pick{u}", [P, 1], I32) for u in range(2)]
        rows_in = [st.sb(f"rows_in{u}", [P, D]) for u in range(2)]
        x_high, x_low = ([st.sb(f"{n}{u}", [P, KT, P], F32R) for u in range(2)] for n in ("x_high", "x_low"))
        silu, hidden = st.sb("silu", [P, HIDDEN]), st.sb("hidden", [P, HIDDEN])
        hidden_t = st.sb("hidden_t", [P, FT, P])
        y = [st.sb(f"y{u}", [P, D]) for u in range(2)]
        ids_loaded, gain_loaded = st.sem("ids_loaded"), st.sem("gain_loaded")
        picked, gathered, stored = ([st.sem(f"{n}{u}") for u in range(2)] for n in ("picked", "gathered", "stored"))
        passed = st.sem("passed")
        gate_high_ready, gate_low_ready, up_high_ready, up_low_ready = (
            st.sem(n) for n in ("gate_high_ready", "gate_low_ready", "up_high_ready", "up_low_ready"))
        x_turned, x_first_ready, x_high_ready, x_low_ready = (
            st.sem(n) for n in ("x_turned", "x_first_ready", "x_high_ready", "x_low_ready"))
        gate_made, up_made, silu_ready, hidden_ready, hidden_turned, hidden_t_ready, made, down_made, y_low, y_high = (
            st.sem(n) for n in ("gate_made", "up_made", "silu_ready", "hidden_ready", "hidden_turned", "hidden_t_ready", "made",
                                "down_made", "y_low", "y_high"))
        block = st.open()
        half = EXPERTS // 2

        def turn_x(pe, n, u, per_u):
            pe.wait_ge(gathered[u], per_u * 16 + 16)
            pe.wait_ge(x_low_ready, n)
            for k in range(KT):
                last = pe.transpose(bank[k // 4][:, (k % 4) * P:(k % 4 + 1) * P], rows_in[u][:, k * P:(k + 1) * P], ident[:])
            last.then_inc(x_turned, 1)

        def lift(pe, n, u):
            pe.wait_ge(x_low_ready, n + 1)
            pe.wait_ge(hidden_ready, n)
            for b, ready, high, low, done in ((2, gate_low_ready, gate_high, w.gate_low[u], gate_made),
                                              (3, up_low_ready, up_high, w.up_low[u], up_made)):
                pe.wait_ge(ready, n + 1)
                for k in range(KT):
                    last = three_passes(pe, bank[b][:], (x_high[u][:, k, :], x_low[u][:, k, :]), (high[:, k, :], low[:, k, :]),
                                        start=(k == 0), stop=(k == KT - 1))
                last.then_inc(done, 1)

        def lower(pe, n, u, per_u):
            pe.wait_ge(hidden_ready, n + 1)
            for k in range(FT):
                last = pe.transpose(bank[4][:, k * P:(k + 1) * P], hidden[:, k * P:(k + 1) * P], ident[:])
            last.then_inc(hidden_turned, 1)
            pe.wait_ge(w.down_loaded[u], per_u * 16 + 16)
            pe.wait_ge(hidden_t_ready, n + 1)
            pe.wait_ge(y_low, n)
            pe.wait_ge(y_high, n)
            for b in range(2):
                for k in range(FT):
                    last = pe.matmul(bank[5 + b][:], hidden_t[:, k, :], w.down[u][:, k, b * BANK:(b + 1) * BANK],
                                     start=(k == 0), stop=(k == FT - 1))
                last.then_inc((made, down_made)[b], 1)

        def split_gate(act, n, u, per_u):
            act.wait_ge(w.gate_loaded[u], per_u * 16 + 16)
            act.wait_ge(gate_made, n)
            split_high(act, gate_high, w.gate[u][:]).then_inc(gate_high_ready, 1)

        def split_up(act, n, u, per_u):
            act.wait_ge(w.up_loaded[u], per_u * 16 + 16)
            act.wait_ge(up_made, n)
            split_high(act, up_high, w.up[u][:]).then_inc(up_high_ready, 1)

        def split_x(act, n, u):
            act.wait_ge(x_turned, n + 1)
            for k in range(KT):
                last = act.activation(x_high[u][:, k, :], bank[k // 4][:, (k % 4) * P:(k % 4 + 1) * P], ACT.Copy, scale=gain[:, k:k + 1])
                if k == 3:
                    last.then_inc(x_first_ready, 1)
            last.then_inc(x_high_ready, 1)

        def gate(act, n):
            act.wait_ge(gate_made, n + 1)
            act.wait_ge(hidden_ready, n)
            act.activation(silu[:], bank[2][:], ACT.Silu).then_inc(silu_ready, 1)

        def take_hidden(act, n):
            act.wait_ge(hidden_turned, n + 1)
            act.activation(hidden_t[:], three(bank[4][:], FT), ACT.Copy).then_inc(hidden_t_ready, 1)

        def out_low(act, n, u, per_u):
            act.wait_ge(made, n + 1)
            act.wait_ge(stored[u], per_u * 16)
            act.activation(y[u][:, 0:BANK], bank[5][:], ACT.Copy).then_inc(y_low, 1)
            act.wait_ge(y_low, n + 1)
            act.wait_ge(y_high, n + 1)
            act.dma_start(y_rows[ds(n * P, P), :], y[u][:]).then_inc(stored[u], 16)

        def low_gate(v, n, u):
            v.wait_ge(gate_high_ready, n + 1)
            split_low(v, w.gate_low[u][:], w.gate[u][:], gate_high).then_inc(gate_low_ready, 1)

        def low_up(v, n, u):
            v.wait_ge(up_high_ready, n + 1)
            split_low(v, w.up_low[u][:], w.up[u][:], up_high).then_inc(up_low_ready, 1)

        def low_x(v, n, u):
            for k in range(KT):
                if k % 4 == 0:
                    v.wait_ge((x_first_ready, x_high_ready)[k // 4], n + 1)
                last = v.scalar_tensor_tensor(out=x_low[u][:, k, :], in0=bank[k // 4][:, (k % 4) * P:(k % 4 + 1) * P],
                                              scalar=gain[:, k:k + 1], in1=x_high[u][:, k, :], op0=ALU.mult, op1=ALU.subtract)
            last.then_inc(x_low_ready, 1)

        def hide(v, n):
            v.wait_ge(silu_ready, n + 1)
            v.wait_ge(up_made, n + 1)
            v.wait_ge(hidden_turned, n)
            v.tensor_tensor(hidden[:], silu[:], bank[3][:], ALU.mult).then_inc(hidden_ready, 1)

        def out_high(v, n, u, per_u):
            v.wait_ge(down_made, n + 1)
            v.wait_ge(stored[u], per_u * 16)
            v.tensor_copy(y[u][:, BANK:D], bank[6][:]).then_inc(y_high, 1)

        def each_more(eng, body):
            def used(i):
                return eng.If(eng.value_load(more[0:1, 1, ds(i, 1)], min_val=0, max_val=1))

            with used(0):
                with eng.Fori(0, MORE_BLOCKS) as i:
                    with used(i):
                        body(i)

        @block.sync
        def _(sp):
            with nc.allow_non_contiguous_dma("a slot's token for each partition"):
                sp.dma_start(ids[:], slot_token.rearrange("(b p) a -> p (b a)", p=P)).then_inc(ids_loaded, 16)
                sp.dma_start(gain[:], a["norm2_gain"].rearrange("(k p) -> p k", p=P)).then_inc(gain_loaded, 16)
            with sp.Fori(1, half) as j:
                for u in range(2):
                    e = j * 2 + u
                    sp.wait_ge(gate_made, e - 1)
                    w.load_gate(sp, e, u)
                    sp.wait_ge(up_made, e - 1)
                    w.load_up(sp, e, u)
                    sp.wait_ge(down_made, e - 1)
                    w.load_down(sp, e, u)

            def load_more(i):
                e = sp.value_load(more[0:1, 0, ds(i, 1)], min_val=0, max_val=EXPERTS - 1)
                sp.wait_ge(down_made, i + EXPERTS)
                w.load_gate(sp, e, 0)
                w.load_up(sp, e, 0)
                w.load_down(sp, e, 0)

            each_more(sp, load_more)

        @block.gpsimd
        def _(pool):
            def fetch(at, u, per_u):
                pool.tensor_copy(pick[u][:], ids[:, at]).then_inc(picked[u], 1)
                pool.wait_ge(picked[u], per_u + 1)
                pool.sem_inc(passed, 1)
                pool.indirect_dma_start(out=rows_in[u][:], out_offset=None, in_=h_rows,
                                        in_offset=bass.IndirectOffsetOnAxis(ap=pick[u][:, 0:1], axis=0)).then_inc(gathered[u], 16)

            def fetch_more(i):
                pool.wait_ge(x_turned, i + EXPERTS)
                pool.wait_ge(gathered[0], (i + half) * 16)
                fetch(ds(i + EXPERTS, 1), 0, i + half)

            pool.wait_ge(ids_loaded, 16)
            for u in range(2):
                fetch(slice(u, u + 1), u, 0)
            with pool.Fori(1, half) as j:
                for u in range(2):
                    pool.wait_ge(x_turned, j * 2 + u - 1)
                    pool.wait_ge(gathered[u], j * 16)
                    fetch(ds(j * 2 + u, 1), u, j)
            each_more(pool, fetch_more)

        @block.tensor
        def _(pe):
            def step(n, j, u):
                lift(pe, n, u)
                turn_x(pe, n + 1, 1 - u, j + u)
                lower(pe, n, u, j)

            def more_block(i):
                n = i + EXPERTS
                turn_x(pe, n, 0, i + half)
                lift(pe, n, 0)
                lower(pe, n, 0, i + half)

            turn_x(pe, 0, 0, 0)
            with pe.Fori(0, half - 1) as j:
                for u in range(2):
                    step(j * 2 + u, j, u)
            step(EXPERTS - 2, half - 1, 0)
            lift(pe, EXPERTS - 1, 1)
            lower(pe, EXPERTS - 1, 1, half - 1)
            each_more(pe, more_block)

        @block.scalar
        def _(act):
            def step(n, j, u):
                gate(act, n)
                split_gate(act, n + 1, 1 - u, j + u)
                take_hidden(act, n)
                split_x(act, n + 1, 1 - u)
                split_up(act, n + 1, 1 - u, j + u)
                out_low(act, n, u, j)

            def more_block(i):
                n = i + EXPERTS
                split_x(act, n, 0)
                split_gate(act, n, 0, i + half)
                split_up(act, n, 0, i + half)
                gate(act, n)
                take_hidden(act, n)
                out_low(act, n, 0, i + half)
                act.wait_ge(stored[0], (i + half) * 16 + 16)
                act.sem_inc(passed, 1)

            split_gate(act, 0, 0, 0)
            act.wait_ge(gain_loaded, 16)
            split_x(act, 0, 0)
            split_up(act, 0, 0, 0)
            with act.Fori(0, half - 1) as j:
                for u in range(2):
                    step(j * 2 + u, j, u)
            step(EXPERTS - 2, half - 1, 0)
            gate(act, EXPERTS - 1)
            take_hidden(act, EXPERTS - 1)
            out_low(act, EXPERTS - 1, 1, half - 1)
            for u in range(2):
                act.wait_ge(stored[u], 16 * half)
            each_more(act, more_block)

        @block.vector
        def _(v):
            def step(n, j, u):
                hide(v, n)
                low_gate(v, n + 1, 1 - u)
                low_x(v, n + 1, 1 - u)
                low_up(v, n + 1, 1 - u)
                out_high(v, n, u, j)

            def more_block(i):
                n = i + EXPERTS
                low_x(v, n, 0)
                low_gate(v, n, 0)
                low_up(v, n, 0)
                hide(v, n)
                out_high(v, n, 0, i + half)

            v.wait_ge(gain_loaded, 16)
            low_gate(v, 0, 0)
            low_x(v, 0, 0)
            low_up(v, 0, 0)
            with v.Fori(0, half - 1) as j:
                for u in range(2):
                    step(j * 2 + u, j, u)
            step(EXPERTS - 2, half - 1, 0)
            hide(v, EXPERTS - 1)
            out_high(v, EXPERTS - 1, 1, half - 1)
            each_more(v, more_block)


def combine_stage(nc, x, squares, y_rows, slot_index, slot_weight, gain_dram, x_dram):
    GROUP = 4
    with Stage(nc, "combine") as st:
        gain = st.sb("gain", [P, D])
        got = st.sb("got", [P, 2, TT, D])
        junk = [st.sb(f"junk{u}", [P, D]) for u in range(2)]
        square, mean, root, rstd = (st.sb(n, [P, TT]) for n in ("square", "mean", "root", "rstd"))
        gathered = [st.sem(f"gathered{t}") for t in range(TT)]
        gain_loaded, stored, added, squared, mean_ready, root_ready, rstd_ready, normed, x_squared = (
            st.sem(n) for n in ("gain_loaded", "stored", "added", "squared", "mean_ready", "root_ready", "rstd_ready", "normed",
                                "x_squared"))
        block = st.open()

        @block.sync
        def _(sp):
            sp.dma_start(gain[:], rows(gain_dram, D)).then_inc(gain_loaded, 16)
            for t in range(TT):
                sp.wait_ge(normed, t + 1)
                sp.dma_start(x_dram[t * P:(t + 1) * P, :], x[:, t, :]).then_inc(stored, 16)
            sp.wait_ge(stored, 16 * TT)

        @block.gpsimd
        def _(pool):
            for t in range(TT):
                for c in range(2):
                    pool.indirect_dma_start(out=got[:, c, t, :], out_offset=None, in_=y_rows,
                                            in_offset=bass.IndirectOffsetOnAxis(ap=slot_index[:, c, t:t + 1], axis=0))\
                        .then_inc(gathered[t], 16)

        @block.vector
        def _(v):
            for g in range(TT // GROUP):
                tiles = range(g * GROUP, (g + 1) * GROUP)
                group = slice(g * GROUP, (g + 1) * GROUP)
                for t in tiles:
                    v.wait_ge(gathered[t], 32)
                    for c in range(2):
                        v.scalar_tensor_tensor(out=x[:, t, :], in0=got[:, c, t, :], scalar=slot_weight[:, c, t:t + 1],
                                               in1=x[:, t, :], op0=ALU.mult, op1=ALU.add).then_inc(added, 1)
                        v.wait_ge(added, 2 * t + c + 1)
                v.wait_ge(squared, (g + 1) * GROUP)
                v.tensor_scalar(mean[:, group], square[:, group], 1.0 / D, EPS, ALU.mult, ALU.add).then_inc(mean_ready, 1)
                v.wait_ge(root_ready, g + 1)
                v.reciprocal(rstd[:, group], root[:, group]).then_inc(rstd_ready, 1)
                v.wait_ge(rstd_ready, g + 1)
                v.wait_ge(gain_loaded, 16)
                for t in tiles:
                    v.scalar_tensor_tensor(out=x[:, t, :], in0=x[:, t, :], scalar=rstd[:, t:t + 1], in1=gain[:], op0=ALU.mult,
                                           op1=ALU.mult).then_inc(normed, 1)

        @block.scalar
        def _(act):
            for g in range(TT // GROUP):
                for t in range(g * GROUP, (g + 1) * GROUP):
                    act.wait_ge(added, 2 * t + 2)
                    if t >= 2:
                        act.wait_ge(squared, t - 1)
                    act.activation(junk[t % 2][:], x[:, t, :], ACT.Square, accum_out=square[:, t:t + 1]).then_inc(squared, 1)
                act.wait_ge(mean_ready, g + 1)
                act.activation(root[:, g * GROUP:(g + 1) * GROUP], mean[:, g * GROUP:(g + 1) * GROUP], ACT.Sqrt).then_inc(root_ready, 1)
            act.wait_ge(squared, TT)
            for t in range(TT):
                act.wait_ge(normed, t + 1)
                square_rows(act, x, t, junk, squares, x_squared)


MLA_HEADS, Q_LORA, KV_LORA, NOPE, ROPE, V_DIM = 8, 256, 128, 64, 32, 64
QK = NOPE + ROPE
SC, SC_TAPS = 256, 3
SSD_HEADS, SSD_HD, SSD_GROUPS, SSD_STATE, SSD_TAPS = 4, 64, 2, 128, 4
SSD = SSD_HEADS * SSD_HD
XBC = SSD + 2 * SSD_GROUPS * SSD_STATE
LATENT = Q_LORA + KV_LORA + ROPE
SC_AT = LATENT
Z_AT = SC_AT + 3 * SC
XBC_AT = Z_AT + SSD
DT_AT = XBC_AT + XBC
TM_COLS = LATENT + SSD + SSD_HEADS
SC_T, XBC_T = 3 * SC // P, XBC // P
MLA_T = MLA_HEADS * V_DIM // P


def wide(psum, b, n):
    return psum[:, b:b + n, :].rearrange("p a b -> p (a b)")


def project2_stage(nc, psum, bank, high, low, feat, a, rows2, latent_squares, xbc):
    with Stage(nc, "project2") as st:
        w_tm, w_tm_low = st.twin("w_tm", [P, KT, TM_COLS])
        w_fm, w_fm_low = zip(*(st.twin(f"w_fm{u}", [P, KT, P]) for u in range(2)))
        w_tm_high = st.sb("w_tm_high", [P, KT, TM_COLS], F32R)
        w_fm_high = [st.sb(f"w_fm_high{u}", [P, KT, P], F32R) for u in range(2)]
        sc = st.sb("sc", [P, SC_T, S])
        acc = st.sb("acc", [P, S])
        junk = [acc[:, n * BANK:(n + 1) * BANK] for n in range(2)]
        latent_squared = [st.sem(f"latent_squared{n}") for n in range(2)]
        taps, bias = st.sb("taps", [P, XBC_T, SSD_TAPS]), st.sb("bias", [P, XBC_T])
        sc_taps = st.sb("sc_taps", [P, SC // P, SC_TAPS])
        const = st.sem("const")
        PIECES = 4
        tm_loaded = [st.sem(f"tm_loaded{n}") for n in range(PIECES + 1)]
        each = KT // PIECES
        tm_parts = [(slice(c * each, (c + 1) * each), slice(0, LATENT)) for c in range(PIECES)] + \
            [(slice(0, KT), slice(LATENT, TM_COLS))]
        fm_loaded = [st.sem(f"fm_loaded{u}") for u in range(2)]
        made = [st.sem(f"made{u}") for u in range(2)]
        tm_high_ready, tm_low_ready = st.sem("tm_high_ready"), st.sem("tm_low_ready")
        fm_high_ready, fm_low_ready = ([st.sem(f"{n}{u}") for u in range(2)] for n in ("fm_high_ready", "fm_low_ready"))
        product, latent_out, z_out, sc_out, scaled, tapped, xbc_out = (
            st.sem(n) for n in ("product", "latent_out", "z_out", "sc_out", "scaled", "tapped", "xbc_out"))
        gated, sc_scaled, sc_order = st.sem("gated"), st.sem("sc_scaled"), st.sem("sc_order")
        block = st.open()

        def cols(w, at, n):
            return w[:, at:at + n].rearrange("(k p) n -> p k n", p=P)

        w_dram = a["w_in_2"]

        @block.sync
        def _(sp):
            for c in range(PIECES):
                sp.dma_start(w_tm[:, c * each:(c + 1) * each, 0:LATENT],
                             cols(w_dram[c * each * P:(c + 1) * each * P, :], 0, LATENT)).then_inc(tm_loaded[c], 16)
            sp.dma_start(w_tm[:, :, LATENT:LATENT + SSD], cols(w_dram, Z_AT, SSD)).then_inc(tm_loaded[PIECES], 16)
            with nc.allow_non_contiguous_dma("a few taps for each channel"):
                sp.dma_start(w_tm[:, :, LATENT + SSD:], cols(w_dram, DT_AT, SSD_HEADS)).then_inc(tm_loaded[PIECES], 16)
                for i in range(SSD_TAPS):
                    sp.dma_start(taps[:, :, i], a["ssd_conv_w_2"][i, :].rearrange("(c p) -> p c", p=P)).then_inc(const, 16)
                sp.dma_start(bias[:], a["ssd_conv_b_2"].rearrange("(c p) -> p c", p=P)).then_inc(const, 16)
                for i in range(SC_TAPS):
                    sp.dma_start(sc_taps[:, :, i], a["sc_conv_w_2"][i, :].rearrange("(c p) -> p c", p=P)).then_inc(const, 16)
            with sp.Fori(0, SC_T) as j:
                for u, at in enumerate((SC_AT, XBC_AT)):
                    sp.wait_ge(made[u], j)
                    sp.dma_start(w_fm[u][:], w_dram[:, ds(j * P + at, P)].rearrange("(k p) n -> p k n", p=P))\
                        .then_inc(fm_loaded[u], 16)

        @block.tensor
        def _(pe):
            for t in range(TT):
                tile = slice(t * P, (t + 1) * P)
                if t >= 4:
                    pe.wait_ge(latent_out, t - 3)
                    pe.wait_ge(z_out, t - 3)
                for n, (lo_, hi) in enumerate(((0, LATENT), (LATENT, TM_COLS))):
                    for k in range(KT):
                        if t == 0 and k % each == 0:
                            pe.wait_ge(tm_low_ready, PIECES + 1 if n else k // each + 1)
                        last = three_passes(pe, bank[2 * (t % 4) + n][:, 0:hi - lo_], (high[:, k, tile], low[:, k, tile]),
                                            (w_tm_high[:, k, lo_:hi], w_tm_low[:, k, lo_:hi]), start=(k == 0), stop=(k == KT - 1))
                    last.then_inc(product, 1)
            pe.wait_ge(latent_out, TT)
            pe.wait_ge(z_out, TT)
            with pe.Fori(0, SC_T) as j:
                for u in range(2):
                    pe.wait_ge(fm_low_ready[u], j + 1)
                    pe.wait_ge((sc_out, tapped)[u], j * (1, 3)[u])
                    for n in range(2):
                        half = slice(n * BANK, (n + 1) * BANK)
                        for k in range(KT):
                            last = three_passes(pe, bank[2 * u + n][:], (w_fm_high[u][:, k, :], w_fm_low[u][:, k, :]),
                                                (high[:, k, half], low[:, k, half]), start=(k == 0), stop=(k == KT - 1))
                    last.then_inc(made[u], 1)

        @block.scalar
        def _(act):
            def split(j, u):
                act.wait_ge(fm_loaded[u], j * 16 + 16)
                split_high(act, w_fm_high[u][:], w_fm[u][:]).then_inc(fm_high_ready[u], 1)

            def take_sc(j):
                act.wait_ge(made[0], j + 1)
                act.activation(sc[:, ds(j, 1), :].rearrange("p a s -> p (a s)"), wide(psum, 0, 2), ACT.Copy).then_inc(sc_out, 1)

            def convolve(j):
                act.wait_ge(made[1], j + 1)
                act.wait_ge(xbc_out, j)
                act.activation(acc[:], wide(psum, 2, 2), ACT.Identity, scale=taps[:, ds(j, 1), SSD_TAPS - 1],
                               bias=bias[:, ds(j, 1)]).then_inc(scaled, 1)
                act.wait_ge(tapped, j * 3 + 3)
                act.activation(xbc[:, ds(j, 1), :].rearrange("p a s -> p (a s)"), acc[:], ACT.Silu).then_inc(xbc_out, 1)

            def scale_first(i):
                act.wait_ge(gated, i + 1)
                act.activation(sc[:, i + 4, :], sc[:, i + 2, :], ACT.Copy, scale=sc_taps[:, i, SC_TAPS - 1:SC_TAPS])\
                    .then_inc(sc_scaled, 1)

            for n, (ks, ns) in enumerate(tm_parts):
                act.wait_ge(tm_loaded[n], 32 if n == PIECES else 16)
                split_high(act, w_tm_high[:, ks, ns], w_tm[:, ks, ns]).then_inc(tm_high_ready, 1)
            for u in range(2):
                split(0, u)
            for t in range(TT):
                act.wait_ge(product, 2 * t + 1)
                act.activation(rows2[:, t, 0:LATENT], bank[2 * (t % 4)][:, 0:LATENT], ACT.Copy)
                for n, (at, width) in enumerate(((0, Q_LORA), (Q_LORA, KV_LORA))):
                    if t:
                        act.wait_ge(latent_squared[n], t)
                    act.activation(junk[n][:, 0:width], bank[2 * (t % 4)][:, at:at + width], ACT.Square,
                                   accum_out=latent_squares[:, n, t:t + 1]).then_inc(latent_squared[n], 1)
                act.wait_ge(latent_squared[1], t + 1)
                act.sem_inc(latent_out, 1)
            act.wait_ge(const, 16 * (SSD_TAPS + 1 + SC_TAPS))
            with act.Fori(0, SC_T - 1) as j:
                take_sc(j)
                split(j + 1, 0)
                convolve(j)
                split(j + 1, 1)
            scale_first(0)
            take_sc(SC_T - 1)
            convolve(SC_T - 1)
            scale_first(1)

        @block.vector
        def _(v):
            def split(j, u):
                v.wait_ge(fm_high_ready[u], j + 1)
                split_low(v, w_fm_low[u][:], w_fm[u][:], w_fm_high[u][:]).then_inc(fm_low_ready[u], 1)

            def convolve(j):
                v.wait_ge(scaled, j + 1)
                for i in range(1, SSD_TAPS):
                    if i > 1:
                        v.wait_ge(tapped, j * 3 + i - 1)
                    v.scalar_tensor_tensor(out=acc[:, i:], in0=wide(psum, 2, 2)[:, 0:S - i],
                                           scalar=taps[:, ds(j, 1), SSD_TAPS - 1 - i], in1=acc[:, i:],
                                           op0=ALU.mult, op1=ALU.add).then_inc(tapped, 1)

            def gate(i):
                v.wait_ge(sc_out, i + 5)
                v.tensor_tensor(sc[:, i + 2, :], sc[:, i + 2, :], sc[:, i + 4, :], ALU.mult).then_inc(gated, 1)

            def short_convolve(i):
                v.wait_ge(sc_scaled, i + 1)
                for n in range(1, SC_TAPS):
                    v.scalar_tensor_tensor(out=sc[:, i + 4, n:], in0=sc[:, i + 2, 0:S - n],
                                           scalar=sc_taps[:, i, SC_TAPS - 1 - n:SC_TAPS - n], in1=sc[:, i + 4, n:],
                                           op0=ALU.mult, op1=ALU.add).then_inc(sc_order, 1)
                    v.wait_ge(sc_order, (SC_TAPS - 1) * i + n)

            for n, (ks, ns) in enumerate(tm_parts):
                v.wait_ge(tm_high_ready, n + 1)
                split_low(v, w_tm_low[:, ks, ns], w_tm[:, ks, ns], w_tm_high[:, ks, ns]).then_inc(tm_low_ready, 1)
            for u in range(2):
                split(0, u)
            for t in range(TT):
                v.wait_ge(product, 2 * t + 2)
                v.tensor_copy(rows2[:, t, LATENT:], bank[2 * (t % 4) + 1][:, 0:SSD + SSD_HEADS]).then_inc(z_out, 1)
            v.wait_ge(const, 16 * (SSD_TAPS + 1 + SC_TAPS))
            with v.Fori(0, XBC_T - 1) as j:
                split(j + 1, 0)
                convolve(j)
                split(j + 1, 1)
            gate(0)
            short_convolve(0)
            convolve(XBC_T - 1)
            gate(1)
            short_convolve(1)
            v.wait_ge(made[1], XBC_T)
            for i in range(2):
                v.tensor_tensor(feat[:, MLA_T + i, :], sc[:, i + 4, :], sc[:, i, :], ALU.mult).then_inc(sc_order, 1)


def mixers2_stage(nc, bank, ident, a, rows2, latent_squares, xbc, feat, q_t, k_t, values, spare):
    R2 = ROPE // 2
    with Stage(nc, "mixers2") as st:
        q_cols, kv_cols = MLA_HEADS * QK, MLA_HEADS * (NOPE + V_DIM)
        w_q = three(spare[:, 0:Q_LORA // P * q_cols], Q_LORA // P)
        w_kv = spare[:, Q_LORA // P * q_cols:Q_LORA // P * q_cols + kv_cols]
        gains = st.sb("gains", [P, 3])
        incl = st.sb("incl", [P, P])
        inv_freq = st.sb("inv_freq", [P, R2])
        pos_i, pos = st.sb("pos_i", [P, TT], I32), st.sb("pos", [P, TT])
        angle, turns, wrap = (st.sb(n, [P, TT, R2]) for n in ("angle", "turns", "wrap"))
        turns_i = st.sb("turns_i", [P, TT, R2], I32)
        cos, sin = st.sb("cos", [P, TT, R2]), st.sb("sin", [P, TT, R2])
        dt_bias, a_log, d_skip = (st.sb(n, [P, SSD_HEADS]) for n in ("dt_bias", "a_log", "d_skip"))
        dt, dt_raw, soft, a_dt = (st.sb(n, [P, TT, SSD_HEADS]) for n in ("dt", "dt_raw", "soft", "a_dt"))
        ssd_gain = st.sb("ssd_gain", [P, SSD // P])
        junk = [st.sb(f"junk{n}", [P, Q_LORA]) for n in range(2)]
        stats = st.sb("stats", [P, 4, 2, TT])
        latent = st.sb("latent", [P, Q_LORA + KV_LORA])
        latent_t = st.sb("latent_t", [P, 3, P])
        q_row = st.sb("q_row", [P, MLA_HEADS + 1, QK])
        k_row = st.sb("k_row", [P, MLA_HEADS, QK])
        rot = st.sb("rot", [P, 4, MLA_HEADS + 1, R2])
        cur = [st.sb(f"cur{u}", [P, XBC_T, P]) for u in range(2)]
        row = st.sb("row", [P, BANK])
        a_wide, decay, pt = (st.sb(n, [P, SSD_HEADS, P]) for n in ("a_wide", "decay", "pt"))
        run, to_end, run_exp, tile_exp, end_gap = (st.sb(n, [P, SSD_HEADS]) for n in ("run", "to_end", "run_exp", "tile_exp", "end_gap"))
        xdt, xdt_end, state = (st.sb(n, [P, SSD]) for n in ("xdt", "xdt_end", "state"))
        part = st.sb("part", [P, SSD])
        y = three(flat(feat[:, 0:TT * SSD // S, :]), TT)
        y_stats = st.sb("y_stats", [P, 4, TT])
        names = ("const rates_loaded angles_loaded w_loaded angle_ready trig_ready soft_asked soft_ready rates_ready dve_order pool_order copied "
                 "squared mean_ready root_ready normed silu_ready latent_ready latent_turned latent_t_ready lifted q_ready k_ready v_ready "
                 "q_rotated heads_turned heads_even heads_odd row_turned row_ready skip_ready a_wide_ready run_made "
                 "run_order scored gap_ready decay_ready gaps_ready mask_order pt_ready xdt_ready y_made y_order y_summed y_ready "
                 "state_made state_order state_ready y_squared y_mean y_root y_rstd y_normed y_turned y_out pool_passed").split()
        s = {n: st.sem(n) for n in names}
        block = st.open()
        with_const = [
            (gains[:, 0:2], a["mla_q_norm_2"].rearrange("(k p) -> p k", p=P)),
            (gains[:, 2:3], a["mla_kv_norm_2"].rearrange("(k p) -> p k", p=P)),
            (ssd_gain[:], a["ssd_norm_2"].rearrange("(k p) -> p k", p=P)),
            (incl[:], a["c_incl"]), (d_skip[:], rows(a["ssd_d_2"], SSD_HEADS))]
        for_rates = [(dt_bias[:], rows(a["ssd_dt_bias_2"], SSD_HEADS)), (a_log[:], rows(a["ssd_a_log_2"], SSD_HEADS))]
        for_angles = [(pos_i[:], a["positions_2"].rearrange("(t p) -> p t", p=P)), (inv_freq[:], a["c_inv_freq"])]
        for_lift = [(w_q, a["mla_w_q_up_2"].rearrange("(k p) n -> p k n", p=P)), (w_kv, a["mla_w_kv_up_2"])]

        @block.sync
        def _(sp):
            with nc.allow_non_contiguous_dma("gains and positions, one to a partition"):
                for loads, done in ((for_rates, "rates_loaded"), (for_angles, "angles_loaded"), (with_const, "const"),
                                    (for_lift, "w_loaded")):
                    for to, of in loads:
                        sp.dma_start(to, of).then_inc(s[done], 16)

        def each_turn(eng, turn):
            turn(0, 0, True, False)
            turn(1, 1, False, False)
            with eng.Fori(1, TT // 2 - 1) as j:
                for u in range(2):
                    turn(j * 2 + u, u, False, False)
            turn(TT - 2, 0, False, False)
            turn(TT - 1, 1, False, True)

        def at_tile(ap, t):
            return ap[:, ds(t, 1), :].rearrange("p a d -> p (a d)")

        @block.gpsimd
        def _(pool):
            def link(ins, count):
                ins.then_inc(s["pool_order"], 1)
                pool.wait_ge(s["pool_order"], count)
                pool.sem_inc(s["pool_passed"], 1)

            def copy_cur(t, u):
                pool.tensor_copy(cur[u][:], xbc[:, :, ds(t * P, P)]).then_inc(s["copied"], 1)

            def turn(t, u, first, last):
                if first:
                    copy_cur(1, 1)
                else:
                    pool.wait_ge(s["state_made"], t)
                    pool.sem_inc(s["pool_passed"], 1)
                    if not last:
                        copy_cur(t + 1, 1 - u)
                    pool.wait_ge(s["heads_turned"], t * 4)
                    pool.sem_inc(s["pool_passed"], 1)
                link(pool.tensor_copy(q_row[:, MLA_HEADS, NOPE:QK],
                                      at_tile(rows2, t)[:, Q_LORA + KV_LORA:LATENT]), t * 7 + 1)
                pool.wait_ge(s["q_ready"], t * 2 + 2)
                pool.sem_inc(s["pool_passed"], 1)
                first_half, second_half = q_row[:, :, NOPE:NOPE + R2], q_row[:, :, NOPE + R2:QK]
                c, n = (x[:, ds(t, 1), :].to_broadcast([P, MLA_HEADS + 1, R2]) for x in (cos, sin))
                link(pool.tensor_tensor(rot[:, 0], first_half, c, ALU.mult), t * 7 + 2)
                link(pool.tensor_tensor(rot[:, 1], second_half, n, ALU.mult), t * 7 + 3)
                link(pool.tensor_tensor(rot[:, 2], second_half, c, ALU.mult), t * 7 + 4)
                link(pool.tensor_tensor(rot[:, 3], first_half, n, ALU.mult), t * 7 + 5)
                link(pool.tensor_tensor(first_half, rot[:, 0], rot[:, 1], ALU.subtract), t * 7 + 6)
                link(pool.tensor_tensor(second_half, rot[:, 2], rot[:, 3], ALU.add), t * 7 + 7)
                pool.tensor_copy(k_row[:, :, NOPE:QK], q_row[:, MLA_HEADS:MLA_HEADS + 1, NOPE:QK]
                                 .to_broadcast([P, MLA_HEADS, ROPE])).then_inc(s["q_rotated"], 1)

            copy_cur(0, 0)
            pool.wait_ge(s["trig_ready"], 2)
            each_turn(pool, turn)

        @block.scalar
        def _(act):
            act.wait_ge(s["mean_ready"], 2)
            act.activation(stats[:, 2, :, :], stats[:, 1, :, :], ACT.Sqrt).then_inc(s["root_ready"], 1)
            act.wait_ge(s["rates_loaded"], 16 * len(for_rates))
            act.wait_ge(s["soft_asked"], 1)
            act.activation(soft[:], soft[:], ACT.Exp, scale=-1.0).then_inc(s["soft_ready"], 1)
            act.activation(a_log[:], a_log[:], ACT.Exp).then_inc(s["rates_ready"], 1)
            act.wait_ge(s["soft_ready"], 1)
            act.activation(soft[:], soft[:], ACT.Ln, bias=1.0).then_inc(s["soft_ready"], 1)
            act.activation(rows2[:, :, LATENT:LATENT + SSD], rows2[:, :, LATENT:LATENT + SSD], ACT.Silu).then_inc(s["silu_ready"], 1)
            for n, to in enumerate((sin, cos)):
                act.wait_ge(s["angle_ready"], n + 1)
                act.activation(to[:], wrap[:] if n else angle[:], ACT.Sin).then_inc(s["trig_ready"], 1)

            def heads_even(t):
                for n, to in enumerate((q_t, k_t)):
                    act.wait_ge(s["heads_turned"], t * 4 + 2 * n + 1)
                    act.activation(to[:, 0:4, ds(t * P, P)], three(bank[1 + 2 * n][0:QK, :], 4), ACT.Copy).then_inc(s["heads_even"], 1)

            def turn(t, u, first, last):
                act.wait_ge(s["row_turned"], t + 1)
                if not first:
                    act.wait_ge(s["state_made"], t)
                    act.wait_ge(s["skip_ready"], t)
                act.activation(row[:], bank[5][:], ACT.Copy).then_inc(s["row_ready"], 1)
                act.wait_ge(s["gap_ready"], t + 1)
                act.activation(decay[:], decay[:], ACT.Exp).then_inc(s["decay_ready"], 1)
                act.wait_ge(s["gaps_ready"], t + 1)
                act.activation(to_end[:], end_gap[:], ACT.Exp).then_inc(s["decay_ready"], 1)
                if not first:
                    act.wait_ge(s["y_summed"], t)
                    act.wait_ge(s["state_ready"], t)
                act.activation(run_exp[:], run[:], ACT.Exp).then_inc(s["decay_ready"], 1)
                act.activation(tile_exp[:], three(bank[6][:], SSD_HEADS)[:, :, P - 1], ACT.Exp).then_inc(s["decay_ready"], 1)
                if not first:
                    heads_even(t - 1)
                for n in range(2):
                    act.wait_ge(s["lifted"], t * 4 + n + 1)
                    act.activation(q_row[:, 4 * n:4 * n + 4, :], three(bank[1 + n][:, 0:4 * QK], 4), ACT.Copy).then_inc(s["q_ready"], 1)
                for n in range(2):
                    act.wait_ge(s["k_ready"], t * 2 + n + 1)
                    act.activation(values[:, ds(t, 1), 4 * V_DIM * n:4 * V_DIM * (n + 1)].rearrange("p a (h d) -> p (a h) d", d=V_DIM),
                                   three(bank[3 + n][:], 4)[:, :, NOPE:], ACT.Copy).then_inc(s["v_ready"], 1)

            each_turn(act, turn)
            heads_even(TT - 1)
            for t in range(TT):
                act.wait_ge(s["y_ready"], t + 1)
                if t >= 2:
                    act.wait_ge(s["y_squared"], t - 1)
                act.activation(junk[t % 2][:], y[:, t, :], ACT.Square, accum_out=y_stats[:, 0, t:t + 1]).then_inc(s["y_squared"], 1)
            act.wait_ge(s["y_mean"], 1)
            act.activation(y_stats[:, 2, :], y_stats[:, 1, :], ACT.Sqrt).then_inc(s["y_root"], 1)
            for i in range(2):
                for half in range(2):
                    act.wait_ge(s["y_turned"], 2 * i + half + 1)
                    act.activation(feat[:, KT - 2 + i, half * BANK:(half + 1) * BANK], bank[2 * i + half][:], ACT.Copy,
                                   scale=ssd_gain[:, i:i + 1]).then_inc(s["y_out"], 1)

        @block.tensor
        def _(pe):
            def heads(t):
                pe.wait_ge(s["q_rotated"], t + 1)
                pe.wait_ge(s["k_ready"], t * 2 + 2)
                pe.wait_ge(s["v_ready"], t * 2 + 2)
                for n in range(4):
                    of = (q_row, k_row)[n // 2]
                    for h in range(4):
                        last = pe.transpose(bank[1 + n][0:QK, h * P:(h + 1) * P], of[:, 4 * (n % 2) + h, :], ident[:])
                    last.then_inc(s["heads_turned"], 1)

            def turn(t, u, first, last):
                pe.wait_ge(s["copied"], t + 1)
                if not first:
                    pe.wait_ge(s["y_summed"], t)
                    pe.wait_ge(s["pt_ready"], t)
                for i in range(4):
                    last_one = pe.transpose(bank[5][:, i * P:(i + 1) * P], cur[u][:, i, :], ident[:])
                last_one.then_inc(s["row_turned"], 1)
                for gr in range(SSD_GROUPS):
                    last_one = pe.matmul(bank[7][:, gr * P:(gr + 1) * P], cur[u][:, 2 + gr, :], cur[u][:, 4 + gr, :], start=True, stop=True)
                last_one.then_inc(s["scored"], 1)
                pe.wait_ge(s["a_wide_ready"], t + 1)
                if not first:
                    pe.wait_ge(s["state_ready"], t)
                for h in range(SSD_HEADS):
                    pe.matmul(bank[6][:, h * P:(h + 1) * P], a_wide[:, h, :], incl[:], start=True, stop=True)
                pe.matmul(bank[7][:, 2 * P:2 * P + SSD_HEADS], incl[:], at_tile(a_dt, t), start=True, stop=True)\
                    .then_inc(s["run_made"], 1)
                pe.wait_ge(s["latent_ready"], t * 2 + 2)
                for i in range(3):
                    last_one = pe.transpose(bank[0][:, i * P:(i + 1) * P], latent[:, i * P:(i + 1) * P], ident[:])
                last_one.then_inc(s["latent_turned"], 1)
                if not first:
                    heads(t - 1)
                pe.wait_ge(s["latent_t_ready"], t + 1)
                if first:
                    pe.wait_ge(s["w_loaded"], 16 * len(for_lift))
                if not first:
                    pe.wait_ge(s["heads_even"], t * 2)
                    pe.wait_ge(s["heads_odd"], t * 2)
                for n in range(2):
                    for k in range(2):
                        last_one = pe.matmul(bank[1 + n][:, 0:4 * QK], latent_t[:, k, :], w_q[:, k, 4 * QK * n:4 * QK * (n + 1)],
                                             start=(k == 0), stop=(k == 1))
                    last_one.then_inc(s["lifted"], 1)
                pe.wait_ge(s["row_ready"], t + 1)
                pe.wait_ge(s["xdt_ready"], t * 2 + 2)
                pe.wait_ge(s["pt_ready"], t + 1)
                for gr in range(SSD_GROUPS):
                    pe.matmul(bank[5][:, gr * P:(gr + 1) * P], cur[u][:, 4 + gr, :], state[:, gr * P:(gr + 1) * P], start=True, stop=True)
                for h in range(SSD_HEADS):
                    at = h * SSD_HD
                    last_one = pe.matmul(bank[5][:, SSD + at:SSD + at + SSD_HD], pt[:, h, :], xdt[:, at:at + SSD_HD], start=True, stop=True)
                last_one.then_inc(s["y_made"], 1)
                pe.wait_ge(s["decay_ready"], t * 4 + 4)
                for gr in range(SSD_GROUPS):
                    last_one = pe.matmul(bank[6][:, gr * P:(gr + 1) * P], row[:, SSD + gr * P:SSD + (gr + 1) * P],
                                         xdt_end[:, gr * P:(gr + 1) * P], start=True, stop=True)
                last_one.then_inc(s["state_made"], 1)
                for n in range(2):
                    pe.matmul(bank[3 + n][:], latent_t[:, 2, :], w_kv[:, n * BANK:(n + 1) * BANK], start=True, stop=True)\
                        .then_inc(s["lifted"], 1)

            pe.wait_ge(s["const"], 16 * len(with_const))
            each_turn(pe, turn)
            heads(TT - 1)
            pe.wait_ge(s["y_normed"], 1)
            pe.wait_ge(s["heads_even"], TT * 2)
            pe.wait_ge(s["heads_odd"], TT * 2)
            for i in range(2):
                for half in range(2):
                    for t in range(4):
                        last_one = pe.transpose(bank[2 * i + half][:, t * P:(t + 1) * P], y[:, 4 * half + t, i * P:(i + 1) * P], ident[:])
                    last_one.then_inc(s["y_turned"], 1)

        @block.vector
        def _(v):
            BEFORE = 22
            steps = [0]

            def link(ins):
                steps[0] += 1
                ins.then_inc(s["dve_order"], 1)
                v.wait_ge(s["dve_order"], steps[0])

            for n, width in enumerate((Q_LORA, KV_LORA)):
                v.tensor_scalar(stats[:, 1, n, :], latent_squares[:, n, :], 1.0 / width, EPS, ALU.mult, ALU.add)\
                    .then_inc(s["mean_ready"], 1)
            link(v.memset(state[:], 0.0))
            v.wait_ge(s["rates_loaded"], 16 * len(for_rates))
            link(v.tensor_tensor(dt_raw[:], rows2[:, :, LATENT + SSD:], per_block(dt_bias[:], TT), ALU.add))
            v.scalar_tensor_tensor(out=soft[:], in0=dt_raw[:], scalar=-1.0, in1=dt_raw[:], op0=ALU.mult, op1=ALU.max)\
                .then_inc(s["soft_asked"], 1)
            v.wait_ge(s["angles_loaded"], 16 * len(for_angles))
            link(v.tensor_copy(pos[:], pos_i[:]))
            link(v.tensor_tensor(angle[:], per_row(pos[:], R2), per_block(inv_freq[:], TT), ALU.mult))
            link(v.tensor_scalar(turns[:], angle[:], float(1 / (2 * np.pi)), None, ALU.mult))
            link(v.tensor_copy(turns_i[:], turns[:]))
            link(v.tensor_copy(turns[:], turns_i[:]))
            two_pi = 2 * np.pi
            high = float(np.float32(6.28125))
            middle = float(np.float32(np.round((two_pi - high) * 2 ** 21) / 2 ** 21))
            for part_of in (high, middle, float(np.float32(two_pi - high - middle))):
                link(v.scalar_tensor_tensor(out=angle[:], in0=turns[:], scalar=-part_of, in1=angle[:], op0=ALU.mult, op1=ALU.add))

            def keep_within(x):
                link(v.tensor_scalar(turns[:], x, float(np.pi), -two_pi, ALU.is_gt, ALU.mult))
                link(v.tensor_tensor(x, x, turns[:], ALU.add))
                link(v.tensor_scalar(turns[:], x, -float(np.pi), two_pi, ALU.is_lt, ALU.mult))
                link(v.tensor_tensor(x, x, turns[:], ALU.add))
                limit = float(np.nextafter(np.float32(np.pi), np.float32(0)))
                return v.tensor_scalar(x, x, limit, -limit, ALU.min, ALU.max)

            keep_within(angle[:]).then_inc(s["angle_ready"], 1)
            v.wait_ge(s["angle_ready"], 1)
            link(v.tensor_scalar(wrap[:], angle[:], float(np.pi / 2), None, ALU.add))
            keep_within(wrap[:]).then_inc(s["angle_ready"], 1)
            v.wait_ge(s["root_ready"], 1)
            link(v.reciprocal(stats[:, 3, :, :], stats[:, 2, :, :]))
            v.wait_ge(s["soft_ready"], 2)
            v.wait_ge(s["rates_ready"], 1)
            link(v.scalar_tensor_tensor(out=dt[:], in0=dt_raw[:], scalar=0.0, in1=soft[:], op0=ALU.max, op1=ALU.add))
            link(v.scalar_tensor_tensor(out=a_dt[:], in0=dt[:], scalar=-1.0, in1=per_block(a_log[:], TT), op0=ALU.mult, op1=ALU.mult))
            assert steps[0] == BEFORE, steps

            def chain(order, t, per):
                done = [0]

                def step(ins):
                    done[0] += 1
                    assert done[0] <= per
                    ins.then_inc(s[order], 1)
                    v.wait_ge(s[order], t * per + done[0])

                return step

            def widen(t):
                v.tensor_copy(a_wide[:], per_row(at_tile(a_dt, t), P)).then_inc(s["a_wide_ready"], 1)
                for n, (at, width) in enumerate(((0, Q_LORA), (Q_LORA, KV_LORA))):
                    v.tensor_scalar(latent[:, at:at + width], at_tile(rows2, t)[:, at:at + width], stats[:, 3, n, ds(t, 1)],
                                    None, ALU.mult).then_inc(s["latent_ready"], 1)

            def heads_odd(t):
                for n, to in enumerate((q_t, k_t)):
                    v.wait_ge(s["heads_turned"], t * 4 + 2 * n + 2)
                    v.tensor_copy(to[:, 4:8, ds(t * P, P)], three(bank[2 + 2 * n][0:QK, :], 4)).then_inc(s["heads_odd"], 1)

            def turn(t, u, first, last):
                step = chain("run_order", t, 2)
                v.wait_ge(s["run_made"], t + 1)
                step(v.tensor_copy(run[:], bank[7][:, 2 * P:2 * P + SSD_HEADS]))
                step(v.tensor_tensor(decay[:], three(bank[6][:], SSD_HEADS), per_row(run[:], P), ALU.subtract))
                v.tensor_scalar(decay[:], decay[:], 0.0, None, ALU.min).then_inc(s["gap_ready"], 1)
                v.tensor_tensor(end_gap[:], three(bank[6][:], SSD_HEADS)[:, :, P - 1], run[:], ALU.subtract).then_inc(s["gaps_ready"], 1)
                v.wait_ge(s["latent_turned"], t + 1)
                v.tensor_tensor(latent_t[:], three(bank[0][:, 0:3 * P], 3), per_row(gains[:], P), ALU.mult).then_inc(s["latent_t_ready"], 1)
                if not first:
                    heads_odd(t - 1)
                v.wait_ge(s["row_ready"], t + 1)
                v.tensor_tensor(three(xdt[:], SSD_HEADS), three(row[:, 0:SSD], SSD_HEADS), per_row(at_tile(dt, t), SSD_HD), ALU.mult)\
                    .then_inc(s["xdt_ready"], 1)
                y_now = at_tile(y, t)
                v.tensor_tensor(three(y_now, SSD_HEADS), three(row[:, 0:SSD], SSD_HEADS), per_row(d_skip[:], SSD_HD), ALU.mult)\
                    .then_inc(s["skip_ready"], 1)
                v.wait_ge(s["decay_ready"], t * 4 + 4)
                v.wait_ge(s["xdt_ready"], t * 2 + 1)
                v.tensor_tensor(three(xdt_end[:], SSD_HEADS), three(xdt[:], SSD_HEADS), per_row(to_end[:], SSD_HD), ALU.mult)\
                    .then_inc(s["xdt_ready"], 1)
                chain("mask_order", t, 1)(v.tensor_tensor(decay[:], decay[:], per_block(incl[:], SSD_HEADS), ALU.mult))
                for gr in range(SSD_GROUPS):
                    each = SSD_HEADS // SSD_GROUPS
                    ins = v.tensor_tensor(pt[:, gr * each:(gr + 1) * each, :], decay[:, gr * each:(gr + 1) * each, :],
                                          per_block(bank[7][:, gr * P:(gr + 1) * P], each), ALU.mult)
                ins.then_inc(s["pt_ready"], 1)
                if not last:
                    widen(t + 1)
                v.wait_ge(s["y_made"], t + 1)
                v.wait_ge(s["skip_ready"], t + 1)
                step = chain("y_order", t, 2)
                step(v.tensor_tensor(three(part[:], SSD_HEADS), three(bank[5][:, 0:SSD], SSD_HEADS), per_row(run_exp[:], SSD_HD), ALU.mult))
                v.tensor_tensor(y_now, y_now, bank[5][:, SSD:2 * SSD], ALU.add).then_inc(s["y_summed"], 1)
                v.wait_ge(s["y_summed"], t + 1)
                step(v.tensor_tensor(y_now, y_now, part[:], ALU.add))
                v.tensor_tensor(y_now, y_now, at_tile(rows2, t)[:, LATENT:LATENT + SSD], ALU.mult).then_inc(s["y_ready"], 1)
                v.wait_ge(s["state_made"], t + 1)
                chain("state_order", t, 1)(v.tensor_tensor(three(state[:], SSD_HEADS), three(state[:], SSD_HEADS),
                                                           per_row(tile_exp[:], SSD_HD), ALU.mult))
                v.tensor_tensor(state[:], state[:], bank[6][:, 0:SSD], ALU.add).then_inc(s["state_ready"], 1)
                for n in range(2):
                    v.wait_ge(s["lifted"], t * 4 + 2 + n + 1)
                    v.tensor_copy(k_row[:, 4 * n:4 * n + 4, 0:NOPE], three(bank[3 + n][:], 4)[:, :, 0:NOPE]).then_inc(s["k_ready"], 1)

            v.wait_ge(s["const"], 16 * len(with_const))
            v.wait_ge(s["silu_ready"], 1)
            widen(0)
            each_turn(v, turn)
            heads_odd(TT - 1)
            v.wait_ge(s["y_squared"], TT)
            v.tensor_scalar(y_stats[:, 1, :], y_stats[:, 0, :], 1.0 / SSD, EPS, ALU.mult, ALU.add).then_inc(s["y_mean"], 1)
            v.wait_ge(s["y_root"], 1)
            v.reciprocal(y_stats[:, 3, :], y_stats[:, 2, :]).then_inc(s["y_rstd"], 1)
            v.wait_ge(s["y_rstd"], 1)
            v.tensor_tensor(y[:], y[:], per_row(y_stats[:, 3, :], SSD), ALU.mult).then_inc(s["y_normed"], 1)


def attention_stage(nc, psum, bank, ident, a, q_t, k_t, values, feat, room):
    scale = QK ** -0.5
    TURNS = MLA_HEADS // 2
    N = 2 * TT
    with Stage(nc, "attention") as st:
        q_now = [st.sb(f"q_now{u}", [QK, S]) for u in range(2)]
        future = st.sb("future", [P, P])
        p = [st.sb(f"p{b}", [P, S]) for b in range(2)]
        p_t = [st.sb(f"p_t{b}", [P, TT, P]) for b in range(2)]
        most, bias, total, share = ([st.sb(f"{n}{b}", [P, 1]) for b in range(2)] for n in ("most", "bias", "total", "share"))
        out = three(room[:, 0:TT * MLA_HEADS * V_DIM], TT)
        const = st.sem("const")
        q_copied, scored = ([st.sem(f"{n}{u}") for u in range(2)] for n in ("q_copied", "scored"))
        pool_passed = st.sem("pool_passed")
        masked, most_ready, bias_ready, exp_ready, turned, low_ready, high_ready, made, share_ready, out_ready = (
            st.sem(n) for n in ("masked", "most_ready", "bias_ready", "exp_ready", "turned", "low_ready",
                                "high_ready", "made", "share_ready", "out_ready"))
        out_turned, even_out, odd_out = st.sem("out_turned"), st.sem("even_out"), st.sem("odd_out")
        block = st.open()

        def tile_of(m):
            return m % TT if m < TT else TT - 1 - m % TT

        def back(j, m):
            return max(j * N + m - 1, 0) if isinstance(j, int) else j * N + m - 1

        def each_turn(eng, turn):
            turn(0, True, False)
            with eng.Fori(1, TURNS - 1) as j:
                turn(j, False, False)
            turn(TURNS - 1, False, True)

        def after(j, m, last):
            return (j, m + 1) if m + 1 < N else None if last else (j + 1, 0)

        def before(j, m, first):
            return (j, m - 1) if m else None if first else (j - 1, N - 1)

        @block.sync
        def _(sp):
            sp.dma_start(future[:], a["c_future"]).then_inc(const, 16)

        @block.gpsimd
        def _(pool):
            with pool.Fori(0, TURNS) as j:
                for u in range(2):
                    pool.wait_ge(scored[u], j * TT)
                    pool.sem_inc(pool_passed, 1)
                    pool.tensor_copy(q_now[u][:], q_t[:, ds(j * 2 + u, 1), :].rearrange("p a s -> p (a s)")).then_inc(q_copied[u], 1)

        @block.tensor
        def _(pe):
            def scores(j, m):
                u, i = m // TT, tile_of(m)
                if m % TT == 0:
                    pe.wait_ge(q_copied[u], j + 1)
                pe.wait_ge(exp_ready, back(j, m))
                for n in range(i // 4 + 1):
                    width = min(BANK, (i + 1) * P - n * BANK)
                    last = pe.matmul(bank[2 * (m % 2) + n][:, 0:width], q_now[u][:, i * P:(i + 1) * P],
                                     k_t[:, ds(j * 2 + u, 1), n * BANK:n * BANK + width].rearrange("p a s -> p (a s)"),
                                     start=True, stop=True)
                last.then_inc(scored[u], 1)

            def turn(j, m):
                pe.wait_ge(exp_ready, j * N + m + 1)
                pe.wait_ge(low_ready, j * N + m)
                pe.wait_ge(high_ready, j * N + m)
                i = tile_of(m)
                for b in range(i + 1):
                    last = pe.transpose(bank[4 + b // 4][:, (b % 4) * P:(b % 4 + 1) * P], p[m % 2][:, b * P:(b + 1) * P], ident[:])
                last.then_inc(turned, 1)

            def weigh(j, m):
                u, i = m // TT, tile_of(m)
                pe.wait_ge(low_ready, j * N + m + 1)
                pe.wait_ge(high_ready, j * N + m + 1)
                pe.wait_ge(out_ready, back(j, m))
                for b in range(i + 1):
                    last = pe.matmul(bank[6 + m % 2][:, 0:V_DIM], p_t[m % 2][:, b, :],
                                     values[:, b, ds((j * 2 + u) * V_DIM, V_DIM)], start=(b == 0), stop=(b == i))
                last.then_inc(made, 1)

            def steps(j, first, last):
                for m in range(N):
                    if after(j, m, last):
                        scores(*after(j, m, last))
                    turn(j, m)
                    if before(j, m, first):
                        weigh(*before(j, m, first))

            scores(0, 0)
            each_turn(pe, steps)
            weigh(TURNS - 1, N - 1)
            pe.wait_ge(out_ready, TURNS * N)
            for t in range(TT):
                for k in range(MLA_T):
                    last = pe.transpose(bank[t][:, k * P:(k + 1) * P], out[:, t, k * P:(k + 1) * P], ident[:])
                last.then_inc(out_turned, 1)

        @block.scalar
        def _(act):
            def steps(j, first, last):
                for m in range(N):
                    i, b = tile_of(m), m % 2
                    act.wait_ge(bias_ready, j * N + m + 1)
                    act.wait_ge(turned, back(j, m))
                    act.wait_ge(share_ready, back(j, m))
                    act.activation(p[b][:, 0:(i + 1) * P], wide(psum, 2 * b, 2)[:, 0:(i + 1) * P], ACT.Exp, bias=bias[b][:, 0:1],
                                   scale=scale, accum_out=total[b][:]).then_inc(exp_ready, 1)
                    act.wait_ge(turned, j * N + m + 1)
                    act.wait_ge(made, back(j, m))
                    low = min(i + 1, 4)
                    act.activation(p_t[b][:, 0:low, :], three(bank[4][:, 0:low * P], low), ACT.Copy).then_inc(low_ready, 1)
            each_turn(act, steps)
            for t in range(0, TT, 2):
                act.wait_ge(out_turned, t + 1)
                act.activation(feat[:, 0:MLA_T, t * P:(t + 1) * P], three(bank[t][:], MLA_T), ACT.Copy).then_inc(even_out, 1)
            act.wait_ge(even_out, TT // 2)

        @block.vector
        def _(v):
            def bound(j, m):
                i, b = tile_of(m), m % 2
                at = wide(psum, 2 * b, 2)
                v.wait_ge(scored[m // TT], j * TT + m % TT + 1)
                v.tensor_tensor(at[:, i * P:(i + 1) * P], at[:, i * P:(i + 1) * P], future[:], ALU.add).then_inc(masked, 1)
                v.wait_ge(masked, j * N + m + 1)
                v.wait_ge(bias_ready, back(j, m))
                v.tensor_reduce(most[b][:], at[:, 0:(i + 1) * P], AX_X, ALU.max).then_inc(most_ready, 1)
                v.wait_ge(most_ready, j * N + m + 1)
                v.wait_ge(exp_ready, back(j, m))
                v.tensor_scalar(bias[b][:], most[b][:], -scale, None, ALU.mult).then_inc(bias_ready, 1)

            def high(j, m):
                i, b = tile_of(m), m % 2
                v.wait_ge(turned, j * N + m + 1)
                v.wait_ge(made, back(j, m))
                if i >= 4:
                    v.tensor_copy(p_t[b][:, 4:i + 1, :], three(bank[5][:, 0:(i - 3) * P], i - 3)).then_inc(high_ready, 1)
                else:
                    v.sem_inc(high_ready, 1)

            def finish(j, m):
                u, i, b = m // TT, tile_of(m), m % 2
                v.wait_ge(exp_ready, j * N + m + 1)
                v.wait_ge(out_ready, back(j, m))
                v.reciprocal(share[b][:], total[b][:]).then_inc(share_ready, 1)
                v.wait_ge(share_ready, j * N + m + 1)
                v.wait_ge(made, j * N + m + 1)
                v.tensor_scalar(out[:, i, ds((j * 2 + u) * V_DIM, V_DIM)], bank[6 + b][:, 0:V_DIM], share[b][:, 0:1], None,
                                ALU.mult).then_inc(out_ready, 1)

            v.wait_ge(const, 16)
            def steps(j, first, last):
                for m in range(N):
                    if after(j, m, last):
                        bound(*after(j, m, last))
                    high(j, m)
                    if before(j, m, first):
                        finish(*before(j, m, first))

            bound(0, 0)
            each_turn(v, steps)
            finish(TURNS - 1, N - 1)
            for t in range(1, TT, 2):
                v.wait_ge(out_turned, t + 1)
                v.tensor_copy(feat[:, 0:MLA_T, t * P:(t + 1) * P], three(bank[t][:], MLA_T)).then_inc(odd_out, 1)
            v.wait_ge(odd_out, TT // 2)


FFN = 2816
FFN_T = FFN // P
FFN_TAPS = 3


def ffn_up_stage(nc, psum, bank, ident, a, high, low, hidden):
    with Stage(nc, "ffn_up") as st:
        tap_rows = st.sb("tap_rows", [2 * FFN_T, FFN_TAPS + 1, P])
        taps = st.sb("taps", [P, FFN_TAPS + 1, 2 * FFN_T])
        w, w_low = zip(*(zip(*(st.twin(f"w{c}{u}", [P, KT, P]) for u in range(2))) for c in range(2)))
        w_high = [[st.sb(f"w_high{c}{u}", [P, KT, P], F32R) for u in range(2)] for c in range(2)]
        acc = [[st.sb(f"acc{c}{u}", [P, S]) for u in range(2)] for c in range(2)]
        taps_loaded, taps_turned, taps_ready = st.sem("taps_loaded"), st.sem("taps_turned"), st.sem("taps_ready")
        loaded, high_ready, low_ready, made, scaled, tapped = (
            [[st.sem(f"{n}{c}{u}") for u in range(2)] for c in range(2)]
            for n in ("loaded", "high_ready", "low_ready", "made", "scaled", "tapped"))
        silu_ready, hidden_ready = ([st.sem(f"{n}{u}") for u in range(2)] for n in ("silu_ready", "hidden_ready"))
        block = st.open()
        last_tap = FFN_TAPS - 1
        TURNS = FFN_T // 2

        @block.sync
        def _(sp):
            sp.dma_start(tap_rows[:, 0:FFN_TAPS, :], a["ffn_conv_w_2"].rearrange("i (c p) -> c i p", p=P)).then_inc(taps_loaded, 16)
            sp.dma_start(tap_rows[:, FFN_TAPS, :], a["ffn_conv_b_2"].rearrange("(c p) -> c p", p=P)).then_inc(taps_loaded, 16)
            with sp.Fori(0, TURNS) as j:
                for u in range(2):
                    for c in range(2):
                        sp.wait_ge(made[c][u], j)
                        sp.dma_start(w[c][u][:], a["ffn_w_up_2"][:, ds((j * 2 + u) * P + c * FFN, P)]
                                     .rearrange("(k p) n -> p k n", p=P)).then_inc(loaded[c][u], 16)

        @block.tensor
        def _(pe):
            pe.wait_ge(taps_loaded, 32)
            n = 2 * FFN_T
            for i in range(FFN_TAPS + 1):
                last = pe.transpose(bank[0][:, i * n:(i + 1) * n], tap_rows[:, i, :], ident[0:n, 0:n])
            last.then_inc(taps_turned, 1)
            pe.wait_ge(taps_ready, 1)
            with pe.Fori(0, TURNS) as j:
                for u in range(2):
                    for c in range(2):
                        pe.wait_ge(low_ready[c][u], j + 1)
                        pe.wait_ge(tapped[c][u], j * last_tap)
                        for h in range(2):
                            half = slice(h * BANK, (h + 1) * BANK)
                            for k in range(KT):
                                last = three_passes(pe, bank[4 * u + 2 * c + h][:], (w_high[c][u][:, k, :], w_low[c][u][:, k, :]),
                                                    (high[:, k, half], low[:, k, half]), start=(k == 0), stop=(k == KT - 1))
                        last.then_inc(made[c][u], 1)

        @block.scalar
        def _(act):
            def split(j, u, c):
                act.wait_ge(loaded[c][u], j * 16 + 16)
                split_high(act, w_high[c][u][:], w[c][u][:]).then_inc(high_ready[c][u], 1)

            def scale(j, u, c):
                at = j * 2 + u + c * FFN_T
                act.wait_ge(made[c][u], j + 1)
                act.wait_ge(hidden_ready[u], j)
                act.activation(acc[c][u][:], wide(psum, 4 * u + 2 * c, 2), ACT.Identity, scale=taps[:, last_tap, ds(at, 1)],
                               bias=taps[:, FFN_TAPS, ds(at, 1)]).then_inc(scaled[c][u], 1)

            def gate(j, u):
                act.wait_ge(tapped[0][u], j * last_tap + last_tap)
                act.activation(acc[0][u][:], acc[0][u][:], ACT.Silu).then_inc(silu_ready[u], 1)

            act.wait_ge(taps_turned, 1)
            act.activation(taps[:], three(bank[0][:, 0:(FFN_TAPS + 1) * 2 * FFN_T], FFN_TAPS + 1), ACT.Copy).then_inc(taps_ready, 1)
            split(0, 0, 0)
            split(0, 0, 1)
            act.wait_ge(taps_ready, 1)

            def turn(j, last):
                for u in range(2):
                    for c in range(2):
                        if u == 0 or not last:
                            split(j + u, 1 - u, c)
                        scale(j, u, c)
                    gate(j, u)

            with act.Fori(0, TURNS - 1) as j:
                turn(j, False)
            turn(TURNS - 1, True)

        @block.vector
        def _(v):
            def split(j, u, c):
                v.wait_ge(high_ready[c][u], j + 1)
                split_low(v, w_low[c][u][:], w[c][u][:], w_high[c][u][:]).then_inc(low_ready[c][u], 1)

            def convolve(j, u, c):
                at = j * 2 + u + c * FFN_T
                v.wait_ge(scaled[c][u], j + 1)
                for i in range(1, FFN_TAPS):
                    v.wait_ge(tapped[c][u], j * last_tap + i - 1)
                    v.scalar_tensor_tensor(out=acc[c][u][:, i:], in0=wide(psum, 4 * u + 2 * c, 2)[:, 0:S - i],
                                           scalar=taps[:, last_tap - i, ds(at, 1)], in1=acc[c][u][:, i:],
                                           op0=ALU.mult, op1=ALU.add).then_inc(tapped[c][u], 1)

            def hide(j, u):
                v.wait_ge(silu_ready[u], j + 1)
                v.wait_ge(tapped[1][u], j * last_tap + last_tap)
                v.tensor_tensor(hidden[:, ds(j * 2 + u, 1), :].rearrange("p a s -> p (a s)"), acc[0][u][:], acc[1][u][:],
                                ALU.mult).then_inc(hidden_ready[u], 1)

            def turn(j, last):
                for u in range(2):
                    for c in range(2):
                        if u == 0 or not last:
                            split(j + u, 1 - u, c)
                        convolve(j, u, c)
                    hide(j, u)

            split(0, 0, 0)
            split(0, 0, 1)
            v.wait_ge(taps_ready, 1)
            with v.Fori(0, TURNS - 1) as j:
                turn(j, False)
            turn(TURNS - 1, True)


def ffn_down_stage(nc, psum, bank, a, hidden, hidden_low, high_parts, x, gain, x_dram, gain_dram, out):
    RING = 3
    AHEAD = 2
    with Stage(nc, "ffn_down") as st:
        beyond = st.sb("beyond", [P, FFN_T - 2 * KT, S], F32R)
        hidden_high = [part[:, k, :] for part in (*high_parts, beyond) for k in range(part.shape[1])]
        w, w_low = zip(*(st.twin(f"w{i}", [P, BANK]) for i in range(RING)))
        w_high = [st.sb(f"w_high{i}", [P, BANK], F32R) for i in range(RING)]
        y = st.sb("y", [P, TT, BANK])
        square = st.sb("square", [P, 2, TT])
        mean, root, rstd = (st.sb(n, [P, TT]) for n in ("mean", "root", "rstd"))
        scaled, junk = hidden[:, 0:TT, 0:BANK], hidden[:, TT, :]
        loaded, w_high_ready, w_low_ready, used = (
            [st.sem(f"{n}{i}") for i in range(RING)] for n in ("loaded", "w_high_ready", "w_low_ready", "used"))
        hidden_high_ready, hidden_low_ready, made, even_out, odd_out, squared, summed, mean_ready, root_ready, rstd_ready = (
            st.sem(n) for n in ("hidden_high_ready", "hidden_low_ready", "made", "even_out", "odd_out", "squared", "summed",
                                "mean_ready", "root_ready", "rstd_ready"))
        x_loaded, gain_loaded, scaled_ready, y_gained, first_added, even_added, odd_added, stored = (
            st.sem(n) for n in ("x_loaded", "gain_loaded", "scaled_ready", "y_gained", "first_added", "even_added", "odd_added", "stored"))
        block = st.open()

        def ring(n, k):
            return (n * FFN_T + k) % RING

        def count(n, k):
            return (n * FFN_T + k) // RING

        @block.sync
        def _(sp):
            for n in range(2):
                for k in range(FFN_T):
                    i = ring(n, k)
                    if n or k >= RING:
                        sp.wait_ge(used[i], count(n, k))
                    sp.dma_start(w[i][:], a["ffn_w_down_2"][k * P:(k + 1) * P, n * BANK:(n + 1) * BANK]).then_inc(loaded[i], 16)
            for k in range(TT - RING + 1, TT + 1):
                sp.wait_ge(used[ring(1, k)], count(1, k) + 1)
            sp.dma_start(gain, rows(gain_dram, D)).then_inc(gain_loaded, 16)
            sp.dma_start(x, x_dram.rearrange("(t p) d -> p t d", p=P)).then_inc(x_loaded, 16)
            for t in range(TT):
                sp.wait_ge(first_added, t + 1)
                sp.wait_ge((even_added, odd_added)[t % 2], t // 2 + 1)
                sp.dma_start(out[t * P:(t + 1) * P, :], x[:, t, :]).then_inc(stored, 16)
            sp.wait_ge(stored, 16 * TT)

        @block.tensor
        def _(pe):
            for n in range(2):
                for k in range(FFN_T):
                    i = ring(n, k)
                    pe.wait_ge(w_low_ready[i], count(n, k) + 1)
                    if n == 0:
                        pe.wait_ge(hidden_low_ready, k + 1)
                    for t in range(TT):
                        if n and k == 0:
                            pe.wait_ge((even_out, odd_out)[t % 2], t // 2 + 1)
                        tile = slice(t * P, (t + 1) * P)
                        last = three_passes(pe, bank[t][:], (hidden_high[k][:, tile], hidden_low[:, k, tile]),
                                            (w_high[i][:], w_low[i][:]), start=(k == 0), stop=(k == FFN_T - 1))
                        if k == FFN_T - 1:
                            last.then_inc((made, used[i])[t == TT - 1], 1)
                    if k < FFN_T - 1:
                        last.then_inc(used[i], 1)

        def wait_made(eng, n, t):
            if t == TT - 1:
                eng.wait_ge(used[ring(n, FFN_T - 1)], count(n, FFN_T - 1) + 1)
            else:
                eng.wait_ge(made, n * (TT - 1) + t + 1)

        @block.scalar
        def _(act):
            def square_of(n, t):
                if n * TT + t:
                    act.wait_ge(squared, n * TT + t)
                act.activation(junk[:, 0:BANK], (y[:, t, :], bank[t][:])[n], ACT.Square, accum_out=square[:, n, t:t + 1])\
                    .then_inc(squared, 1)

            def split_w(n, k):
                i = ring(n, k)
                act.wait_ge(loaded[i], 16 * (count(n, k) + 1))
                split_high(act, w_high[i][:], w[i][:]).then_inc(w_high_ready[i], 1)

            for k in range(FFN_T):
                split_high(act, hidden_high[k], hidden[:, k, :]).then_inc(hidden_high_ready, 1)
                split_w(0, k)
            for k in range(AHEAD):
                split_w(1, k)
            for t in range(0, TT, 2):
                wait_made(act, 0, t)
                act.activation(y[:, t, :], bank[t][:], ACT.Copy).then_inc(even_out, 1)
            for k in range(AHEAD, FFN_T):
                split_w(1, k)
            act.wait_ge(used[ring(1, TT)], count(1, TT) + 1)
            act.wait_ge(even_out, TT // 2)
            act.wait_ge(odd_out, TT // 2)
            for t in range(TT):
                square_of(0, t)
            for t in range(TT):
                wait_made(act, 1, t)
                square_of(1, t)
            act.wait_ge(mean_ready, 1)
            act.activation(root[:], mean[:], ACT.Sqrt).then_inc(root_ready, 1)

        @block.vector
        def _(v):
            def split_w(n, k):
                i = ring(n, k)
                v.wait_ge(w_high_ready[i], count(n, k) + 1)
                split_low(v, w_low[i][:], w[i][:], w_high[i][:]).then_inc(w_low_ready[i], 1)

            for k in range(FFN_T):
                v.wait_ge(hidden_high_ready, k + 1)
                split_low(v, hidden_low[:, k, :], hidden[:, k, :], hidden_high[k]).then_inc(hidden_low_ready, 1)
                split_w(0, k)
            for k in range(AHEAD):
                split_w(1, k)
            for t in range(1, TT, 2):
                wait_made(v, 0, t)
                v.tensor_copy(y[:, t, :], bank[t][:]).then_inc(odd_out, 1)
            for k in range(AHEAD, FFN_T):
                split_w(1, k)
            v.wait_ge(gain_loaded, 16)
            v.wait_ge(squared, TT)
            v.tensor_tensor(y[:], y[:], per_block(gain[:, 0:BANK], TT), ALU.mult).then_inc(y_gained, 1)
            v.wait_ge(x_loaded, 16)
            v.wait_ge(squared, 2 * TT)
            v.tensor_tensor(mean[:], square[:, 0, :], square[:, 1, :], ALU.add).then_inc(summed, 1)
            v.wait_ge(summed, 1)
            v.tensor_scalar(mean[:], mean[:], 1.0 / D, EPS, ALU.mult, ALU.add).then_inc(mean_ready, 1)
            v.wait_ge(root_ready, 1)
            v.reciprocal(rstd[:], root[:]).then_inc(rstd_ready, 1)
            v.wait_ge(rstd_ready, 1)
            v.wait_ge(y_gained, 1)
            first, second = slice(0, BANK), slice(BANK, D)
            for t in range(TT):
                v.scalar_tensor_tensor(out=scaled[:, t, :], in0=bank[t][:], scalar=rstd[:, t:t + 1], in1=gain[:, second],
                                       op0=ALU.mult, op1=ALU.mult).then_inc(scaled_ready, 1)
                v.scalar_tensor_tensor(out=x[:, t, first], in0=y[:, t, :], scalar=rstd[:, t:t + 1], in1=x[:, t, first],
                                       op0=ALU.mult, op1=ALU.add).then_inc(first_added, 1)
                if t % 2:
                    v.wait_ge(scaled_ready, t + 1)
                    v.tensor_tensor(x[:, t, second], x[:, t, second], scaled[:, t, :], ALU.add).then_inc(odd_added, 1)

        @block.gpsimd
        def _(pool):
            pool.wait_ge(x_loaded, 16)
            for t in range(0, TT, 2):
                pool.wait_ge(scaled_ready, t + 1)
                pool.tensor_tensor(x[:, t, BANK:D], x[:, t, BANK:D], scaled[:, t, :], ALU.add).then_inc(even_added, 1)


def program(nc, a, out):
    with ExitStack() as ctx:
        def sb(name, shape, dt=F32):
            return ctx.enter_context(nc.sbuf_tensor(name, shape, dt))

        psum = ctx.enter_context(nc.psum_tensor("psum", [P, 8, BANK], F32))
        bank = [psum[:, i, :] for i in range(8)]
        ident = sb("ident", [P, P])
        squares = sb("squares", [P, TT])
        proj = nc.dram_tensor("proj", [S + 1, IN_COLS], F32).ap()
        h_rows = nc.dram_tensor("h_rows", [S, D], F32).ap()
        y_rows = nc.dram_tensor("y_rows", [SLOT_BLOCKS * P, D], F32).ap()
        with nc.sbuf_tensor("high1", [P, KT, S], F32R) as high, nc.sbuf_tensor("low1", [P, KT, S], F32R) as low:
            with nc.sbuf_tensor("x_rows", [P, TT, D], F32) as x:
                load_stage(nc, x, squares, ident, a["x"], a["c_ident"], proj[0:1, :])
                norm_stage(nc, "norm1", bank, ident, x, squares, a["norm1_gain"], high, low=low)
            project_stage(nc, "project", bank, high, low, a["w_in"], 480, IN_COLS // 480, proj[1:S + 1, :],
                          y_rows[EXPERTS * P:, :])
        mixed = nc.dram_tensor("mixed", [TT, P, KT * P], F32).ap()
        mix_stage(nc, bank, ident, a, proj, mixed)
        feat, = overlay(nc, ("feat", [P, KT, S], F32))
        part = sb("part", [P, KT, S], F32R)
        x2_dram = nc.dram_tensor("x2_rows", [S, D], F32).ap()
        with nc.sbuf_tensor("h", [P, TT, D], F32) as x:
            with ExitStack() as routed:
                def sb1(name, shape, dt=F32):
                    return routed.enter_context(nc.sbuf_tensor(name, shape, dt))

                add_product_stage(nc, "out1", bank, feat, part, a["w_out"], x, squares, x_dram=a["x"], feat_dram=mixed)
                token_ids = sb1("token_ids", [P, TT], I32)
                slot_weight = sb1("slot_weight", [P, 2, TT])
                slot_index = sb1("slot_index", [P, 2, TT], I32)
                more = sb1("more", [1, 2, MORE_BLOCKS], I32)
                slot_token = nc.dram_tensor("slot_token", [SLOT_BLOCKS * P, 1], I32).ap()
                norm_stage(nc, "norm2", bank, ident, x, squares, a["norm2_gain"], feat, h_rows)
                with ExitStack() as weights:
                    w = ExpertWeights(nc, weights, a)
                    route_stage(nc, bank, ident, a, feat, token_ids, slot_weight, slot_index, more, slot_token, w.load_first)
                    expert_stage(nc, bank, ident, a, w, part, more, slot_token, h_rows, y_rows)
                combine_stage(nc, x, squares, y_rows, slot_index, slot_weight, a["final_norm_gain"], x2_dram)
            mixers2(nc, a, psum, bank, ident, feat, part, x, squares)
        second_half(nc, a, out, psum, bank, ident, feat, part, squares, x2_dram)


def mixers2(nc, a, psum, bank, ident, feat, part, x, squares):
    with ExitStack() as ctx:
        def sb(name, shape, dt=F32):
            return ctx.enter_context(nc.sbuf_tensor(name, shape, dt))

        xbc = sb("xbc", [P, XBC_T, S])
        latent_squares = sb("latent_squares", [P, 2, TT])
        room = flat(x)
        rows2, spare = three(room[:, 0:TT * TM_COLS], TT), room[:, TT * TM_COLS:]
        with nc.sbuf_tensor("low3", [P, KT, S], F32R) as low:
            norm_stage(nc, "norm3", bank, ident, x, squares, a["norm_mix_pre_2"], part, low=low)
            project2_stage(nc, psum, bank, part, low, feat, a, rows2, latent_squares, xbc)
        q_t, k_t = sb("q_t", [QK, MLA_HEADS, S]), sb("k_t", [QK, MLA_HEADS, S])
        values = sb("values", [P, TT, MLA_HEADS * V_DIM])
        mixers2_stage(nc, bank, ident, a, rows2, latent_squares, xbc, feat, q_t, k_t, values, spare)
        attention_stage(nc, psum, bank, ident, a, q_t, k_t, values, feat, room)


def second_half(nc, a, out, psum, bank, ident, feat, part, squares, x2_dram):
    x3_dram = nc.dram_tensor("x3_rows", [S, D], F32).ap()
    x, w = overlay(nc, ("x2", [P, TT, D], F32), ("w_out2", [P, KT, D], F32))
    _, w_low, w_high = overlay(nc, ("x2_place", [P, TT, D], F32), ("w_out2_low", [P, KT, D], F32R),
                               ("w_out2_high", [P, KT, D], F32R))
    hidden, low_plain = overlay(nc, ("hidden", [P, FFN_T, S], F32), ("low4_plain", [P, KT, S], F32))
    with nc.sbuf_tensor("hidden_low", [P, FFN_T, S], F32R) as hidden_low, nc.sbuf_tensor("low4", [P, KT, S], F32R) as low:
        add_product_stage(nc, "out2", bank, feat, part, a["w_out_2"], x, squares, x2_dram, a["norm_mix_post_2"], x3_dram,
                          weights=(w, w_low, w_high))
        norm_stage(nc, "norm4", bank, ident, x, squares, a["norm_ffn_pre_2"], part, low=low)
        ffn_up_stage(nc, psum, bank, ident, a, part, low, hidden)
        ffn_down_stage(nc, psum, bank, a, hidden, hidden_low, (part, low), feat[:], low_plain[:, 0, :], x3_dram,
                       a["norm_ffn_post_2"], out)


def kernel(**inputs):
    import concourse.bacc as bacc
    from concourse import mybir as types
    from concourse.bass_utils import run_bass_kernel_spmd

    nc = bacc.Bacc("TRN2", target_bir_lowering=False, num_devices=1)
    arrays, args = {}, {}
    for name, value in lay_out(inputs).items():
        arrays[f"in_{name}_dram"] = value
        args[name] = nc.dram_tensor(f"in_{name}_dram", value.shape, types.dt.from_np(value.dtype), kind="ExternalInput").ap()
    out = nc.dram_tensor("out_0_dram", [S, D], types.dt.float32, kind="ExternalOutput").ap()
    program(nc, args, out)
    r = run_bass_kernel_spmd(nc, [arrays], core_ids=[0])
    return r.results[0]["out_0_dram"].reshape(1, S, D)
```
